# Optimizing a Trainium2 kernel written in Bass

```python
import math
import jax
import jax.numpy as jnp
from jax import lax
import numpy as np

D_MODEL = 1024
BATCH = 1
SEQ = 1024
DEPTH = 1
DEC_BATCH = 8
DEC_SEQ = 4
PAST_LEN = 4096
PAGE_SIZE = 128

HEAD_DIM = 64
ATT_HEADS = 8
ATT_KV_HEADS = 2
ATT_REP = ATT_HEADS // ATT_KV_HEADS
CMP_BLOCK = 32
CMP_STRIDE = 16
CMP_HIDDEN = 64
SEL_BLOCK = 64
SEL_TOPN = 16
WINDOW = 512
SEL_Q_BLOCK = 64
WIN_Q_BLOCK = 128
N_BUCKETS = 32
MAX_DISTANCE = 128
SSD_HEADS = 8
SSD_HEAD_DIM = 64
SSD_GROUPS = 2
SSD_REP = SSD_HEADS // SSD_GROUPS
SSD_STATE = 64
SSD_CONV = 4
SSD_CHUNK = 128
D_ATT = ATT_HEADS * HEAD_DIM
D_SSD = SSD_HEADS * SSD_HEAD_DIM
D_MIX = D_ATT + D_SSD
D_KV = ATT_KV_HEADS * HEAD_DIM
D_CONV = D_SSD + 2 * SSD_GROUPS * SSD_STATE
D_FF = ((8 * D_MODEL // 3 + 255) // 256) * 256
OFF_KV = D_ATT
OFF_GATE = OFF_KV + 6 * D_KV
OFF_Z = OFF_GATE + 3 * ATT_HEADS
OFF_XBC = OFF_Z + D_SSD
OFF_DT = OFF_XBC + D_CONV
D_IN = OFF_DT + SSD_HEADS
RMS_EPS = 1e-6
SEL_FORCE = 1e30

kernel_name = 'hymba_nsa_ssd_step'

def rmsnorm(x, g):
    xf = x.astype(jnp.float32)
    y = xf * lax.rsqrt(jnp.mean(xf * xf, axis=-1, keepdims=True) + RMS_EPS)
    return (y * g.astype(jnp.float32)).astype(x.dtype)

def rel_bucket(dist):
    n = jnp.maximum(dist, 0)
    max_exact = N_BUCKETS // 2
    nf = jnp.maximum(n, 1).astype(jnp.float32)
    large = max_exact + (jnp.log(nf / max_exact) / math.log(MAX_DISTANCE / max_exact)
                         * (N_BUCKETS - max_exact)).astype(jnp.int32)
    large = jnp.minimum(large, N_BUCKETS - 1)
    return jnp.where(n < max_exact, n, large)

def masked_softmax(s, mask):
    s = jnp.where(mask, s.astype(jnp.float32), -1e30)
    m = jnp.max(s, axis=-1, keepdims=True)
    e = jnp.where(mask, jnp.exp(s - m), 0.0)
    return e / jnp.maximum(jnp.sum(e, axis=-1, keepdims=True), 1e-30)

def attend_shared(q, q_pos, k, v, k_pos, mask, rel_bias):
    s = jnp.einsum('...qgrd,...kgd->...qgrk', q, k).astype(jnp.float32) * (HEAD_DIM ** -0.5)
    dist = q_pos[..., :, None] - k_pos[..., None, :]
    bias = rel_bias[rel_bucket(dist)]
    bias = bias.reshape(bias.shape[:-1] + (ATT_KV_HEADS, ATT_REP))
    bias = jnp.moveaxis(bias, -3, -1)
    p = masked_softmax(s + bias, mask[..., :, None, None, :])
    o = jnp.einsum('...qgrk,...kgd->...qgrd', p.astype(v.dtype), v)
    return o, p

def attend_gathered(q, q_pos, kg, vg, k_pos, rel_bias):
    s = jnp.einsum('bqgrd,bqgkd->bqgrk', q, kg).astype(jnp.float32) * (HEAD_DIM ** -0.5)
    dist = q_pos[None, :, None, None] - k_pos
    g_i = jnp.arange(ATT_KV_HEADS)[None, None, :, None]
    bias = rel_bias.reshape(N_BUCKETS, ATT_KV_HEADS, ATT_REP)[rel_bucket(dist), g_i]
    p = masked_softmax(s + jnp.swapaxes(bias, -1, -2), (dist >= 0)[:, :, :, None, :])
    return jnp.einsum('bqgrk,bqgkd->bqgrd', p.astype(vg.dtype), vg)

def compress(rows, pe, w1, w2):
    B, L = rows.shape[:2]
    n_sub = L // CMP_STRIDE
    n_part = CMP_BLOCK // CMP_STRIDE
    n_blk = n_sub - n_part + 1
    sub = rows[:, :n_sub * CMP_STRIDE].reshape(B, n_sub, CMP_STRIDE, ATT_KV_HEADS, HEAD_DIM)
    u = jnp.einsum('bnsgd,jsdh->bjngh', sub, w1.reshape(n_part, CMP_STRIDE, HEAD_DIM, CMP_HIDDEN))
    pre = jnp.einsum('sd,sdh->h', pe, w1)
    for j in range(n_part):
        pre = pre + u[:, j, j:j + n_blk]
    return jnp.einsum('bngh,hd->bngd', jax.nn.silu(pre), w2)

def cmp_branch(q, q_pos, kc_rows, vc_rows, W):
    kc = rmsnorm(compress(kc_rows, W['cmp_pe'][0], W['cmp_w1'][0], W['cmp_w2'][0]), W['k_norm'])
    vc = compress(vc_rows, W['cmp_pe'][1], W['cmp_w1'][1], W['cmp_w2'][1])
    e = CMP_STRIDE * jnp.arange(kc.shape[1], dtype=jnp.int32) + (CMP_BLOCK - 1)
    mask = e[None, :] <= q_pos[:, None]
    return attend_shared(q, q_pos, kc, vc, e, mask, W['rel_bias'])

def select_blocks(p_cmp, q_pos, n_sel, k_top):
    imp = jnp.sum(p_cmp, axis=3)
    ratio = SEL_BLOCK // CMP_STRIDE
    imp = jnp.concatenate([imp, jnp.zeros(imp.shape[:-1] + (1,), imp.dtype)], axis=-1)[..., :ratio * n_sel]
    grp = imp.reshape(imp.shape[:-1] + (n_sel, ratio))
    prev = jnp.concatenate([jnp.zeros(grp.shape[:-2] + (1,), grp.dtype), grp[..., :-1, ratio - 1]], axis=-1)
    score = jnp.sum(grp, axis=-1) + prev
    j = jnp.arange(n_sel, dtype=jnp.int32)
    cur = (q_pos // SEL_BLOCK)[None, :, None, None]
    forced = (j == 0) | (j == cur) | (j == cur - 1)
    score = jnp.where(forced, SEL_FORCE, jnp.where(j <= cur, score, -SEL_FORCE))
    _, idx = lax.top_k(score, k_top)
    return idx

def sel_branch_prompt(q, pos, idx, ks, vs, rel_bias):
    B, T = q.shape[:2]
    k_top = idx.shape[-1]
    kb = ks.reshape(B, T // SEL_BLOCK, SEL_BLOCK, ATT_KV_HEADS, HEAD_DIM)
    vb = vs.reshape(B, T // SEL_BLOCK, SEL_BLOCK, ATT_KV_HEADS, HEAD_DIM)
    b_i = jnp.arange(B)[:, None, None, None]
    g_i = jnp.arange(ATT_KV_HEADS)[None, None, :, None]
    offs = jnp.arange(SEL_BLOCK, dtype=jnp.int32)
    nqb = T // SEL_Q_BLOCK

    def one_block(args):
        qb, ib, pb = args
        kg = kb[b_i, ib, :, g_i].reshape(B, SEL_Q_BLOCK, ATT_KV_HEADS, k_top * SEL_BLOCK, HEAD_DIM)
        vg = vb[b_i, ib, :, g_i].reshape(B, SEL_Q_BLOCK, ATT_KV_HEADS, k_top * SEL_BLOCK, HEAD_DIM)
        kpos = (ib[..., None] * SEL_BLOCK + offs).reshape(B, SEL_Q_BLOCK, ATT_KV_HEADS, k_top * SEL_BLOCK)
        return attend_gathered(qb, pb, kg, vg, kpos, rel_bias)

    q_blocks = jnp.swapaxes(q.reshape(B, nqb, SEL_Q_BLOCK, ATT_KV_HEADS, ATT_REP, HEAD_DIM), 0, 1)
    i_blocks = jnp.swapaxes(idx.reshape(B, nqb, SEL_Q_BLOCK, ATT_KV_HEADS, k_top), 0, 1)
    p_blocks = pos.reshape(nqb, SEL_Q_BLOCK)
    o = lax.map(one_block, (q_blocks, i_blocks, p_blocks))
    return jnp.swapaxes(o, 0, 1).reshape(B, T, ATT_KV_HEADS, ATT_REP, HEAD_DIM)

def sel_branch_sample(q, pos, idx, ks, vs, c_ks, c_vs, page_table, rel_bias):
    B, S = q.shape[:2]
    k_top = idx.shape[-1]
    per_page = c_ks.shape[1] // SEL_BLOCK
    b_i = jnp.arange(B)[:, None, None, None]
    g_i = jnp.arange(ATT_KV_HEADS)[None, None, :, None]
    phys = page_table[b_i, idx // per_page]
    off = idx % per_page

    def gather(cache, new_rows):
        cr = cache.reshape(cache.shape[0], per_page, SEL_BLOCK, ATT_KV_HEADS, HEAD_DIM)
        past = cr[phys, off, :, g_i].reshape(B, S, ATT_KV_HEADS, k_top * SEL_BLOCK, HEAD_DIM)
        new = jnp.broadcast_to(jnp.swapaxes(new_rows, 1, 2)[:, None], (B, S, ATT_KV_HEADS, S, HEAD_DIM))
        return jnp.concatenate([past, new], axis=3)

    kpos_past = (idx[..., None] * SEL_BLOCK + jnp.arange(SEL_BLOCK, dtype=jnp.int32)).reshape(
        B, S, ATT_KV_HEADS, k_top * SEL_BLOCK)
    kpos_new = jnp.broadcast_to(pos, (B, S, ATT_KV_HEADS, S))
    kpos = jnp.concatenate([kpos_past, kpos_new], axis=3)
    return attend_gathered(q, pos, gather(c_ks, ks), gather(c_vs, vs), kpos, rel_bias)

def win_branch_prompt(q, pos, kw, vw, rel_bias):
    B, T = q.shape[:2]
    nq = T // WIN_Q_BLOCK
    nwb = WINDOW // WIN_Q_BLOCK

    def band(t):
        tp = jnp.concatenate([jnp.zeros((B, WINDOW, ATT_KV_HEADS, HEAD_DIM), t.dtype), t], axis=1)
        tp = tp.reshape(B, nq + nwb, WIN_Q_BLOCK, ATT_KV_HEADS, HEAD_DIM)
        return jnp.concatenate([tp[:, m:m + nq] for m in range(nwb + 1)], axis=2)

    qpos = pos.reshape(nq, WIN_Q_BLOCK)
    kpos = (jnp.arange(nq, dtype=jnp.int32)[:, None] * WIN_Q_BLOCK - WINDOW
            + jnp.arange((nwb + 1) * WIN_Q_BLOCK, dtype=jnp.int32)[None, :])
    dist = qpos[:, :, None] - kpos[:, None, :]
    mask = (dist >= 0) & (dist < WINDOW) & (kpos[:, None, :] >= 0)
    o, _ = attend_shared(q.reshape(B, nq, WIN_Q_BLOCK, ATT_KV_HEADS, ATT_REP, HEAD_DIM),
                         qpos, band(kw), band(vw), kpos, mask, rel_bias)
    return o.reshape(B, T, ATT_KV_HEADS, ATT_REP, HEAD_DIM)

def causal_conv(xbc, buf, w, b):
    L = xbc.shape[1]
    xp = jnp.concatenate([buf.astype(xbc.dtype), xbc], axis=1)
    out = b
    for k in range(SSD_CONV):
        out = out + xp[:, k:k + L] * w[k]
    return jax.nn.silu(out), xp[:, L:]

def ssd_scan(x, dt, A, Bm, Cm, h0, chunk):
    b, L = x.shape[:2]
    c = L // chunk
    xr = x.reshape(b, c, chunk, SSD_GROUPS, SSD_REP, SSD_HEAD_DIM)
    dtr = dt.reshape(b, c, chunk, SSD_GROUPS, SSD_REP)
    Br = Bm.reshape(b, c, chunk, SSD_GROUPS, SSD_STATE)
    Cr = Cm.reshape(b, c, chunk, SSD_GROUPS, SSD_STATE)
    acum = jnp.cumsum(dtr * A, axis=2)
    xdt = xr * dtr[..., None]
    causal = jnp.tril(jnp.ones((chunk, chunk), bool))[:, :, None, None]
    seg = acum[:, :, :, None] - acum[:, :, None, :]
    decay = jnp.where(causal, jnp.exp(jnp.where(causal, seg, 0.0)), 0.0)
    scores = jnp.einsum('bclgn,bcsgn->bclsg', Cr, Br)[..., None] * decay
    y_diag = jnp.einsum('bclsgr,bcsgrp->bclgrp', scores, xdt)
    to_end = jnp.exp(acum[:, :, -1:] - acum)
    states = jnp.einsum('bcsgn,bcsgr,bcsgrp->bcgrpn', Br, to_end, xdt)
    chunk_decay = jnp.exp(acum[:, :, -1])

    def step(h, inp):
        st, dec = inp
        return h * dec[..., None, None] + st, h

    h_last, h_in = lax.scan(step, h0, (jnp.moveaxis(states, 1, 0), jnp.moveaxis(chunk_decay, 1, 0)))
    h_in = jnp.moveaxis(h_in, 0, 1)
    y_off = jnp.einsum('bclgn,bcgrpn,bclgr->bclgrp', Cr, h_in, jnp.exp(acum))
    return (y_diag + y_off).reshape(b, L, SSD_GROUPS, SSD_REP, SSD_HEAD_DIM), h_last

def ssd_mixer(z, xbc, dt_raw, conv_buf, h0, W, chunk):
    B, L = z.shape[:2]
    f = jnp.float32
    xbc, new_buf = causal_conv(xbc, conv_buf, W['conv_w'], W['conv_b'])
    xs = xbc[..., :D_SSD].astype(f).reshape(B, L, SSD_GROUPS, SSD_REP, SSD_HEAD_DIM)
    Bm = xbc[..., D_SSD:D_SSD + SSD_GROUPS * SSD_STATE].astype(f).reshape(B, L, SSD_GROUPS, SSD_STATE)
    Cm = xbc[..., D_SSD + SSD_GROUPS * SSD_STATE:].astype(f).reshape(B, L, SSD_GROUPS, SSD_STATE)
    dt = jax.nn.softplus(dt_raw.astype(f) + W['dt_bias'].astype(f)).reshape(B, L, SSD_GROUPS, SSD_REP)
    A = -jnp.exp(W['a_log'].astype(f)).reshape(SSD_GROUPS, SSD_REP)
    h0r = h0.astype(f).reshape(B, SSD_GROUPS, SSD_REP, SSD_HEAD_DIM, SSD_STATE)
    y, h = ssd_scan(xs, dt, A, Bm, Cm, h0r, chunk)
    y = y + W['d_skip'].astype(f).reshape(SSD_GROUPS, SSD_REP)[..., None] * xs
    y = y.reshape(B, L, D_SSD) * jax.nn.silu(z.astype(f))
    y = rmsnorm(y.reshape(B, L, SSD_GROUPS, D_SSD // SSD_GROUPS),
                W['ssd_norm'].reshape(SSD_GROUPS, D_SSD // SSD_GROUPS)).reshape(B, L, D_SSD)
    return y.astype(z.dtype), new_buf, h.reshape(B, SSD_HEADS, SSD_HEAD_DIM, SSD_STATE).astype(h0.dtype)

def project(x, W):
    B, L = x.shape[:2]
    p = rmsnorm(x, W['norm_mix']) @ W['w_in']
    q, kv, gate, z, xbc, dt_raw = jnp.split(p, [OFF_KV, OFF_GATE, OFF_Z, OFF_XBC, OFF_DT], axis=-1)
    q = rmsnorm(q.reshape(B, L, ATT_KV_HEADS, ATT_REP, HEAD_DIM), W['q_norm'])
    kc, vc, ks, vs, kw, vw = [t.reshape(B, L, ATT_KV_HEADS, HEAD_DIM) for t in jnp.split(kv, 6, axis=-1)]
    ks = rmsnorm(ks, W['k_norm'])
    kw = rmsnorm(kw, W['k_norm'])
    gate = jax.nn.sigmoid(gate.astype(jnp.float32)).reshape(B, L, ATT_KV_HEADS, ATT_REP, 3)
    return q, kc, vc, ks, vs, kw, vw, gate, z, xbc, dt_raw

def combine(gate, o_cmp, o_sel, o_win):
    return gate[..., 0:1] * o_cmp + gate[..., 1:2] * o_sel + gate[..., 2:3] * o_win

def finish(x, o_att, y_ssd, W):
    B, L = x.shape[:2]
    mix = jnp.concatenate([o_att.reshape(B, L, D_ATT).astype(x.dtype), y_ssd.astype(x.dtype)], axis=-1)
    h = x + mix @ W['w_out']
    u = rmsnorm(h, W['norm_ffn'])
    return h + (jax.nn.silu(u @ W['w_gate']) * (u @ W['w_up'])) @ W['w_down']

def prompt_layer(x, W):
    B, T = x.shape[:2]
    pos = jnp.arange(T, dtype=jnp.int32)
    q, kc, vc, ks, vs, kw, vw, gate, z, xbc, dt_raw = project(x, W)
    o_cmp, p_cmp = cmp_branch(q, pos, kc, vc, W)
    n_sel = T // SEL_BLOCK
    idx = select_blocks(p_cmp, pos, n_sel, min(SEL_TOPN, n_sel))
    o_sel = sel_branch_prompt(q, pos, idx, ks, vs, W['rel_bias'])
    o_win = win_branch_prompt(q, pos, kw, vw, W['rel_bias'])
    o_att = combine(gate, o_cmp, o_sel, o_win)
    conv0 = jnp.zeros((B, SSD_CONV - 1, D_CONV), x.dtype)
    h0 = jnp.zeros((B, SSD_HEADS, SSD_HEAD_DIM, SSD_STATE), jnp.float32)
    y_ssd, conv_state, ssm_state = ssd_mixer(z, xbc, dt_raw, conv0, h0, W, min(SSD_CHUNK, T))
    y = finish(x, o_att, y_ssd, W)
    wb = min(WINDOW, T)
    return y, (kc, vc, ks, vs, kw[:, T - wb:], vw[:, T - wb:], conv_state, ssm_state)

def sample_layer(x, c_kc, c_vc, c_ks, c_vs, c_kw, c_vw, s_conv, s_ssm, page_table, W):
    B, S = x.shape[:2]
    past = page_table.shape[1] * c_kc.shape[1]
    pos = past + jnp.arange(S, dtype=jnp.int32)
    q, kc, vc, ks, vs, kw, vw, gate, z, xbc, dt_raw = project(x, W)

    def gather_all(cache):
        return cache[page_table].reshape(B, past, ATT_KV_HEADS, HEAD_DIM)

    o_cmp, p_cmp = cmp_branch(q, pos, jnp.concatenate([gather_all(c_kc), kc], axis=1),
                              jnp.concatenate([gather_all(c_vc), vc], axis=1), W)
    n_sel = past // SEL_BLOCK
    idx = select_blocks(p_cmp, pos, n_sel, min(SEL_TOPN - 1, n_sel))
    o_sel = sel_branch_sample(q, pos, idx, ks, vs, c_ks, c_vs, page_table, W['rel_bias'])
    lb = c_kw.shape[1]
    kwin = jnp.concatenate([c_kw, kw], axis=1)
    vwin = jnp.concatenate([c_vw, vw], axis=1)
    kpos = past - lb + jnp.arange(lb + S, dtype=jnp.int32)
    dist = pos[:, None] - kpos[None, :]
    o_win, _ = attend_shared(q, pos, kwin, vwin, kpos, (dist >= 0) & (dist < WINDOW), W['rel_bias'])
    o_att = combine(gate, o_cmp, o_sel, o_win)
    y_ssd, conv_state, ssm_state = ssd_mixer(z, xbc, dt_raw, s_conv, s_ssm, W, S)
    y = finish(x, o_att, y_ssd, W)
    return y, (kc, vc, ks, vs, kwin[:, S:], vwin[:, S:], conv_state, ssm_state)

def setup_inputs(seed: int = 0) -> dict:
    key = jax.random.key(seed)
    ks = jax.random.split(key, 32)
    f32 = jnp.float32

    def nrm(k, shape, scale):
        return jax.random.normal(k, shape, f32) * scale

    n_pages = PAST_LEN // PAGE_SIZE
    n_phys = (DEC_BATCH * n_pages * 5) // 4
    win_buf = min(WINDOW, PAST_LEN)
    page_table = jax.random.permutation(ks[0], n_phys)[:DEC_BATCH * n_pages].reshape(
        DEC_BATCH, n_pages).astype(jnp.int32)
    kv_page = (DEPTH, n_phys, PAGE_SIZE, ATT_KV_HEADS, HEAD_DIM)
    kv_win = (DEPTH, DEC_BATCH, win_buf, ATT_KV_HEADS, HEAD_DIM)
    dt0 = jnp.exp(jax.random.uniform(ks[1], (DEPTH, SSD_HEADS), f32, math.log(1e-3), math.log(1e-1)))
    return {
        'x_prompt': nrm(ks[2], (BATCH, SEQ, D_MODEL), 1.0),
        'x_sample': nrm(ks[3], (DEC_BATCH, DEC_SEQ, D_MODEL), 1.0),
        'cache_k_cmp': nrm(ks[4], kv_page, 1.0),
        'cache_v_cmp': nrm(ks[5], kv_page, 1.0),
        'cache_k_sel': nrm(ks[6], kv_page, 1.0),
        'cache_v_sel': nrm(ks[7], kv_page, 1.0),
        'cache_k_win': nrm(ks[8], kv_win, 1.0),
        'cache_v_win': nrm(ks[9], kv_win, 1.0),
        'state_conv': nrm(ks[10], (DEPTH, DEC_BATCH, SSD_CONV - 1, D_CONV), 1.0),
        'state_ssm': nrm(ks[11], (DEPTH, DEC_BATCH, SSD_HEADS, SSD_HEAD_DIM, SSD_STATE), 0.5),
        'page_table': page_table,
        'norm_mix': 1.0 + nrm(ks[12], (DEPTH, D_MODEL), 0.02),
        'w_in': nrm(ks[13], (DEPTH, D_MODEL, D_IN), D_MODEL ** -0.5),
        'q_norm': 1.0 + nrm(ks[14], (DEPTH, HEAD_DIM), 0.02),
        'k_norm': 1.0 + nrm(ks[15], (DEPTH, HEAD_DIM), 0.02),
        'cmp_pe': nrm(ks[16], (DEPTH, 2, CMP_BLOCK, HEAD_DIM), 0.1),
        'cmp_w1': nrm(ks[17], (DEPTH, 2, CMP_BLOCK, HEAD_DIM, CMP_HIDDEN), (CMP_BLOCK * HEAD_DIM) ** -0.5),
        'cmp_w2': nrm(ks[18], (DEPTH, 2, CMP_HIDDEN, HEAD_DIM), CMP_HIDDEN ** -0.5),
        'rel_bias': nrm(ks[19], (N_BUCKETS, ATT_HEADS), 0.3),
        'conv_w': nrm(ks[20], (DEPTH, SSD_CONV, D_CONV), SSD_CONV ** -0.5),
        'conv_b': nrm(ks[21], (DEPTH, D_CONV), 0.02),
        'dt_bias': dt0 + jnp.log(-jnp.expm1(-dt0)),
        'a_log': jnp.log(jax.random.uniform(ks[22], (DEPTH, SSD_HEADS), f32, 1.0, 16.0)),
        'd_skip': 1.0 + nrm(ks[23], (DEPTH, SSD_HEADS), 0.02),
        'ssd_norm': 1.0 + nrm(ks[24], (DEPTH, D_SSD), 0.02),
        'w_out': nrm(ks[25], (DEPTH, D_MIX, D_MODEL), D_MIX ** -0.5),
        'norm_ffn': 1.0 + nrm(ks[26], (DEPTH, D_MODEL), 0.02),
        'w_gate': nrm(ks[27], (DEPTH, D_MODEL, D_FF), D_MODEL ** -0.5),
        'w_up': nrm(ks[28], (DEPTH, D_MODEL, D_FF), D_MODEL ** -0.5),
        'w_down': nrm(ks[29], (DEPTH, D_FF, D_MODEL), D_FF ** -0.5),
    }

def reference(x_prompt, x_sample, cache_k_cmp, cache_v_cmp, cache_k_sel, cache_v_sel,
              cache_k_win, cache_v_win, state_conv, state_ssm, page_table,
              norm_mix, w_in, q_norm, k_norm, cmp_pe, cmp_w1, cmp_w2, rel_bias,
              conv_w, conv_b, dt_bias, a_log, d_skip, ssd_norm, w_out, norm_ffn,
              w_gate, w_up, w_down):
    y_prompt, y_sample = x_prompt, x_sample
    prompt_states, sample_states = [], []
    for l in range(DEPTH):
        W = dict(norm_mix=norm_mix[l], w_in=w_in[l], q_norm=q_norm[l], k_norm=k_norm[l],
                 cmp_pe=cmp_pe[l], cmp_w1=cmp_w1[l], cmp_w2=cmp_w2[l], rel_bias=rel_bias,
                 conv_w=conv_w[l], conv_b=conv_b[l], dt_bias=dt_bias[l], a_log=a_log[l],
                 d_skip=d_skip[l], ssd_norm=ssd_norm[l], w_out=w_out[l], norm_ffn=norm_ffn[l],
                 w_gate=w_gate[l], w_up=w_up[l], w_down=w_down[l])
        y_prompt, st_p = prompt_layer(y_prompt, W)
        y_sample, st_s = sample_layer(y_sample, cache_k_cmp[l], cache_v_cmp[l], cache_k_sel[l],
                                      cache_v_sel[l], cache_k_win[l], cache_v_win[l],
                                      state_conv[l], state_ssm[l], page_table, W)
        prompt_states.append(st_p)
        sample_states.append(st_s)
    p_k_cmp, p_v_cmp, p_k_sel, p_v_sel, p_k_win, p_v_win, p_conv, p_ssm = [
        jnp.stack(a) for a in zip(*prompt_states)]
    s_k_cmp, s_v_cmp, s_k_sel, s_v_sel, s_k_win, s_v_win, s_conv, s_ssm = [
        jnp.stack(a) for a in zip(*sample_states)]
    return (y_prompt, y_sample,
            p_k_cmp, p_v_cmp, p_k_sel, p_v_sel, p_k_win, p_v_win, p_conv, p_ssm,
            s_k_cmp, s_v_cmp, s_k_sel, s_v_sel, s_k_win, s_v_win, s_conv, s_ssm)


_drawn_inputs = setup_inputs


def setup_inputs(seed=0):
    import zlib

    import numpy as np

    out = dict(_drawn_inputs(seed))
    spreads = {}
    factors = {'cache_k_cmp': 2.974,
     'cache_v_cmp': 3.388,
     'cache_k_sel': 4.001,
     'cache_v_sel': 3.169,
     'q_norm': 8.0,
     'k_norm': 3.018,
     'cmp_pe': 2.975,
     'rel_bias': 3.297,
     'd_skip': 4.87,
     'ssd_norm': 4.522,
     'norm_ffn': 4.46}
    for name, (base, spread) in spreads.items():
        noise = np.random.default_rng([zlib.crc32(name.encode()), seed]).standard_normal(out[name].shape)
        drawn = base * np.exp(spread * noise) if base else spread * noise
        out[name] = jnp.asarray(drawn.astype(out[name].dtype))
    for name, factor in factors.items():
        out[name] = (out[name] * factor).astype(out[name].dtype)
    return out
```

```python
import math
from collections import namedtuple
from contextlib import ExitStack, contextmanager

import numpy as np

import concourse.bass as bass
from concourse import mybir
from concourse.alu_op_type import AluOpType as ALU

ACT = mybir.ActivationFunctionType
AX = mybir.AxisListType
F32 = mybir.dt.float32
U32 = mybir.dt.uint32
I32 = mybir.dt.int32

P = 128
DM, SEQ, DB, DS, PAST, PAGE = 1024, 1024, 8, 4, 4096, 128
HD, NH, NG, REP = 64, 8, 2, 4
CSTRIDE, CHID, SELB, TOPN, WIN = 16, 64, 64, 15, 512
NBUCK, MAXDIST = 32, 128
DKV = NG * HD
DATT, DSSD, DCONV = NH * HD, 512, 768
DFF = 2816
OFF_GATE = DATT + 6 * DKV
OFF_Z = OFF_GATE + 3 * NH
OFF_XBC = OFF_Z + DSSD
OFF_DT = OFF_XBC + DCONV
DIN = OFF_DT + 8
EPS = 1e-6
NEG = -1e30
NT = SEQ // P
NS = DB * DS
KT = DM // P
TOK = SEQ + NS
B4 = 4
BIASW = 384
PZ_Z, PZ_XBC, PZ_DT, PZ_GATE = 0, DSSD, DSSD + DCONV, DSSD + DCONV + 8
PZ = PZ_GATE + 3 * NH

CONST_COLS = {}


def _shape_constants():
    p = np.arange(P)
    row_s = (p // REP) % DS
    t = np.arange(NS)
    parts = {
        "ident": np.eye(P),
        "ones": np.ones((P, P)),
        "tri": p[:, None] <= p[None, :],
        "after": np.where(p[:, None] <= p[None, :], 0.0, NEG),
        "far": np.where(p[None, :] > p[:, None], 0.0, NEG),
        "rep_sum": (p[:, None] // REP) == (p[None, :] // REP),
        "s_tri": np.pad(((t[:, None] // DS) == (t[None, :] // DS)) & (t[:, None] <= t[None, :]), ((0, P - NS), (0, 0))),
        "s_after": np.pad(np.where(((t[:, None] // DS) == (t[None, :] // DS)) & (t[:, None] <= t[None, :]), 0.0, NEG),
                          ((0, P - NS), (0, 0))),
        "s_ones": np.pad((t[:, None] // DS) == (t[None, :] // DS), ((0, P - NS), (0, 0))),
        "s_of_b": np.pad((t[:, None] // DS) == np.arange(DB)[None, :], ((0, P - NS), (0, 0))),
        "win_old": np.where(np.arange(4)[None, :] <= row_s[:, None], NEG, 0.0),
        "page_of": (8 * p[:, None] <= p[None, :]) & (p[None, :] < 8 * p[:, None] + 8),
        "p_mod": (p % 8)[:, None],
        "eps": np.full((P, 1), EPS),
        "zero": np.zeros((P, 1)),
        "one": np.ones((P, 1)),
    }
    at, out = 0, []
    for name, a in parts.items():
        CONST_COLS[name] = (at, at + a.shape[1])
        at += a.shape[1]
        out.append(np.asarray(a, np.float32))
    return np.concatenate(out, axis=1)


def _bucket_columns():
    oh = np.zeros((NBUCK + 1, BIASW), np.float32)
    for y in range(BIASW):
        n = 255 - y
        if n < 0:
            oh[NBUCK, y] = 1.0
            continue
        half = NBUCK // 2
        if n < half:
            b = n
        else:
            b = half + int(np.float32(np.log(np.float32(n) / np.float32(half))) / np.float32(math.log(MAXDIST / half))
                           * np.float32(NBUCK - half))
        b = min(b, NBUCK - 1)
        oh[b, y] += 1.0
        oh[NBUCK - 1, y] -= 1.0
    return oh


CONSTS = _shape_constants()
BUCKETS = _bucket_columns()


def named(**values):
    return namedtuple("Named", list(values))(**values)


class Buffers:
    pass


@contextmanager
def stage(nc, names):
    with ExitStack() as ctx:
        found = {}
        nums = []
        for name in names.split():
            count = 1
            if "*" in name:
                name, count = name.split("*")
            sems = [ctx.enter_context(nc.semaphore(f"{name}_{i}")) for i in range(int(count))]
            nums += [x.num for x in sems]
            found[name] = sems[0] if count == 1 else sems
        yield named(**found)
        with nc.Block() as block:
            @block.sync
            def _(sp):
                for n in sorted(nums):
                    sp.sem_clear(range(n, n + 1))


class Chain:

    def __init__(self, engine, sem):
        self.engine, self.sem, self.n = engine, sem, 0

    def __call__(self, instruction):
        self.n += 1
        instruction.then_inc(self.sem, 1)
        self.engine.wait_ge(self.sem, self.n)
        return instruction


def load_setup(nc, io, m):
    c = m.c
    with stage(nc, "loaded filled bias_mm bias_row bias_stored tables head_decay scaled page_float page_mm") as s:
        with nc.Block() as block:
            @block.sync
            def _(sp):
                loads = [
                    (m.consts[:, :], io.consts), (m.onehot[:, :], io.buckets),
                    (m.gmix[:, :], io.norm_mix.rearrange("o (c p) -> p (o c)", p=P)),
                    (m.gffn[:, :], io.norm_ffn.rearrange("o (c p) -> p (o c)", p=P)),
                    (m.qn[:, :], bass.AP(io.q_norm.tensor, 0, [[0, P], [1, HD]])),
                    (m.kn[:, :], bass.AP(io.k_norm.tensor, 0, [[0, P], [1, HD]])),
                    (m.convb[:, :], io.conv_b.rearrange("o (c p) -> p (o c)", p=P)),
                    (m.dtb[:, :], bass.AP(io.dt_bias.tensor, 0, [[0, P], [1, 8]])),
                    (m.alog[:, :], bass.AP(io.a_log.tensor, 0, [[0, P], [1, 8]])),
                    (m.dskip[:, :], bass.AP(io.d_skip.tensor, 0, [[0, P], [1, 8]])),
                    (m.ssdn[:, :], bass.AP(io.ssd_norm.tensor, 0, [[0, P], [1, DSSD]])),
                    (m.pages[:, :], bass.AP(io.page_table.tensor, 0, [[1, 16], [16, 16]])),
                ] + [(m.convw[:, k, :], io.conv_w[0, k, :].rearrange("(c p) -> p c", p=P)) for k in range(4)]
                for dst, src in loads:
                    sp.dma_start(dst, src, allow_slow_non_contiguous=True).then_inc(s.loaded, 16)
                sp.wait_ge(s.filled, 1)
                sp.dma_start(m.relx[0:NBUCK, :], io.rel_bias).then_inc(s.loaded, 16)
                sp.wait_ge(s.bias_row, 1)
                sp.dma_start(m.bias_dram, m.biasrow[:, :].unsqueeze(1).broadcast_to([NH, P, BIASW])).then_inc(s.bias_stored, 16)
                sp.wait_ge(s.bias_stored, 16)
                t = m.bias_dram.tensor
                for b in range(B4):
                    for g in range(NG):
                        p0 = b * 32 + g * 16
                        for q in range(DS):
                            sp.dma_start(m.srow[p0 + q * REP:p0 + (q + 1) * REP, :],
                                         bass.AP(t, g * REP * P * BIASW + 127 - q, [[P * BIASW, REP], [1, 132]])).then_inc(s.tables, 16)
                sp.wait_ge(s.tables, 16 * 32)

            @block.vector
            def _(dve):
                chain = Chain(dve, s.scaled)
                nc.vector.memset(m.relx[:, :], NEG).then_inc(s.filled, 1)
                dve.wait_ge(s.loaded, 16 * 17)
                nc.vector.tensor_copy(m.pagef[:, :], m.pages[:, :]).then_inc(s.page_float, 1)
                dve.wait_ge(s.page_mm, 1)
                chain(nc.vector.tensor_scalar(m.rowf[:, :], m.bank[1][:, 0:2 * DB], 8.0, c("p_mod"), ALU.mult, ALU.add))
                nc.vector.tensor_copy(m.rows[:, :], m.rowf[:, :])
                nc.vector.tensor_scalar(m.qn[:, :], m.qn[:, :], float(HD) ** -0.5, None, ALU.mult)
                dve.wait_ge(s.head_decay, 1)
                nc.vector.tensor_scalar(m.alog[:, :], m.alog[:, :], -1.0, None, ALU.mult)
                dve.wait_ge(s.bias_mm, 1)
                nc.vector.tensor_copy(m.biasrow[:, :], m.bank[0][0:NH, 0:BIASW]).then_inc(s.bias_row, 1)

            @block.scalar
            def _(act):
                act.wait_ge(s.loaded, 16 * 17)
                nc.scalar.activation(m.alog[:, :], m.alog[:, :], ACT.Exp).then_inc(s.head_decay, 1)

            @block.tensor
            def _(pe):
                pe.wait_ge(s.page_float, 1)
                nc.tensor.matmul(m.bank[1][:, 0:2 * DB], c("page_of")[0:16, :], m.pagef[:, :],
                                 start=True, stop=True).then_inc(s.page_mm, 1)
                pe.wait_ge(s.loaded, 16 * 17)
                nc.tensor.matmul(m.bank[0][0:NH, 0:BIASW], m.relx[:, :], m.onehot[:, :],
                                 start=True, stop=True).then_inc(s.bias_mm, 1)


def project(nc, io, m, w, tiles):
    c = m.c
    n = len(tiles)
    chunks = [(0, 512), (512, 1024), (1024, OFF_Z), (OFF_Z, OFF_XBC), (OFF_XBC, OFF_XBC + 512), (OFF_XBC + 512, DIN)]
    TA, TB = m.bank[6], m.bank[7]
    with stage(nc, "x_loaded*2 w_loaded x_square x_rstd x_scaled x_turned u_ready projected low_taken high_taken "
                   "squared head_sums head_rstd normed qk_turned qk_taken stored*2 act_c dve_c") as s:
        with nc.Block() as block:
            @block.sync
            def _(sp):
                def load_x(j):
                    if j >= 2:
                        sp.wait_ge(s.x_turned, 2 * (j - 1))
                    sp.dma_start(w.x[0:tiles[j].rows, j % 2, :], tiles[j].x).then_inc(s.x_loaded[j % 2], 16)

                load_x(0)
                if w.first:
                    wv = io.w_in.rearrange("o (c p) n -> p (o c) n", p=P)
                    for k in range(KT):
                        sp.dma_start(w.w[:, k, :], wv[:, k, :]).then_inc(s.w_loaded, 16)
                if n > 1:
                    load_x(1)
                for j in range(n):
                    t = tiles[j]
                    sp.wait_ge(s.normed, j + 1)
                    sp.wait_ge(s.low_taken, 3 * (j + 1))
                    for dst, src in ((t.kc, w.kv[0:t.rows, j % 2, 0, :]), (t.vc, w.kv[0:t.rows, j % 2, 1, :]),
                                     (t.ks, w.qk[0:t.rows, j % 2, 4, :]), (t.vs, w.kv[0:t.rows, j % 2, 3, :]),
                                     (t.kw, w.qk[0:t.rows, j % 2, 5, :]), (t.vw, w.kv[0:t.rows, j % 2, 5, :])):
                        sp.dma_start(dst, src).then_inc(s.stored[j % 2], 16)
                    if j + 2 < n:
                        load_x(j + 2)
                for k in range(min(n, 2)):
                    sp.wait_ge(s.stored[k], 16 * 6 * len(range(k, n, 2)))

            @block.tensor
            def _(pe):
                def turn_x(j):
                    r = tiles[j].rows
                    pe.wait_ge(s.x_scaled, j + 1)
                    if j >= 1:
                        pe.wait_ge(s.u_ready, 2 * j)
                    if j >= 2:
                        pe.wait_ge(s.qk_taken, 2 * (j - 1))
                    for k in range(KT):
                        bank = (TA, TB)[k // 4]
                        i = nc.tensor.transpose(bank[:, (k % 4) * P:(k % 4) * P + r],
                                                w.x[0:r, j % 2, k * P:(k + 1) * P], c("ident")[0:r, 0:r])
                        if k % 4 == 3:
                            i.then_inc(s.x_turned, 1)

                def turn_heads(j):
                    r = tiles[j].rows
                    pe.wait_ge(s.normed, j + 1)
                    pe.wait_ge(s.u_ready, 2 * min(j + 2, n))
                    for k in range(6):
                        bank = (TA, TB)[k // 4]
                        i = nc.tensor.transpose(bank[:, (k % 4) * P:(k % 4) * P + r], w.qk[0:r, j % 2, k, :],
                                                c("ident")[0:r, 0:r])
                        if k in (3, 5):
                            i.then_inc(s.qk_turned, 1)

                def multiply(j, cs):
                    r = tiles[j].rows
                    for i in cs:
                        a, b = chunks[i]
                        if j >= 1:
                            if i < 3:
                                pe.wait_ge(s.low_taken, 3 * (j - 1) + i + 1)
                            else:
                                pe.wait_ge(s.high_taken, 3 * (j - 1) + i - 2)
                        for k in range(KT):
                            mm = nc.tensor.matmul(m.bank[i][0:r, 0:b - a], w.u[:, j % 2, k, 0:r], w.w[:, k, a:b],
                                                  start=(k == 0), stop=(k == KT - 1))
                        mm.then_inc(s.projected, 1)

                turn_x(0)
                if w.first:
                    pe.wait_ge(s.w_loaded, 16 * KT)
                for j in range(n):
                    pe.wait_ge(s.u_ready, 2 * (j + 1))
                    multiply(j, (0, 1, 2))
                    if j >= 1:
                        turn_heads(j - 1)
                    if j + 1 < n:
                        turn_x(j + 1)
                    multiply(j, (3, 4, 5))
                if n > 1:
                    pe.wait_ge(s.qk_taken, 2 * (n - 1))
                turn_heads(n - 1)

            @block.scalar
            def _(act):
                chain = Chain(act, s.act_c)

                def statistics(j):
                    r = tiles[j].rows
                    act.wait_ge(s.x_loaded[j % 2], 16 * (j // 2 + 1))
                    if j >= 2:
                        act.wait_ge(s.x_scaled, j - 1)
                    chain(nc.scalar.activation(w.junk[0:r, :], w.x[0:r, j % 2, :], ACT.Square,
                                               accum_out=w.ss[0:r, j % 2:j % 2 + 1]))
                    chain(nc.scalar.activation(w.ss[0:r, 2:3], w.ss[0:r, j % 2:j % 2 + 1], ACT.Ln, scale=1.0 / DM,
                                               bias=c("eps")[0:r, :]))
                    nc.scalar.activation(w.ss[0:r, 4 + j % 2:5 + j % 2], w.ss[0:r, 2:3], ACT.Exp,
                                         scale=-0.5).then_inc(s.x_rstd, 1)

                def take_heads(j):
                    t = tiles[j]
                    act.wait_ge(s.qk_turned, 2 * j + 1)
                    nc.scalar.activation(t.qT, TA[:, :].rearrange("p (r q) -> p r q", r=4)[:, :, 0:t.rows],
                                         ACT.Copy).then_inc(s.qk_taken, 1)
                    act.wait_ge(s.qk_turned, 2 * j + 2)
                    nc.scalar.activation(t.ksT, TB[:, 0:t.rows], ACT.Copy)
                    nc.scalar.activation(t.kwT, TB[:, P:P + t.rows], ACT.Copy).then_inc(s.qk_taken, 1)

                statistics(0)
                for j in range(n):
                    t, r = tiles[j], tiles[j].rows
                    if j + 1 < n:
                        statistics(j + 1)
                    act.wait_ge(s.projected, 6 * j + 1)
                    if j >= 1:
                        act.wait_ge(s.normed, j)
                    if j >= 2:
                        act.wait_ge(s.stored[j % 2], 16 * 6 * (j // 2))
                    nc.scalar.activation(w.q[0:r, :], m.bank[0][0:r, :], ACT.Copy).then_inc(s.low_taken, 1)
                    act.wait_ge(s.projected, 6 * j + 2)
                    nc.scalar.activation(w.kv[0:r, j % 2, 0:4, :], m.bank[1][0:r, :].rearrange("p (a b) -> p a b", a=4),
                                         ACT.Copy).then_inc(s.low_taken, 1)
                    act.wait_ge(s.projected, 6 * j + 3)
                    nc.scalar.activation(w.kv[0:r, j % 2, 4:6, :],
                                         m.bank[2][0:r, 0:256].rearrange("p (a b) -> p a b", a=2), ACT.Copy)
                    nc.scalar.activation(t.gate, m.bank[2][0:r, 256:280], ACT.Copy).then_inc(s.low_taken, 1)
                    act.wait_ge(s.low_taken, 3 * (j + 1))
                    if j >= 1:
                        act.wait_ge(s.head_sums, j)
                    nc.scalar.activation(w.sq[0:r, 0:512], w.q[0:r, :], ACT.Square)
                    nc.scalar.activation(w.sq[0:r, 512:640], w.kv[0:r, j % 2, 2, :], ACT.Square)
                    nc.scalar.activation(w.sq[0:r, 640:768], w.kv[0:r, j % 2, 4, :], ACT.Square).then_inc(s.squared, 1)
                    nc.scalar.activation(t.v[:, 0, :], w.kv[0:r, j % 2, 3, :], ACT.Copy)
                    nc.scalar.activation(t.v[:, 1, :], w.kv[0:r, j % 2, 5, :], ACT.Copy)
                    if j >= 1:
                        take_heads(j - 1)
                    act.wait_ge(s.head_sums, j + 1)
                    chain(nc.scalar.activation(w.hs[0:r, 12:24], w.hs[0:r, 0:12], ACT.Ln, scale=1.0 / HD,
                                               bias=c("eps")[0:r, :]))
                    nc.scalar.activation(w.hs[0:r, 24:36], w.hs[0:r, 12:24], ACT.Exp,
                                         scale=-0.5).then_inc(s.head_rstd, 1)
                take_heads(n - 1)

            @block.vector
            def _(dve):
                chain = Chain(dve, s.dve_c)

                def make_u(j):
                    r = tiles[j].rows
                    dve.wait_ge(s.x_rstd, j + 1)
                    nc.vector.tensor_scalar(w.x[0:r, j % 2, :], w.x[0:r, j % 2, :], w.ss[0:r, 4 + j % 2:5 + j % 2], None,
                                            ALU.mult).then_inc(s.x_scaled, 1)
                    for h in range(2):
                        dve.wait_ge(s.x_turned, 2 * j + h + 1)
                        if j >= 2:
                            dve.wait_ge(s.projected, 6 * (j - 1))
                        nc.vector.tensor_tensor(w.u[:, j % 2, 4 * h:4 * h + 4, 0:r],
                                                (TA, TB)[h][:, :].rearrange("p (k q) -> p k q", k=4)[:, :, 0:r],
                                                m.gmix[:, 4 * h:4 * h + 4].unsqueeze(2).broadcast_to([P, 4, r]),
                                                ALU.mult).then_inc(s.u_ready, 1)

                make_u(0)
                for j in range(n):
                    t, r = tiles[j], tiles[j].rows
                    if j + 1 < n:
                        make_u(j + 1)
                    for i, (a, b) in ((3, (PZ_Z, PZ_Z + 512)), (4, (PZ_XBC, PZ_XBC + 512)), (5, (PZ_XBC + 512, PZ_GATE))):
                        dve.wait_ge(s.projected, 6 * j + i + 1)
                        nc.vector.tensor_copy(t.pz[:, a:b], m.bank[i][0:r, 0:b - a]).then_inc(s.high_taken, 1)
                    dve.wait_ge(s.squared, j + 1)
                    if j >= 1:
                        dve.wait_ge(s.head_rstd, j)
                    nc.vector.tensor_reduce(w.hs[0:r, 0:12], w.sq[0:r, :].rearrange("p (h d) -> p h d", d=HD), AX.X,
                                            ALU.add).then_inc(s.head_sums, 1)
                    dve.wait_ge(s.head_rstd, j + 1)
                    if j >= 2:
                        dve.wait_ge(s.stored[j % 2], 16 * 6 * (j // 2))
                        dve.wait_ge(s.qk_turned, 2 * (j - 1))
                    nc.vector.tensor_tensor(
                        w.qk[0:r, j % 2, 0:4, :].rearrange("p r (g d) -> p g r d", g=NG),
                        w.q[0:r, :].rearrange("p (g r d) -> p g r d", g=NG, r=REP),
                        w.hs[0:r, 24:32].rearrange("p (g r) -> p g r", g=NG).unsqueeze(3).broadcast_to([r, NG, REP, HD]),
                        ALU.mult)
                    chain(nc.vector.tensor_tensor(
                        w.qk[0:r, j % 2, 4:6, :].rearrange("p b (g d) -> p b g d", g=NG),
                        w.kv[0:r, j % 2, 2:6:2, :].rearrange("p b (g d) -> p b g d", g=NG),
                        w.hs[0:r, 32:36].rearrange("p (b g) -> p b g", g=NG).unsqueeze(3).broadcast_to([r, 2, NG, HD]),
                        ALU.mult))
                    nc.vector.tensor_tensor(
                        w.qk[0:r, j % 2, 0:4, :].rearrange("p r (g d) -> p (r g) d", g=NG),
                        w.qk[0:r, j % 2, 0:4, :].rearrange("p r (g d) -> p (r g) d", g=NG),
                        m.qn[0:r, :].unsqueeze(1).broadcast_to([r, NH, HD]), ALU.mult)
                    nc.vector.tensor_tensor(
                        w.qk[0:r, j % 2, 4:6, :].rearrange("p r (g d) -> p (r g) d", g=NG),
                        w.qk[0:r, j % 2, 4:6, :].rearrange("p r (g d) -> p (r g) d", g=NG),
                        m.kn[0:r, :].unsqueeze(1).broadcast_to([r, 4, HD]), ALU.mult).then_inc(s.normed, 1)


def stage_pointwise(nc, io, m):
    c = m.c
    sb = Region(nc, m.att_end, m.end)
    m.dt = nc.alloc_sbuf_tensor_at("dt", [P, NT + 1, 16], F32, offset=m.dt_start)
    t1 = sb("dt_low", [P, NT + 1, 8])
    t2 = sb("dt_exp", [P, NT + 1, 8])
    parts = [(slice(0, P), slice(0, NT)), (slice(0, NS), slice(NT, NT + 1))]
    with stage(nc, "act_c dve_c low_ready log_ready stored") as s:
        with nc.Block() as block:
            @block.sync
            def _(sp):
                sp.dma_start(io.p_conv[0, 0, :, :], m.pz[P - 3:P, NT - 1, PZ_XBC:PZ_XBC + DCONV]).then_inc(s.stored, 16)
                for b in range(DB):
                    sp.dma_start(io.s_conv[0, b, :, :],
                                 m.pz[b * DS + 1:(b + 1) * DS, NT, PZ_XBC:PZ_XBC + DCONV]).then_inc(s.stored, 16)
                sp.wait_ge(s.stored, 16 * (1 + DB))

            @block.scalar
            def _(act):
                for rows, tiles in parts:
                    nc.scalar.activation(m.gates[rows, tiles, :], m.pz[rows, tiles, PZ_GATE:PZ], ACT.Sigmoid)
                for rows, tiles in parts:
                    z = m.pz[rows, tiles, PZ_Z:PZ_Z + DSSD]
                    nc.scalar.activation(z, z, ACT.Silu)
                chain = Chain(act, s.act_c)
                act.wait_ge(s.low_ready, 1)
                for rows, tiles in parts:
                    chain(nc.scalar.activation(t2[rows, tiles, :], t1[rows, tiles, :], ACT.Exp))
                for rows, tiles in parts:
                    nc.scalar.activation(t2[rows, tiles, :], t2[rows, tiles, :], ACT.Ln,
                                         bias=c("one")[rows, :]).then_inc(s.log_ready, 1)

            @block.vector
            def _(dve):
                chain = Chain(dve, s.dve_c)
                for rows, tiles in parts:
                    n = tiles.stop - tiles.start
                    r = rows.stop
                    x, low = m.dt[rows, tiles, 0:8], t1[rows, tiles, :]
                    chain(nc.vector.tensor_tensor(x, m.pz[rows, tiles, PZ_DT:PZ_DT + 8],
                                                  m.dtb[rows, :].unsqueeze(1).broadcast_to([r, n, 8]), ALU.add))
                    chain(nc.vector.tensor_scalar(low, x, -1.0, None, ALU.mult))
                    chain(nc.vector.tensor_tensor(low, low, x, ALU.min))
                nc.vector.tensor_scalar(t1[0:1, 0, 0:1], t1[0:1, 0, 0:1], 1.0, None, ALU.mult).then_inc(s.low_ready, 1)
                dve.wait_ge(s.log_ready, 2)
                for rows, tiles in parts:
                    n = tiles.stop - tiles.start
                    r = rows.stop
                    x = m.dt[rows, tiles, 0:8]
                    chain(nc.vector.tensor_scalar(x, x, 0.0, None, ALU.max))
                    chain(nc.vector.tensor_tensor(x, x, t2[rows, tiles, :], ALU.add))
                    nc.vector.tensor_tensor(m.dt[rows, tiles, 8:16], x,
                                            m.alog[rows, :].unsqueeze(1).broadcast_to([r, n, 8]), ALU.mult)


def stage_conv(nc, io, m):
    c = m.c
    NCB = DCONV // P
    sb = Region(nc, m.qT_start, m.mix_start)
    m.xc = sb("conv_out", [P, NCB, TOK])
    m.conv_end = sb.at
    raw = sb("conv_in", [P, NCB, 3 + SEQ])
    raws = sb("conv_in_s", [P, NCB, DB, 3 + DS])
    state = sb("conv_state", [DB * 3, DCONV])
    with stage(nc, "state_loaded padded turned taken tapped summed sample_taken dve_c") as s:
        with nc.Block() as block:
            @block.sync
            def _(sp):
                sp.dma_start(state[:, :], io.state_conv.rearrange("o b k c -> (o b k) c")).then_inc(s.state_loaded, 16)

            @block.gpsimd
            def _(pool):
                nc.gpsimd.memset(raw[:, :, 0:3], 0.0).then_inc(s.padded, 1)

            @block.tensor
            def _(pe):
                for b in range(NCB):
                    for h in range(2):
                        n = 2 * b + h
                        if n >= 6:
                            pe.wait_ge(s.taken, n - 5)
                        for k in range(4):
                            i = nc.tensor.transpose(m.bank[n % 6][:, k * P:(k + 1) * P],
                                                    m.pz[:, 4 * h + k, PZ_XBC + b * P:PZ_XBC + (b + 1) * P], c("ident"))
                        i.then_inc(s.turned, 1)
                pe.wait_ge(s.state_loaded, 16)
                for b in range(NCB):
                    nc.tensor.transpose(m.bank[6][:, b * NS:(b + 1) * NS],
                                        m.pz[0:NS, NT, PZ_XBC + b * P:PZ_XBC + (b + 1) * P], c("ident")[0:NS, 0:NS])
                    i = nc.tensor.transpose(m.bank[7][:, b * 24:(b + 1) * 24], state[:, b * P:(b + 1) * P],
                                            c("ident")[0:24, 0:24])
                i.then_inc(s.turned, 1)

            @block.scalar
            def _(act):
                act.wait_ge(s.padded, 1)
                for b in range(NCB):
                    for h in range(2):
                        n = 2 * b + h
                        act.wait_ge(s.turned, n + 1)
                        nc.scalar.activation(raw[:, b, 3 + 512 * h:3 + 512 * (h + 1)], m.bank[n % 6][:, :],
                                             ACT.Copy).then_inc(s.taken, 1)
                    act.wait_ge(s.taken, 2 * b + 2)
                    nc.scalar.activation(m.xc[:, b, 0:SEQ], raw[:, b, 0:SEQ], ACT.Identity, bias=m.convb[:, b:b + 1],
                                         scale=m.convw[:, 0, b:b + 1]).then_inc(s.tapped, 1)
                act.wait_ge(s.turned, 2 * NCB + 1)
                nc.scalar.activation(raws[:, :, :, 3:3 + DS], m.bank[6][:, 0:NCB * NS].rearrange(
                    "p (c b t) -> p c b t", c=NCB, b=DB), ACT.Copy)
                nc.scalar.activation(raws[:, :, :, 0:3], m.bank[7][:, 0:NCB * 24].rearrange(
                    "p (c b t) -> p c b t", c=NCB, b=DB), ACT.Copy).then_inc(s.sample_taken, 1)
                act.wait_ge(s.sample_taken, 1)
                for b in range(NCB):
                    nc.scalar.activation(m.xc[:, b, SEQ:TOK].rearrange("p (b t) -> p b t", b=DB), raws[:, b, :, 0:DS],
                                         ACT.Identity, bias=m.convb[:, b:b + 1],
                                         scale=m.convw[:, 0, b:b + 1]).then_inc(s.tapped, 1)
                for b in range(NCB):
                    act.wait_ge(s.summed, b + 1)
                    nc.scalar.activation(m.xc[:, b, 0:SEQ], m.xc[:, b, 0:SEQ], ACT.Silu)
                act.wait_ge(s.summed, 2 * NCB)
                nc.scalar.activation(m.xc[:, :, SEQ:TOK], m.xc[:, :, SEQ:TOK], ACT.Silu)

            @block.vector
            def _(dve):
                chain = Chain(dve, s.dve_c)
                for b in range(NCB):
                    dve.wait_ge(s.tapped, b + 1)
                    for k in range(1, 4):
                        i = nc.vector.scalar_tensor_tensor(m.xc[:, b, 0:SEQ], raw[:, b, k:k + SEQ], m.convw[:, k, b:b + 1],
                                                           m.xc[:, b, 0:SEQ], ALU.mult, ALU.add)
                        if k < 3:
                            chain(i)
                    i.then_inc(s.summed, 1)
                for b in range(NCB):
                    dve.wait_ge(s.tapped, NCB + b + 1)
                    out = m.xc[:, b, SEQ:TOK].rearrange("p (b t) -> p b t", b=DB)
                    for k in range(1, 4):
                        i = nc.vector.scalar_tensor_tensor(out, raws[:, b, :, k:k + DS], m.convw[:, k, b:b + 1],
                                                           out, ALU.mult, ALU.add)
                        if k < 3:
                            chain(i)
                    i.then_inc(s.summed, 1)


def ssd_chunks(nc, m, w, chunks):
    c = m.c
    n = len(chunks)
    R = chunks[0].rows
    sample = chunks[0].sample
    tri, after, ones = (("s_tri", "s_after", "s_ones") if sample else ("tri", "after", "ones"))
    tri, after, ones = c(tri)[0:R, 0:R], c(after)[0:R, 0:R], c(ones)[0:R, 0:R]
    heads = lambda ap: ap.unsqueeze(2).broadcast_to([R, 8, HD])
    with stage(nc, "xs_ready dt_ready td_ready turned sums_ready x_taken small_taken diff_ready ex_ready cb_ready "
                   "acb_ready seg_done e_ready m_ready xdt_ready xe_ready yo_ready yd_ready st_ready state_ready "
                   "state_scaled xd_ready y_ready yr_ready y_done act_c dve_c pe_c") as s:
        with nc.Block() as block:
            @block.tensor
            def _(pe):
                chain = Chain(pe, s.pe_c)

                def front(j):
                    q = j % 2
                    pe.wait_ge(s.xs_ready, j + 1)
                    if j >= 1:
                        pe.wait_ge(s.x_taken, j)
                        pe.wait_ge(s.small_taken, j)
                    for k in range(4):
                        nc.tensor.transpose(m.bank[0][0:R, k * P:(k + 1) * P], w.xs[:, q, k, 0:R], c("ident"))
                    nc.tensor.transpose(m.bank[1][0:R, 0:P], w.xs[:, q, 4, 0:R], c("ident")).then_inc(s.turned, 1)
                    pe.wait_ge(s.dt_ready, j + 1)
                    nc.tensor.matmul(m.bank[1][0:R, P:P + 8], tri, w.dt[0:R, q, 8:16], start=True, stop=True)
                    nc.tensor.matmul(m.bank[1][0:R, P + 8:P + 16], ones, w.dt[0:R, q, 8:16], start=True,
                                     stop=True).then_inc(s.sums_ready, 1)
                    if j >= 1:
                        pe.wait_ge(s.m_ready, j)
                        pe.wait_ge(s.seg_done, j)
                    for g in range(NG):
                        mm = nc.tensor.matmul(m.bank[2][0:R, g * P:g * P + R], w.xs[64 * g:64 * g + 64, q, 4, 0:R],
                                              w.xs[64 * g:64 * g + 64, q, 5, 0:R], start=True, stop=True)
                        chain(mm)
                    nc.tensor.nop().then_inc(s.cb_ready, 1)
                    pe.wait_ge(s.td_ready, j + 1)
                    for h in range(2):
                        mm = nc.tensor.matmul(m.bank[4 + h][0:R, 0:4 * R], c("ones")[0:R, 0:R],
                                              w.td[0:R, 4 * h:4 * h + 4, 0:R], start=True, stop=True)
                    mm.then_inc(s.acb_ready, 1)

                def back(j):
                    q = j % 2
                    if j >= 1:
                        pe.wait_ge(s.y_ready, j)
                        pe.wait_ge(s.state_ready, j)
                    if not sample:
                        for g in range(NG):
                            mm = nc.tensor.matmul(m.bank[6][0:R, 256 * g:256 * (g + 1)],
                                                  w.xs[64 * g:64 * g + 64, q, 5, 0:R],
                                                  w.state[64 * g:64 * g + 64, :], start=True, stop=True)
                            chain(mm)
                    else:
                        for g in range(NG):
                            for b in range(DB):
                                mm = nc.tensor.matmul(m.bank[6][0:R, 256 * g:256 * (g + 1)],
                                                      w.cm[64 * g:64 * g + 64, b, :], w.s0[64 * g:64 * g + 64, b, :],
                                                      start=(b == 0), stop=(b == DB - 1))
                            chain(mm)
                    nc.tensor.nop().then_inc(s.yo_ready, 1)
                    pe.wait_ge(s.m_ready, j + 1)
                    pe.wait_ge(s.xdt_ready, j + 1)
                    for h in range(8):
                        mm = nc.tensor.matmul(m.bank[7][0:R, HD * h:HD * (h + 1)], w.seg[0:R, h, 0:R],
                                              w.xdt[0:R, HD * h:HD * (h + 1)], start=True, stop=True)
                    mm.then_inc(s.yd_ready, 1)
                    if not sample:
                        pe.wait_ge(s.xe_ready, j + 1)
                        nc.tensor.matmul(m.bank[3][:, :], w.small[0:R, q, 0:P], w.xe[0:R, :], start=True,
                                         stop=True).then_inc(s.st_ready, 1)

                front(0)
                for j in range(n):
                    back(j)
                    if j + 1 < n:
                        front(j + 1)

            @block.scalar
            def _(act):
                chain = Chain(act, s.act_c)

                def slice_chunk(j):
                    if j >= 2:
                        act.wait_ge(s.yo_ready, j - 1)
                    nc.scalar.activation(w.xs[:, j % 2, :, 0:R], chunks[j].xc, ACT.Copy).then_inc(s.xs_ready, 1)

                slice_chunk(0)
                for j in range(n):
                    q = j % 2
                    act.wait_ge(s.turned, j + 1)
                    if j >= 1:
                        act.wait_ge(s.xe_ready, j)
                        act.wait_ge(s.xd_ready, j)
                    nc.scalar.activation(w.xt[0:R, :], m.bank[0][0:R, :], ACT.Copy).then_inc(s.x_taken, 1)
                    act.wait_ge(s.diff_ready, j + 1)
                    if j >= 2:
                        act.wait_ge(s.y_ready, j - 1)
                    nc.scalar.activation(w.ex[0:R, q, :], w.small[0:R, q, P:P + 24], ACT.Exp).then_inc(s.ex_ready, 1)
                    act.wait_ge(s.seg_done, j + 1)
                    nc.scalar.activation(w.seg[0:R, :, 0:R], w.seg[0:R, :, 0:R], ACT.Exp).then_inc(s.e_ready, 1)
                    if j + 1 < n:
                        slice_chunk(j + 1)
                    act.wait_ge(s.y_ready, j + 1)
                    for g in range(NG):
                        chain(nc.scalar.activation(w.junk[0:R, :], w.y[0:R, q, 256 * g:256 * (g + 1)], ACT.Square,
                                                   accum_out=w.yr[0:R, q, g:g + 1]))
                    chain(nc.scalar.activation(w.yr[0:R, q, 2:4], w.yr[0:R, q, 0:2], ACT.Ln, scale=1.0 / 256,
                                               bias=c("eps")[0:R, :]))
                    nc.scalar.activation(w.yr[0:R, q, 4:6], w.yr[0:R, q, 2:4], ACT.Exp, scale=-0.5).then_inc(s.yr_ready, 1)

            @block.gpsimd
            def _(pool):
                for j in range(n):
                    pool.wait_ge(s.x_taken, j + 1)
                    if j >= 1:
                        pool.wait_ge(s.y_ready, j)
                    nc.gpsimd.tensor_tensor(w.xd[0:R, :].rearrange("p (h d) -> p h d", h=8),
                                            w.xt[0:R, :].rearrange("p (h d) -> p h d", h=8), heads(m.dskip[0:R, :]),
                                            ALU.mult).then_inc(s.xd_ready, 1)

            @block.vector
            def _(dve):
                chain = Chain(dve, s.dve_c)

                def steps(j):
                    q = j % 2
                    if j >= 2:
                        dve.wait_ge(s.xe_ready, j - 1)
                    nc.vector.tensor_copy(w.dt[0:R, q, :], chunks[j].dt).then_inc(s.dt_ready, 1)
                    dve.wait_ge(s.dt_ready, j + 1)
                    if j >= 1:
                        dve.wait_ge(s.acb_ready, j)
                    nc.vector.tensor_tensor(w.td[0:R, :, 0:R], tri.unsqueeze(1).broadcast_to([R, 8, R]),
                                            w.dt[0:R, q, 8:16].unsqueeze(2).broadcast_to([R, 8, R]),
                                            ALU.mult).then_inc(s.td_ready, 1)

                def finish(j):
                    q = j % 2
                    dve.wait_ge(s.yr_ready, j + 1)
                    for g in range(NG):
                        i = nc.vector.scalar_tensor_tensor(chunks[j].out[:, 256 * g:256 * (g + 1)],
                                                           w.y[0:R, q, 256 * g:256 * (g + 1)], w.yr[0:R, q, 4 + g:5 + g],
                                                           m.ssdn[0:R, 256 * g:256 * (g + 1)], ALU.mult, ALU.mult)
                    i.then_inc(s.y_done, 1)

                steps(0)
                for j in range(n):
                    q = j % 2
                    ch = chunks[j]
                    dve.wait_ge(s.sums_ready, j + 1)
                    if j >= 2:
                        dve.wait_ge(s.ex_ready, j - 1)
                    nc.vector.tensor_copy(w.small[0:R, q, 0:P + 16], m.bank[1][0:R, 0:P + 16]).then_inc(s.small_taken, 1)
                    dve.wait_ge(s.small_taken, j + 1)
                    nc.vector.tensor_tensor(w.small[0:R, q, P + 16:P + 24], w.small[0:R, q, P + 8:P + 16],
                                            w.small[0:R, q, P:P + 8], ALU.subtract).then_inc(s.diff_ready, 1)
                    dve.wait_ge(s.acb_ready, j + 1)
                    if j >= 1:
                        dve.wait_ge(s.yd_ready, j)
                    for h in range(8):
                        i = nc.vector.scalar_tensor_tensor(w.seg[0:R, h, 0:R],
                                                           m.bank[4 + h // 4][0:R, (h % 4) * R:(h % 4 + 1) * R],
                                                           w.small[0:R, q, P + h:P + h + 1], after,
                                                           ALU.subtract, ALU.add)
                    i.then_inc(s.seg_done, 1)
                    if j >= 1:
                        finish(j - 1)
                    dve.wait_ge(s.x_taken, j + 1)
                    nc.vector.tensor_tensor(w.xdt[0:R, :].rearrange("p (h d) -> p h d", h=8),
                                            w.xt[0:R, :].rearrange("p (h d) -> p h d", h=8), heads(w.dt[0:R, q, 0:8]),
                                            ALU.mult).then_inc(s.xdt_ready, 1)
                    dve.wait_ge(s.xdt_ready, j + 1)
                    dve.wait_ge(s.ex_ready, j + 1)
                    if j >= 1:
                        dve.wait_ge(s.state_ready, j)
                    nc.vector.tensor_tensor(w.xe[0:R, :].rearrange("p (h d) -> p h d", h=8),
                                            w.xdt[0:R, :].rearrange("p (h d) -> p h d", h=8), heads(w.ex[0:R, q, 16:24]),
                                            ALU.mult).then_inc(s.xe_ready, 1)
                    dve.wait_ge(s.e_ready, j + 1)
                    dve.wait_ge(s.cb_ready, j + 1)
                    for g in range(NG):
                        i = nc.vector.tensor_tensor(w.seg[0:R, 4 * g:4 * g + 4, 0:R], w.seg[0:R, 4 * g:4 * g + 4, 0:R],
                                                    m.bank[2][0:R, g * P:g * P + R].unsqueeze(1).broadcast_to([R, 4, R]),
                                                    ALU.mult)
                    i.then_inc(s.m_ready, 1)
                    if j + 1 < n:
                        steps(j + 1)
                    dve.wait_ge(s.yo_ready, j + 1)
                    if not sample:
                        for g in range(NG):
                            st = w.state[64 * g:64 * g + 64, :].rearrange("p (r d) -> p r d", r=4)
                            chain(nc.vector.tensor_tensor(
                                st, st, w.ex[64 * g:64 * g + 64, q, 8 + 4 * g:12 + 4 * g].unsqueeze(2).broadcast_to(
                                    [64, 4, HD]), ALU.mult))
                        dve.wait_ge(s.st_ready, j + 1)
                        for g in range(NG):
                            i = nc.vector.tensor_tensor(w.state[64 * g:64 * g + 64, :], w.state[64 * g:64 * g + 64, :],
                                                        m.bank[3][64 * g:64 * g + 64, 256 * g:256 * (g + 1)], ALU.add)
                        i.then_inc(s.state_ready, 1)
                    y = w.y[0:R, q, :]
                    if j >= 2:
                        dve.wait_ge(s.y_done, j - 1)
                    chain(nc.vector.tensor_tensor(y.rearrange("p (h d) -> p h d", h=8),
                                                  m.bank[6][0:R, :].rearrange("p (h d) -> p h d", h=8),
                                                  heads(w.ex[0:R, q, 0:8]), ALU.mult))
                    dve.wait_ge(s.yd_ready, j + 1)
                    chain(nc.vector.tensor_tensor(y, y, m.bank[7][0:R, :], ALU.add))
                    dve.wait_ge(s.xd_ready, j + 1)
                    chain(nc.vector.tensor_tensor(y, y, w.xd[0:R, :], ALU.add))
                    nc.vector.tensor_tensor(y, y, ch.z, ALU.mult).then_inc(s.y_ready, 1)
                finish(n - 1)


def stage_ssd(nc, io, m):
    c = m.c
    sb = Region(nc, m.conv_end, m.mix_start)
    w = Buffers()
    w.xs = sb("chunk", [P, 2, 6, P])
    w.dt = sb("chunk_dt", [P, 2, 16])
    w.td = sb("dt_steps", [P, 8, P])
    w.small = sb("b_and_sums", [P, 2, P + 24])
    w.ex = sb("decays", [P, 2, 24])
    w.seg = sb("seg", [P, 8, P])
    w.xt = sb("x_tok", [P, DSSD])
    w.xdt = sb("xdt", [P, DSSD])
    w.xe = sb("x_to_end", [P, DSSD])
    w.xd = sb("x_skip", [P, DSSD])
    w.y = sb("y_ssd", [P, 2, DSSD])
    w.yr = sb("y_rstd", [P, 2, 6])
    w.junk = sb("junk_y", [P, 256])
    w.state = sb("state", [P, 256])
    w.s0 = sb("state0", [P, DB, 256])
    w.cm = sb("c_masked", [P, DB, NS])
    w.bm = sb("b_masked", [NS, DB, P])
    w.db = sb("dta_of_b", [NS, DB, 8])
    w.dec = sb("decay_of_b", [P, DB, 8])
    w.hin = sb("state_in", [P, DB, 2, NG, HD])
    w.hout = sb("state_out", [P, DB, 2, NG, HD])
    hd = lambda ap: ap.rearrange("o b (i h) p n -> (h p) (o b) i n", h=2)

    with stage(nc, "loaded zeroed turned taken") as s:
        with nc.Block() as block:
            @block.sync
            def _(sp):
                for i in range(4):
                    sp.dma_start(w.hin[:, :, i % 2, i // 2, :], hd(io.state_ssm)[:, :, i, :]).then_inc(s.loaded, 16)

            @block.gpsimd
            def _(pool):
                nc.gpsimd.memset(w.state[:, :], 0.0)
                nc.gpsimd.memset(w.cm[:, :, :], 0.0).then_inc(s.zeroed, 1)

            @block.tensor
            def _(pe):
                pe.wait_ge(s.loaded, 64)
                for b in range(DB):
                    for i in range(2):
                        t = nc.tensor.transpose(m.bank[b // 2][:, ((b % 2) * 2 + i) * P:((b % 2) * 2 + i + 1) * P],
                                                w.hin[:, b, i, :, :], c("ident"))
                t.then_inc(s.turned, 1)

            @block.vector
            def _(dve):
                dve.wait_ge(s.zeroed, 1)
                nc.vector.tensor_copy(bass.AP(w.cm[:, :, :].tensor, 0, [[DB * NS, P], [NS + DS, DB], [1, DS]]),
                                      m.xc[:, 5, SEQ:TOK].rearrange("p (b t) -> p b t", b=DB))
                dve.wait_ge(s.turned, 1)
                for k in range(4):
                    nc.vector.tensor_copy(w.s0[:, 2 * k:2 * k + 2, :], m.bank[k][:, :].rearrange("p (b x) -> p b x", b=2))

    with nc.Fori(0, NT // PER) as turn:
        chunks = []
        for j in range(PER):
            i = turn * PER + j
            flat = lambda ap: ap.rearrange("p o c -> p (o c)")
            chunks.append(named(rows=P, sample=False, xc=m.xc[:, :, bass.ds(i * P, P)],
                               dt=flat(m.dt[:, bass.ds(i, 1), :]), z=flat(m.pz[:, bass.ds(i, 1), PZ_Z:PZ_Z + DSSD]),
                               out=flat(m.mix[:, bass.ds(i, 1), DATT:DM])))
        ssd_chunks(nc, m, w, chunks)
    ssd_chunks(nc, m, w, [named(rows=NS, sample=True, xc=m.xc[:, :, SEQ:TOK], dt=m.dt[0:NS, NT, :],
                               z=m.pz[0:NS, NT, PZ_Z:PZ_Z + DSSD], out=m.mix[0:NS, NT, DATT:DM])])

    with stage(nc, "dta_ready sums_ready decayed b_ready multiplied scaled added turned taken stored") as s:
        with nc.Block() as block:
            @block.tensor
            def _(pe):
                pe.wait_ge(s.dta_ready, 1)
                nc.tensor.matmul(m.bank[7][:, 0:64], c("ones")[0:NS, :], w.db[:, :, :], start=True,
                                 stop=True).then_inc(s.sums_ready, 1)
                pe.wait_ge(s.b_ready, 1)
                for b in range(DB):
                    if b >= 4:
                        pe.wait_ge(s.added, b - 3)
                    nc.tensor.matmul(m.bank[b % 4][:, :], w.bm[:, b, :], w.xe[0:NS, :], start=True,
                                     stop=True).then_inc(s.multiplied, 1)
                for b in range(DB + 1):
                    src = w.s0[:, b, :] if b < DB else w.state[:, :]
                    if b < DB:
                        pe.wait_ge(s.added, b + 1)
                    if b >= 2:
                        pe.wait_ge(s.taken, b - 1)
                    for i in range(2):
                        t = nc.tensor.transpose(m.bank[4 + b % 2][:, i * P:(i + 1) * P], src[:, i * P:(i + 1) * P],
                                                c("ident"))
                    t.then_inc(s.turned, 1)

            @block.scalar
            def _(act):
                act.wait_ge(s.sums_ready, 1)
                nc.scalar.activation(w.dec[:, :, :], m.bank[7][:, 0:64].rearrange("p (b h) -> p b h", b=DB),
                                     ACT.Exp).then_inc(s.decayed, 1)
                for b in range(DB + 1):
                    act.wait_ge(s.turned, b + 1)
                    dst = w.hout[:, b, :, :, :] if b < DB else w.hin[:, 0, :, :, :]
                    nc.scalar.activation(dst.rearrange("p i g n -> p (i g n)"), m.bank[4 + b % 2][:, 0:256],
                                         ACT.Copy).then_inc(s.taken, 1)

            @block.vector
            def _(dve):
                nc.vector.tensor_tensor(w.db[:, :, :], m.dt[0:NS, NT, 8:16].unsqueeze(1).broadcast_to([NS, DB, 8]),
                                        c("s_of_b")[0:NS, :].unsqueeze(2).broadcast_to([NS, DB, 8]),
                                        ALU.mult).then_inc(s.dta_ready, 1)
                nc.vector.tensor_tensor(w.bm[:, :, :], w.small[0:NS, 0, 0:P].unsqueeze(1).broadcast_to([NS, DB, P]),
                                        c("s_of_b")[0:NS, :].unsqueeze(2).broadcast_to([NS, DB, P]),
                                        ALU.mult).then_inc(s.b_ready, 1)
                dve.wait_ge(s.decayed, 1)
                for b in range(DB):
                    for g in range(NG):
                        st = w.s0[64 * g:64 * g + 64, b, :].rearrange("p (r d) -> p r d", r=4)
                        i = nc.vector.tensor_tensor(st, st, w.dec[64 * g:64 * g + 64, b, 4 * g:4 * g + 4].unsqueeze(
                            2).broadcast_to([64, 4, HD]), ALU.mult)
                    i.then_inc(s.scaled, 1)
                    dve.wait_ge(s.scaled, b + 1)
                    dve.wait_ge(s.multiplied, b + 1)
                    for g in range(NG):
                        i = nc.vector.tensor_tensor(w.s0[64 * g:64 * g + 64, b, :], w.s0[64 * g:64 * g + 64, b, :],
                                                    m.bank[b % 4][64 * g:64 * g + 64, 256 * g:256 * (g + 1)], ALU.add)
                    i.then_inc(s.added, 1)

            @block.sync
            def _(sp):
                sp.wait_ge(s.taken, DB + 1)
                for i in range(4):
                    sp.dma_start(hd(io.s_ssm)[:, :, i, :], w.hout[:, :, i % 2, i // 2, :]).then_inc(s.stored, 16)
                    sp.dma_start(hd(io.p_ssm)[:, 0, i, :], w.hin[:, 0, i % 2, i // 2, :]).then_inc(s.stored, 16)
                sp.wait_ge(s.stored, 16 * 8)


SUBS = PAGE // CSTRIDE
CW = CSTRIDE * DKV


def load_compression(nc, io, m, sb):
    w = m.cmp = Buffers()
    w.w1 = sb("cmp_w1", [P, 2, 8, 2, CHID])
    w.w2 = sb("cmp_w2", [CHID, 2, HD])
    w.pe = sb("cmp_pe", [P, 2, 16])
    w.pre = sb("cmp_pe_sum", [CHID, 2])
    with stage(nc, "loaded summed") as s:
        with nc.Block() as block:
            @block.sync
            def _(sp):
                for kv in range(2):
                    for j in range(2):
                        src = io.cmp_w1[0, kv, 16 * j:16 * (j + 1), :, :].rearrange("(q s) d h -> (s d) q h", s=2)
                        sp.dma_start(w.w1[:, kv, :, j, :], src).then_inc(s.loaded, 16)
                    sp.dma_start(w.w2[:, kv, :], io.cmp_w2[0, kv, :, :]).then_inc(s.loaded, 16)
                    sp.dma_start(w.pe[:, kv, :], io.cmp_pe[0, kv, :, :].rearrange("(q s) d -> (s d) q", s=2),
                                 allow_slow_non_contiguous=True).then_inc(s.loaded, 16)
                sp.wait_ge(s.loaded, 16 * 8)

            @block.tensor
            def _(pe):
                pe.wait_ge(s.loaded, 16 * 8)
                for kv in range(2):
                    for n in range(16):
                        mm = nc.tensor.matmul(m.bank[0][0:CHID, kv:kv + 1], w.w1[:, kv, n % 8, n // 8, :],
                                              w.pe[:, kv, n:n + 1], start=(n == 0), stop=(n == 15))
                mm.then_inc(s.summed, 1)

            @block.vector
            def _(dve):
                dve.wait_ge(s.summed, 1)
                nc.vector.tensor_copy(w.pre[:, :], m.bank[0][0:CHID, 0:2])


def stage_prompt_compress(nc, io, m):
    c = m.c
    sb = Region(nc, m.att_end, m.mix_start)
    N = SEQ // CSTRIDE
    m.kcT = sb("kcT", [P, N])
    m.vc = sb("vc", [N, DKV])
    m.bias = sb("bias", [P, NH, 256])
    m.prompt_att_start = sb.at
    load_compression(nc, io, m, sb)
    w = m.cmp
    x = sb("rows16", [N, 2, CW])
    xr = sb("rows16_by_group", [N, 2, CW])
    xt = sb("rows16_T", [P, 2, 8, NG, N])
    up = sb("second_half", [CHID, 2, NG, N])
    hid = sb("hidden", [CHID, 2, NG, N])
    kc = sb("kc_tok", [N, DKV])
    sq = sb("kc_square", [N, DKV])
    st = sb("kc_stats", [N, 6])
    with stage(nc, "loaded*2 grouped turned taken summed shifted added hidden_done projected kc_raw squared stats rstd "
                   "normed kc_turned bias_loaded zeroed act_c dve_c") as s:
        with nc.Block() as block:
            @block.sync
            def _(sp):
                for kv, src in enumerate((io.p_k_cmp, io.p_v_cmp)):
                    sp.dma_start(x[:, kv, :], src.rearrange("a b (n s) g d -> (a b n) (s g d)", s=CSTRIDE)
                                 ).then_inc(s.loaded[kv], 16)
                t = m.bias_dram.tensor
                sp.dma_start(m.bias[:, :, :], bass.AP(t, 127, [[BIASW - 1, P], [P * BIASW, NH], [1, 256]])).then_inc(s.bias_loaded, 16)
                sp.wait_ge(s.bias_loaded, 16)

            @block.gpsimd
            def _(pool):
                nc.gpsimd.memset(hid[:, :, :, :], 0.0).then_inc(s.zeroed, 1)

            @block.tensor
            def _(pe):
                for kv in range(2):
                    pe.wait_ge(s.grouped, kv + 1)
                    for a in range(4):
                        n = 4 * kv + a
                        if n >= 2:
                            pe.wait_ge(s.taken, n - 1)
                        for k in range(4):
                            g, q = k % 2, 2 * a + k // 2
                            t = nc.tensor.transpose(m.bank[n % 2][:, k * N:(k + 1) * N],
                                                    xr[:, kv, g * 1024 + q * P:g * 1024 + (q + 1) * P], c("ident")[0:N, 0:N])
                        t.then_inc(s.turned, 1)
                    pe.wait_ge(s.taken, 4 * kv + 4)
                    for q in range(8):
                        mm = nc.tensor.matmul(m.bank[2 + kv][:, 0:NG * N], w.w1[:, kv, q, :, :].rearrange("p j h -> p (j h)"),
                                              xt[:, kv, q, :, :], start=(q == 0), stop=(q == 7))
                    mm.then_inc(s.summed, 1)
                for kv in range(2):
                    pe.wait_ge(s.hidden_done, kv + 1)
                    for g in range(NG):
                        mm = nc.tensor.matmul(m.bank[4 + kv][0:N, g * HD:(g + 1) * HD], hid[:, kv, g, :], w.w2[:, kv, :],
                                              start=True, stop=True)
                    mm.then_inc(s.projected, 1)
                pe.wait_ge(s.normed, 1)
                nc.tensor.transpose(m.bank[6][:, 0:N], kc[:, :], c("ident")[0:N, 0:N]).then_inc(s.kc_turned, 1)

            @block.scalar
            def _(act):
                chain = Chain(act, s.act_c)
                act.wait_ge(s.zeroed, 1)
                for kv in range(2):
                    act.wait_ge(s.summed, kv + 1)
                    nc.scalar.activation(up[:, kv, :, :], m.bank[2 + kv][CHID:P, 0:NG * N].rearrange(
                        "p (g n) -> p g n", g=NG), ACT.Copy).then_inc(s.shifted, 1)
                    act.wait_ge(s.added, kv + 1)
                    nc.scalar.activation(hid[:, kv, :, 0:N - 1], up[:, kv, :, 0:N - 1], ACT.Silu,
                                         bias=w.pre[:, kv:kv + 1]).then_inc(s.hidden_done, 1)
                act.wait_ge(s.kc_raw, 1)
                nc.scalar.activation(sq[:, :], kc[:, :], ACT.Square).then_inc(s.squared, 1)
                act.wait_ge(s.stats, 1)
                chain(nc.scalar.activation(st[:, 2:4], st[:, 0:2], ACT.Ln, scale=1.0 / HD, bias=c("eps")[0:N, :]))
                nc.scalar.activation(st[:, 4:6], st[:, 2:4], ACT.Exp, scale=-0.5).then_inc(s.rstd, 1)

            @block.vector
            def _(dve):
                chain = Chain(dve, s.dve_c)
                for kv in range(2):
                    dve.wait_ge(s.loaded[kv], 16)
                    nc.vector.tensor_copy(xr[:, kv, :].rearrange("p (g s d) -> p g s d", g=NG, s=CSTRIDE),
                                          x[:, kv, :].rearrange("p (s g d) -> p g s d", g=NG, s=CSTRIDE)
                                          ).then_inc(s.grouped, 1)
                    for a in range(4):
                        n = 4 * kv + a
                        dve.wait_ge(s.turned, n + 1)
                        nc.vector.tensor_copy(xt[:, kv, 2 * a:2 * a + 2, :, :],
                                              m.bank[n % 2][:, 0:4 * N].rearrange("p (q g n) -> p q g n", q=2, g=NG)
                                              ).then_inc(s.taken, 1)
                for kv in range(2):
                    dve.wait_ge(s.shifted, kv + 1)
                    nc.vector.tensor_tensor(up[:, kv, :, 0:N - 1], up[:, kv, :, 1:N],
                                            m.bank[2 + kv][0:CHID, 0:NG * N].rearrange("p (g n) -> p g n", g=NG)[:, :, 0:N - 1],
                                            ALU.add).then_inc(s.added, 1)
                dve.wait_ge(s.projected, 2)
                nc.vector.tensor_copy(m.vc[:, :], m.bank[5][0:N, 0:DKV])
                nc.vector.tensor_copy(kc[:, :], m.bank[4][0:N, 0:DKV]).then_inc(s.kc_raw, 1)
                dve.wait_ge(s.squared, 1)
                nc.vector.tensor_reduce(st[:, 0:2], sq[:, :].rearrange("p (g d) -> p g d", g=NG), AX.X,
                                        ALU.add).then_inc(s.stats, 1)
                dve.wait_ge(s.rstd, 1)
                k3 = kc[:, :].rearrange("p (g d) -> p g d", g=NG)
                chain(nc.vector.tensor_tensor(k3, k3, st[:, 4:6].unsqueeze(2).broadcast_to([N, NG, HD]), ALU.mult))
                nc.vector.tensor_tensor(k3, k3, m.kn[0:N, :].unsqueeze(1).broadcast_to([N, NG, HD]),
                                        ALU.mult).then_inc(s.normed, 1)
                dve.wait_ge(s.kc_turned, 1)
                nc.vector.tensor_copy(m.kcT[:, :], m.bank[6][:, 0:N])


def stage_prompt_attention(nc, io, m):
    c = m.c
    assert SEQ // SELB <= 16
    sb = Region(nc, m.prompt_att_start, m.mix_start)
    qp = sb("q_padded", [P, NG, NT, P])
    psel = sb("p_sel", [P, 2, SEQ])
    pwc = sb("p_win_cmp", [P, 2, 768])
    pt = sb("p_T", [P, 4, 512])
    negmax = sb("neg_max", [P, NG * NT, 3])
    sums = sb("row_sums", [P, NG * NT, 3])
    scale = sb("row_scale", [P, NG * NT, 3])
    CMP, SEL, WINB = 0, 1, 2
    CC = 640
    units = [(t, g) for t in range(NT) for g in range(NG)]

    def parts(n):
        t, g = units[n // 2]
        if n % 2 == 0:
            return [(SEL, k, k * P, P) for k in range(t + 1)]
        lo = max(0, t - 4)
        return [(WINB, k, (k - lo) * P, P) for k in range(lo, t + 1)] + [(CMP, 0, CC, 8 * t + 7)]

    def groups(n):
        p = parts(n)
        return [p[i:i + 4] for i in range(0, len(p), 4)]

    first_group = [0]
    for n in range(2 * len(units)):
        first_group.append(first_group[-1] + len(groups(n)))

    with stage(nc, "zeroed") as s:
        with nc.Block() as block:
            @block.gpsimd
            def _(pool):
                nc.gpsimd.memset(qp[:, :, :, :], 0.0)

    with nc.Fori(0, REP) as r, stage(
            nc, "q_ready scored prepared exp_done turned copied_v copied_a weighted finished dve_c act_c") as s:
        with nc.Block() as block:
            @block.tensor
            def _(pe):
                def scores(n):
                    t, g = units[n // 2]
                    if n >= 2:
                        pe.wait_ge(s.exp_done, n - 1)
                    if n % 2 == 0:
                        for a in range(0, (t + 1) * P, 512):
                            b = min(a + 512, (t + 1) * P)
                            mm = nc.tensor.matmul(m.psum[:, a:b], qp[:, g, t, :], m.ksT[:, a:b], start=True, stop=True)
                    else:
                        lo = max(0, t - 4) * P
                        for a in range(lo, (t + 1) * P, 512):
                            b = min(a + 512, (t + 1) * P)
                            nc.tensor.matmul(m.psum[:, 1024 + a - lo:1024 + b - lo], qp[:, g, t, :], m.kwT[:, a:b],
                                             start=True, stop=True)
                        mm = nc.tensor.matmul(m.psum[:, 1024 + CC:1024 + CC + 8 * t + 7], qp[:, g, t, :],
                                              m.kcT[:, 0:8 * t + 7], start=True, stop=True)
                    mm.then_inc(s.scored, 1)

                def copied(G, at_least):
                    pe.wait_ge(s.copied_a if G % 2 else s.copied_v, at_least)

                def turn(n, i):
                    G = first_group[n] + i
                    src = psel if n % 2 == 0 else pwc
                    if G >= 2:
                        copied(G, G // 2)
                    for k, (_, _, col, width) in enumerate(groups(n)[i]):
                        x = nc.tensor.transpose(m.bank[4 + G % 2][0:width, k * P:(k + 1) * P],
                                                src[:, (n // 2) % 2, col:col + width], c("ident"))
                    x.then_inc(s.turned, 1)

                def weight(n, i):
                    t, g = units[n // 2]
                    G = first_group[n] + i
                    copied(G, G // 2 + 1)
                    lo = max(0, t - 4)
                    for k, (br, kt, col, width) in enumerate(groups(n)[i]):
                        v = (m.vc[0:width, g * HD:(g + 1) * HD] if br == CMP else
                             m.v[:, kt, 0 if br == SEL else 1, g * HD:(g + 1) * HD])
                        mm = nc.tensor.matmul(m.bank[6 + (n // 2) % 2][:, br * HD:(br + 1) * HD],
                                              pt[0:width, G % 4, k * P:(k + 1) * P], v,
                                              start=(br == CMP or kt == (0 if br == SEL else lo)),
                                              stop=(br == CMP or kt == t))
                    mm.then_inc(s.weighted, 1)

                pe.wait_ge(s.q_ready, 2)
                scores(0)
                scores(1)
                for n in range(2 * len(units)):
                    if n + 2 < 2 * len(units):
                        scores(n + 2)
                    pe.wait_ge(s.exp_done, n + 1)
                    if n % 2 == 0 and n >= 4:
                        pe.wait_ge(s.finished, n // 2 - 1)
                    k = len(groups(n))
                    for i in range(k):
                        turn(n, i)
                        if i:
                            weight(n, i - 1)
                    weight(n, k - 1)

            def copy_group(engine, sem, copy, n, i):
                G = first_group[n] + i
                engine.wait_ge(s.turned, G + 1)
                if G >= 4:
                    engine.wait_ge(s.weighted, G - 3)
                p = groups(n)[i]
                whole = [x for x in p if x[3] == P]
                if whole:
                    x = copy(pt[:, G % 4, 0:len(whole) * P], m.bank[4 + G % 2][:, 0:len(whole) * P])
                if len(whole) < len(p):
                    k, width = len(p) - 1, p[-1][3]
                    x = copy(pt[0:width, G % 4, k * P:(k + 1) * P], m.bank[4 + G % 2][0:width, k * P:(k + 1) * P])
                x.then_inc(sem, 1)

            @block.scalar
            def _(act):
                def exps(n):
                    t, g = units[n // 2]
                    u = n // 2
                    act.wait_ge(s.prepared, n + 1)
                    if n >= 4:
                        act.wait_ge(s.weighted, first_group[n - 3])
                    if n % 2 == 0:
                        act_ = nc.scalar.activation(psel[:, u % 2, 0:(t + 1) * P], m.psum[:, 0:(t + 1) * P], ACT.Exp,
                                                    bias=negmax[:, u, SEL:SEL + 1], accum_out=sums[:, u, SEL:SEL + 1])
                    else:
                        k = min(t, 4) + 1
                        nc.scalar.activation(pwc[:, u % 2, 0:k * P], m.psum[:, 1024:1024 + k * P], ACT.Exp,
                                             bias=negmax[:, u, WINB:WINB + 1], accum_out=sums[:, u, WINB:WINB + 1])
                        act_ = nc.scalar.activation(pwc[:, u % 2, CC:CC + 8 * t + 7], m.psum[:, 1024 + CC:1024 + CC + 8 * t + 7],
                                                    ACT.Exp, bias=negmax[:, u, CMP:CMP + 1],
                                                    accum_out=sums[:, u, CMP:CMP + 1])
                    act_.then_inc(s.exp_done, 1)

                exps(0)
                for n in range(2 * len(units)):
                    if n + 1 < 2 * len(units):
                        exps(n + 1)
                    for i in range(len(groups(n))):
                        if (first_group[n] + i) % 2:
                            copy_group(act, s.copied_a, lambda o, a: nc.scalar.activation(o, a, ACT.Copy), n, i)

            @block.vector
            def _(dve):
                chain = Chain(dve, s.dve_c)
                for g in range(NG):
                    rows = slice(64 * g, 64 * g + 64)
                    nc.vector.tensor_copy(qp[rows, g, :, :],
                                          m.qT[rows, :, bass.ds(r, 1), :].rearrange("p t o q -> p t (o q)")
                                          ).then_inc(s.q_ready, 1)

                def add(region, table):
                    chain(nc.vector.tensor_tensor(region, region, table, ALU.add))

                def top(region, u, br):
                    return nc.vector.tensor_reduce(negmax[:, u, br:br + 1], region, AX.X, ALU.max, negate=True)

                def prepare(n):
                    t, g = units[n // 2]
                    u = n // 2
                    bias = m.bias[:, bass.ds(g * REP + r, 1), :].rearrange("p o k -> p (o k)")
                    dve.wait_ge(s.scored, n + 1)
                    if n % 2 == 0:
                        lo = max(0, t - 1)
                        add(m.psum[:, lo * P:(t + 1) * P], bias[:, 0:256] if t else bias[:, P:256])
                        i = top(m.psum[:, 0:(t + 1) * P], u, SEL)
                    else:
                        k = min(t, 4) + 1
                        lo = max(0, k - 2)
                        add(m.psum[:, 1024 + lo * P:1024 + k * P], bias[:, 0:256] if t else bias[:, P:256])
                        if t >= 4:
                            add(m.psum[:, 1024:1024 + P], c("far"))
                        top(m.psum[:, 1024:1024 + k * P], u, WINB)
                        first = max(0, 8 * t - 9)
                        col = 159 + 16 * (first - 8 * t)
                        add(m.psum[:, 1024 + CC + first:1024 + CC + 8 * t + 7], bias[:, col:256:16])
                        chain(top(m.psum[:, 1024 + CC:1024 + CC + 8 * t + 7], u, CMP))
                        i = nc.vector.tensor_scalar(negmax[:, u, CMP:CMP + 1], negmax[:, u, CMP:CMP + 1], 1e29, None,
                                                    ALU.min)
                    i.then_inc(s.prepared, 1)

                def finish(u):
                    t, g = units[u]
                    out = m.mix[:, t, bass.ds((g * REP + r) * HD, HD)]
                    gate = m.gates[:, t, bass.ds((g * REP + r) * 3, 3)]
                    o = m.bank[6 + u % 2]
                    chain(nc.vector.tensor_scalar(scale[:, u, :], sums[:, u, :], 1e-30, None, ALU.max))
                    chain(nc.vector.reciprocal(scale[:, u, :], scale[:, u, :]))
                    chain(nc.vector.tensor_tensor(scale[:, u, :], scale[:, u, :], gate, ALU.mult))
                    dve.wait_ge(s.weighted, first_group[2 * u + 2])
                    chain(nc.vector.tensor_scalar(out, o[:, 0:HD], scale[:, u, 0:1], None, ALU.mult))
                    chain(nc.vector.scalar_tensor_tensor(out, o[:, HD:2 * HD], scale[:, u, 1:2], out, ALU.mult, ALU.add))
                    nc.vector.scalar_tensor_tensor(out, o[:, 2 * HD:3 * HD], scale[:, u, 2:3], out, ALU.mult,
                                                   ALU.add).then_inc(s.finished, 1)

                prepare(0)
                for n in range(2 * len(units)):
                    if n + 1 < 2 * len(units):
                        prepare(n + 1)
                    for i in range(len(groups(n))):
                        if (first_group[n] + i) % 2 == 0:
                            copy_group(dve, s.copied_v, nc.vector.tensor_copy, n, i)
                    if n % 2:
                        dve.wait_ge(s.exp_done, n + 1)
                        finish(n // 2)


def prepare_sample_attention(nc, io, m, w):
    with stage(nc, "gates_out gates_in kept zeroed placed") as s:
        with nc.Block() as block:
            @block.sync
            def _(sp):
                rows = lambda o: o.rearrange("o b t g d -> (o b) t (g d)")
                for dst, old, new in ((io.s_k_win, io.cache_k_win, io.kw_new), (io.s_v_win, io.cache_v_win, io.vw_new)):
                    sp.dma_start(rows(dst)[:, 0:WIN - DS, :], rows(old)[:, DS:WIN, :]).then_inc(s.kept, 16)
                    sp.dma_start(rows(dst)[:, WIN - DS:WIN, :], new.rearrange("(b t) c -> b t c", b=DB)).then_inc(s.kept, 16)
                sp.dma_start(m.gate_dram, m.gates[0:NS, NT, :]).then_inc(s.gates_out, 16)
                sp.wait_ge(s.gates_out, 16)
                for hb in range(2):
                    for b in range(B4):
                        for g in range(NG):
                            src = bass.AP(m.gate_dram.tensor, (hb * 16 + b * DS) * 24 + g * 12, [[24, DS], [3, REP], [1, 3]])
                            sp.dma_start(w.gate[b * 32 + g * 16:b * 32 + g * 16 + 16, hb, :], src).then_inc(s.gates_in, 16)
                sp.wait_ge(s.gates_in, 16 * 16)
                sp.wait_ge(s.kept, 16 * 4)

            @block.gpsimd
            def _(pool):
                nc.gpsimd.memset(w.q_all[:, :, :, :], 0.0).then_inc(s.zeroed, 1)
                nc.gpsimd.memset(w.hid[:, :, :], 0.0)
                nc.gpsimd.memset(w.pc[:, :], 0.0)
                nc.gpsimd.memset(w.imp[:, :], 0.0)
                nc.gpsimd.memset(w.score[:, SCORES - 1:SCORES], 2e30)

            @block.vector
            def _(dve):
                dve.wait_ge(s.zeroed, 1)
                for g in range(NG):
                    rows = slice(64 * g, 64 * g + 64)
                    for b in range(B4):
                        for hb in range(2):
                            q0 = (hb * B4 + b) * DS
                            nc.vector.tensor_copy(
                                w.q_all[rows, hb, b, b * 32 + g * 16:b * 32 + g * 16 + 16].rearrange("p (t r) -> p r t", t=DS),
                                m.qTs[rows, :, q0:q0 + DS])


SCORES = PAST // SELB + 1
RING = 4


def sample_attention_turn(nc, io, m, w, hb):
    c = m.c
    NA, NB_, NC_ = 16, 8, 8
    caches = [io.cache_k_cmp, io.cache_v_cmp, io.cache_k_sel, io.cache_v_sel]
    chunks = [(caches[kv], b, h) for b in range(B4) for kv in range(2) for h in range(2)]
    chunks += [(caches[2], b, h) for h in range(2) for b in range(B4)]
    chunks += [(caches[3], b, h) for b in range(B4) for h in range(2)]
    fill_a = lambda u, i: 8 * u + i
    fill_b = lambda k, i: 64 + i if k == 0 else 70 + 4 * (k - 1) + i
    fill_k = lambda i: 68 + i
    fill_w = lambda b: 98 + b
    fill_p = lambda i: 102 + i
    PCMP, PWIN, PNEW, PSEL = 0, 2, 6, 8
    p_pieces = ([(w.pc, k * P, P) for k in range(2)] + [(w.sw, k * P, P) for k in range(4)] +
                [(w.ss, PAST, DS), (w.sw, WIN, DS)] + [(w.ss, k * P, P) for k in range(32)])

    with stage(nc, "rows_ready v_used win_loaded kn_ready q_ready grouped turned copied_v copied_a summed "
                   "shifted added hidden_done projected taken squared k_sums k_rstd k_normed c_scored c_ready c_exp "
                   "c_weights imp_done masked s_scored s_taken w_scored n_scored w_taken w_ready s_ready w_exp s_exp "
                   "p_final o_ready stored dve_c act_c") as s:
        with nc.Block() as block:
            @block.sync
            def _(sp):
                for dst, src in ((w.wk, io.cache_k_win), (w.wv, io.cache_v_win)):
                    v = src.rearrange("o b (p k) g d -> p (o b) (k g d)", k=4)
                    sp.dma_start(dst[:, :, :], v[:, bass.ds(hb * B4, B4), :]).then_inc(s.win_loaded, 16)
                vs = io.s_v_sel.rearrange("o b t g d -> t (o b) (g d)")
                vw = io.vw_new.rearrange("(b t) c -> t b c", b=DB)
                sp.dma_start(w.vn[:, :, 0, :], vs[:, bass.ds(hb * B4, B4), :]).then_inc(s.win_loaded, 16)
                sp.dma_start(w.vn[:, :, 1, :], vw[:, bass.ds(hb * B4, B4), :]).then_inc(s.win_loaded, 16)
                sp.wait_ge(s.o_ready, 1)
                for b in range(B4):
                    for g in range(NG):
                        dst = m.o_dram[bass.ds(hb * B4 * DS + b * DS, DS), :].rearrange("t (g r d) -> t g r d", g=NG, r=REP)
                        sp.dma_start(dst[:, g, :, :], w.os[g * 16:g * 16 + 16, b, g * HD:(g + 1) * HD]
                                     ).then_inc(s.stored, 16)
                sp.wait_ge(s.stored, 16 * 8)

            @block.gpsimd
            def _(pool):
                pool.wait_ge(s.rows_ready, 1)
                for n, (cache, b, h) in enumerate(chunks):
                    k = n - RING
                    if 0 <= k < NA:
                        pool.wait_ge(s.grouped, k + 1)
                    elif NA <= k < NA + NB_:
                        pool.wait_ge(s.turned, fill_b(k - NA, 3) + 1)
                    elif k >= 0:
                        pool.wait_ge(s.v_used, k - NA - NB_ + 1)
                    nc.gpsimd.indirect_dma_start(
                        w.ring[:, n % RING, :], None,
                        cache.rearrange("o n (a s) g d -> (o n a) (s g d)", s=CSTRIDE),
                        bass.IndirectOffsetOnAxis(ap=w.rows[:, 2 * b + h:2 * b + h + 1], axis=0)
                    ).then_inc(w.landed[n % RING], 16)

            def chunk_here(engine, n):
                engine.wait_ge(w.landed[n % RING], hb * (16 * len(chunks) // RING) + 16 * (n // RING + 1))

            @block.tensor
            def _(pe):
                def bank_free(f):
                    if f >= 2:
                        pe.wait_ge(s.copied_a if f % 2 else s.copied_v, f // 2)

                def turn(f, pieces):
                    bank_free(f)
                    for k, (src, width) in enumerate(pieces):
                        x = nc.tensor.transpose(m.bank[4 + f % 2][0:width, k * P:(k + 1) * P], src, c("ident"))
                    x.then_inc(s.turned, 1)

                def copied(f):
                    pe.wait_ge(s.copied_a if f % 2 else s.copied_v, f // 2 + 1)

                def turn_a(u, i):
                    n = 2 * u + i // 4
                    pe.wait_ge(s.grouped, n + 1)
                    a = i % 4
                    turn(fill_a(u, i), [(w.xr[:, n % 2, g * 1024 + q * P:g * 1024 + (q + 1) * P], P)
                                        for q in (2 * a, 2 * a + 1) for g in range(NG)])

                def project(u):
                    pe.wait_ge(s.hidden_done, u + 1)
                    if u >= 2:
                        pe.wait_ge(s.taken, u - 1)
                    for h in range(2):
                        for g in range(NG):
                            mm = nc.tensor.matmul(m.bank[2 + u % 2][:, (2 * h + g) * HD:(2 * h + g + 1) * HD],
                                                  w.hid[:, g, h * P:(h + 1) * P], m.cmp.w2[:, u % 2, :],
                                                  start=True, stop=True)
                    mm.then_inc(s.projected, 1)

                for i in range(8):
                    turn_a(0, i)
                for u in range(8):
                    if u >= 2:
                        pe.wait_ge(s.added, u - 1)
                    for q in range(8):
                        if q == 0:
                            copied(fill_a(u, 6))
                            copied(fill_a(u, 7))
                        mm = nc.tensor.matmul(m.bank[u % 2][:, :], m.cmp.w1[:, u % 2, q, :, :].rearrange("p j h -> p (j h)"),
                                              w.xt[:, u % 2, q, :, :], start=(q == 0), stop=(q == 7))
                        if q == 7:
                            mm.then_inc(s.summed, 1)
                        if u < 7:
                            turn_a(u + 1, q)
                    if u:
                        project(u - 1)
                project(7)

                def turn_b(k, i):
                    if i == 0:
                        chunk_here(pe, NA + k)
                    x = w.ring[:, (NA + k) % RING, :]
                    turn(fill_b(k, i), [(x[:, (4 * i + j) * P:(4 * i + j + 1) * P], P) for j in range(4)])

                for i in range(4):
                    turn_b(0, i)
                pe.wait_ge(s.k_normed, 1)
                for i in range(2):
                    turn(fill_k(i), [(w.kraw[:, (4 * i + j) * P:(4 * i + j + 1) * P], P) for j in range(4)])
                copied(fill_k(0))
                copied(fill_k(1))
                pe.wait_ge(s.q_ready, 1)
                for b in range(B4):
                    mm = nc.tensor.matmul(m.bank[6][:, 0:255], w.q[:, b, :], w.kcT[:, b * 256:b * 256 + 255],
                                          start=(b == 0), stop=(b == B4 - 1))
                mm.then_inc(s.c_scored, 1)
                for k in range(NB_):
                    if k == B4:
                        pe.wait_ge(s.s_taken, 4)
                    if k == 2:
                        pe.wait_ge(s.c_weights, 1)
                        nc.tensor.matmul(m.bank[7][:, 0:255], c("rep_sum"), w.pc[:, 0:255], start=True,
                                         stop=True).then_inc(s.imp_done, 1)
                    if k == 0:
                        pe.wait_ge(s.taken, 8)
                        pe.wait_ge(s.added, 8)
                    for i in range(4):
                        copied(fill_b(k, i))
                        mm = nc.tensor.matmul(m.bank[i][:, :], w.q[:, k % B4, :], w.kt[:, k % 2, i * 512:(i + 1) * 512],
                                              start=(k % B4 == 0), stop=(k % B4 == B4 - 1))
                        if i == 3:
                            mm.then_inc(s.s_scored, 1)
                        if k + 1 < NB_:
                            turn_b(k + 1, i)
                pe.wait_ge(s.win_loaded, 64)
                for b in range(B4):
                    turn(fill_w(b), [(w.wk[:, b, j * P:(j + 1) * P], P) for j in range(4)])
                pe.wait_ge(s.c_exp, 1)
                for b in range(B4):
                    copied(fill_w(b))
                    mm = nc.tensor.matmul(m.bank[6][:, :], w.q[:, b, :], w.kt[:, 0, b * 512:(b + 1) * 512],
                                          start=(b == 0), stop=(b == B4 - 1))
                mm.then_inc(s.w_scored, 1)
                pe.wait_ge(s.masked, 1)
                pe.wait_ge(s.kn_ready, 1)
                for br in range(2):
                    for b in range(B4):
                        mm = nc.tensor.matmul(m.bank[7][:, 4 * br:4 * br + 4], w.q[:, b, :], w.kn[:, br, b * DS:(b + 1) * DS],
                                              start=(b == 0), stop=(b == B4 - 1))
                mm.then_inc(s.n_scored, 1)
                pe.wait_ge(s.p_final, 3)
                for i in range(10):
                    turn(fill_p(i), [(src[:, col:col + width], width) for src, col, width in p_pieces[4 * i:4 * i + 4]])
                copied(fill_p(8))
                copied(fill_p(9))
                pe.wait_ge(s.w_taken, 2)
                for b in range(B4):
                    terms = [(w.pt[:, PCMP + h, :], w.vc[:, b, h, :]) for h in range(2)]
                    terms += [(w.pt[:, PWIN + k, :], w.wv[:, b, k * P:(k + 1) * P]) for k in range(4)]
                    terms += [(w.pt[0:DS, PNEW + br, :], w.vn[:, b, br, :]) for br in range(2)]
                    terms += [(w.pt[:, PSEL + k, :], None) for k in range(32)]
                    for n, (weights, v) in enumerate(terms):
                        h, k = divmod(n - PSEL, 16)
                        if v is None:
                            chunk = NA + NB_ + 2 * b + h
                            if k == 0:
                                chunk_here(pe, chunk)
                            v = w.ring[:, chunk % RING, k * P:(k + 1) * P]
                        mm = nc.tensor.matmul(m.bank[7][0:32, b * P:(b + 1) * P], weights[:, b * 32:(b + 1) * 32], v,
                                              start=(n == 0), stop=(n == len(terms) - 1))
                        if n >= PSEL and k == 15:
                            mm.then_inc(s.v_used, 1)

            def copy(engine, f, dst, src_view=None, width=P):
                act = engine is w.act
                engine.wait_ge(s.turned, f + 1)
                src = m.bank[4 + f % 2][0:width, :] if src_view is None else src_view(m.bank[4 + f % 2])
                x = nc.scalar.activation(dst, src, ACT.Copy) if act else nc.vector.tensor_copy(dst, src)
                x.then_inc(s.copied_a if act else s.copied_v, 1)

            def copy_a(engine, u, i):
                if i < 2 and u >= 2:
                    engine.wait_ge(s.summed, u - 1)
                h, a = divmod(i, 4)
                copy(engine, fill_a(u, i), w.xt[:, u % 2, 2 * a:2 * a + 2, :, h * P:(h + 1) * P],
                     lambda bank: bank[:, :].rearrange("p (q g n) -> p q g n", q=2, g=NG))

            def copy_b(engine, k, i):
                if k >= 2 and i < 2:
                    engine.wait_ge(s.s_scored, k - 1)
                copy(engine, fill_b(k, i), w.kt[:, k % 2, i * 512:(i + 1) * 512])

            def copy_w(engine, b):
                if b < 2:
                    engine.wait_ge(s.s_scored, NB_ - 1)
                copy(engine, fill_w(b), w.kt[:, 0, b * 512:(b + 1) * 512])

            def copy_p(engine, i):
                if i == 1:
                    engine.wait_ge(s.turned, fill_p(1) + 1)
                    bank = m.bank[4 + fill_p(1) % 2]
                    nc.scalar.activation(w.pt[:, 4:6, :].rearrange("p a b -> p (a b)"), bank[:, 0:256], ACT.Copy)
                    nc.scalar.activation(w.pt[0:DS, 6:8, :].rearrange("p a b -> p (a b)"), bank[0:DS, 256:512],
                                         ACT.Copy).then_inc(s.copied_a, 1)
                else:
                    copy(engine, fill_p(i), w.pt[:, 4 * i:4 * i + 4, :].rearrange("p a b -> p (a b)"))

            @block.scalar
            def _(act):
                w.act = act
                chain = Chain(act, s.act_c)
                nc.scalar.activation(w.q[:, :, :], w.q_all[:, bass.ds(hb, 1), :, :].rearrange("p o b q -> p (o b) q"),
                                     ACT.Copy).then_inc(s.q_ready, 1)
                for i in (1, 3, 5, 7):
                    copy_a(act, 0, i)
                for u in range(8):
                    if u < 7:
                        for i in (1, 3, 5, 7):
                            copy_a(act, u + 1, i)
                    act.wait_ge(s.summed, u + 1)
                    if u >= 1:
                        act.wait_ge(s.hidden_done, u)
                    nc.scalar.activation(w.up[:, :, :], m.bank[u % 2][CHID:P, :].rearrange("p (g n) -> p g n", g=NG),
                                         ACT.Copy).then_inc(s.shifted, 1)
                    act.wait_ge(s.added, u + 1)
                    if u >= 1:
                        act.wait_ge(s.projected, u)
                    nc.scalar.activation(w.hid[:, :, 0:255], w.up[:, :, 0:255], ACT.Silu,
                                         bias=m.cmp.pre[:, u % 2:u % 2 + 1]).then_inc(s.hidden_done, 1)
                for i in (1, 3):
                    copy_b(act, 0, i)
                act.wait_ge(s.taken, 7)
                act.wait_ge(s.turned, 64)
                nc.scalar.activation(w.sq[:, :], w.kraw[:, :], ACT.Square).then_inc(s.squared, 1)
                act.wait_ge(s.k_sums, 1)
                chain(nc.scalar.activation(w.kst[:, 16:32], w.kst[:, 0:16], ACT.Ln, scale=1.0 / HD, bias=c("eps")))
                nc.scalar.activation(w.kst[:, 32:48], w.kst[:, 16:32], ACT.Exp, scale=-0.5).then_inc(s.k_rstd, 1)
                copy(act, fill_k(1), w.kcT[:, 512:1024])
                act.wait_ge(s.c_ready, 1)
                nc.scalar.activation(w.pc[:, 0:255], m.bank[6][:, 0:255], ACT.Exp, bias=w.nm[:, 0:1],
                                     accum_out=w.sum[:, 0:1]).then_inc(s.c_exp, 1)
                for k in range(1, NB_):
                    for i in (1, 3):
                        copy_b(act, k, i)
                for b in (1, 3):
                    copy_w(act, b)
                act.wait_ge(s.w_ready, 1)
                nc.scalar.activation(w.sw[:, :], w.sw[:, :], ACT.Exp, bias=w.nm[:, 1:2],
                                     accum_out=w.sum[:, 1:2]).then_inc(s.w_exp, 1)
                act.wait_ge(s.s_ready, 1)
                nc.scalar.activation(w.ss[:, :], w.ss[:, :], ACT.Exp, bias=w.nm[:, 2:3],
                                     accum_out=w.sum[:, 2:3]).then_inc(s.s_exp, 1)
                for i in (1, 3, 5, 7, 9):
                    copy_p(act, i)
                act.wait_ge(s.v_used, 8)
                nc.scalar.activation(w.os[:, :, :].rearrange("p b x -> p (b x)"), m.bank[7][0:32, :],
                                     ACT.Copy).then_inc(s.o_ready, 1)

            @block.vector
            def _(dve):
                chain = Chain(dve, s.dve_c)
                nc.vector.tensor_copy(w.rows[:, :], m.rows[:, bass.ds(hb * 2 * B4, 2 * B4)]).then_inc(s.rows_ready, 1)
                nc.vector.tensor_copy(w.kn[:, 0, :], m.ksTs[:, bass.ds(hb * 16, 16)])
                nc.vector.tensor_copy(w.kn[:, 1, :], m.kwTs[:, bass.ds(hb * 16, 16)]).then_inc(s.kn_ready, 1)
                nc.vector.tensor_copy(w.gt[:, :], w.gate[:, bass.ds(hb, 1), :].rearrange("p o x -> p (o x)"))

                def group(n):
                    chunk_here(dve, n)
                    if n >= 2:
                        dve.wait_ge(s.turned, 4 * (n - 1))
                    nc.vector.tensor_copy(w.xr[:, n % 2, :].rearrange("p (g s d) -> p g s d", g=NG, s=CSTRIDE),
                                          w.ring[:, n % RING, :].rearrange("p (s g d) -> p g s d", g=NG, s=CSTRIDE)
                                          ).then_inc(s.grouped, 1)

                def take(u):
                    dve.wait_ge(s.projected, u + 1)
                    dst = (w.kraw[:, (u // 2) * 256:(u // 2 + 1) * 256] if u % 2 == 0 else
                           w.vc[:, u // 2, :, :].rearrange("p h x -> p (h x)"))
                    nc.vector.tensor_copy(dst, m.bank[2 + u % 2][:, 0:256]).then_inc(s.taken, 1)

                group(0)
                group(1)
                for i in (0, 2, 4, 6):
                    copy_a(dve, 0, i)
                for u in range(8):
                    if u < 7:
                        group(2 * u + 2)
                        for i in (0, 2):
                            copy_a(dve, u + 1, i)
                        group(2 * u + 3)
                        for i in (4, 6):
                            copy_a(dve, u + 1, i)
                    if u:
                        take(u - 1)
                    dve.wait_ge(s.shifted, u + 1)
                    nc.vector.tensor_tensor(w.up[:, :, 0:255], w.up[:, :, 1:256],
                                            m.bank[u % 2][0:CHID, :].rearrange("p (g n) -> p g n", g=NG)[:, :, 0:255],
                                            ALU.add).then_inc(s.added, 1)
                take(7)
                for i in (0, 2):
                    copy_b(dve, 0, i)
                dve.wait_ge(s.squared, 1)
                nc.vector.tensor_reduce(w.kst[:, 0:16], w.sq[:, :].rearrange("p (a d) -> p a d", d=HD), AX.X,
                                        ALU.add).then_inc(s.k_sums, 1)
                dve.wait_ge(s.k_rstd, 1)
                k3 = w.kraw[:, :].rearrange("p (a d) -> p a d", d=HD)
                chain(nc.vector.tensor_tensor(k3, k3, w.kst[:, 32:48].unsqueeze(2).broadcast_to([P, 16, HD]), ALU.mult))
                nc.vector.tensor_tensor(k3, k3, m.kn[:, :].unsqueeze(1).broadcast_to([P, 16, HD]),
                                        ALU.mult).then_inc(s.k_normed, 1)
                copy(dve, fill_k(0), w.kcT[:, 0:512])
                dve.wait_ge(s.c_scored, 1)
                near = m.bank[6][:, 247:255]
                chain(nc.vector.tensor_tensor(near, near, m.srow[:, 15:128:16], ALU.add))
                nc.vector.tensor_reduce(w.nm[:, 0:1], m.bank[6][:, 0:255], AX.X, ALU.max,
                                        negate=True).then_inc(s.c_ready, 1)
                for k in (1,):
                    for i in (0, 2):
                        copy_b(dve, k, i)
                dve.wait_ge(s.c_exp, 1)
                chain(nc.vector.tensor_scalar(w.rs[:, 0:1], w.sum[:, 0:1], 1e-30, None, ALU.max))
                chain(nc.vector.reciprocal(w.rs[:, 0:1], w.rs[:, 0:1]))
                nc.vector.tensor_scalar(w.pc[:, 0:255], w.pc[:, 0:255], w.rs[:, 0:1], None, ALU.mult
                                        ).then_inc(s.c_weights, 1)
                for i in (0, 2):
                    copy_b(dve, 2, i)
                dve.wait_ge(s.imp_done, 1)
                chain(nc.vector.tensor_copy(w.imp[:, 1:256], m.bank[7][:, 0:255]))
                chain(nc.vector.tensor_reduce(w.score[:, 0:64], w.imp[:, 1:257].rearrange("p (j x) -> p j x", x=4),
                                              AX.X, ALU.add))
                chain(nc.vector.tensor_tensor(w.score[:, 0:64], w.score[:, 0:64], w.imp[:, 0:256:4], ALU.add))
                chain(nc.vector.memset(w.score[:, 0:64:63], 1e30))
                chain(nc.vector.max(w.top[:, 0:8], w.score[:, :]))
                chain(nc.vector.match_replace(w.left[:, :], w.top[:, 0:8], w.score[:, :], -1.0))
                chain(nc.vector.max(w.top[:, 8:16], w.left[:, :]))
                chain(nc.vector.match_replace(w.left[:, :], w.top[:, 8:16], w.left[:, :], -1.0))
                nc.vector.tensor_scalar(w.mask[:, :], w.left[:, 0:64], 0.0, NEG, ALU.is_ge, ALU.mult).then_inc(s.masked, 1)
                nc.vector.tensor_scalar(w.pc[:, 0:255], w.pc[:, 0:255], w.gt[:, 0:1], None,
                                        ALU.mult).then_inc(s.p_final, 1)
                dve.wait_ge(s.masked, 1)
                dve.wait_ge(s.p_final, 1)
                for k in (3,):
                    for i in (0, 2):
                        copy_b(dve, k, i)

                def take_scores(h):
                    dve.wait_ge(s.s_scored, 4 * (h + 1))
                    for i in range(4):
                        nc.vector.tensor_tensor(
                            w.ss[:, h * 2048 + i * 512:h * 2048 + (i + 1) * 512].rearrange("p (s j x) -> p s j x", s=4, x=4),
                            m.bank[i][:, :].rearrange("p (s j x) -> p s j x", s=4, x=4),
                            w.mask[:, 32 * h:32 * h + 32].unsqueeze(1).unsqueeze(3).broadcast_to([P, 4, 32, 4]),
                            ALU.add).then_inc(s.s_taken, 1)

                for i in (0, 2):
                    copy_b(dve, 4, i)
                take_scores(0)
                for k in range(5, NB_):
                    for i in (0, 2):
                        copy_b(dve, k, i)
                for b in (0, 2):
                    copy_w(dve, b)
                dve.wait_ge(s.w_scored, 1)
                nc.vector.tensor_copy(w.sw[:, 0:WIN], m.bank[6][:, :]).then_inc(s.w_taken, 1)
                dve.wait_ge(s.n_scored, 1)
                nc.vector.tensor_tensor(w.sw[:, WIN:WIN + DS], m.bank[7][:, 4:8], m.srow[:, P:P + DS], ALU.add)
                nc.vector.tensor_tensor(w.ss[:, PAST:PAST + DS], m.bank[7][:, 0:4], m.srow[:, P:P + DS],
                                        ALU.add).then_inc(s.w_taken, 1)
                dve.wait_ge(s.w_taken, 2)
                old = w.sw[:, 0:WIN].rearrange("p (k n) -> p k n", k=4)
                chain(nc.vector.tensor_tensor(old[:, :, 0], old[:, :, 0], c("win_old"), ALU.add))
                chain(nc.vector.tensor_tensor(old[:, :, 96:128], old[:, :, 96:128],
                                              m.srow[:, 0:P].rearrange("p (n k) -> p k n", k=4), ALU.add))
                nc.vector.tensor_reduce(w.nm[:, 1:2], w.sw[:, :], AX.X, ALU.max, negate=True).then_inc(s.w_ready, 1)
                take_scores(1)
                dve.wait_ge(s.s_taken, 8)
                near = w.ss[:, 2048:4096].rearrange("p (s n) -> p s n", s=16)[:, :, 120:128]
                chain(nc.vector.tensor_tensor(near, near, m.srow[:, 0:P].rearrange("p (n s) -> p s n", s=16), ALU.add))
                nc.vector.tensor_reduce(w.nm[:, 2:3], w.ss[:, :], AX.X, ALU.max, negate=True).then_inc(s.s_ready, 1)
                for k, (buf, done) in enumerate(((w.sw, s.w_exp), (w.ss, s.s_exp))):
                    a = slice(k + 1, k + 2)
                    dve.wait_ge(done, 1)
                    chain(nc.vector.tensor_scalar(w.rs[:, a], w.sum[:, a], 1e-30, None, ALU.max))
                    chain(nc.vector.reciprocal(w.rs[:, a], w.rs[:, a]))
                    gate = w.gt[:, 2:3] if k == 0 else w.gt[:, 1:2]
                    nc.vector.tensor_scalar(buf[:, :], buf[:, :], w.rs[:, a], gate, ALU.mult,
                                            ALU.mult).then_inc(s.p_final, 1)
                for i in (0, 2, 4, 6, 8):
                    copy_p(dve, i)


def stage_sample_attention(nc, io, m):
    sb = Region(nc, m.sample_end, m.mix_start)
    m.gate_dram = nc.dram_tensor("gates_by_token", (NS, 3 * NH), F32, kind="Internal").ap()
    m.o_dram = nc.dram_tensor("attention_by_token", (NS, DATT), F32, kind="Internal").ap()
    w = Buffers()
    load_compression(nc, io, m, sb)
    w.ring = sb("cache_ring", [P, RING, CW])
    both = sb("rows_T_or_weights_T", [P, 2 * 8 * NG * 256])
    w.xt = both[:, :].rearrange("p (u q g n) -> p u q g n", u=2, q=8, g=NG)
    w.pt = both[:, 0:40 * P].rearrange("p (k n) -> p k n", k=40)
    both = sb("rows_grouped_or_scores", [P, PAST + DS])
    w.xr = both[:, 0:2 * CW].rearrange("p (k x) -> p k x", k=2)
    w.sq = both[:, 0:1024]
    w.ss = both[:, :]
    w.kt = sb("keys_T", [P, 2, CW])
    w.wk = sb("win_k", [P, B4, 4 * DKV])
    w.wv = sb("win_v", [P, B4, 4 * DKV])
    w.vn = sb("new_v", [DS, B4, 2, DKV])
    w.kn = sb("new_k", [P, 2, 16])
    w.up = sb("second_half_s", [CHID, NG, 256])
    w.hid = sb("hidden_s", [CHID, NG, 256])
    w.kraw = sb("kc_s", [P, 1024])
    w.kcT = sb("kcT_s", [P, 1024])
    w.vc = sb("vc_s", [P, B4, 2, DKV])
    w.kst = sb("kc_stats_s", [P, 48])
    w.pc = sb("p_cmp_s", [P, 256])
    w.imp = sb("importance", [P, 257])
    w.score = sb("score", [P, SCORES])
    w.left = sb("not_selected", [P, SCORES])
    w.top = sb("top", [P, 16])
    w.mask = sb("block_mask", [P, 64])
    w.sw = sb("p_win_s", [P, WIN + DS])
    w.os = sb("out_s", [32, B4, P])
    w.q_all = sb("q_padded_all", [P, 2, B4, P])
    w.q = sb("q_padded_s", [P, B4, P])
    w.gate = sb("gate_rows", [P, 2, 3])
    w.gt = sb("gate_rows_now", [P, 3])
    w.rows = sb("rows_now", [P, 2 * B4], U32)
    w.nm = sb("neg_max_s", [P, 3])
    w.sum = sb("row_sums_s", [P, 3])
    w.rs = sb("row_scale_s", [P, 3])
    prepare_sample_attention(nc, io, m, w)
    with ExitStack() as ctx:
        w.landed = [ctx.enter_context(nc.semaphore(f"ring_landed_{i}")) for i in range(RING)]
        with nc.Fori(0, 2) as hb:
            sample_attention_turn(nc, io, m, w, hb)
    with stage(nc, "loaded") as s:
        with nc.Block() as block:
            @block.sync
            def _(sp):
                sp.dma_start(m.mix[0:NS, NT, 0:DATT], m.o_dram).then_inc(s.loaded, 16)
                sp.wait_ge(s.loaded, 16)


def finish_mixer(nc, m, w, tiles):
    c = m.c
    n = len(tiles)
    with stage(nc, "x_loaded*2 w_loaded copied turned mT_ready mixed h_ready h_normed h_turned u_taken h_rstd act_c") as s:
        with nc.Block() as block:
            @block.sync
            def _(sp):
                for j in range(n):
                    if j >= 2:
                        sp.wait_ge(s.h_ready, 2 * (j - 1))
                    sp.dma_start(w.x[0:tiles[j].rows, j % 2, :], tiles[j].x).then_inc(s.x_loaded[j % 2], 16)

            @block.scalar
            def _(act):
                chain = Chain(act, s.act_c)

                def statistics(j):
                    t, r = tiles[j], tiles[j].rows
                    act.wait_ge(s.h_ready, 2 * j + 2)
                    chain(nc.scalar.activation(w.junk[0:r, :], t.mix, ACT.Square, accum_out=w.ss[0:r, 0:1]))
                    chain(nc.scalar.activation(w.ss[0:r, 1:2], w.ss[0:r, 0:1], ACT.Ln, scale=1.0 / DM,
                                               bias=c("eps")[0:r, :]))
                    nc.scalar.activation(w.ss[0:r, 2 + j % 2:3 + j % 2], w.ss[0:r, 1:2], ACT.Exp,
                                         scale=-0.5).then_inc(s.h_rstd, 1)

                for j in range(n):
                    t, r = tiles[j], tiles[j].rows
                    if j >= 2:
                        act.wait_ge(s.turned, 2 * (j - 1))
                    nc.scalar.activation(w.mt[0:r, j % 2, :], t.mix, ACT.Copy).then_inc(s.copied, 1)
                    if j >= 1:
                        statistics(j - 1)
                statistics(n - 1)

            @block.tensor
            def _(pe):
                def turn(src, j, banks, sem):
                    r = tiles[j].rows
                    for k in range(KT):
                        i = nc.tensor.transpose(m.bank[banks[k // 4]][:, (k % 4) * P:(k % 4) * P + r],
                                                src[0:r, j % 2, k * P:(k + 1) * P], c("ident")[0:r, 0:r])
                        if k % 4 == 3:
                            i.then_inc(sem, 1)

                def turn_mix(j):
                    pe.wait_ge(s.copied, j + 1)
                    if j >= 1:
                        pe.wait_ge(s.mT_ready, 2 * j)
                    turn(w.mt, j, (6, 7), s.turned)

                def turn_h(j):
                    pe.wait_ge(s.h_normed, j + 1)
                    if j >= 1:
                        pe.wait_ge(s.u_taken, 2 * j)
                    turn(w.hn, j, (4, 5), s.h_turned)

                turn_mix(0)
                for j in range(n):
                    r = tiles[j].rows
                    if j + 1 < n:
                        turn_mix(j + 1)
                    pe.wait_ge(s.mT_ready, 2 * j + 2)
                    if j >= 2:
                        pe.wait_ge(s.h_ready, 2 * (j - 1))
                    for h in range(2):
                        for k in range(KT):
                            mm = nc.tensor.matmul(m.bank[2 * (j % 2) + h][0:r, :], w.mT[:, j % 2, k, 0:r],
                                                  w.w[:, k, h * 512:(h + 1) * 512], start=(k == 0), stop=(k == KT - 1))
                        mm.then_inc(s.mixed, 1)
                    if j >= 1:
                        turn_h(j - 1)
                turn_h(n - 1)

            @block.vector
            def _(dve):
                def take_mix(j):
                    r = tiles[j].rows
                    for h in range(2):
                        dve.wait_ge(s.turned, 2 * j + h + 1)
                        if j >= 2:
                            dve.wait_ge(s.mixed, 2 * (j - 1))
                        nc.vector.tensor_copy(w.mT[:, j % 2, 4 * h:4 * h + 4, 0:r],
                                              m.bank[6 + h][:, :].rearrange("p (k q) -> p k q", k=4)[:, :, 0:r]
                                              ).then_inc(s.mT_ready, 1)

                def take_u(j):
                    t, r = tiles[j], tiles[j].rows
                    dve.wait_ge(s.h_rstd, j + 1)
                    if j >= 2:
                        dve.wait_ge(s.h_turned, 2 * (j - 1))
                    nc.vector.tensor_scalar(w.hn[0:r, j % 2, :], t.mix, w.ss[0:r, 2 + j % 2:3 + j % 2], None,
                                            ALU.mult).then_inc(s.h_normed, 1)
                    for h in range(2):
                        dve.wait_ge(s.h_turned, 2 * j + h + 1)
                        nc.vector.tensor_tensor(t.u[h], m.bank[4 + h][:, :].rearrange("p (k q) -> p k q", k=4)[:, :, 0:r],
                                                m.gffn[:, 4 * h:4 * h + 4].unsqueeze(2).broadcast_to([P, 4, r]),
                                                ALU.mult).then_inc(s.u_taken, 1)

                take_mix(0)
                for j in range(n):
                    t, r = tiles[j], tiles[j].rows
                    if j + 1 < n:
                        take_mix(j + 1)
                    dve.wait_ge(s.x_loaded[j % 2], 16 * (j // 2 + 1))
                    dve.wait_ge(s.copied, j + 1)
                    for h in range(2):
                        dve.wait_ge(s.mixed, 2 * j + h + 1)
                        nc.vector.tensor_tensor(t.mix[:, h * 512:(h + 1) * 512], m.bank[2 * (j % 2) + h][0:r, :],
                                                w.x[0:r, j % 2, h * 512:(h + 1) * 512], ALU.add).then_inc(s.h_ready, 1)
                    if j >= 1:
                        take_u(j - 1)
                take_u(n - 1)


def stage_finish_mixer(nc, io, m):
    m.gT_start = m.mix_start - 22 * TOK * 4
    m.u2 = nc.alloc_sbuf_tensor_at("u2", [P, KT, TOK], F32, offset=m.gT_start - KT * TOK * 4)
    sb = Region(nc, m.gT_start, m.mix_start)
    w = Buffers()
    w.w = sb("w_out", [P, KT, DM])
    w.x = sb("x_again", [P, 2, DM])
    w.mt = sb("mix_tile", [P, 2, DM])
    w.mT = sb("mixT", [P, 2, KT, P])
    w.hn = sb("h_tile", [P, 2, DM])
    w.junk = sb("junk2", [P, DM], mybir.dt.bfloat16)
    w.ss = sb("ss2", [P, 4])
    with stage(nc, "w_loaded") as s:
        with nc.Block() as block:
            @block.sync
            def _(sp):
                for k in range(KT):
                    sp.dma_start(w.w[:, k, :], io.w_out[0, k * P:(k + 1) * P, :]).then_inc(s.w_loaded, 16)
                sp.wait_ge(s.w_loaded, 16 * KT)
    xp = io.x_prompt.rearrange("o (n p) c -> p (o n) c", p=P)
    with nc.Fori(0, NT // PER) as turn:
        tiles = []
        for j in range(PER):
            i = turn * PER + j
            tiles.append(named(rows=P, x=xp[:, bass.ds(i, 1), :],
                              mix=m.mix[:, bass.ds(i, 1), :].rearrange("p o c -> p (o c)"),
                              u=[m.u2[:, 4 * h:4 * h + 4, bass.ds(i * P, P)] for h in range(2)]))
        finish_mixer(nc, m, w, tiles)
    finish_mixer(nc, m, w, [named(rows=NS, x=io.x_sample.rearrange("b t c -> (b t) c"), mix=m.mix[0:NS, NT, :],
                                 u=[m.u2[:, 4 * h:4 * h + 4, SEQ:TOK] for h in range(2)])])


FT = DFF // P
TCH = [(i * 352, (i + 1) * 352) for i in range(3)]


def stage_ffn_up(nc, io, m):
    U = 2
    sb = Region(nc, m.base_end, m.gT_start - KT * TOK * 4)
    wslot = sb("w_gate_up", [P, U, 2, KT, P])
    e = sb("exp_gate", [P, 3, 352])
    m.gT = nc.alloc_sbuf_tensor_at("gT", [P, FT, TOK], F32, offset=m.gT_start)
    wg = io.w_gate.rearrange("o (c p) (f q) -> p (o c) f q", p=P, q=P)
    wu = io.w_up.rearrange("o (c p) (f q) -> p (o c) f q", p=P, q=P)

    with stage(nc, "loaded") as s:
        with nc.Block() as block:
            @block.sync
            def _(sp):
                for f in range(U):
                    for a, src in enumerate((wg, wu)):
                        sp.dma_start(wslot[:, f, a, :, :], src[:, :, f, :]).then_inc(s.loaded, 16)
                sp.wait_ge(s.loaded, 16 * 2 * U)
    def body(turn, fetch):
        with stage(nc, "fetched multiplied exp_done piece_done dve_c") as s:
            with nc.Block() as block:
                @block.sync
                def _(sp):
                    for f in range(U if fetch else 0):
                        sp.wait_ge(s.multiplied, 6 * (f + 1))
                        for a, src in enumerate((wg, wu)):
                            sp.dma_start(wslot[:, f, a, :, :],
                                         src[:, :, bass.ds(turn * U + U + f, 1), :].rearrange("p c o q -> p (c o) q")
                                         ).then_inc(s.fetched, 16)
                    if fetch:
                        sp.wait_ge(s.fetched, 16 * 2 * U)

                @block.tensor
                def _(pe):
                    for f in range(U):
                        for t, (a, b) in enumerate(TCH):
                            n = 3 * f + t
                            if n >= 4:
                                pe.wait_ge(s.piece_done, n - 3)
                            for side in range(2):
                                for k in range(KT):
                                    mm = nc.tensor.matmul(m.bank[2 * (n % 4) + side][:, 0:352], wslot[:, f, side, k, :],
                                                          m.u2[:, k, a:b], start=(k == 0), stop=(k == KT - 1))
                                mm.then_inc(s.multiplied, 1)

                @block.scalar
                def _(act):
                    for n in range(3 * U):
                        act.wait_ge(s.multiplied, 2 * n + 1)
                        if n >= 3:
                            act.wait_ge(s.piece_done, n - 2)
                        nc.scalar.activation(e[:, n % 3, :], m.bank[2 * (n % 4)][:, 0:352], ACT.Exp,
                                             scale=-1.0).then_inc(s.exp_done, 1)

                @block.vector
                def _(dve):
                    chain = Chain(dve, s.dve_c)
                    for n in range(3 * U):
                        f, (a, b) = n // 3, TCH[n % 3]
                        x = e[:, n % 3, :]
                        dve.wait_ge(s.exp_done, n + 1)
                        chain(nc.vector.tensor_scalar(x, x, 1.0, None, ALU.add))
                        chain(nc.vector.reciprocal(x, x))
                        chain(nc.vector.tensor_tensor(x, x, m.bank[2 * (n % 4)][:, 0:352], ALU.mult))
                        dve.wait_ge(s.multiplied, 2 * n + 2)
                        nc.vector.tensor_tensor(
                            m.gT[:, bass.ds(turn * U + f, 1), a:b].rearrange("p o t -> p (o t)"), x,
                            m.bank[2 * (n % 4) + 1][:, 0:352], ALU.mult).then_inc(s.piece_done, 1)

    with nc.Fori(0, FT // U - 1) as turn:
        body(turn, fetch=True)
    body(FT // U - 1, fetch=False)


def stage_ffn_down(nc, io, m):
    NC, U = 256, 2
    sb = Region(nc, m.base_end, m.gT_start)
    wslot = sb("w_down", [P, U, FT, NC])
    y = sb("y_tile", [P, 4, NC])
    wd = io.w_down.rearrange("o (f p) n -> p (o f) n", p=P)
    yp = io.y_prompt.rearrange("o (n p) c -> p (o n) c", p=P)
    ysm = io.y_sample.rearrange("b t c -> (b t) c")
    with stage(nc, "loaded") as s:
        with nc.Block() as block:
            @block.sync
            def _(sp):
                for q in range(U):
                    sp.dma_start(wslot[:, q, :, :], wd[:, :, q * NC:(q + 1) * NC]).then_inc(s.loaded, 16)
                sp.wait_ge(s.loaded, 16 * U)
    for turn in range(DM // NC // U):
        fetch = turn == 0
        with stage(nc, "fetched multiplied y_ready stored*4") as s:
            units = [(q, t) for q in range(U) for t in range(NT + 1)]
            with nc.Block() as block:
                @block.sync
                def _(sp):
                    for i, (q, t) in enumerate(units):
                        rows = P if t < NT else NS
                        sp.wait_ge(s.y_ready, i + 1)
                        col = (turn * U + q) * NC
                        dst = yp[:, t, col:col + NC] if t < NT else ysm[:, col:col + NC]
                        sp.dma_start(dst, y[0:rows, i % 4, :]).then_inc(s.stored[i % 4], 16)
                        if t == NT and fetch:
                            ahead = (U + q) * NC
                            sp.dma_start(wslot[:, q, :, :], wd[:, :, ahead:ahead + NC]).then_inc(s.fetched, 16)
                    for k in range(4):
                        sp.wait_ge(s.stored[k], 16 * len(range(k, len(units), 4)))
                    if fetch:
                        sp.wait_ge(s.fetched, 16 * U)

                @block.tensor
                def _(pe):
                    for i, (q, t) in enumerate(units):
                        rows = P if t < NT else NS
                        if i >= 8:
                            pe.wait_ge(s.y_ready, i - 7)
                        for f in range(FT):
                            mm = nc.tensor.matmul(m.bank[i % 8][0:rows, 0:NC], m.gT[:, f, t * P:t * P + rows],
                                                  wslot[:, q, f, :], start=(f == 0), stop=(f == FT - 1))
                        mm.then_inc(s.multiplied, 1)

                @block.vector
                def _(dve):
                    for i, (q, t) in enumerate(units):
                        rows = P if t < NT else NS
                        dve.wait_ge(s.multiplied, i + 1)
                        if i >= 4:
                            dve.wait_ge(s.stored[i % 4], 16 * (i // 4))
                        nc.vector.tensor_tensor(y[0:rows, i % 4, :], m.bank[i % 8][0:rows, 0:NC],
                                                m.mix[0:rows, t, (turn * U + q) * NC:(turn * U + q + 1) * NC],
                                                ALU.add).then_inc(s.y_ready, 1)


class Region:

    def __init__(self, nc, start, end):
        self.nc, self.at, self.end = nc, start, end

    def __call__(self, name, shape, dtype=F32):
        size = int(np.prod(shape[1:])) * (2 if dtype == mybir.dt.bfloat16 else 4)
        t = self.nc.alloc_sbuf_tensor_at(name, list(shape), dtype, offset=self.at)
        self.at += -(-size // 32) * 32
        assert self.at <= self.end, (name, self.at, self.end)
        return t


class Memory:

    def __init__(self, nc):
        self.psum = nc.alloc_psum_tensor("banks", [P, 8 * 512], F32)
        self.bank = [self.psum[:, i * 512:(i + 1) * 512] for i in range(8)]
        start, end = -(-nc.sbuf_base // 32) * 32, nc.sbuf_usable_end // 32 * 32
        sb = Region(nc, start, end)
        self.consts = sb("consts", list(CONSTS.shape))
        self.gmix = sb("gmix", [P, KT])
        self.gffn = sb("gffn", [P, KT])
        self.qn = sb("qn", [P, HD])
        self.kn = sb("kn", [P, HD])
        self.convw = sb("convw", [P, 4, 6])
        self.convb = sb("convb", [P, 6])
        self.dtb = sb("dtb", [P, 8])
        self.alog = sb("alog", [P, 8])
        self.dskip = sb("dskip", [P, 8])
        self.ssdn = sb("ssdn", [P, DSSD])
        self.rows = sb("rows", [P, 2 * DB], U32)
        self.srow = sb("srow", [P, 132])
        self.gates = sb("gates", [P, NT + 1, 3 * NH])
        self.bias_dram = nc.dram_tensor("bias_by_distance", (NH, P, BIASW), F32, kind="Internal").ap()
        self.base_end = sb.at
        self.qTs = sb("qTs", [P, REP, NS])
        self.ksTs = sb("ksTs", [P, NS])
        self.kwTs = sb("kwTs", [P, NS])
        self.dt_start = sb.at
        sb("dt_place", [P, NT + 1, 16])
        self.sample_end = sb.at
        self.pz = sb("pz", [P, NT + 1, PZ])
        self.pz_end = sb.at
        self.qT_start = sb.at
        self.qT = sb("qT", [P, NT, REP, P])
        self.ksT = sb("ksT", [P, SEQ])
        self.kwT = sb("kwT", [P, SEQ])
        self.v = sb("v", [P, NT + 1, 2, DKV])
        self.att_end = sb.at
        self.end = end
        self.mix_start = end - (NT + 1) * DM * 4
        self.mix = nc.alloc_sbuf_tensor_at("mix", [P, NT + 1, DM], F32, offset=self.mix_start)

    def c(self, name):
        a, b = CONST_COLS[name]
        return self.consts[:, a:b]


def stage_setup(nc, io, m):
    sb = Region(nc, m.sample_end, m.end)
    m.relx = sb("relx", [NBUCK + 1, NH])
    m.onehot = sb("onehot", [NBUCK + 1, BIASW])
    m.biasrow = sb("biasrow", [NH, BIASW])
    m.pages = sb("pages", [16, 2 * DB], I32)
    m.pagef = sb("pagef", [16, 2 * DB])
    m.rowf = sb("rowf", [P, 2 * DB])

    load_setup(nc, io, m)


PER = 4


def stage_projection(nc, io, m):
    sb = Region(nc, m.att_end, m.end)
    w = Buffers()
    w.w = sb("w_in", [P, KT, DIN])
    w.x = sb("x_tile", [P, 2, DM])
    w.u = sb("u_tile", [P, 2, KT, P])
    w.q = sb("q_raw", [P, DATT])
    w.kv = sb("kv_raw", [P, 2, 6, DKV])
    w.qk = sb("qk_normed", [P, 2, 6, P])
    w.sq = sb("squares", [P, 768])
    w.junk = sb("junk", [P, DM], mybir.dt.bfloat16)
    w.ss = sb("ss", [P, 6])
    w.hs = sb("hs", [P, 36])
    tokens = lambda ap, i: ap.rearrange("(n p) c -> p n c", p=P)[:, bass.ds(i, 1), :]
    kv_rows = lambda o: o.rearrange("a b t g d -> (a b t) (g d)")
    with nc.Fori(0, NT // PER) as turn:
        tiles = []
        for j in range(PER):
            i = turn * PER + j
            tiles.append(named(
                rows=P, x=tokens(io.x_prompt.rearrange("o t c -> (o t) c"), i),
                kc=tokens(kv_rows(io.p_k_cmp), i), vc=tokens(kv_rows(io.p_v_cmp), i),
                ks=tokens(kv_rows(io.p_k_sel), i), vs=tokens(kv_rows(io.p_v_sel), i),
                kw=kv_rows(io.p_k_win)[j * P:(j + 1) * P, :], vw=kv_rows(io.p_v_win)[j * P:(j + 1) * P, :],
                qT=m.qT[:, bass.ds(i, 1), :, :].rearrange("p o r q -> p (o r) q"),
                ksT=m.ksT[:, bass.ds(i * P, P)], kwT=m.kwT[:, bass.ds(i * P, P)],
                v=m.v[:, bass.ds(i, 1), :, :].rearrange("p o b d -> p (o b) d"),
                pz=m.pz[:, bass.ds(i, 1), :].rearrange("p o c -> p (o c)"),
                gate=m.pz[:, bass.ds(i, 1), PZ_GATE:PZ].rearrange("p o c -> p (o c)")))
        w.first = True
        project(nc, io, m, w, tiles)
    w.first = False
    project(nc, io, m, w, [named(
        rows=NS, x=io.x_sample.rearrange("b t c -> (b t) c"), kc=kv_rows(io.s_k_cmp), vc=kv_rows(io.s_v_cmp),
        ks=kv_rows(io.s_k_sel), vs=kv_rows(io.s_v_sel), kw=io.kw_new, vw=io.vw_new,
        qT=m.qTs[:, :, :], ksT=m.ksTs[:, :], kwT=m.kwTs[:, :], v=m.v[0:NS, NT, :, :], pz=m.pz[0:NS, NT, :],
        gate=m.pz[0:NS, NT, PZ_GATE:PZ])])


def program(nc, io):
    m = Memory(nc)
    for f in STAGES:
        f(nc, io, m)


STAGES = [stage_setup, stage_projection, stage_pointwise, stage_prompt_compress,
          stage_prompt_attention, stage_conv, stage_ssd, stage_sample_attention,
          stage_finish_mixer, stage_ffn_up, stage_ffn_down]


_INS = ['x_prompt', 'x_sample', 'cache_k_cmp', 'cache_v_cmp', 'cache_k_sel', 'cache_v_sel', 'cache_k_win', 'cache_v_win',
        'state_conv', 'state_ssm', 'page_table', 'norm_mix', 'w_in', 'q_norm', 'k_norm', 'cmp_pe', 'cmp_w1', 'cmp_w2',
        'rel_bias', 'conv_w', 'conv_b', 'dt_bias', 'a_log', 'd_skip', 'ssd_norm', 'w_out', 'norm_ffn', 'w_gate', 'w_up',
        'w_down']
_OUTS = [('y_prompt', (1, SEQ, DM)), ('y_sample', (DB, DS, DM))] + \
    [(f'p_{n}', (1, 1, SEQ, NG, HD)) for n in ('k_cmp', 'v_cmp', 'k_sel', 'v_sel')] + \
    [(f'p_{n}', (1, 1, WIN, NG, HD)) for n in ('k_win', 'v_win')] + \
    [('p_conv', (1, 1, 3, DCONV)), ('p_ssm', (1, 1, 8, HD, HD))] + \
    [(f's_{n}', (1, DB, DS, NG, HD)) for n in ('k_cmp', 'v_cmp', 'k_sel', 'v_sel')] + \
    [(f's_{n}', (1, DB, WIN, NG, HD)) for n in ('k_win', 'v_win')] + \
    [('s_conv', (1, DB, 3, DCONV)), ('s_ssm', (1, DB, 8, HD, HD))]


def kernel(**inputs):
    import numpy as _np
    import concourse.bacc as _bacc
    from concourse.bass_utils import run_bass_kernel_spmd as _run

    nc = _bacc.Bacc("TRN2", target_bir_lowering=False, num_devices=1)
    aps, arrays = {}, {}
    given = {name: inputs[name] for name in _INS}
    given["consts"], given["buckets"] = CONSTS, BUCKETS
    for name, a in given.items():
        a = _np.ascontiguousarray(a)
        arrays[f"in_{name}"] = a
        aps[name] = nc.dram_tensor(f"in_{name}", a.shape, mybir.dt.from_np(a.dtype), kind="ExternalInput").ap()
    for name, shape in _OUTS:
        aps[name] = nc.dram_tensor(f"out_{name}", shape, F32, kind="ExternalOutput").ap()
    for name in ("kw_new", "vw_new"):
        aps[name] = nc.dram_tensor(name, (NS, DKV), F32, kind="Internal").ap()
    program(nc, named(**aps))
    r = _run(nc, [arrays], core_ids=[0])
    return tuple(r.results[0][f"out_{name}"] for name, _ in _OUTS)
```

```python
import math
from collections import namedtuple
from contextlib import ExitStack, contextmanager

import numpy as np

import concourse.bass as bass
from concourse import mybir
from concourse.alu_op_type import AluOpType as ALU

ACT = mybir.ActivationFunctionType
AX = mybir.AxisListType
F32 = mybir.dt.float32
U32 = mybir.dt.uint32
I32 = mybir.dt.int32

P = 128
DM, SEQ, DB, DS, PAST, PAGE = 1024, 1024, 8, 4, 4096, 128
HD, NH, NG, REP = 64, 8, 2, 4
CSTRIDE, CHID, SELB, TOPN, WIN = 16, 64, 64, 15, 512
NBUCK, MAXDIST = 32, 128
DKV = NG * HD
DATT, DSSD, DCONV = NH * HD, 512, 768
DFF = 2816
OFF_GATE = DATT + 6 * DKV
OFF_Z = OFF_GATE + 3 * NH
OFF_XBC = OFF_Z + DSSD
OFF_DT = OFF_XBC + DCONV
DIN = OFF_DT + 8
EPS = 1e-6
NEG = -1e30
NT = SEQ // P
NS = DB * DS
KT = DM // P
TOK = SEQ + NS
B4 = 4
BIASW = 384
PZ_Z, PZ_XBC, PZ_DT, PZ_GATE = 0, DSSD, DSSD + DCONV, DSSD + DCONV + 8
PZ = PZ_GATE + 3 * NH

CONST_COLS = {}


def _shape_constants():
    p = np.arange(P)
    row_s = (p // REP) % DS
    t = np.arange(NS)
    parts = {
        "ident": np.eye(P),
        "ones": np.ones((P, P)),
        "tri": p[:, None] <= p[None, :],
        "after": np.where(p[:, None] <= p[None, :], 0.0, NEG),
        "far": np.where(p[None, :] > p[:, None], 0.0, NEG),
        "rep_sum": (p[:, None] // REP) == (p[None, :] // REP),
        "s_tri": np.pad(((t[:, None] // DS) == (t[None, :] // DS)) & (t[:, None] <= t[None, :]), ((0, P - NS), (0, 0))),
        "s_after": np.pad(np.where(((t[:, None] // DS) == (t[None, :] // DS)) & (t[:, None] <= t[None, :]), 0.0, NEG),
                          ((0, P - NS), (0, 0))),
        "s_ones": np.pad((t[:, None] // DS) == (t[None, :] // DS), ((0, P - NS), (0, 0))),
        "s_of_b": np.pad((t[:, None] // DS) == np.arange(DB)[None, :], ((0, P - NS), (0, 0))),
        "win_old": np.where(np.arange(4)[None, :] <= row_s[:, None], NEG, 0.0),
        "page_of": (8 * p[:, None] <= p[None, :]) & (p[None, :] < 8 * p[:, None] + 8),
        "p_mod": (p % 8)[:, None],
        "eps": np.full((P, 1), EPS),
        "zero": np.zeros((P, 1)),
        "one": np.ones((P, 1)),
    }
    at, out = 0, []
    for name, a in parts.items():
        CONST_COLS[name] = (at, at + a.shape[1])
        at += a.shape[1]
        out.append(np.asarray(a, np.float32))
    return np.concatenate(out, axis=1)


def _bucket_columns():
    oh = np.zeros((NBUCK + 1, BIASW), np.float32)
    for y in range(BIASW):
        n = 255 - y
        if n < 0:
            oh[NBUCK, y] = 1.0
            continue
        half = NBUCK // 2
        if n < half:
            b = n
        else:
            b = half + int(np.float32(np.log(np.float32(n) / np.float32(half))) / np.float32(math.log(MAXDIST / half))
                           * np.float32(NBUCK - half))
        b = min(b, NBUCK - 1)
        oh[b, y] += 1.0
        oh[NBUCK - 1, y] -= 1.0
    return oh


CONSTS = _shape_constants()
BUCKETS = _bucket_columns()


def named(**values):
    return namedtuple("Named", list(values))(**values)


class Buffers:
    pass


@contextmanager
def stage(nc, names):
    with ExitStack() as ctx:
        found = {}
        nums = []
        for name in names.split():
            count = 1
            if "*" in name:
                name, count = name.split("*")
            sems = [ctx.enter_context(nc.semaphore(f"{name}_{i}")) for i in range(int(count))]
            nums += [x.num for x in sems]
            found[name] = sems[0] if count == 1 else sems
        yield named(**found)
        with nc.Block() as block:
            @block.sync
            def _(sp):
                for n in sorted(nums):
                    sp.sem_clear(range(n, n + 1))


class Chain:

    def __init__(self, engine, sem):
        self.engine, self.sem, self.n = engine, sem, 0

    def __call__(self, instruction):
        self.n += 1
        instruction.then_inc(self.sem, 1)
        self.engine.wait_ge(self.sem, self.n)
        return instruction


def load_setup(nc, io, m):
    c = m.c
    with stage(nc, "loaded filled bias_mm bias_row bias_stored tables head_decay scaled page_float page_mm") as s:
        with nc.Block() as block:
            @block.sync
            def _(sp):
                loads = [
                    (m.consts[:, :], io.consts), (m.onehot[:, :], io.buckets),
                    (m.gmix[:, :], io.norm_mix.rearrange("o (c p) -> p (o c)", p=P)),
                    (m.gffn[:, :], io.norm_ffn.rearrange("o (c p) -> p (o c)", p=P)),
                    (m.qn[:, :], bass.AP(io.q_norm.tensor, 0, [[0, P], [1, HD]])),
                    (m.kn[:, :], bass.AP(io.k_norm.tensor, 0, [[0, P], [1, HD]])),
                    (m.convb[:, :], io.conv_b.rearrange("o (c p) -> p (o c)", p=P)),
                    (m.dtb[:, :], bass.AP(io.dt_bias.tensor, 0, [[0, P], [1, 8]])),
                    (m.alog[:, :], bass.AP(io.a_log.tensor, 0, [[0, P], [1, 8]])),
                    (m.dskip[:, :], bass.AP(io.d_skip.tensor, 0, [[0, P], [1, 8]])),
                    (m.ssdn[:, :], bass.AP(io.ssd_norm.tensor, 0, [[0, P], [1, DSSD]])),
                    (m.pages[:, :], bass.AP(io.page_table.tensor, 0, [[1, 16], [16, 16]])),
                ] + [(m.convw[:, k, :], io.conv_w[0, k, :].rearrange("(c p) -> p c", p=P)) for k in range(4)]
                for dst, src in loads:
                    sp.dma_start(dst, src, allow_slow_non_contiguous=True).then_inc(s.loaded, 16)
                sp.wait_ge(s.filled, 1)
                sp.dma_start(m.relx[0:NBUCK, :], io.rel_bias).then_inc(s.loaded, 16)
                sp.wait_ge(s.bias_row, 1)
                sp.dma_start(m.bias_dram, m.biasrow[:, :].unsqueeze(1).broadcast_to([NH, P, BIASW])).then_inc(s.bias_stored, 16)
                sp.wait_ge(s.bias_stored, 16)
                t = m.bias_dram.tensor
                for b in range(B4):
                    for g in range(NG):
                        p0 = b * 32 + g * 16
                        for q in range(DS):
                            sp.dma_start(m.srow[p0 + q * REP:p0 + (q + 1) * REP, :],
                                         bass.AP(t, g * REP * P * BIASW + 127 - q, [[P * BIASW, REP], [1, 132]])).then_inc(s.tables, 16)
                sp.wait_ge(s.tables, 16 * 32)

            @block.vector
            def _(dve):
                chain = Chain(dve, s.scaled)
                nc.vector.memset(m.relx[:, :], NEG).then_inc(s.filled, 1)
                dve.wait_ge(s.loaded, 16 * 17)
                nc.vector.tensor_copy(m.pagef[:, :], m.pages[:, :]).then_inc(s.page_float, 1)
                dve.wait_ge(s.page_mm, 1)
                chain(nc.vector.tensor_scalar(m.rowf[:, :], m.bank[1][:, 0:2 * DB], 8.0, c("p_mod"), ALU.mult, ALU.add))
                nc.vector.tensor_copy(m.rows[:, :], m.rowf[:, :])
                nc.vector.tensor_scalar(m.qn[:, :], m.qn[:, :], float(HD) ** -0.5, None, ALU.mult)
                dve.wait_ge(s.head_decay, 1)
                nc.vector.tensor_scalar(m.alog[:, :], m.alog[:, :], -1.0, None, ALU.mult)
                dve.wait_ge(s.bias_mm, 1)
                nc.vector.tensor_copy(m.biasrow[:, :], m.bank[0][0:NH, 0:BIASW]).then_inc(s.bias_row, 1)

            @block.scalar
            def _(act):
                act.wait_ge(s.loaded, 16 * 17)
                nc.scalar.activation(m.alog[:, :], m.alog[:, :], ACT.Exp).then_inc(s.head_decay, 1)

            @block.tensor
            def _(pe):
                pe.wait_ge(s.page_float, 1)
                nc.tensor.matmul(m.bank[1][:, 0:2 * DB], c("page_of")[0:16, :], m.pagef[:, :],
                                 start=True, stop=True).then_inc(s.page_mm, 1)
                pe.wait_ge(s.loaded, 16 * 17)
                nc.tensor.matmul(m.bank[0][0:NH, 0:BIASW], m.relx[:, :], m.onehot[:, :],
                                 start=True, stop=True).then_inc(s.bias_mm, 1)


def project(nc, io, m, w, tiles):
    c = m.c
    n = len(tiles)
    chunks = [(0, 512), (512, 1024), (1024, OFF_Z), (OFF_Z, OFF_XBC), (OFF_XBC, OFF_XBC + 512), (OFF_XBC + 512, DIN)]
    TA, TB = m.bank[6], m.bank[7]
    with stage(nc, "x_loaded*2 w_loaded x_square x_rstd x_scaled x_turned u_ready projected low_taken high_taken "
                   "squared head_sums head_rstd normed qk_turned qk_taken stored*2 act_c dve_c") as s:
        with nc.Block() as block:
            @block.sync
            def _(sp):
                def load_x(j):
                    if j >= 2:
                        sp.wait_ge(s.x_turned, 2 * (j - 1))
                    sp.dma_start(w.x[0:tiles[j].rows, j % 2, :], tiles[j].x).then_inc(s.x_loaded[j % 2], 16)

                load_x(0)
                if w.first:
                    wv = io.w_in.rearrange("o (c p) n -> p (o c) n", p=P)
                    for k in range(KT):
                        sp.dma_start(w.w[:, k, :], wv[:, k, :]).then_inc(s.w_loaded, 16)
                if n > 1:
                    load_x(1)
                for j in range(n):
                    t = tiles[j]
                    sp.wait_ge(s.normed, j + 1)
                    sp.wait_ge(s.low_taken, 3 * (j + 1))
                    for dst, src in ((t.kc, w.kv[0:t.rows, j % 2, 0, :]), (t.vc, w.kv[0:t.rows, j % 2, 1, :]),
                                     (t.ks, w.qk[0:t.rows, j % 2, 4, :]), (t.vs, w.kv[0:t.rows, j % 2, 3, :]),
                                     (t.kw, w.qk[0:t.rows, j % 2, 5, :]), (t.vw, w.kv[0:t.rows, j % 2, 5, :])):
                        sp.dma_start(dst, src).then_inc(s.stored[j % 2], 16)
                    if j + 2 < n:
                        load_x(j + 2)
                for k in range(min(n, 2)):
                    sp.wait_ge(s.stored[k], 16 * 6 * len(range(k, n, 2)))

            @block.tensor
            def _(pe):
                def turn_x(j):
                    r = tiles[j].rows
                    pe.wait_ge(s.x_scaled, j + 1)
                    if j >= 1:
                        pe.wait_ge(s.u_ready, 2 * j)
                    if j >= 2:
                        pe.wait_ge(s.qk_taken, 2 * (j - 1))
                    for k in range(KT):
                        bank = (TA, TB)[k // 4]
                        i = nc.tensor.transpose(bank[:, (k % 4) * P:(k % 4) * P + r],
                                                w.x[0:r, j % 2, k * P:(k + 1) * P], c("ident")[0:r, 0:r])
                        if k % 4 == 3:
                            i.then_inc(s.x_turned, 1)

                def turn_heads(j):
                    r = tiles[j].rows
                    pe.wait_ge(s.normed, j + 1)
                    pe.wait_ge(s.u_ready, 2 * min(j + 2, n))
                    for k in range(6):
                        bank = (TA, TB)[k // 4]
                        i = nc.tensor.transpose(bank[:, (k % 4) * P:(k % 4) * P + r], w.qk[0:r, j % 2, k, :],
                                                c("ident")[0:r, 0:r])
                        if k in (3, 5):
                            i.then_inc(s.qk_turned, 1)

                def multiply(j, cs):
                    r = tiles[j].rows
                    for i in cs:
                        a, b = chunks[i]
                        if j >= 1:
                            if i < 3:
                                pe.wait_ge(s.low_taken, 3 * (j - 1) + i + 1)
                            else:
                                pe.wait_ge(s.high_taken, 3 * (j - 1) + i - 2)
                        for k in range(KT):
                            mm = nc.tensor.matmul(m.bank[i][0:r, 0:b - a], w.u[:, j % 2, k, 0:r], w.w[:, k, a:b],
                                                  start=(k == 0), stop=(k == KT - 1))
                        mm.then_inc(s.projected, 1)

                turn_x(0)
                if w.first:
                    pe.wait_ge(s.w_loaded, 16 * KT)
                for j in range(n):
                    pe.wait_ge(s.u_ready, 2 * (j + 1))
                    multiply(j, (0, 1, 2))
                    if j >= 1:
                        turn_heads(j - 1)
                    if j + 1 < n:
                        turn_x(j + 1)
                    multiply(j, (3, 4, 5))
                if n > 1:
                    pe.wait_ge(s.qk_taken, 2 * (n - 1))
                turn_heads(n - 1)

            @block.scalar
            def _(act):
                chain = Chain(act, s.act_c)

                def statistics(j):
                    r = tiles[j].rows
                    act.wait_ge(s.x_loaded[j % 2], 16 * (j // 2 + 1))
                    if j >= 2:
                        act.wait_ge(s.x_scaled, j - 1)
                    chain(nc.scalar.activation(w.junk[0:r, :], w.x[0:r, j % 2, :], ACT.Square,
                                               accum_out=w.ss[0:r, j % 2:j % 2 + 1]))
                    chain(nc.scalar.activation(w.ss[0:r, 2:3], w.ss[0:r, j % 2:j % 2 + 1], ACT.Ln, scale=1.0 / DM,
                                               bias=c("eps")[0:r, :]))
                    nc.scalar.activation(w.ss[0:r, 4 + j % 2:5 + j % 2], w.ss[0:r, 2:3], ACT.Exp,
                                         scale=-0.5).then_inc(s.x_rstd, 1)

                def take_heads(j):
                    t = tiles[j]
                    act.wait_ge(s.qk_turned, 2 * j + 1)
                    nc.scalar.activation(t.qT, TA[:, :].rearrange("p (r q) -> p r q", r=4)[:, :, 0:t.rows],
                                         ACT.Copy).then_inc(s.qk_taken, 1)
                    act.wait_ge(s.qk_turned, 2 * j + 2)
                    nc.scalar.activation(t.ksT, TB[:, 0:t.rows], ACT.Copy)
                    nc.scalar.activation(t.kwT, TB[:, P:P + t.rows], ACT.Copy).then_inc(s.qk_taken, 1)

                statistics(0)
                for j in range(n):
                    t, r = tiles[j], tiles[j].rows
                    if j + 1 < n:
                        statistics(j + 1)
                    act.wait_ge(s.projected, 6 * j + 1)
                    if j >= 1:
                        act.wait_ge(s.normed, j)
                    if j >= 2:
                        act.wait_ge(s.stored[j % 2], 16 * 6 * (j // 2))
                    nc.scalar.activation(w.q[0:r, :], m.bank[0][0:r, :], ACT.Copy).then_inc(s.low_taken, 1)
                    act.wait_ge(s.projected, 6 * j + 2)
                    nc.scalar.activation(w.kv[0:r, j % 2, 0:4, :], m.bank[1][0:r, :].rearrange("p (a b) -> p a b", a=4),
                                         ACT.Copy).then_inc(s.low_taken, 1)
                    act.wait_ge(s.projected, 6 * j + 3)
                    nc.scalar.activation(w.kv[0:r, j % 2, 4:6, :],
                                         m.bank[2][0:r, 0:256].rearrange("p (a b) -> p a b", a=2), ACT.Copy)
                    nc.scalar.activation(t.gate, m.bank[2][0:r, 256:280], ACT.Copy).then_inc(s.low_taken, 1)
                    act.wait_ge(s.low_taken, 3 * (j + 1))
                    if j >= 1:
                        act.wait_ge(s.head_sums, j)
                    nc.scalar.activation(w.sq[0:r, 0:512], w.q[0:r, :], ACT.Square)
                    nc.scalar.activation(w.sq[0:r, 512:640], w.kv[0:r, j % 2, 2, :], ACT.Square)
                    nc.scalar.activation(w.sq[0:r, 640:768], w.kv[0:r, j % 2, 4, :], ACT.Square).then_inc(s.squared, 1)
                    nc.scalar.activation(t.v[:, 0, :], w.kv[0:r, j % 2, 3, :], ACT.Copy)
                    nc.scalar.activation(t.v[:, 1, :], w.kv[0:r, j % 2, 5, :], ACT.Copy)
                    if j >= 1:
                        take_heads(j - 1)
                    act.wait_ge(s.head_sums, j + 1)
                    chain(nc.scalar.activation(w.hs[0:r, 12:24], w.hs[0:r, 0:12], ACT.Ln, scale=1.0 / HD,
                                               bias=c("eps")[0:r, :]))
                    nc.scalar.activation(w.hs[0:r, 24:36], w.hs[0:r, 12:24], ACT.Exp,
                                         scale=-0.5).then_inc(s.head_rstd, 1)
                take_heads(n - 1)

            @block.vector
            def _(dve):
                chain = Chain(dve, s.dve_c)

                def make_u(j):
                    r = tiles[j].rows
                    dve.wait_ge(s.x_rstd, j + 1)
                    nc.vector.tensor_scalar(w.x[0:r, j % 2, :], w.x[0:r, j % 2, :], w.ss[0:r, 4 + j % 2:5 + j % 2], None,
                                            ALU.mult).then_inc(s.x_scaled, 1)
                    for h in range(2):
                        dve.wait_ge(s.x_turned, 2 * j + h + 1)
                        if j >= 2:
                            dve.wait_ge(s.projected, 6 * (j - 1))
                        nc.vector.tensor_tensor(w.u[:, j % 2, 4 * h:4 * h + 4, 0:r],
                                                (TA, TB)[h][:, :].rearrange("p (k q) -> p k q", k=4)[:, :, 0:r],
                                                m.gmix[:, 4 * h:4 * h + 4].unsqueeze(2).broadcast_to([P, 4, r]),
                                                ALU.mult).then_inc(s.u_ready, 1)

                make_u(0)
                for j in range(n):
                    t, r = tiles[j], tiles[j].rows
                    if j + 1 < n:
                        make_u(j + 1)
                    for i, (a, b) in ((3, (PZ_Z, PZ_Z + 512)), (4, (PZ_XBC, PZ_XBC + 512)), (5, (PZ_XBC + 512, PZ_GATE))):
                        dve.wait_ge(s.projected, 6 * j + i + 1)
                        nc.vector.tensor_copy(t.pz[:, a:b], m.bank[i][0:r, 0:b - a]).then_inc(s.high_taken, 1)
                    dve.wait_ge(s.squared, j + 1)
                    if j >= 1:
                        dve.wait_ge(s.head_rstd, j)
                    nc.vector.tensor_reduce(w.hs[0:r, 0:12], w.sq[0:r, :].rearrange("p (h d) -> p h d", d=HD), AX.X,
                                            ALU.add).then_inc(s.head_sums, 1)
                    dve.wait_ge(s.head_rstd, j + 1)
                    if j >= 2:
                        dve.wait_ge(s.stored[j % 2], 16 * 6 * (j // 2))
                        dve.wait_ge(s.qk_turned, 2 * (j - 1))
                    nc.vector.tensor_tensor(
                        w.qk[0:r, j % 2, 0:4, :].rearrange("p r (g d) -> p g r d", g=NG),
                        w.q[0:r, :].rearrange("p (g r d) -> p g r d", g=NG, r=REP),
                        w.hs[0:r, 24:32].rearrange("p (g r) -> p g r", g=NG).unsqueeze(3).broadcast_to([r, NG, REP, HD]),
                        ALU.mult)
                    chain(nc.vector.tensor_tensor(
                        w.qk[0:r, j % 2, 4:6, :].rearrange("p b (g d) -> p b g d", g=NG),
                        w.kv[0:r, j % 2, 2:6:2, :].rearrange("p b (g d) -> p b g d", g=NG),
                        w.hs[0:r, 32:36].rearrange("p (b g) -> p b g", g=NG).unsqueeze(3).broadcast_to([r, 2, NG, HD]),
                        ALU.mult))
                    nc.vector.tensor_tensor(
                        w.qk[0:r, j % 2, 0:4, :].rearrange("p r (g d) -> p (r g) d", g=NG),
                        w.qk[0:r, j % 2, 0:4, :].rearrange("p r (g d) -> p (r g) d", g=NG),
                        m.qn[0:r, :].unsqueeze(1).broadcast_to([r, NH, HD]), ALU.mult)
                    nc.vector.tensor_tensor(
                        w.qk[0:r, j % 2, 4:6, :].rearrange("p r (g d) -> p (r g) d", g=NG),
                        w.qk[0:r, j % 2, 4:6, :].rearrange("p r (g d) -> p (r g) d", g=NG),
                        m.kn[0:r, :].unsqueeze(1).broadcast_to([r, 4, HD]), ALU.mult).then_inc(s.normed, 1)


def stage_pointwise(nc, io, m):
    c = m.c
    sb = Region(nc, m.att_end, m.end)
    m.dt = nc.alloc_sbuf_tensor_at("dt", [P, NT + 1, 16], F32, offset=m.dt_start)
    t1 = sb("dt_low", [P, NT + 1, 8])
    t2 = sb("dt_exp", [P, NT + 1, 8])
    parts = [(slice(0, P), slice(0, NT)), (slice(0, NS), slice(NT, NT + 1))]
    with stage(nc, "act_c dve_c low_ready log_ready stored") as s:
        with nc.Block() as block:
            @block.sync
            def _(sp):
                sp.dma_start(io.p_conv[0, 0, :, :], m.pz[P - 3:P, NT - 1, PZ_XBC:PZ_XBC + DCONV]).then_inc(s.stored, 16)
                for b in range(DB):
                    sp.dma_start(io.s_conv[0, b, :, :],
                                 m.pz[b * DS + 1:(b + 1) * DS, NT, PZ_XBC:PZ_XBC + DCONV]).then_inc(s.stored, 16)
                sp.wait_ge(s.stored, 16 * (1 + DB))

            @block.scalar
            def _(act):
                for rows, tiles in parts:
                    nc.scalar.activation(m.gates[rows, tiles, :], m.pz[rows, tiles, PZ_GATE:PZ], ACT.Sigmoid)
                for rows, tiles in parts:
                    z = m.pz[rows, tiles, PZ_Z:PZ_Z + DSSD]
                    nc.scalar.activation(z, z, ACT.Silu)
                chain = Chain(act, s.act_c)
                act.wait_ge(s.low_ready, 1)
                for rows, tiles in parts:
                    chain(nc.scalar.activation(t2[rows, tiles, :], t1[rows, tiles, :], ACT.Exp))
                for rows, tiles in parts:
                    nc.scalar.activation(t2[rows, tiles, :], t2[rows, tiles, :], ACT.Ln,
                                         bias=c("one")[rows, :]).then_inc(s.log_ready, 1)

            @block.vector
            def _(dve):
                chain = Chain(dve, s.dve_c)
                for rows, tiles in parts:
                    n = tiles.stop - tiles.start
                    r = rows.stop
                    x, low = m.dt[rows, tiles, 0:8], t1[rows, tiles, :]
                    chain(nc.vector.tensor_tensor(x, m.pz[rows, tiles, PZ_DT:PZ_DT + 8],
                                                  m.dtb[rows, :].unsqueeze(1).broadcast_to([r, n, 8]), ALU.add))
                    chain(nc.vector.tensor_scalar(low, x, -1.0, None, ALU.mult))
                    chain(nc.vector.tensor_tensor(low, low, x, ALU.min))
                nc.vector.tensor_scalar(t1[0:1, 0, 0:1], t1[0:1, 0, 0:1], 1.0, None, ALU.mult).then_inc(s.low_ready, 1)
                dve.wait_ge(s.log_ready, 2)
                for rows, tiles in parts:
                    n = tiles.stop - tiles.start
                    r = rows.stop
                    x = m.dt[rows, tiles, 0:8]
                    chain(nc.vector.tensor_scalar(x, x, 0.0, None, ALU.max))
                    chain(nc.vector.tensor_tensor(x, x, t2[rows, tiles, :], ALU.add))
                    nc.vector.tensor_tensor(m.dt[rows, tiles, 8:16], x,
                                            m.alog[rows, :].unsqueeze(1).broadcast_to([r, n, 8]), ALU.mult)


def stage_conv(nc, io, m):
    c = m.c
    NCB = DCONV // P
    sb = Region(nc, m.qT_start, m.mix_start)
    m.xc = sb("conv_out", [P, NCB, TOK])
    m.conv_end = sb.at
    raw = sb("conv_in", [P, NCB, 3 + SEQ])
    raws = sb("conv_in_s", [P, NCB, DB, 3 + DS])
    state = sb("conv_state", [DB * 3, DCONV])
    with stage(nc, "state_loaded padded turned taken tapped summed sample_taken dve_c") as s:
        with nc.Block() as block:
            @block.sync
            def _(sp):
                sp.dma_start(state[:, :], io.state_conv.rearrange("o b k c -> (o b k) c")).then_inc(s.state_loaded, 16)

            @block.gpsimd
            def _(pool):
                nc.gpsimd.memset(raw[:, :, 0:3], 0.0).then_inc(s.padded, 1)

            @block.tensor
            def _(pe):
                for b in range(NCB):
                    for h in range(2):
                        n = 2 * b + h
                        if n >= 6:
                            pe.wait_ge(s.taken, n - 5)
                        for k in range(4):
                            i = nc.tensor.transpose(m.bank[n % 6][:, k * P:(k + 1) * P],
                                                    m.pz[:, 4 * h + k, PZ_XBC + b * P:PZ_XBC + (b + 1) * P], c("ident"))
                        i.then_inc(s.turned, 1)
                pe.wait_ge(s.state_loaded, 16)
                for b in range(NCB):
                    nc.tensor.transpose(m.bank[6][:, b * NS:(b + 1) * NS],
                                        m.pz[0:NS, NT, PZ_XBC + b * P:PZ_XBC + (b + 1) * P], c("ident")[0:NS, 0:NS])
                    i = nc.tensor.transpose(m.bank[7][:, b * 24:(b + 1) * 24], state[:, b * P:(b + 1) * P],
                                            c("ident")[0:24, 0:24])
                i.then_inc(s.turned, 1)

            @block.scalar
            def _(act):
                act.wait_ge(s.padded, 1)
                for b in range(NCB):
                    for h in range(2):
                        n = 2 * b + h
                        act.wait_ge(s.turned, n + 1)
                        nc.scalar.activation(raw[:, b, 3 + 512 * h:3 + 512 * (h + 1)], m.bank[n % 6][:, :],
                                             ACT.Copy).then_inc(s.taken, 1)
                    act.wait_ge(s.taken, 2 * b + 2)
                    nc.scalar.activation(m.xc[:, b, 0:SEQ], raw[:, b, 0:SEQ], ACT.Identity, bias=m.convb[:, b:b + 1],
                                         scale=m.convw[:, 0, b:b + 1]).then_inc(s.tapped, 1)
                act.wait_ge(s.turned, 2 * NCB + 1)
                nc.scalar.activation(raws[:, :, :, 3:3 + DS], m.bank[6][:, 0:NCB * NS].rearrange(
                    "p (c b t) -> p c b t", c=NCB, b=DB), ACT.Copy)
                nc.scalar.activation(raws[:, :, :, 0:3], m.bank[7][:, 0:NCB * 24].rearrange(
                    "p (c b t) -> p c b t", c=NCB, b=DB), ACT.Copy).then_inc(s.sample_taken, 1)
                act.wait_ge(s.sample_taken, 1)
                for b in range(NCB):
                    nc.scalar.activation(m.xc[:, b, SEQ:TOK].rearrange("p (b t) -> p b t", b=DB), raws[:, b, :, 0:DS],
                                         ACT.Identity, bias=m.convb[:, b:b + 1],
                                         scale=m.convw[:, 0, b:b + 1]).then_inc(s.tapped, 1)
                for b in range(NCB):
                    act.wait_ge(s.summed, b + 1)
                    nc.scalar.activation(m.xc[:, b, 0:SEQ], m.xc[:, b, 0:SEQ], ACT.Silu)
                act.wait_ge(s.summed, 2 * NCB)
                nc.scalar.activation(m.xc[:, :, SEQ:TOK], m.xc[:, :, SEQ:TOK], ACT.Silu)

            @block.vector
            def _(dve):
                chain = Chain(dve, s.dve_c)
                for b in range(NCB):
                    dve.wait_ge(s.tapped, b + 1)
                    for k in range(1, 4):
                        i = nc.vector.scalar_tensor_tensor(m.xc[:, b, 0:SEQ], raw[:, b, k:k + SEQ], m.convw[:, k, b:b + 1],
                                                           m.xc[:, b, 0:SEQ], ALU.mult, ALU.add)
                        if k < 3:
                            chain(i)
                    i.then_inc(s.summed, 1)
                for b in range(NCB):
                    dve.wait_ge(s.tapped, NCB + b + 1)
                    out = m.xc[:, b, SEQ:TOK].rearrange("p (b t) -> p b t", b=DB)
                    for k in range(1, 4):
                        i = nc.vector.scalar_tensor_tensor(out, raws[:, b, :, k:k + DS], m.convw[:, k, b:b + 1],
                                                           out, ALU.mult, ALU.add)
                        if k < 3:
                            chain(i)
                    i.then_inc(s.summed, 1)


def ssd_chunks(nc, m, w, chunks):
    c = m.c
    n = len(chunks)
    R = chunks[0].rows
    sample = chunks[0].sample
    tri, after, ones = (("s_tri", "s_after", "s_ones") if sample else ("tri", "after", "ones"))
    tri, after, ones = c(tri)[0:R, 0:R], c(after)[0:R, 0:R], c(ones)[0:R, 0:R]
    heads = lambda ap: ap.unsqueeze(2).broadcast_to([R, 8, HD])
    with stage(nc, "xs_ready dt_ready td_ready turned sums_ready x_taken small_taken diff_ready ex_ready cb_ready "
                   "acb_ready seg_done e_ready m_ready xdt_ready xe_ready yo_ready yd_ready st_ready state_ready "
                   "state_scaled xd_ready y_ready yr_ready y_done act_c dve_c pe_c") as s:
        with nc.Block() as block:
            @block.tensor
            def _(pe):
                chain = Chain(pe, s.pe_c)

                def front(j):
                    q = j % 2
                    pe.wait_ge(s.xs_ready, j + 1)
                    if j >= 1:
                        pe.wait_ge(s.x_taken, j)
                        pe.wait_ge(s.small_taken, j)
                    for k in range(4):
                        nc.tensor.transpose(m.bank[0][0:R, k * P:(k + 1) * P], w.xs[:, q, k, 0:R], c("ident"))
                    nc.tensor.transpose(m.bank[1][0:R, 0:P], w.xs[:, q, 4, 0:R], c("ident")).then_inc(s.turned, 1)
                    pe.wait_ge(s.dt_ready, j + 1)
                    nc.tensor.matmul(m.bank[1][0:R, P:P + 8], tri, w.dt[0:R, q, 8:16], start=True, stop=True)
                    nc.tensor.matmul(m.bank[1][0:R, P + 8:P + 16], ones, w.dt[0:R, q, 8:16], start=True,
                                     stop=True).then_inc(s.sums_ready, 1)
                    if j >= 1:
                        pe.wait_ge(s.m_ready, j)
                        pe.wait_ge(s.seg_done, j)
                    for g in range(NG):
                        mm = nc.tensor.matmul(m.bank[2][0:R, g * P:g * P + R], w.xs[64 * g:64 * g + 64, q, 4, 0:R],
                                              w.xs[64 * g:64 * g + 64, q, 5, 0:R], start=True, stop=True)
                        chain(mm)
                    nc.tensor.nop().then_inc(s.cb_ready, 1)
                    pe.wait_ge(s.td_ready, j + 1)
                    for h in range(2):
                        mm = nc.tensor.matmul(m.bank[4 + h][0:R, 0:4 * R], c("ones")[0:R, 0:R],
                                              w.td[0:R, 4 * h:4 * h + 4, 0:R], start=True, stop=True)
                    mm.then_inc(s.acb_ready, 1)

                def back(j):
                    q = j % 2
                    if j >= 1:
                        pe.wait_ge(s.y_ready, j)
                        pe.wait_ge(s.state_ready, j)
                    if not sample:
                        for g in range(NG):
                            mm = nc.tensor.matmul(m.bank[6][0:R, 256 * g:256 * (g + 1)],
                                                  w.xs[64 * g:64 * g + 64, q, 5, 0:R],
                                                  w.state[64 * g:64 * g + 64, :], start=True, stop=True)
                            chain(mm)
                    else:
                        for g in range(NG):
                            for b in range(DB):
                                mm = nc.tensor.matmul(m.bank[6][0:R, 256 * g:256 * (g + 1)],
                                                      w.cm[64 * g:64 * g + 64, b, :], w.s0[64 * g:64 * g + 64, b, :],
                                                      start=(b == 0), stop=(b == DB - 1))
                            chain(mm)
                    nc.tensor.nop().then_inc(s.yo_ready, 1)
                    pe.wait_ge(s.m_ready, j + 1)
                    pe.wait_ge(s.xdt_ready, j + 1)
                    for h in range(8):
                        mm = nc.tensor.matmul(m.bank[7][0:R, HD * h:HD * (h + 1)], w.seg[0:R, h, 0:R],
                                              w.xdt[0:R, HD * h:HD * (h + 1)], start=True, stop=True)
                    mm.then_inc(s.yd_ready, 1)
                    if not sample:
                        pe.wait_ge(s.xe_ready, j + 1)
                        nc.tensor.matmul(m.bank[3][:, :], w.small[0:R, q, 0:P], w.xe[0:R, :], start=True,
                                         stop=True).then_inc(s.st_ready, 1)

                front(0)
                for j in range(n):
                    back(j)
                    if j + 1 < n:
                        front(j + 1)

            @block.scalar
            def _(act):
                chain = Chain(act, s.act_c)

                def slice_chunk(j):
                    if j >= 2:
                        act.wait_ge(s.yo_ready, j - 1)
                    nc.scalar.activation(w.xs[:, j % 2, :, 0:R], chunks[j].xc, ACT.Copy).then_inc(s.xs_ready, 1)

                slice_chunk(0)
                for j in range(n):
                    q = j % 2
                    act.wait_ge(s.turned, j + 1)
                    if j >= 1:
                        act.wait_ge(s.xe_ready, j)
                        act.wait_ge(s.xd_ready, j)
                    nc.scalar.activation(w.xt[0:R, :], m.bank[0][0:R, :], ACT.Copy).then_inc(s.x_taken, 1)
                    act.wait_ge(s.diff_ready, j + 1)
                    if j >= 2:
                        act.wait_ge(s.y_ready, j - 1)
                    nc.scalar.activation(w.ex[0:R, q, :], w.small[0:R, q, P:P + 24], ACT.Exp).then_inc(s.ex_ready, 1)
                    act.wait_ge(s.seg_done, j + 1)
                    nc.scalar.activation(w.seg[0:R, :, 0:R], w.seg[0:R, :, 0:R], ACT.Exp).then_inc(s.e_ready, 1)
                    if j + 1 < n:
                        slice_chunk(j + 1)
                    act.wait_ge(s.y_ready, j + 1)
                    for g in range(NG):
                        chain(nc.scalar.activation(w.junk[0:R, :], w.y[0:R, q, 256 * g:256 * (g + 1)], ACT.Square,
                                                   accum_out=w.yr[0:R, q, g:g + 1]))
                    chain(nc.scalar.activation(w.yr[0:R, q, 2:4], w.yr[0:R, q, 0:2], ACT.Ln, scale=1.0 / 256,
                                               bias=c("eps")[0:R, :]))
                    nc.scalar.activation(w.yr[0:R, q, 4:6], w.yr[0:R, q, 2:4], ACT.Exp, scale=-0.5).then_inc(s.yr_ready, 1)

            @block.gpsimd
            def _(pool):
                for j in range(n):
                    pool.wait_ge(s.x_taken, j + 1)
                    if j >= 1:
                        pool.wait_ge(s.y_ready, j)
                    nc.gpsimd.tensor_tensor(w.xd[0:R, :].rearrange("p (h d) -> p h d", h=8),
                                            w.xt[0:R, :].rearrange("p (h d) -> p h d", h=8), heads(m.dskip[0:R, :]),
                                            ALU.mult).then_inc(s.xd_ready, 1)

            @block.vector
            def _(dve):
                chain = Chain(dve, s.dve_c)

                def steps(j):
                    q = j % 2
                    if j >= 2:
                        dve.wait_ge(s.xe_ready, j - 1)
                    nc.vector.tensor_copy(w.dt[0:R, q, :], chunks[j].dt).then_inc(s.dt_ready, 1)
                    dve.wait_ge(s.dt_ready, j + 1)
                    if j >= 1:
                        dve.wait_ge(s.acb_ready, j)
                    nc.vector.tensor_tensor(w.td[0:R, :, 0:R], tri.unsqueeze(1).broadcast_to([R, 8, R]),
                                            w.dt[0:R, q, 8:16].unsqueeze(2).broadcast_to([R, 8, R]),
                                            ALU.mult).then_inc(s.td_ready, 1)

                def finish(j):
                    q = j % 2
                    dve.wait_ge(s.yr_ready, j + 1)
                    for g in range(NG):
                        i = nc.vector.scalar_tensor_tensor(chunks[j].out[:, 256 * g:256 * (g + 1)],
                                                           w.y[0:R, q, 256 * g:256 * (g + 1)], w.yr[0:R, q, 4 + g:5 + g],
                                                           m.ssdn[0:R, 256 * g:256 * (g + 1)], ALU.mult, ALU.mult)
                    i.then_inc(s.y_done, 1)

                steps(0)
                for j in range(n):
                    q = j % 2
                    ch = chunks[j]
                    dve.wait_ge(s.sums_ready, j + 1)
                    if j >= 2:
                        dve.wait_ge(s.ex_ready, j - 1)
                    nc.vector.tensor_copy(w.small[0:R, q, 0:P + 16], m.bank[1][0:R, 0:P + 16]).then_inc(s.small_taken, 1)
                    dve.wait_ge(s.small_taken, j + 1)
                    nc.vector.tensor_tensor(w.small[0:R, q, P + 16:P + 24], w.small[0:R, q, P + 8:P + 16],
                                            w.small[0:R, q, P:P + 8], ALU.subtract).then_inc(s.diff_ready, 1)
                    dve.wait_ge(s.acb_ready, j + 1)
                    if j >= 1:
                        dve.wait_ge(s.yd_ready, j)
                    for h in range(8):
                        i = nc.vector.scalar_tensor_tensor(w.seg[0:R, h, 0:R],
                                                           m.bank[4 + h // 4][0:R, (h % 4) * R:(h % 4 + 1) * R],
                                                           w.small[0:R, q, P + h:P + h + 1], after,
                                                           ALU.subtract, ALU.add)
                    i.then_inc(s.seg_done, 1)
                    if j >= 1:
                        finish(j - 1)
                    dve.wait_ge(s.x_taken, j + 1)
                    nc.vector.tensor_tensor(w.xdt[0:R, :].rearrange("p (h d) -> p h d", h=8),
                                            w.xt[0:R, :].rearrange("p (h d) -> p h d", h=8), heads(w.dt[0:R, q, 0:8]),
                                            ALU.mult).then_inc(s.xdt_ready, 1)
                    dve.wait_ge(s.xdt_ready, j + 1)
                    dve.wait_ge(s.ex_ready, j + 1)
                    if j >= 1:
                        dve.wait_ge(s.state_ready, j)
                    nc.vector.tensor_tensor(w.xe[0:R, :].rearrange("p (h d) -> p h d", h=8),
                                            w.xdt[0:R, :].rearrange("p (h d) -> p h d", h=8), heads(w.ex[0:R, q, 16:24]),
                                            ALU.mult).then_inc(s.xe_ready, 1)
                    dve.wait_ge(s.e_ready, j + 1)
                    dve.wait_ge(s.cb_ready, j + 1)
                    for g in range(NG):
                        i = nc.vector.tensor_tensor(w.seg[0:R, 4 * g:4 * g + 4, 0:R], w.seg[0:R, 4 * g:4 * g + 4, 0:R],
                                                    m.bank[2][0:R, g * P:g * P + R].unsqueeze(1).broadcast_to([R, 4, R]),
                                                    ALU.mult)
                    i.then_inc(s.m_ready, 1)
                    if j + 1 < n:
                        steps(j + 1)
                    dve.wait_ge(s.yo_ready, j + 1)
                    if not sample:
                        for g in range(NG):
                            st = w.state[64 * g:64 * g + 64, :].rearrange("p (r d) -> p r d", r=4)
                            chain(nc.vector.tensor_tensor(
                                st, st, w.ex[64 * g:64 * g + 64, q, 8 + 4 * g:12 + 4 * g].unsqueeze(2).broadcast_to(
                                    [64, 4, HD]), ALU.mult))
                        dve.wait_ge(s.st_ready, j + 1)
                        for g in range(NG):
                            i = nc.vector.tensor_tensor(w.state[64 * g:64 * g + 64, :], w.state[64 * g:64 * g + 64, :],
                                                        m.bank[3][64 * g:64 * g + 64, 256 * g:256 * (g + 1)], ALU.add)
                        i.then_inc(s.state_ready, 1)
                    y = w.y[0:R, q, :]
                    if j >= 2:
                        dve.wait_ge(s.y_done, j - 1)
                    chain(nc.vector.tensor_tensor(y.rearrange("p (h d) -> p h d", h=8),
                                                  m.bank[6][0:R, :].rearrange("p (h d) -> p h d", h=8),
                                                  heads(w.ex[0:R, q, 0:8]), ALU.mult))
                    dve.wait_ge(s.yd_ready, j + 1)
                    chain(nc.vector.tensor_tensor(y, y, m.bank[7][0:R, :], ALU.add))
                    dve.wait_ge(s.xd_ready, j + 1)
                    chain(nc.vector.tensor_tensor(y, y, w.xd[0:R, :], ALU.add))
                    nc.vector.tensor_tensor(y, y, ch.z, ALU.mult).then_inc(s.y_ready, 1)
                finish(n - 1)


def stage_ssd(nc, io, m):
    c = m.c
    sb = Region(nc, m.conv_end, m.mix_start)
    w = Buffers()
    w.xs = sb("chunk", [P, 2, 6, P])
    w.dt = sb("chunk_dt", [P, 2, 16])
    w.td = sb("dt_steps", [P, 8, P])
    w.small = sb("b_and_sums", [P, 2, P + 24])
    w.ex = sb("decays", [P, 2, 24])
    w.seg = sb("seg", [P, 8, P])
    w.xt = sb("x_tok", [P, DSSD])
    w.xdt = sb("xdt", [P, DSSD])
    w.xe = sb("x_to_end", [P, DSSD])
    w.xd = sb("x_skip", [P, DSSD])
    w.y = sb("y_ssd", [P, 2, DSSD])
    w.yr = sb("y_rstd", [P, 2, 6])
    w.junk = sb("junk_y", [P, 256])
    w.state = sb("state", [P, 256])
    w.s0 = sb("state0", [P, DB, 256])
    w.cm = sb("c_masked", [P, DB, NS])
    w.bm = sb("b_masked", [NS, DB, P])
    w.db = sb("dta_of_b", [NS, DB, 8])
    w.dec = sb("decay_of_b", [P, DB, 8])
    w.hin = sb("state_in", [P, DB, 2, NG, HD])
    w.hout = sb("state_out", [P, DB, 2, NG, HD])
    hd = lambda ap: ap.rearrange("o b (i h) p n -> (h p) (o b) i n", h=2)

    with stage(nc, "loaded zeroed turned taken") as s:
        with nc.Block() as block:
            @block.sync
            def _(sp):
                for i in range(4):
                    sp.dma_start(w.hin[:, :, i % 2, i // 2, :], hd(io.state_ssm)[:, :, i, :]).then_inc(s.loaded, 16)

            @block.gpsimd
            def _(pool):
                nc.gpsimd.memset(w.state[:, :], 0.0)
                nc.gpsimd.memset(w.cm[:, :, :], 0.0).then_inc(s.zeroed, 1)

            @block.tensor
            def _(pe):
                pe.wait_ge(s.loaded, 64)
                for b in range(DB):
                    for i in range(2):
                        t = nc.tensor.transpose(m.bank[b // 2][:, ((b % 2) * 2 + i) * P:((b % 2) * 2 + i + 1) * P],
                                                w.hin[:, b, i, :, :], c("ident"))
                t.then_inc(s.turned, 1)

            @block.vector
            def _(dve):
                dve.wait_ge(s.zeroed, 1)
                nc.vector.tensor_copy(bass.AP(w.cm[:, :, :].tensor, 0, [[DB * NS, P], [NS + DS, DB], [1, DS]]),
                                      m.xc[:, 5, SEQ:TOK].rearrange("p (b t) -> p b t", b=DB))
                dve.wait_ge(s.turned, 1)
                for k in range(4):
                    nc.vector.tensor_copy(w.s0[:, 2 * k:2 * k + 2, :], m.bank[k][:, :].rearrange("p (b x) -> p b x", b=2))

    with nc.Fori(0, NT // PER) as turn:
        chunks = []
        for j in range(PER):
            i = turn * PER + j
            flat = lambda ap: ap.rearrange("p o c -> p (o c)")
            chunks.append(named(rows=P, sample=False, xc=m.xc[:, :, bass.ds(i * P, P)],
                               dt=flat(m.dt[:, bass.ds(i, 1), :]), z=flat(m.pz[:, bass.ds(i, 1), PZ_Z:PZ_Z + DSSD]),
                               out=flat(m.mix[:, bass.ds(i, 1), DATT:DM])))
        ssd_chunks(nc, m, w, chunks)
    ssd_chunks(nc, m, w, [named(rows=NS, sample=True, xc=m.xc[:, :, SEQ:TOK], dt=m.dt[0:NS, NT, :],
                               z=m.pz[0:NS, NT, PZ_Z:PZ_Z + DSSD], out=m.mix[0:NS, NT, DATT:DM])])

    with stage(nc, "dta_ready sums_ready decayed b_ready multiplied scaled added turned taken stored") as s:
        with nc.Block() as block:
            @block.tensor
            def _(pe):
                pe.wait_ge(s.dta_ready, 1)
                nc.tensor.matmul(m.bank[7][:, 0:64], c("ones")[0:NS, :], w.db[:, :, :], start=True,
                                 stop=True).then_inc(s.sums_ready, 1)
                pe.wait_ge(s.b_ready, 1)
                for b in range(DB):
                    if b >= 4:
                        pe.wait_ge(s.added, b - 3)
                    nc.tensor.matmul(m.bank[b % 4][:, :], w.bm[:, b, :], w.xe[0:NS, :], start=True,
                                     stop=True).then_inc(s.multiplied, 1)
                for b in range(DB + 1):
                    src = w.s0[:, b, :] if b < DB else w.state[:, :]
                    if b < DB:
                        pe.wait_ge(s.added, b + 1)
                    if b >= 2:
                        pe.wait_ge(s.taken, b - 1)
                    for i in range(2):
                        t = nc.tensor.transpose(m.bank[4 + b % 2][:, i * P:(i + 1) * P], src[:, i * P:(i + 1) * P],
                                                c("ident"))
                    t.then_inc(s.turned, 1)

            @block.scalar
            def _(act):
                act.wait_ge(s.sums_ready, 1)
                nc.scalar.activation(w.dec[:, :, :], m.bank[7][:, 0:64].rearrange("p (b h) -> p b h", b=DB),
                                     ACT.Exp).then_inc(s.decayed, 1)
                for b in range(DB + 1):
                    act.wait_ge(s.turned, b + 1)
                    dst = w.hout[:, b, :, :, :] if b < DB else w.hin[:, 0, :, :, :]
                    nc.scalar.activation(dst.rearrange("p i g n -> p (i g n)"), m.bank[4 + b % 2][:, 0:256],
                                         ACT.Copy).then_inc(s.taken, 1)

            @block.vector
            def _(dve):
                nc.vector.tensor_tensor(w.db[:, :, :], m.dt[0:NS, NT, 8:16].unsqueeze(1).broadcast_to([NS, DB, 8]),
                                        c("s_of_b")[0:NS, :].unsqueeze(2).broadcast_to([NS, DB, 8]),
                                        ALU.mult).then_inc(s.dta_ready, 1)
                nc.vector.tensor_tensor(w.bm[:, :, :], w.small[0:NS, 0, 0:P].unsqueeze(1).broadcast_to([NS, DB, P]),
                                        c("s_of_b")[0:NS, :].unsqueeze(2).broadcast_to([NS, DB, P]),
                                        ALU.mult).then_inc(s.b_ready, 1)
                dve.wait_ge(s.decayed, 1)
                for b in range(DB):
                    for g in range(NG):
                        st = w.s0[64 * g:64 * g + 64, b, :].rearrange("p (r d) -> p r d", r=4)
                        i = nc.vector.tensor_tensor(st, st, w.dec[64 * g:64 * g + 64, b, 4 * g:4 * g + 4].unsqueeze(
                            2).broadcast_to([64, 4, HD]), ALU.mult)
                    i.then_inc(s.scaled, 1)
                    dve.wait_ge(s.scaled, b + 1)
                    dve.wait_ge(s.multiplied, b + 1)
                    for g in range(NG):
                        i = nc.vector.tensor_tensor(w.s0[64 * g:64 * g + 64, b, :], w.s0[64 * g:64 * g + 64, b, :],
                                                    m.bank[b % 4][64 * g:64 * g + 64, 256 * g:256 * (g + 1)], ALU.add)
                    i.then_inc(s.added, 1)

            @block.sync
            def _(sp):
                sp.wait_ge(s.taken, DB + 1)
                for i in range(4):
                    sp.dma_start(hd(io.s_ssm)[:, :, i, :], w.hout[:, :, i % 2, i // 2, :]).then_inc(s.stored, 16)
                    sp.dma_start(hd(io.p_ssm)[:, 0, i, :], w.hin[:, 0, i % 2, i // 2, :]).then_inc(s.stored, 16)
                sp.wait_ge(s.stored, 16 * 8)


SUBS = PAGE // CSTRIDE
CW = CSTRIDE * DKV


def load_compression(nc, io, m, sb):
    w = m.cmp = Buffers()
    w.w1 = sb("cmp_w1", [P, 2, 8, 2, CHID])
    w.w2 = sb("cmp_w2", [CHID, 2, HD])
    w.pe = sb("cmp_pe", [P, 2, 16])
    w.pre = sb("cmp_pe_sum", [CHID, 2])
    with stage(nc, "loaded summed") as s:
        with nc.Block() as block:
            @block.sync
            def _(sp):
                for kv in range(2):
                    for j in range(2):
                        src = io.cmp_w1[0, kv, 16 * j:16 * (j + 1), :, :].rearrange("(q s) d h -> (s d) q h", s=2)
                        sp.dma_start(w.w1[:, kv, :, j, :], src).then_inc(s.loaded, 16)
                    sp.dma_start(w.w2[:, kv, :], io.cmp_w2[0, kv, :, :]).then_inc(s.loaded, 16)
                    sp.dma_start(w.pe[:, kv, :], io.cmp_pe[0, kv, :, :].rearrange("(q s) d -> (s d) q", s=2),
                                 allow_slow_non_contiguous=True).then_inc(s.loaded, 16)
                sp.wait_ge(s.loaded, 16 * 8)

            @block.tensor
            def _(pe):
                pe.wait_ge(s.loaded, 16 * 8)
                for kv in range(2):
                    for n in range(16):
                        mm = nc.tensor.matmul(m.bank[0][0:CHID, kv:kv + 1], w.w1[:, kv, n % 8, n // 8, :],
                                              w.pe[:, kv, n:n + 1], start=(n == 0), stop=(n == 15))
                mm.then_inc(s.summed, 1)

            @block.vector
            def _(dve):
                dve.wait_ge(s.summed, 1)
                nc.vector.tensor_copy(w.pre[:, :], m.bank[0][0:CHID, 0:2])


def stage_prompt_compress(nc, io, m):
    c = m.c
    sb = Region(nc, m.att_end, m.mix_start)
    N = SEQ // CSTRIDE
    m.kcT = sb("kcT", [P, N])
    m.vc = sb("vc", [N, DKV])
    m.bias = sb("bias", [P, NH, 256])
    m.prompt_att_start = sb.at
    load_compression(nc, io, m, sb)
    w = m.cmp
    x = sb("rows16", [N, 2, CW])
    xr = sb("rows16_by_group", [N, 2, CW])
    xt = sb("rows16_T", [P, 2, 8, NG, N])
    up = sb("second_half", [CHID, 2, NG, N])
    hid = sb("hidden", [CHID, 2, NG, N])
    kc = sb("kc_tok", [N, DKV])
    sq = sb("kc_square", [N, DKV])
    st = sb("kc_stats", [N, 6])
    with stage(nc, "loaded*2 grouped turned taken summed shifted added hidden_done projected kc_raw squared stats rstd "
                   "normed kc_turned bias_loaded zeroed act_c dve_c") as s:
        with nc.Block() as block:
            @block.sync
            def _(sp):
                for kv, src in enumerate((io.p_k_cmp, io.p_v_cmp)):
                    sp.dma_start(x[:, kv, :], src.rearrange("a b (n s) g d -> (a b n) (s g d)", s=CSTRIDE)
                                 ).then_inc(s.loaded[kv], 16)
                t = m.bias_dram.tensor
                sp.dma_start(m.bias[:, :, :], bass.AP(t, 127, [[BIASW - 1, P], [P * BIASW, NH], [1, 256]])).then_inc(s.bias_loaded, 16)
                sp.wait_ge(s.bias_loaded, 16)

            @block.gpsimd
            def _(pool):
                nc.gpsimd.memset(hid[:, :, :, :], 0.0).then_inc(s.zeroed, 1)

            @block.tensor
            def _(pe):
                for kv in range(2):
                    pe.wait_ge(s.grouped, kv + 1)
                    for a in range(4):
                        n = 4 * kv + a
                        if n >= 2:
                            pe.wait_ge(s.taken, n - 1)
                        for k in range(4):
                            g, q = k % 2, 2 * a + k // 2
                            t = nc.tensor.transpose(m.bank[n % 2][:, k * N:(k + 1) * N],
                                                    xr[:, kv, g * 1024 + q * P:g * 1024 + (q + 1) * P], c("ident")[0:N, 0:N])
                        t.then_inc(s.turned, 1)
                    pe.wait_ge(s.taken, 4 * kv + 4)
                    for q in range(8):
                        mm = nc.tensor.matmul(m.bank[2 + kv][:, 0:NG * N], w.w1[:, kv, q, :, :].rearrange("p j h -> p (j h)"),
                                              xt[:, kv, q, :, :], start=(q == 0), stop=(q == 7))
                    mm.then_inc(s.summed, 1)
                for kv in range(2):
                    pe.wait_ge(s.hidden_done, kv + 1)
                    for g in range(NG):
                        mm = nc.tensor.matmul(m.bank[4 + kv][0:N, g * HD:(g + 1) * HD], hid[:, kv, g, :], w.w2[:, kv, :],
                                              start=True, stop=True)
                    mm.then_inc(s.projected, 1)
                pe.wait_ge(s.normed, 1)
                nc.tensor.transpose(m.bank[6][:, 0:N], kc[:, :], c("ident")[0:N, 0:N]).then_inc(s.kc_turned, 1)

            @block.scalar
            def _(act):
                chain = Chain(act, s.act_c)
                act.wait_ge(s.zeroed, 1)
                for kv in range(2):
                    act.wait_ge(s.summed, kv + 1)
                    nc.scalar.activation(up[:, kv, :, :], m.bank[2 + kv][CHID:P, 0:NG * N].rearrange(
                        "p (g n) -> p g n", g=NG), ACT.Copy).then_inc(s.shifted, 1)
                    act.wait_ge(s.added, kv + 1)
                    nc.scalar.activation(hid[:, kv, :, 0:N - 1], up[:, kv, :, 0:N - 1], ACT.Silu,
                                         bias=w.pre[:, kv:kv + 1]).then_inc(s.hidden_done, 1)
                act.wait_ge(s.kc_raw, 1)
                nc.scalar.activation(sq[:, :], kc[:, :], ACT.Square).then_inc(s.squared, 1)
                act.wait_ge(s.stats, 1)
                chain(nc.scalar.activation(st[:, 2:4], st[:, 0:2], ACT.Ln, scale=1.0 / HD, bias=c("eps")[0:N, :]))
                nc.scalar.activation(st[:, 4:6], st[:, 2:4], ACT.Exp, scale=-0.5).then_inc(s.rstd, 1)

            @block.vector
            def _(dve):
                chain = Chain(dve, s.dve_c)
                for kv in range(2):
                    dve.wait_ge(s.loaded[kv], 16)
                    nc.vector.tensor_copy(xr[:, kv, :].rearrange("p (g s d) -> p g s d", g=NG, s=CSTRIDE),
                                          x[:, kv, :].rearrange("p (s g d) -> p g s d", g=NG, s=CSTRIDE)
                                          ).then_inc(s.grouped, 1)
                    for a in range(4):
                        n = 4 * kv + a
                        dve.wait_ge(s.turned, n + 1)
                        nc.vector.tensor_copy(xt[:, kv, 2 * a:2 * a + 2, :, :],
                                              m.bank[n % 2][:, 0:4 * N].rearrange("p (q g n) -> p q g n", q=2, g=NG)
                                              ).then_inc(s.taken, 1)
                for kv in range(2):
                    dve.wait_ge(s.shifted, kv + 1)
                    nc.vector.tensor_tensor(up[:, kv, :, 0:N - 1], up[:, kv, :, 1:N],
                                            m.bank[2 + kv][0:CHID, 0:NG * N].rearrange("p (g n) -> p g n", g=NG)[:, :, 0:N - 1],
                                            ALU.add).then_inc(s.added, 1)
                dve.wait_ge(s.projected, 2)
                nc.vector.tensor_copy(m.vc[:, :], m.bank[5][0:N, 0:DKV])
                nc.vector.tensor_copy(kc[:, :], m.bank[4][0:N, 0:DKV]).then_inc(s.kc_raw, 1)
                dve.wait_ge(s.squared, 1)
                nc.vector.tensor_reduce(st[:, 0:2], sq[:, :].rearrange("p (g d) -> p g d", g=NG), AX.X,
                                        ALU.add).then_inc(s.stats, 1)
                dve.wait_ge(s.rstd, 1)
                k3 = kc[:, :].rearrange("p (g d) -> p g d", g=NG)
                chain(nc.vector.tensor_tensor(k3, k3, st[:, 4:6].unsqueeze(2).broadcast_to([N, NG, HD]), ALU.mult))
                nc.vector.tensor_tensor(k3, k3, m.kn[0:N, :].unsqueeze(1).broadcast_to([N, NG, HD]),
                                        ALU.mult).then_inc(s.normed, 1)
                dve.wait_ge(s.kc_turned, 1)
                nc.vector.tensor_copy(m.kcT[:, :], m.bank[6][:, 0:N])


def stage_prompt_attention(nc, io, m):
    c = m.c
    assert SEQ // SELB <= 16
    sb = Region(nc, m.prompt_att_start, m.mix_start)
    qp = sb("q_padded", [P, NG, NT, P])
    psel = sb("p_sel", [P, 2, SEQ])
    pwc = sb("p_win_cmp", [P, 2, 768])
    pt = sb("p_T", [P, 4, 512])
    negmax = sb("neg_max", [P, NG * NT, 3])
    sums = sb("row_sums", [P, NG * NT, 3])
    scale = sb("row_scale", [P, NG * NT, 3])
    CMP, SEL, WINB = 0, 1, 2
    CC = 640
    units = [(t, g) for t in range(NT) for g in range(NG)]

    def parts(n):
        t, g = units[n // 2]
        if n % 2 == 0:
            return [(SEL, k, k * P, P) for k in range(t + 1)]
        lo = max(0, t - 4)
        return [(WINB, k, (k - lo) * P, P) for k in range(lo, t + 1)] + [(CMP, 0, CC, 8 * t + 7)]

    def groups(n):
        p = parts(n)
        return [p[i:i + 4] for i in range(0, len(p), 4)]

    first_group = [0]
    for n in range(2 * len(units)):
        first_group.append(first_group[-1] + len(groups(n)))

    with stage(nc, "zeroed") as s:
        with nc.Block() as block:
            @block.gpsimd
            def _(pool):
                nc.gpsimd.memset(qp[:, :, :, :], 0.0)

    with nc.Fori(0, REP) as r, stage(
            nc, "q_ready scored prepared exp_done turned copied_v copied_a weighted finished dve_c act_c") as s:
        with nc.Block() as block:
            @block.tensor
            def _(pe):
                def scores(n):
                    t, g = units[n // 2]
                    if n >= 2:
                        pe.wait_ge(s.exp_done, n - 1)
                    if n % 2 == 0:
                        for a in range(0, (t + 1) * P, 512):
                            b = min(a + 512, (t + 1) * P)
                            mm = nc.tensor.matmul(m.psum[:, a:b], qp[:, g, t, :], m.ksT[:, a:b], start=True, stop=True)
                    else:
                        lo = max(0, t - 4) * P
                        for a in range(lo, (t + 1) * P, 512):
                            b = min(a + 512, (t + 1) * P)
                            nc.tensor.matmul(m.psum[:, 1024 + a - lo:1024 + b - lo], qp[:, g, t, :], m.kwT[:, a:b],
                                             start=True, stop=True)
                        mm = nc.tensor.matmul(m.psum[:, 1024 + CC:1024 + CC + 8 * t + 7], qp[:, g, t, :],
                                              m.kcT[:, 0:8 * t + 7], start=True, stop=True)
                    mm.then_inc(s.scored, 1)

                def copied(G, at_least):
                    pe.wait_ge(s.copied_a if G % 2 else s.copied_v, at_least)

                def turn(n, i):
                    G = first_group[n] + i
                    src = psel if n % 2 == 0 else pwc
                    if G >= 2:
                        copied(G, G // 2)
                    for k, (_, _, col, width) in enumerate(groups(n)[i]):
                        x = nc.tensor.transpose(m.bank[4 + G % 2][0:width, k * P:(k + 1) * P],
                                                src[:, (n // 2) % 2, col:col + width], c("ident"))
                    x.then_inc(s.turned, 1)

                def weight(n, i):
                    t, g = units[n // 2]
                    G = first_group[n] + i
                    copied(G, G // 2 + 1)
                    lo = max(0, t - 4)
                    for k, (br, kt, col, width) in enumerate(groups(n)[i]):
                        v = (m.vc[0:width, g * HD:(g + 1) * HD] if br == CMP else
                             m.v[:, kt, 0 if br == SEL else 1, g * HD:(g + 1) * HD])
                        mm = nc.tensor.matmul(m.bank[6 + (n // 2) % 2][:, br * HD:(br + 1) * HD],
                                              pt[0:width, G % 4, k * P:(k + 1) * P], v,
                                              start=(br == CMP or kt == (0 if br == SEL else lo)),
                                              stop=(br == CMP or kt == t))
                    mm.then_inc(s.weighted, 1)

                pe.wait_ge(s.q_ready, 2)
                scores(0)
                scores(1)
                for n in range(2 * len(units)):
                    if n + 2 < 2 * len(units):
                        scores(n + 2)
                    pe.wait_ge(s.exp_done, n + 1)
                    if n % 2 == 0 and n >= 4:
                        pe.wait_ge(s.finished, n // 2 - 1)
                    k = len(groups(n))
                    for i in range(k):
                        turn(n, i)
                        if i:
                            weight(n, i - 1)
                    weight(n, k - 1)

            def copy_group(engine, sem, copy, n, i):
                G = first_group[n] + i
                engine.wait_ge(s.turned, G + 1)
                if G >= 4:
                    engine.wait_ge(s.weighted, G - 3)
                p = groups(n)[i]
                whole = [x for x in p if x[3] == P]
                if whole:
                    x = copy(pt[:, G % 4, 0:len(whole) * P], m.bank[4 + G % 2][:, 0:len(whole) * P])
                if len(whole) < len(p):
                    k, width = len(p) - 1, p[-1][3]
                    x = copy(pt[0:width, G % 4, k * P:(k + 1) * P], m.bank[4 + G % 2][0:width, k * P:(k + 1) * P])
                x.then_inc(sem, 1)

            @block.scalar
            def _(act):
                def exps(n):
                    t, g = units[n // 2]
                    u = n // 2
                    act.wait_ge(s.prepared, n + 1)
                    if n >= 4:
                        act.wait_ge(s.weighted, first_group[n - 3])
                    if n % 2 == 0:
                        act_ = nc.scalar.activation(psel[:, u % 2, 0:(t + 1) * P], m.psum[:, 0:(t + 1) * P], ACT.Exp,
                                                    bias=negmax[:, u, SEL:SEL + 1], accum_out=sums[:, u, SEL:SEL + 1])
                    else:
                        k = min(t, 4) + 1
                        nc.scalar.activation(pwc[:, u % 2, 0:k * P], m.psum[:, 1024:1024 + k * P], ACT.Exp,
                                             bias=negmax[:, u, WINB:WINB + 1], accum_out=sums[:, u, WINB:WINB + 1])
                        act_ = nc.scalar.activation(pwc[:, u % 2, CC:CC + 8 * t + 7], m.psum[:, 1024 + CC:1024 + CC + 8 * t + 7],
                                                    ACT.Exp, bias=negmax[:, u, CMP:CMP + 1],
                                                    accum_out=sums[:, u, CMP:CMP + 1])
                    act_.then_inc(s.exp_done, 1)

                exps(0)
                for n in range(2 * len(units)):
                    if n + 1 < 2 * len(units):
                        exps(n + 1)
                    for i in range(len(groups(n))):
                        if (first_group[n] + i) % 2:
                            copy_group(act, s.copied_a, lambda o, a: nc.scalar.activation(o, a, ACT.Copy), n, i)

            @block.vector
            def _(dve):
                chain = Chain(dve, s.dve_c)
                for g in range(NG):
                    rows = slice(64 * g, 64 * g + 64)
                    nc.vector.tensor_copy(qp[rows, g, :, :],
                                          m.qT[rows, :, bass.ds(r, 1), :].rearrange("p t o q -> p t (o q)")
                                          ).then_inc(s.q_ready, 1)

                def add(region, table):
                    chain(nc.vector.tensor_tensor(region, region, table, ALU.add))

                def top(region, u, br):
                    return nc.vector.tensor_reduce(negmax[:, u, br:br + 1], region, AX.X, ALU.max, negate=True)

                def prepare(n):
                    t, g = units[n // 2]
                    u = n // 2
                    bias = m.bias[:, bass.ds(g * REP + r, 1), :].rearrange("p o k -> p (o k)")
                    dve.wait_ge(s.scored, n + 1)
                    if n % 2 == 0:
                        lo = max(0, t - 1)
                        add(m.psum[:, lo * P:(t + 1) * P], bias[:, 0:256] if t else bias[:, P:256])
                        i = top(m.psum[:, 0:(t + 1) * P], u, SEL)
                    else:
                        k = min(t, 4) + 1
                        lo = max(0, k - 2)
                        add(m.psum[:, 1024 + lo * P:1024 + k * P], bias[:, 0:256] if t else bias[:, P:256])
                        if t >= 4:
                            add(m.psum[:, 1024:1024 + P], c("far"))
                        top(m.psum[:, 1024:1024 + k * P], u, WINB)
                        first = max(0, 8 * t - 9)
                        col = 159 + 16 * (first - 8 * t)
                        add(m.psum[:, 1024 + CC + first:1024 + CC + 8 * t + 7], bias[:, col:256:16])
                        chain(top(m.psum[:, 1024 + CC:1024 + CC + 8 * t + 7], u, CMP))
                        i = nc.vector.tensor_scalar(negmax[:, u, CMP:CMP + 1], negmax[:, u, CMP:CMP + 1], 1e29, None,
                                                    ALU.min)
                    i.then_inc(s.prepared, 1)

                def finish(u):
                    t, g = units[u]
                    out = m.mix[:, t, bass.ds((g * REP + r) * HD, HD)]
                    gate = m.gates[:, t, bass.ds((g * REP + r) * 3, 3)]
                    o = m.bank[6 + u % 2]
                    chain(nc.vector.tensor_scalar(scale[:, u, :], sums[:, u, :], 1e-30, None, ALU.max))
                    chain(nc.vector.reciprocal(scale[:, u, :], scale[:, u, :]))
                    chain(nc.vector.tensor_tensor(scale[:, u, :], scale[:, u, :], gate, ALU.mult))
                    dve.wait_ge(s.weighted, first_group[2 * u + 2])
                    chain(nc.vector.tensor_scalar(out, o[:, 0:HD], scale[:, u, 0:1], None, ALU.mult))
                    chain(nc.vector.scalar_tensor_tensor(out, o[:, HD:2 * HD], scale[:, u, 1:2], out, ALU.mult, ALU.add))
                    nc.vector.scalar_tensor_tensor(out, o[:, 2 * HD:3 * HD], scale[:, u, 2:3], out, ALU.mult,
                                                   ALU.add).then_inc(s.finished, 1)

                prepare(0)
                for n in range(2 * len(units)):
                    if n + 1 < 2 * len(units):
                        prepare(n + 1)
                    for i in range(len(groups(n))):
                        if (first_group[n] + i) % 2 == 0:
                            copy_group(dve, s.copied_v, nc.vector.tensor_copy, n, i)
                    if n % 2:
                        dve.wait_ge(s.exp_done, n + 1)
                        finish(n // 2)


def prepare_sample_attention(nc, io, m, w):
    with stage(nc, "gates_out gates_in kept zeroed placed") as s:
        with nc.Block() as block:
            @block.sync
            def _(sp):
                rows = lambda o: o.rearrange("o b t g d -> (o b) t (g d)")
                for dst, old, new in ((io.s_k_win, io.cache_k_win, io.kw_new), (io.s_v_win, io.cache_v_win, io.vw_new)):
                    sp.dma_start(rows(dst)[:, 0:WIN - DS, :], rows(old)[:, DS:WIN, :]).then_inc(s.kept, 16)
                    sp.dma_start(rows(dst)[:, WIN - DS:WIN, :], new.rearrange("(b t) c -> b t c", b=DB)).then_inc(s.kept, 16)
                sp.dma_start(m.gate_dram, m.gates[0:NS, NT, :]).then_inc(s.gates_out, 16)
                sp.wait_ge(s.gates_out, 16)
                for hb in range(2):
                    for b in range(B4):
                        for g in range(NG):
                            src = bass.AP(m.gate_dram.tensor, (hb * 16 + b * DS) * 24 + g * 12, [[24, DS], [3, REP], [1, 3]])
                            sp.dma_start(w.gate[b * 32 + g * 16:b * 32 + g * 16 + 16, hb, :], src).then_inc(s.gates_in, 16)
                sp.wait_ge(s.gates_in, 16 * 16)
                sp.wait_ge(s.kept, 16 * 4)

            @block.gpsimd
            def _(pool):
                nc.gpsimd.memset(w.q_all[:, :, :, :], 0.0).then_inc(s.zeroed, 1)
                nc.gpsimd.memset(w.hid[:, :, :], 0.0)
                nc.gpsimd.memset(w.pc[:, :], 0.0)
                nc.gpsimd.memset(w.imp[:, :], 0.0)
                nc.gpsimd.memset(w.score[:, SCORES - 1:SCORES], 2e30)

            @block.vector
            def _(dve):
                dve.wait_ge(s.zeroed, 1)
                for g in range(NG):
                    rows = slice(64 * g, 64 * g + 64)
                    for b in range(B4):
                        for hb in range(2):
                            q0 = (hb * B4 + b) * DS
                            nc.vector.tensor_copy(
                                w.q_all[rows, hb, b, b * 32 + g * 16:b * 32 + g * 16 + 16].rearrange("p (t r) -> p r t", t=DS),
                                m.qTs[rows, :, q0:q0 + DS])


SCORES = PAST // SELB + 1
RING = 4


def sample_attention_turn(nc, io, m, w, hb):
    c = m.c
    NA, NB_, NC_ = 16, 8, 8
    caches = [io.cache_k_cmp, io.cache_v_cmp, io.cache_k_sel, io.cache_v_sel]
    chunks = [(caches[kv], b, h) for b in range(B4) for kv in range(2) for h in range(2)]
    chunks += [(caches[2], b, h) for h in range(2) for b in range(B4)]
    chunks += [(caches[3], b, h) for b in range(B4) for h in range(2)]
    fill_a = lambda u, i: 8 * u + i
    fill_b = lambda k, i: 64 + i if k == 0 else 70 + 4 * (k - 1) + i
    fill_k = lambda i: 68 + i
    fill_w = lambda b: 98 + b
    fill_p = lambda i: 102 + i
    PCMP, PWIN, PNEW, PSEL = 0, 2, 6, 8
    p_pieces = ([(w.pc, k * P, P) for k in range(2)] + [(w.sw, k * P, P) for k in range(4)] +
                [(w.ss, PAST, DS), (w.sw, WIN, DS)] + [(w.ss, k * P, P) for k in range(32)])

    with stage(nc, "rows_ready v_used win_loaded kn_ready q_ready grouped turned copied_v copied_a summed "
                   "shifted added hidden_done projected taken squared k_sums k_rstd k_normed c_scored c_ready c_exp "
                   "c_weights imp_done masked s_scored s_taken w_scored n_scored w_taken w_ready s_ready w_exp s_exp "
                   "p_final o_ready stored dve_c act_c") as s:
        with nc.Block() as block:
            @block.sync
            def _(sp):
                for dst, src in ((w.wk, io.cache_k_win), (w.wv, io.cache_v_win)):
                    v = src.rearrange("o b (p k) g d -> p (o b) (k g d)", k=4)
                    sp.dma_start(dst[:, :, :], v[:, bass.ds(hb * B4, B4), :]).then_inc(s.win_loaded, 16)
                vs = io.s_v_sel.rearrange("o b t g d -> t (o b) (g d)")
                vw = io.vw_new.rearrange("(b t) c -> t b c", b=DB)
                sp.dma_start(w.vn[:, :, 0, :], vs[:, bass.ds(hb * B4, B4), :]).then_inc(s.win_loaded, 16)
                sp.dma_start(w.vn[:, :, 1, :], vw[:, bass.ds(hb * B4, B4), :]).then_inc(s.win_loaded, 16)
                sp.wait_ge(s.o_ready, 1)
                for b in range(B4):
                    for g in range(NG):
                        dst = m.o_dram[bass.ds(hb * B4 * DS + b * DS, DS), :].rearrange("t (g r d) -> t g r d", g=NG, r=REP)
                        sp.dma_start(dst[:, g, :, :], w.os[g * 16:g * 16 + 16, b, g * HD:(g + 1) * HD]
                                     ).then_inc(s.stored, 16)
                sp.wait_ge(s.stored, 16 * 8)

            @block.gpsimd
            def _(pool):
                pool.wait_ge(s.rows_ready, 1)
                for n, (cache, b, h) in enumerate(chunks):
                    k = n - RING
                    if 0 <= k < NA:
                        pool.wait_ge(s.grouped, k + 1)
                    elif NA <= k < NA + NB_:
                        pool.wait_ge(s.turned, fill_b(k - NA, 3) + 1)
                    elif k >= 0:
                        pool.wait_ge(s.v_used, k - NA - NB_ + 1)
                    nc.gpsimd.indirect_dma_start(
                        w.ring[:, n % RING, :], None,
                        cache.rearrange("o n (a s) g d -> (o n a) (s g d)", s=CSTRIDE),
                        bass.IndirectOffsetOnAxis(ap=w.rows[:, 2 * b + h:2 * b + h + 1], axis=0)
                    ).then_inc(w.landed[n % RING], 16)

            def chunk_here(engine, n):
                engine.wait_ge(w.landed[n % RING], hb * (16 * len(chunks) // RING) + 16 * (n // RING + 1))

            @block.tensor
            def _(pe):
                def bank_free(f):
                    if f >= 2:
                        pe.wait_ge(s.copied_a if f % 2 else s.copied_v, f // 2)

                def turn(f, pieces):
                    bank_free(f)
                    for k, (src, width) in enumerate(pieces):
                        x = nc.tensor.transpose(m.bank[4 + f % 2][0:width, k * P:(k + 1) * P], src, c("ident"))
                    x.then_inc(s.turned, 1)

                def copied(f):
                    pe.wait_ge(s.copied_a if f % 2 else s.copied_v, f // 2 + 1)

                def turn_a(u, i):
                    n = 2 * u + i // 4
                    pe.wait_ge(s.grouped, n + 1)
                    a = i % 4
                    turn(fill_a(u, i), [(w.xr[:, n % 2, g * 1024 + q * P:g * 1024 + (q + 1) * P], P)
                                        for q in (2 * a, 2 * a + 1) for g in range(NG)])

                def project(u):
                    pe.wait_ge(s.hidden_done, u + 1)
                    if u >= 2:
                        pe.wait_ge(s.taken, u - 1)
                    for h in range(2):
                        for g in range(NG):
                            mm = nc.tensor.matmul(m.bank[2 + u % 2][:, (2 * h + g) * HD:(2 * h + g + 1) * HD],
                                                  w.hid[:, g, h * P:(h + 1) * P], m.cmp.w2[:, u % 2, :],
                                                  start=True, stop=True)
                    mm.then_inc(s.projected, 1)

                for i in range(8):
                    turn_a(0, i)
                for u in range(8):
                    if u >= 2:
                        pe.wait_ge(s.added, u - 1)
                    for q in range(8):
                        if q == 0:
                            copied(fill_a(u, 6))
                            copied(fill_a(u, 7))
                        mm = nc.tensor.matmul(m.bank[u % 2][:, :], m.cmp.w1[:, u % 2, q, :, :].rearrange("p j h -> p (j h)"),
                                              w.xt[:, u % 2, q, :, :], start=(q == 0), stop=(q == 7))
                        if q == 7:
                            mm.then_inc(s.summed, 1)
                        if u < 7:
                            turn_a(u + 1, q)
                    if u:
                        project(u - 1)
                project(7)

                def turn_b(k, i):
                    if i == 0:
                        chunk_here(pe, NA + k)
                    x = w.ring[:, (NA + k) % RING, :]
                    turn(fill_b(k, i), [(x[:, (4 * i + j) * P:(4 * i + j + 1) * P], P) for j in range(4)])

                for i in range(4):
                    turn_b(0, i)
                pe.wait_ge(s.k_normed, 1)
                for i in range(2):
                    turn(fill_k(i), [(w.kraw[:, (4 * i + j) * P:(4 * i + j + 1) * P], P) for j in range(4)])
                copied(fill_k(0))
                copied(fill_k(1))
                pe.wait_ge(s.q_ready, 1)
                for b in range(B4):
                    mm = nc.tensor.matmul(m.bank[6][:, 0:255], w.q[:, b, :], w.kcT[:, b * 256:b * 256 + 255],
                                          start=(b == 0), stop=(b == B4 - 1))
                mm.then_inc(s.c_scored, 1)
                for k in range(NB_):
                    if k == B4:
                        pe.wait_ge(s.s_taken, 4)
                    if k == 2:
                        pe.wait_ge(s.c_weights, 1)
                        nc.tensor.matmul(m.bank[7][:, 0:255], c("rep_sum"), w.pc[:, 0:255], start=True,
                                         stop=True).then_inc(s.imp_done, 1)
                    if k == 0:
                        pe.wait_ge(s.taken, 8)
                        pe.wait_ge(s.added, 8)
                    for i in range(4):
                        copied(fill_b(k, i))
                        mm = nc.tensor.matmul(m.bank[i][:, :], w.q[:, k % B4, :], w.kt[:, k % 2, i * 512:(i + 1) * 512],
                                              start=(k % B4 == 0), stop=(k % B4 == B4 - 1))
                        if i == 3:
                            mm.then_inc(s.s_scored, 1)
                        if k + 1 < NB_:
                            turn_b(k + 1, i)
                pe.wait_ge(s.win_loaded, 64)
                for b in range(B4):
                    turn(fill_w(b), [(w.wk[:, b, j * P:(j + 1) * P], P) for j in range(4)])
                pe.wait_ge(s.c_exp, 1)
                for b in range(B4):
                    copied(fill_w(b))
                    mm = nc.tensor.matmul(m.bank[6][:, :], w.q[:, b, :], w.kt[:, 0, b * 512:(b + 1) * 512],
                                          start=(b == 0), stop=(b == B4 - 1))
                mm.then_inc(s.w_scored, 1)
                pe.wait_ge(s.masked, 1)
                pe.wait_ge(s.kn_ready, 1)
                for br in range(2):
                    for b in range(B4):
                        mm = nc.tensor.matmul(m.bank[7][:, 4 * br:4 * br + 4], w.q[:, b, :], w.kn[:, br, b * DS:(b + 1) * DS],
                                              start=(b == 0), stop=(b == B4 - 1))
                mm.then_inc(s.n_scored, 1)
                pe.wait_ge(s.p_final, 3)
                for i in range(10):
                    turn(fill_p(i), [(src[:, col:col + width], width) for src, col, width in p_pieces[4 * i:4 * i + 4]])
                copied(fill_p(8))
                copied(fill_p(9))
                pe.wait_ge(s.w_taken, 2)
                for b in range(B4):
                    terms = [(w.pt[:, PCMP + h, :], w.vc[:, b, h, :]) for h in range(2)]
                    terms += [(w.pt[:, PWIN + k, :], w.wv[:, b, k * P:(k + 1) * P]) for k in range(4)]
                    terms += [(w.pt[0:DS, PNEW + br, :], w.vn[:, b, br, :]) for br in range(2)]
                    terms += [(w.pt[:, PSEL + k, :], None) for k in range(32)]
                    for n, (weights, v) in enumerate(terms):
                        h, k = divmod(n - PSEL, 16)
                        if v is None:
                            chunk = NA + NB_ + 2 * b + h
                            if k == 0:
                                chunk_here(pe, chunk)
                            v = w.ring[:, chunk % RING, k * P:(k + 1) * P]
                        mm = nc.tensor.matmul(m.bank[7][0:32, b * P:(b + 1) * P], weights[:, b * 32:(b + 1) * 32], v,
                                              start=(n == 0), stop=(n == len(terms) - 1))
                        if n >= PSEL and k == 15:
                            mm.then_inc(s.v_used, 1)

            def copy(engine, f, dst, src_view=None, width=P):
                act = engine is w.act
                engine.wait_ge(s.turned, f + 1)
                src = m.bank[4 + f % 2][0:width, :] if src_view is None else src_view(m.bank[4 + f % 2])
                x = nc.scalar.activation(dst, src, ACT.Copy) if act else nc.vector.tensor_copy(dst, src)
                x.then_inc(s.copied_a if act else s.copied_v, 1)

            def copy_a(engine, u, i):
                if i < 2 and u >= 2:
                    engine.wait_ge(s.summed, u - 1)
                h, a = divmod(i, 4)
                copy(engine, fill_a(u, i), w.xt[:, u % 2, 2 * a:2 * a + 2, :, h * P:(h + 1) * P],
                     lambda bank: bank[:, :].rearrange("p (q g n) -> p q g n", q=2, g=NG))

            def copy_b(engine, k, i):
                if k >= 2 and i < 2:
                    engine.wait_ge(s.s_scored, k - 1)
                copy(engine, fill_b(k, i), w.kt[:, k % 2, i * 512:(i + 1) * 512])

            def copy_w(engine, b):
                if b < 2:
                    engine.wait_ge(s.s_scored, NB_ - 1)
                copy(engine, fill_w(b), w.kt[:, 0, b * 512:(b + 1) * 512])

            def copy_p(engine, i):
                if i == 1:
                    engine.wait_ge(s.turned, fill_p(1) + 1)
                    bank = m.bank[4 + fill_p(1) % 2]
                    nc.scalar.activation(w.pt[:, 4:6, :].rearrange("p a b -> p (a b)"), bank[:, 0:256], ACT.Copy)
                    nc.scalar.activation(w.pt[0:DS, 6:8, :].rearrange("p a b -> p (a b)"), bank[0:DS, 256:512],
                                         ACT.Copy).then_inc(s.copied_a, 1)
                else:
                    copy(engine, fill_p(i), w.pt[:, 4 * i:4 * i + 4, :].rearrange("p a b -> p (a b)"))

            @block.scalar
            def _(act):
                w.act = act
                chain = Chain(act, s.act_c)
                nc.scalar.activation(w.q[:, :, :], w.q_all[:, bass.ds(hb, 1), :, :].rearrange("p o b q -> p (o b) q"),
                                     ACT.Copy).then_inc(s.q_ready, 1)
                for i in (1, 3, 5, 7):
                    copy_a(act, 0, i)
                for u in range(8):
                    if u < 7:
                        for i in (1, 3, 5, 7):
                            copy_a(act, u + 1, i)
                    act.wait_ge(s.summed, u + 1)
                    if u >= 1:
                        act.wait_ge(s.hidden_done, u)
                    nc.scalar.activation(w.up[:, :, :], m.bank[u % 2][CHID:P, :].rearrange("p (g n) -> p g n", g=NG),
                                         ACT.Copy).then_inc(s.shifted, 1)
                    act.wait_ge(s.added, u + 1)
                    if u >= 1:
                        act.wait_ge(s.projected, u)
                    nc.scalar.activation(w.hid[:, :, 0:255], w.up[:, :, 0:255], ACT.Silu,
                                         bias=m.cmp.pre[:, u % 2:u % 2 + 1]).then_inc(s.hidden_done, 1)
                for i in (1, 3):
                    copy_b(act, 0, i)
                act.wait_ge(s.taken, 7)
                act.wait_ge(s.turned, 64)
                nc.scalar.activation(w.sq[:, :], w.kraw[:, :], ACT.Square).then_inc(s.squared, 1)
                act.wait_ge(s.k_sums, 1)
                chain(nc.scalar.activation(w.kst[:, 16:32], w.kst[:, 0:16], ACT.Ln, scale=1.0 / HD, bias=c("eps")))
                nc.scalar.activation(w.kst[:, 32:48], w.kst[:, 16:32], ACT.Exp, scale=-0.5).then_inc(s.k_rstd, 1)
                copy(act, fill_k(1), w.kcT[:, 512:1024])
                act.wait_ge(s.c_ready, 1)
                nc.scalar.activation(w.pc[:, 0:255], m.bank[6][:, 0:255], ACT.Exp, bias=w.nm[:, 0:1],
                                     accum_out=w.sum[:, 0:1]).then_inc(s.c_exp, 1)
                for k in range(1, NB_):
                    for i in (1, 3):
                        copy_b(act, k, i)
                for b in (1, 3):
                    copy_w(act, b)
                act.wait_ge(s.w_ready, 1)
                nc.scalar.activation(w.sw[:, :], w.sw[:, :], ACT.Exp, bias=w.nm[:, 1:2],
                                     accum_out=w.sum[:, 1:2]).then_inc(s.w_exp, 1)
                act.wait_ge(s.s_ready, 1)
                nc.scalar.activation(w.ss[:, :], w.ss[:, :], ACT.Exp, bias=w.nm[:, 2:3],
                                     accum_out=w.sum[:, 2:3]).then_inc(s.s_exp, 1)
                for i in (1, 3, 5, 7, 9):
                    copy_p(act, i)
                act.wait_ge(s.v_used, 8)
                nc.scalar.activation(w.os[:, :, :].rearrange("p b x -> p (b x)"), m.bank[7][0:32, :],
                                     ACT.Copy).then_inc(s.o_ready, 1)

            @block.vector
            def _(dve):
                chain = Chain(dve, s.dve_c)
                nc.vector.tensor_copy(w.rows[:, :], m.rows[:, bass.ds(hb * 2 * B4, 2 * B4)]).then_inc(s.rows_ready, 1)
                nc.vector.tensor_copy(w.kn[:, 0, :], m.ksTs[:, bass.ds(hb * 16, 16)])
                nc.vector.tensor_copy(w.kn[:, 1, :], m.kwTs[:, bass.ds(hb * 16, 16)]).then_inc(s.kn_ready, 1)
                nc.vector.tensor_copy(w.gt[:, :], w.gate[:, bass.ds(hb, 1), :].rearrange("p o x -> p (o x)"))

                def group(n):
                    chunk_here(dve, n)
                    if n >= 2:
                        dve.wait_ge(s.turned, 4 * (n - 1))
                    nc.vector.tensor_copy(w.xr[:, n % 2, :].rearrange("p (g s d) -> p g s d", g=NG, s=CSTRIDE),
                                          w.ring[:, n % RING, :].rearrange("p (s g d) -> p g s d", g=NG, s=CSTRIDE)
                                          ).then_inc(s.grouped, 1)

                def take(u):
                    dve.wait_ge(s.projected, u + 1)
                    dst = (w.kraw[:, (u // 2) * 256:(u // 2 + 1) * 256] if u % 2 == 0 else
                           w.vc[:, u // 2, :, :].rearrange("p h x -> p (h x)"))
                    nc.vector.tensor_copy(dst, m.bank[2 + u % 2][:, 0:256]).then_inc(s.taken, 1)

                group(0)
                group(1)
                for i in (0, 2, 4, 6):
                    copy_a(dve, 0, i)
                for u in range(8):
                    if u < 7:
                        group(2 * u + 2)
                        for i in (0, 2):
                            copy_a(dve, u + 1, i)
                        group(2 * u + 3)
                        for i in (4, 6):
                            copy_a(dve, u + 1, i)
                    if u:
                        take(u - 1)
                    dve.wait_ge(s.shifted, u + 1)
                    nc.vector.tensor_tensor(w.up[:, :, 0:255], w.up[:, :, 1:256],
                                            m.bank[u % 2][0:CHID, :].rearrange("p (g n) -> p g n", g=NG)[:, :, 0:255],
                                            ALU.add).then_inc(s.added, 1)
                take(7)
                for i in (0, 2):
                    copy_b(dve, 0, i)
                dve.wait_ge(s.squared, 1)
                nc.vector.tensor_reduce(w.kst[:, 0:16], w.sq[:, :].rearrange("p (a d) -> p a d", d=HD), AX.X,
                                        ALU.add).then_inc(s.k_sums, 1)
                dve.wait_ge(s.k_rstd, 1)
                k3 = w.kraw[:, :].rearrange("p (a d) -> p a d", d=HD)
                chain(nc.vector.tensor_tensor(k3, k3, w.kst[:, 32:48].unsqueeze(2).broadcast_to([P, 16, HD]), ALU.mult))
                nc.vector.tensor_tensor(k3, k3, m.kn[:, :].unsqueeze(1).broadcast_to([P, 16, HD]),
                                        ALU.mult).then_inc(s.k_normed, 1)
                copy(dve, fill_k(0), w.kcT[:, 0:512])
                dve.wait_ge(s.c_scored, 1)
                near = m.bank[6][:, 247:255]
                chain(nc.vector.tensor_tensor(near, near, m.srow[:, 15:128:16], ALU.add))
                nc.vector.tensor_reduce(w.nm[:, 0:1], m.bank[6][:, 0:255], AX.X, ALU.max,
                                        negate=True).then_inc(s.c_ready, 1)
                for k in (1,):
                    for i in (0, 2):
                        copy_b(dve, k, i)
                dve.wait_ge(s.c_exp, 1)
                chain(nc.vector.tensor_scalar(w.rs[:, 0:1], w.sum[:, 0:1], 1e-30, None, ALU.max))
                chain(nc.vector.reciprocal(w.rs[:, 0:1], w.rs[:, 0:1]))
                nc.vector.tensor_scalar(w.pc[:, 0:255], w.pc[:, 0:255], w.rs[:, 0:1], None, ALU.mult
                                        ).then_inc(s.c_weights, 1)
                for i in (0, 2):
                    copy_b(dve, 2, i)
                dve.wait_ge(s.imp_done, 1)
                chain(nc.vector.tensor_copy(w.imp[:, 1:256], m.bank[7][:, 0:255]))
                chain(nc.vector.tensor_reduce(w.score[:, 0:64], w.imp[:, 1:257].rearrange("p (j x) -> p j x", x=4),
                                              AX.X, ALU.add))
                chain(nc.vector.tensor_tensor(w.score[:, 0:64], w.score[:, 0:64], w.imp[:, 0:256:4], ALU.add))
                chain(nc.vector.memset(w.score[:, 0:64:63], 1e30))
                chain(nc.vector.max(w.top[:, 0:8], w.score[:, :]))
                chain(nc.vector.match_replace(w.left[:, :], w.top[:, 0:8], w.score[:, :], -1.0))
                chain(nc.vector.max(w.top[:, 8:16], w.left[:, :]))
                chain(nc.vector.match_replace(w.left[:, :], w.top[:, 8:16], w.left[:, :], -1.0))
                nc.vector.tensor_scalar(w.mask[:, :], w.left[:, 0:64], 0.0, NEG, ALU.is_ge, ALU.mult).then_inc(s.masked, 1)
                nc.vector.tensor_scalar(w.pc[:, 0:255], w.pc[:, 0:255], w.gt[:, 0:1], None,
                                        ALU.mult).then_inc(s.p_final, 1)
                dve.wait_ge(s.masked, 1)
                dve.wait_ge(s.p_final, 1)
                for k in (3,):
                    for i in (0, 2):
                        copy_b(dve, k, i)

                def take_scores(h):
                    dve.wait_ge(s.s_scored, 4 * (h + 1))
                    for i in range(4):
                        nc.vector.tensor_tensor(
                            w.ss[:, h * 2048 + i * 512:h * 2048 + (i + 1) * 512].rearrange("p (s j x) -> p s j x", s=4, x=4),
                            m.bank[i][:, :].rearrange("p (s j x) -> p s j x", s=4, x=4),
                            w.mask[:, 32 * h:32 * h + 32].unsqueeze(1).unsqueeze(3).broadcast_to([P, 4, 32, 4]),
                            ALU.add).then_inc(s.s_taken, 1)

                for i in (0, 2):
                    copy_b(dve, 4, i)
                take_scores(0)
                for k in range(5, NB_):
                    for i in (0, 2):
                        copy_b(dve, k, i)
                for b in (0, 2):
                    copy_w(dve, b)
                dve.wait_ge(s.w_scored, 1)
                nc.vector.tensor_copy(w.sw[:, 0:WIN], m.bank[6][:, :]).then_inc(s.w_taken, 1)
                dve.wait_ge(s.n_scored, 1)
                nc.vector.tensor_tensor(w.sw[:, WIN:WIN + DS], m.bank[7][:, 4:8], m.srow[:, P:P + DS], ALU.add)
                nc.vector.tensor_tensor(w.ss[:, PAST:PAST + DS], m.bank[7][:, 0:4], m.srow[:, P:P + DS],
                                        ALU.add).then_inc(s.w_taken, 1)
                dve.wait_ge(s.w_taken, 2)
                old = w.sw[:, 0:WIN].rearrange("p (k n) -> p k n", k=4)
                chain(nc.vector.tensor_tensor(old[:, :, 0], old[:, :, 0], c("win_old"), ALU.add))
                chain(nc.vector.tensor_tensor(old[:, :, 96:128], old[:, :, 96:128],
                                              m.srow[:, 0:P].rearrange("p (n k) -> p k n", k=4), ALU.add))
                nc.vector.tensor_reduce(w.nm[:, 1:2], w.sw[:, :], AX.X, ALU.max, negate=True).then_inc(s.w_ready, 1)
                take_scores(1)
                dve.wait_ge(s.s_taken, 8)
                near = w.ss[:, 2048:4096].rearrange("p (s n) -> p s n", s=16)[:, :, 120:128]
                chain(nc.vector.tensor_tensor(near, near, m.srow[:, 0:P].rearrange("p (n s) -> p s n", s=16), ALU.add))
                nc.vector.tensor_reduce(w.nm[:, 2:3], w.ss[:, :], AX.X, ALU.max, negate=True).then_inc(s.s_ready, 1)
                for k, (buf, done) in enumerate(((w.sw, s.w_exp), (w.ss, s.s_exp))):
                    a = slice(k + 1, k + 2)
                    dve.wait_ge(done, 1)
                    chain(nc.vector.tensor_scalar(w.rs[:, a], w.sum[:, a], 1e-30, None, ALU.max))
                    chain(nc.vector.reciprocal(w.rs[:, a], w.rs[:, a]))
                    gate = w.gt[:, 2:3] if k == 0 else w.gt[:, 1:2]
                    nc.vector.tensor_scalar(buf[:, :], buf[:, :], w.rs[:, a], gate, ALU.mult,
                                            ALU.mult).then_inc(s.p_final, 1)
                for i in (0, 2, 4, 6, 8):
                    copy_p(dve, i)


def stage_sample_attention(nc, io, m):
    sb = Region(nc, m.sample_end, m.mix_start)
    m.gate_dram = nc.dram_tensor("gates_by_token", (NS, 3 * NH), F32, kind="Internal").ap()
    m.o_dram = nc.dram_tensor("attention_by_token", (NS, DATT), F32, kind="Internal").ap()
    w = Buffers()
    load_compression(nc, io, m, sb)
    w.ring = sb("cache_ring", [P, RING, CW])
    both = sb("rows_T_or_weights_T", [P, 2 * 8 * NG * 256])
    w.xt = both[:, :].rearrange("p (u q g n) -> p u q g n", u=2, q=8, g=NG)
    w.pt = both[:, 0:40 * P].rearrange("p (k n) -> p k n", k=40)
    both = sb("rows_grouped_or_scores", [P, PAST + DS])
    w.xr = both[:, 0:2 * CW].rearrange("p (k x) -> p k x", k=2)
    w.sq = both[:, 0:1024]
    w.ss = both[:, :]
    w.kt = sb("keys_T", [P, 2, CW])
    w.wk = sb("win_k", [P, B4, 4 * DKV])
    w.wv = sb("win_v", [P, B4, 4 * DKV])
    w.vn = sb("new_v", [DS, B4, 2, DKV])
    w.kn = sb("new_k", [P, 2, 16])
    w.up = sb("second_half_s", [CHID, NG, 256])
    w.hid = sb("hidden_s", [CHID, NG, 256])
    w.kraw = sb("kc_s", [P, 1024])
    w.kcT = sb("kcT_s", [P, 1024])
    w.vc = sb("vc_s", [P, B4, 2, DKV])
    w.kst = sb("kc_stats_s", [P, 48])
    w.pc = sb("p_cmp_s", [P, 256])
    w.imp = sb("importance", [P, 257])
    w.score = sb("score", [P, SCORES])
    w.left = sb("not_selected", [P, SCORES])
    w.top = sb("top", [P, 16])
    w.mask = sb("block_mask", [P, 64])
    w.sw = sb("p_win_s", [P, WIN + DS])
    w.os = sb("out_s", [32, B4, P])
    w.q_all = sb("q_padded_all", [P, 2, B4, P])
    w.q = sb("q_padded_s", [P, B4, P])
    w.gate = sb("gate_rows", [P, 2, 3])
    w.gt = sb("gate_rows_now", [P, 3])
    w.rows = sb("rows_now", [P, 2 * B4], U32)
    w.nm = sb("neg_max_s", [P, 3])
    w.sum = sb("row_sums_s", [P, 3])
    w.rs = sb("row_scale_s", [P, 3])
    prepare_sample_attention(nc, io, m, w)
    with ExitStack() as ctx:
        w.landed = [ctx.enter_context(nc.semaphore(f"ring_landed_{i}")) for i in range(RING)]
        with nc.Fori(0, 2) as hb:
            sample_attention_turn(nc, io, m, w, hb)
    with stage(nc, "loaded") as s:
        with nc.Block() as block:
            @block.sync
            def _(sp):
                sp.dma_start(m.mix[0:NS, NT, 0:DATT], m.o_dram).then_inc(s.loaded, 16)
                sp.wait_ge(s.loaded, 16)


F32R = mybir.dt.float32r
HI, LO = 0, 1
TERMS = ((HI, HI), (HI, LO), (LO, HI))


def stage_finish_mixer(nc, io, m):
    c = m.c
    low = Region(nc, m.base_end, m.mix_start)
    m.u2 = low("u_parts", [P, 2, KT, TOK], F32R)
    m.gT_start = low.at
    raw = nc.alloc_sbuf_tensor_at("w_out_raw", [P, KT, DM], F32, offset=m.base_end)
    wo = low("w_out", [P, 2, KT, DM], F32R)
    mT = low("mixT", [P, 2, 2, KT, P], F32R)
    x = low("x_again", [P, 3, DM])
    ut = low("u_whole", [P, KT, P])
    ss = nc.alloc_sbuf_tensor_at("ss2", [P, 4], F32, offset=low.at)
    xp = io.x_prompt.rearrange("o (n p) c -> p (o n) c", p=P)
    hp = io.h_dram[0:SEQ, :].rearrange("(n p) c -> p n c", p=P)
    n = NT + 1
    rows = [P] * NT + [NS]
    four = lambda bank, r: bank[:, :].rearrange("p (k q) -> p k q", k=4)[:, :, 0:r]
    with stage(nc, "x_loaded*3 w_loaded*8 w_hi w_split turned mT_hi mT_ready mixed h_ready h_stored h_normed "
                   "h_turned u_whole u_hi u_taken h_rstd act_c") as s:
        with nc.Block() as block:
            @block.sync
            def _(sp):
                def store(j):
                    sp.wait_ge(s.h_ready, 2 * j + 2)
                    sp.dma_start(hp[:, j, :] if j < NT else io.h_dram[SEQ:TOK, :], m.mix[0:rows[j], j, :]
                                 ).then_inc(s.h_stored, 16)

                for j in range(n):
                    if j >= 3:
                        sp.wait_ge(s.h_turned, 2 * (j - 2))
                    sp.dma_start(x[0:rows[j], j % 3, :], xp[:, j, :] if j < NT else
                                 io.x_sample.rearrange("b t c -> (b t) c")).then_inc(s.x_loaded[j % 3], 16)
                    if j == 0:
                        for k in range(KT):
                            sp.dma_start(raw[:, k, :], io.w_out[0, k * P:(k + 1) * P, :]).then_inc(s.w_loaded[k], 16)
                    if j >= 3:
                        store(j - 3)
                for j in range(n - 3, n):
                    store(j)
                sp.wait_ge(s.h_stored, 16 * n)

            @block.scalar
            def _(act):
                chain = Chain(act, s.act_c)

                def mix_hi(j):
                    for h in range(2):
                        act.wait_ge(s.turned, 2 * j + h + 1)
                        if j >= 2:
                            act.wait_ge(s.mixed, 2 * (j - 1))
                        nc.scalar.activation(mT[:, j % 2, HI, 4 * h:4 * h + 4, 0:rows[j]], four(m.bank[6 + h], rows[j]),
                                             ACT.Copy).then_inc(s.mT_hi, 1)

                def statistics(j):
                    r = rows[j]
                    act.wait_ge(s.h_ready, 2 * j + 2)
                    chain(nc.scalar.activation(x[0:r, j % 3, :], m.mix[0:r, j, :], ACT.Square, accum_out=ss[0:r, 0:1]))
                    chain(nc.scalar.activation(ss[0:r, 1:2], ss[0:r, 0:1], ACT.Ln, scale=1.0 / DM, bias=c("eps")[0:r, :]))
                    nc.scalar.activation(ss[0:r, 2 + j % 2:3 + j % 2], ss[0:r, 1:2], ACT.Exp,
                                         scale=-0.5).then_inc(s.h_rstd, 1)

                mix_hi(0)
                for k in range(KT):
                    act.wait_ge(s.w_loaded[k], 16)
                    nc.scalar.activation(wo[:, HI, k, :], raw[:, k, :], ACT.Copy).then_inc(s.w_hi, 1)
                for j in range(n + 1):
                    if j + 1 < n:
                        mix_hi(j + 1)
                    if j >= 1:
                        i = j - 1
                        statistics(i)
                        for h in range(2):
                            act.wait_ge(s.u_whole, 2 * i + h + 1)
                            nc.scalar.activation(m.u2[:, HI, 4 * h:4 * h + 4, i * P:i * P + rows[i]],
                                                 ut[:, 4 * h:4 * h + 4, 0:rows[i]], ACT.Copy).then_inc(s.u_hi, 1)

            @block.tensor
            def _(pe):
                def turn(src, r, banks, sem):
                    for k in range(KT):
                        i = nc.tensor.transpose(m.bank[banks[k // 4]][:, (k % 4) * P:(k % 4) * P + r],
                                                src[:, k * P:(k + 1) * P], c("ident")[0:r, 0:r])
                        if k % 4 == 3:
                            i.then_inc(sem, 1)

                def turn_mix(j):
                    if j >= 1:
                        pe.wait_ge(s.mT_ready, 2 * j)
                    turn(m.mix[0:rows[j], j, :], rows[j], (6, 7), s.turned)

                def turn_h(j):
                    pe.wait_ge(s.h_normed, j + 1)
                    if j >= 1:
                        pe.wait_ge(s.u_whole, 2 * j)
                    turn(x[0:rows[j], j % 3, :], rows[j], (4, 5), s.h_turned)

                turn_mix(0)
                for j in range(n):
                    r = rows[j]
                    if j + 1 < n:
                        turn_mix(j + 1)
                    pe.wait_ge(s.mT_ready, 2 * j + 2)
                    if j >= 2:
                        pe.wait_ge(s.h_ready, 2 * (j - 1))
                    for h in range(2):
                        for k in range(KT):
                            if j == 0 and h == 0:
                                pe.wait_ge(s.w_split, k + 1)
                            for a, b in TERMS:
                                mm = nc.tensor.matmul(m.bank[2 * (j % 2) + h][0:r, :], mT[:, j % 2, a, k, 0:r],
                                                      wo[:, b, k, h * 512:(h + 1) * 512],
                                                      start=(k == 0 and (a, b) == TERMS[0]),
                                                      stop=(k == KT - 1 and (a, b) == TERMS[-1]))
                        mm.then_inc(s.mixed, 1)
                    if j >= 1:
                        turn_h(j - 1)
                turn_h(n - 1)

            @block.vector
            def _(dve):
                def mix_lo(j):
                    for h in range(2):
                        dve.wait_ge(s.mT_hi, 2 * j + h + 1)
                        nc.vector.tensor_tensor(mT[:, j % 2, LO, 4 * h:4 * h + 4, 0:rows[j]], four(m.bank[6 + h], rows[j]),
                                                mT[:, j % 2, HI, 4 * h:4 * h + 4, 0:rows[j]].bitcast(F32),
                                                ALU.subtract).then_inc(s.mT_ready, 1)

                mix_lo(0)
                for k in range(KT):
                    dve.wait_ge(s.w_hi, k + 1)
                    nc.vector.tensor_tensor(wo[:, LO, k, :], raw[:, k, :], wo[:, HI, k, :].bitcast(F32),
                                            ALU.subtract).then_inc(s.w_split, 1)
                for j in range(n + 1):
                    if j + 1 < n:
                        mix_lo(j + 1)
                    if j >= 1:
                        i = j - 1
                        r = rows[i]
                        dve.wait_ge(s.x_loaded[i % 3], 16 * (i // 3 + 1))
                        for h in range(2):
                            dve.wait_ge(s.mixed, 2 * i + h + 1)
                            part = m.mix[0:r, i, h * 512:(h + 1) * 512]
                            nc.vector.tensor_tensor(part, m.bank[2 * (i % 2) + h][0:r, :],
                                                    x[0:r, i % 3, h * 512:(h + 1) * 512], ALU.add).then_inc(s.h_ready, 1)
                        dve.wait_ge(s.h_rstd, i + 1)
                        nc.vector.tensor_scalar(x[0:r, i % 3, :], m.mix[0:r, i, :], ss[0:r, 2 + i % 2:3 + i % 2], None,
                                                ALU.mult).then_inc(s.h_normed, 1)
                        for h in range(2):
                            dve.wait_ge(s.h_turned, 2 * i + h + 1)
                            if i >= 1:
                                dve.wait_ge(s.u_taken, 2 * (i - 1) + h + 1)
                            nc.vector.tensor_tensor(ut[:, 4 * h:4 * h + 4, 0:r], four(m.bank[4 + h], r),
                                                    m.gffn[:, 4 * h:4 * h + 4].unsqueeze(2).broadcast_to([P, 4, r]),
                                                    ALU.mult).then_inc(s.u_whole, 1)
                        for h in range(2):
                            dve.wait_ge(s.u_hi, 2 * i + h + 1)
                            nc.vector.tensor_tensor(m.u2[:, LO, 4 * h:4 * h + 4, i * P:i * P + r],
                                                    ut[:, 4 * h:4 * h + 4, 0:r],
                                                    m.u2[:, HI, 4 * h:4 * h + 4, i * P:i * P + r].bitcast(F32),
                                                    ALU.subtract).then_inc(s.u_taken, 1)


FT = DFF // P
PIECE = TOK // 3


def stage_ffn_up(nc, io, m):
    U = 2
    UNITS = [(f, side) for f in range(U) for side in range(2)]
    sb = Region(nc, m.gT_start, m.end)
    m.gT = sb("gT", [P, FT, TOK])
    m.after_gT = sb.at
    raw = sb("w_raw", [P, 2, KT, P])
    wp = sb("w_parts", [P, len(UNITS), 2, KT, P], F32R)
    e = sb("silu_gate", [P, 2, PIECE])
    sides = [io.w_gate.rearrange("o (c p) (f q) -> p (o c) f q", p=P, q=P),
             io.w_up.rearrange("o (c p) (f q) -> p (o c) f q", p=P, q=P)]
    last = FT // U - 1

    with stage(nc, "landed*2 w_hi w_split multiplied silu_done piece_done") as s:
        with nc.Block() as block:
            @block.sync
            def _(sp):
                def load(t, i):
                    f, side = UNITS[i]
                    sp.dma_start(raw[:, side, :, :],
                                 sides[side][:, :, bass.ds(t * U + f, 1), :].rearrange("p c o q -> p (c o) q")
                                 ).then_inc(s.landed[side], 16)

                for i in range(4):
                    if i >= 2:
                        sp.wait_ge(s.w_split, i - 1)
                    load(0, i)
                with sp.Fori(0, last) as t:
                    for i in range(4):
                        sp.wait_ge(s.w_split, t * 4 + 3 + i)
                        load(t + 1, i)

            @block.scalar
            def _(act):
                def hi(t, i):
                    f, side = UNITS[i]
                    act.wait_ge(s.landed[side], t * (16 * U) + 16 * (f + 1))
                    nc.scalar.activation(wp[:, i, HI, :, :], raw[:, side, :, :], ACT.Copy).then_inc(s.w_hi, 1)

                def turn(t, more):
                    for f in range(U):
                        for q in range(3):
                            act.wait_ge(s.multiplied, t * 12 + 6 * f + q + 1)
                            act.wait_ge(s.piece_done, t * 6 + 3 * f + q + 2)
                            nc.scalar.activation(e[:, (3 * f + q) % 2, :], m.bank[q][:, 0:PIECE], ACT.Silu).then_inc(s.silu_done, 1)
                        if more:
                            for i in (2 * f, 2 * f + 1):
                                act.wait_ge(s.multiplied, t * 12 + 3 * i + 3)
                                hi(t + 1, i)

                for i in range(4):
                    hi(0, i)
                with act.Fori(0, last) as t:
                    turn(t, True)
                turn(last, False)

            @block.tensor
            def _(pe):
                def turn(t):
                    for i, (f, side) in enumerate(UNITS):
                        pe.wait_ge(s.w_split, t * 4 + i + 1)
                        for q in range(3):
                            pe.wait_ge(s.piece_done, t * 6 + 3 * f + q + 1)
                            for k in range(KT):
                                for a, b in TERMS:
                                    mm = nc.tensor.matmul(m.bank[3 * side + q][:, 0:PIECE], wp[:, i, a, k, :],
                                                          m.u2[:, b, k, q * PIECE:(q + 1) * PIECE],
                                                          start=(k == 0 and (a, b) == TERMS[0]),
                                                          stop=(k == KT - 1 and (a, b) == TERMS[-1]))
                            mm.then_inc(s.multiplied, 1)

                with pe.Fori(0, last) as t:
                    turn(t)
                turn(last)

            @block.vector
            def _(dve):
                def lo(t, i):
                    dve.wait_ge(s.w_hi, t * 4 + i + 1)
                    nc.vector.tensor_tensor(wp[:, i, LO, :, :], raw[:, UNITS[i][1], :, :],
                                            wp[:, i, HI, :, :].bitcast(F32), ALU.subtract).then_inc(s.w_split, 1)

                def turn(t, more):
                    for f in range(U):
                        for q in range(3):
                            dve.wait_ge(s.silu_done, t * 6 + 3 * f + q + 1)
                            dve.wait_ge(s.multiplied, t * 12 + 6 * f + 3 + q + 1)
                            nc.vector.tensor_tensor(
                                m.gT[:, bass.ds(t * U + f, 1), q * PIECE:(q + 1) * PIECE].rearrange("p o t -> p (o t)"),
                                e[:, (3 * f + q) % 2, :], m.bank[3 + q][:, 0:PIECE], ALU.mult).then_inc(s.piece_done, 1)
                        if more:
                            lo(t + 1, 2 * f)
                            lo(t + 1, 2 * f + 1)

                nc.vector.memset(e[:, :, 0:1], 0.0).then_inc(s.piece_done, 3)
                for i in range(4):
                    lo(0, i)
                with dve.Fori(0, last) as t:
                    turn(t, True)
                turn(last, False)


def stage_ffn_down(nc, io, m):
    NC, GR, RG, RW = 512, 2, 4, 4
    NGR = FT // GR
    IN_B = 19
    a, b = Region(nc, m.base_end, m.gT_start), Region(nc, m.after_gT, m.end)
    whi = a("w_down_hi", [P, FT, NC], F32R)
    wlo_a = a("w_down_lo_a", [P, FT - IN_B, NC], F32R)
    gp = a("g_parts", [P, RG, 2, GR, P], F32R)
    raw = a("w_down_raw", [P, RW, NC])
    wlo_b = b("w_down_lo_b", [P, IN_B, NC], F32R)
    y = b("y_tile", [P, 2, NC])
    part_of = lambda part, f: (whi[:, f, :] if part == HI else wlo_b[:, f, :] if f < IN_B
                               else wlo_a[:, f - IN_B, :])
    wd = io.w_down.rearrange("o (f p) n -> p (o f) n", p=P)
    yp = io.y_prompt.rearrange("o (n p) c -> p (o n) c", p=P)
    hp = io.h_dram[0:SEQ, :].rearrange("(n p) c -> p n c", p=P)
    ysm = io.y_sample.rearrange("b t c -> (b t) c")
    HALVES, PER_HALF = DM // NC, NT + 1

    def tile(at, t):
        half, j = at // PER_HALF, at % PER_HALF + 2 * t
        sample = at % PER_HALF == NT
        rows = NS if sample else P
        cols = slice(half * NC, (half + 1) * NC)
        return named(at=at, t=t, n=at + 2 * t, slot=at % 2, uses=at // 2 + t, half=half, rows=rows,
                     opens=at % PER_HALF == 0,
                     h=io.h_dram[SEQ:TOK, cols] if sample else hp[:, bass.ds(j, 1), cols],
                     y=ysm[:, cols] if sample else yp[:, bass.ds(j, 1), cols],
                     tokens=slice(SEQ, TOK) if sample else bass.ds(j * P, P))

    def over_tiles(engine, body):
        for half in range(HALVES):
            start = half * PER_HALF
            body(tile(start, 0))
            body(tile(start + 1, 0))
            with engine.Fori(0, (NT - 2) // 2) as t:
                body(tile(start + 2, t))
                body(tile(start + 3, t))
            body(tile(start + NT, 0))

    with stage(nc, "landed*4 w_hi w_split g_hi g_split used h_loaded*2 y_ready stored*2") as s:
        def group_free(engine, x, g):
            if g >= RG:
                engine.wait_ge(s.used, x.n * NGR + g - RG + 1)
            elif x.at > 0:
                before = max(k for k in range(NGR) if k % RG == g)
                engine.wait_ge(s.used, (x.n - 1) * NGR + before + 1)

        with nc.Block() as block:
            @block.sync
            def _(sp):
                def store(x):
                    sp.wait_ge(s.y_ready, x.n + 1)
                    sp.dma_start(x.y, y[0:x.rows, x.slot, :]).then_inc(s.stored[x.slot], 16)

                def body(x):
                    if x.at >= 2:
                        sp.wait_ge(s.stored[x.slot], x.uses * 16)
                    sp.dma_start(y[0:x.rows, x.slot, :], x.h).then_inc(s.h_loaded[x.slot], 16)
                    if x.opens:
                        for f in range(FT):
                            i = x.half * FT + f
                            if i >= RW:
                                sp.wait_ge(s.w_split, i - RW + 1)
                            sp.dma_start(raw[:, i % RW, :], wd[:, f, x.half * NC:(x.half + 1) * NC]
                                         ).then_inc(s.landed[i % RW], 16)
                    if x.at >= 1:
                        store(tile(x.at - 1, x.t))

                over_tiles(sp, body)
                last = HALVES * PER_HALF - 1
                store(tile(last, 0))
                for k in range(2):
                    sp.wait_ge(s.stored[k], 16 * (HALVES * PER_HALF // 2))

            @block.scalar
            def _(act):
                def body(x):
                    for g in range(NGR):
                        if x.opens:
                            if x.half > 0:
                                act.wait_ge(s.used, (x.at - 1) * NGR + g + 1)
                            for f in range(g * GR, (g + 1) * GR):
                                i = x.half * FT + f
                                act.wait_ge(s.landed[i % RW], 16 * (i // RW + 1))
                                nc.scalar.activation(part_of(HI, f), raw[:, i % RW, :], ACT.Copy).then_inc(s.w_hi, 1)
                        group_free(act, x, g)
                        nc.scalar.activation(gp[:, g % RG, HI, :, 0:x.rows], m.gT[:, g * GR:(g + 1) * GR, x.tokens],
                                             ACT.Copy).then_inc(s.g_hi, 1)

                over_tiles(act, body)

            @block.tensor
            def _(pe):
                def body(x):
                    if x.at >= 2:
                        pe.wait_ge(s.y_ready, x.n - 1)
                    for g in range(NGR):
                        if x.opens:
                            pe.wait_ge(s.w_split, x.half * FT + (g + 1) * GR)
                        pe.wait_ge(s.g_split, x.n * NGR + g + 1)
                        for k in range(GR):
                            f = g * GR + k
                            for pa, pb in TERMS:
                                mm = nc.tensor.matmul(m.bank[x.slot][0:x.rows, :], gp[:, g % RG, pa, k, 0:x.rows],
                                                      part_of(pb, f), start=(f == 0 and (pa, pb) == TERMS[0]),
                                                      stop=(f == FT - 1 and (pa, pb) == TERMS[-1]))
                        mm.then_inc(s.used, 1)

                over_tiles(pe, body)

            @block.vector
            def _(dve):
                def take(x):
                    dve.wait_ge(s.used, (x.n + 1) * NGR)
                    dve.wait_ge(s.h_loaded[x.slot], x.uses * 16 + 16)
                    nc.vector.tensor_tensor(y[0:x.rows, x.slot, :], m.bank[x.slot][0:x.rows, :],
                                            y[0:x.rows, x.slot, :], ALU.add).then_inc(s.y_ready, 1)

                def body(x):
                    for g in range(NGR):
                        if x.opens:
                            for f in range(g * GR, (g + 1) * GR):
                                i = x.half * FT + f
                                dve.wait_ge(s.w_hi, i + 1)
                                nc.vector.tensor_tensor(part_of(LO, f), raw[:, i % RW, :], part_of(HI, f).bitcast(F32),
                                                        ALU.subtract).then_inc(s.w_split, 1)
                        dve.wait_ge(s.g_hi, x.n * NGR + g + 1)
                        nc.vector.tensor_tensor(gp[:, g % RG, LO, :, 0:x.rows], m.gT[:, g * GR:(g + 1) * GR, x.tokens],
                                                gp[:, g % RG, HI, :, 0:x.rows].bitcast(F32),
                                                ALU.subtract).then_inc(s.g_split, 1)
                        if g == RG - 1 and x.at >= 1:
                            take(tile(x.at - 1, x.t))

                over_tiles(dve, body)
                take(tile(HALVES * PER_HALF - 1, 0))


class Region:

    def __init__(self, nc, start, end):
        self.nc, self.at, self.end = nc, start, end

    def __call__(self, name, shape, dtype=F32):
        size = int(np.prod(shape[1:])) * (2 if dtype == mybir.dt.bfloat16 else 4)
        t = self.nc.alloc_sbuf_tensor_at(name, list(shape), dtype, offset=self.at)
        self.at += -(-size // 32) * 32
        assert self.at <= self.end, (name, self.at, self.end)
        return t


class Memory:

    def __init__(self, nc):
        self.psum = nc.alloc_psum_tensor("banks", [P, 8 * 512], F32)
        self.bank = [self.psum[:, i * 512:(i + 1) * 512] for i in range(8)]
        start, end = -(-nc.sbuf_base // 32) * 32, nc.sbuf_usable_end // 32 * 32
        sb = Region(nc, start, end)
        self.consts = sb("consts", list(CONSTS.shape))
        self.gmix = sb("gmix", [P, KT])
        self.gffn = sb("gffn", [P, KT])
        self.qn = sb("qn", [P, HD])
        self.kn = sb("kn", [P, HD])
        self.convw = sb("convw", [P, 4, 6])
        self.convb = sb("convb", [P, 6])
        self.dtb = sb("dtb", [P, 8])
        self.alog = sb("alog", [P, 8])
        self.dskip = sb("dskip", [P, 8])
        self.ssdn = sb("ssdn", [P, DSSD])
        self.rows = sb("rows", [P, 2 * DB], U32)
        self.srow = sb("srow", [P, 132])
        self.gates = sb("gates", [P, NT + 1, 3 * NH])
        self.bias_dram = nc.dram_tensor("bias_by_distance", (NH, P, BIASW), F32, kind="Internal").ap()
        self.base_end = sb.at
        self.qTs = sb("qTs", [P, REP, NS])
        self.ksTs = sb("ksTs", [P, NS])
        self.kwTs = sb("kwTs", [P, NS])
        self.dt_start = sb.at
        sb("dt_place", [P, NT + 1, 16])
        self.sample_end = sb.at
        self.pz = sb("pz", [P, NT + 1, PZ])
        self.pz_end = sb.at
        self.qT_start = sb.at
        self.qT = sb("qT", [P, NT, REP, P])
        self.ksT = sb("ksT", [P, SEQ])
        self.kwT = sb("kwT", [P, SEQ])
        self.v = sb("v", [P, NT + 1, 2, DKV])
        self.att_end = sb.at
        self.end = end
        self.mix_start = end - (NT + 1) * DM * 4
        self.mix = nc.alloc_sbuf_tensor_at("mix", [P, NT + 1, DM], F32, offset=self.mix_start)

    def c(self, name):
        a, b = CONST_COLS[name]
        return self.consts[:, a:b]


def stage_setup(nc, io, m):
    sb = Region(nc, m.sample_end, m.end)
    m.relx = sb("relx", [NBUCK + 1, NH])
    m.onehot = sb("onehot", [NBUCK + 1, BIASW])
    m.biasrow = sb("biasrow", [NH, BIASW])
    m.pages = sb("pages", [16, 2 * DB], I32)
    m.pagef = sb("pagef", [16, 2 * DB])
    m.rowf = sb("rowf", [P, 2 * DB])

    load_setup(nc, io, m)


PER = 4


def stage_projection(nc, io, m):
    sb = Region(nc, m.att_end, m.end)
    w = Buffers()
    w.w = sb("w_in", [P, KT, DIN])
    w.x = sb("x_tile", [P, 2, DM])
    w.u = sb("u_tile", [P, 2, KT, P])
    w.q = sb("q_raw", [P, DATT])
    w.kv = sb("kv_raw", [P, 2, 6, DKV])
    w.qk = sb("qk_normed", [P, 2, 6, P])
    w.sq = sb("squares", [P, 768])
    w.junk = sb("junk", [P, DM], mybir.dt.bfloat16)
    w.ss = sb("ss", [P, 6])
    w.hs = sb("hs", [P, 36])
    tokens = lambda ap, i: ap.rearrange("(n p) c -> p n c", p=P)[:, bass.ds(i, 1), :]
    kv_rows = lambda o: o.rearrange("a b t g d -> (a b t) (g d)")
    with nc.Fori(0, NT // PER) as turn:
        tiles = []
        for j in range(PER):
            i = turn * PER + j
            tiles.append(named(
                rows=P, x=tokens(io.x_prompt.rearrange("o t c -> (o t) c"), i),
                kc=tokens(kv_rows(io.p_k_cmp), i), vc=tokens(kv_rows(io.p_v_cmp), i),
                ks=tokens(kv_rows(io.p_k_sel), i), vs=tokens(kv_rows(io.p_v_sel), i),
                kw=kv_rows(io.p_k_win)[j * P:(j + 1) * P, :], vw=kv_rows(io.p_v_win)[j * P:(j + 1) * P, :],
                qT=m.qT[:, bass.ds(i, 1), :, :].rearrange("p o r q -> p (o r) q"),
                ksT=m.ksT[:, bass.ds(i * P, P)], kwT=m.kwT[:, bass.ds(i * P, P)],
                v=m.v[:, bass.ds(i, 1), :, :].rearrange("p o b d -> p (o b) d"),
                pz=m.pz[:, bass.ds(i, 1), :].rearrange("p o c -> p (o c)"),
                gate=m.pz[:, bass.ds(i, 1), PZ_GATE:PZ].rearrange("p o c -> p (o c)")))
        w.first = True
        project(nc, io, m, w, tiles)
    w.first = False
    project(nc, io, m, w, [named(
        rows=NS, x=io.x_sample.rearrange("b t c -> (b t) c"), kc=kv_rows(io.s_k_cmp), vc=kv_rows(io.s_v_cmp),
        ks=kv_rows(io.s_k_sel), vs=kv_rows(io.s_v_sel), kw=io.kw_new, vw=io.vw_new,
        qT=m.qTs[:, :, :], ksT=m.ksTs[:, :], kwT=m.kwTs[:, :], v=m.v[0:NS, NT, :, :], pz=m.pz[0:NS, NT, :],
        gate=m.pz[0:NS, NT, PZ_GATE:PZ])])


def program(nc, io):
    m = Memory(nc)
    for f in STAGES:
        f(nc, io, m)


STAGES = [stage_setup, stage_projection, stage_pointwise, stage_prompt_compress,
          stage_prompt_attention, stage_conv, stage_ssd, stage_sample_attention,
          stage_finish_mixer, stage_ffn_up, stage_ffn_down]


_INS = ['x_prompt', 'x_sample', 'cache_k_cmp', 'cache_v_cmp', 'cache_k_sel', 'cache_v_sel', 'cache_k_win', 'cache_v_win',
        'state_conv', 'state_ssm', 'page_table', 'norm_mix', 'w_in', 'q_norm', 'k_norm', 'cmp_pe', 'cmp_w1', 'cmp_w2',
        'rel_bias', 'conv_w', 'conv_b', 'dt_bias', 'a_log', 'd_skip', 'ssd_norm', 'w_out', 'norm_ffn', 'w_gate', 'w_up',
        'w_down']
_OUTS = [('y_prompt', (1, SEQ, DM)), ('y_sample', (DB, DS, DM))] + \
    [(f'p_{n}', (1, 1, SEQ, NG, HD)) for n in ('k_cmp', 'v_cmp', 'k_sel', 'v_sel')] + \
    [(f'p_{n}', (1, 1, WIN, NG, HD)) for n in ('k_win', 'v_win')] + \
    [('p_conv', (1, 1, 3, DCONV)), ('p_ssm', (1, 1, 8, HD, HD))] + \
    [(f's_{n}', (1, DB, DS, NG, HD)) for n in ('k_cmp', 'v_cmp', 'k_sel', 'v_sel')] + \
    [(f's_{n}', (1, DB, WIN, NG, HD)) for n in ('k_win', 'v_win')] + \
    [('s_conv', (1, DB, 3, DCONV)), ('s_ssm', (1, DB, 8, HD, HD))]

_SCRATCH = [("kw_new", (NS, DKV)), ("vw_new", (NS, DKV)), ("h_dram", (TOK, DM))]


def kernel(**inputs):
    import numpy as _np
    import concourse.bacc as _bacc
    from concourse.bass_utils import run_bass_kernel_spmd as _run

    nc = _bacc.Bacc("TRN2", target_bir_lowering=False, num_devices=1)
    aps, arrays = {}, {}
    given = {name: inputs[name] for name in _INS}
    given["consts"], given["buckets"] = CONSTS, BUCKETS
    for name, a in given.items():
        a = _np.ascontiguousarray(a)
        arrays[f"in_{name}"] = a
        aps[name] = nc.dram_tensor(f"in_{name}", a.shape, mybir.dt.from_np(a.dtype), kind="ExternalInput").ap()
    for name, shape in _OUTS:
        aps[name] = nc.dram_tensor(f"out_{name}", shape, F32, kind="ExternalOutput").ap()
    for name, shape in _SCRATCH:
        aps[name] = nc.dram_tensor(name, shape, F32, kind="Internal").ap()
    program(nc, named(**aps))
    r = _run(nc, [arrays], core_ids=[0])
    return tuple(r.results[0][f"out_{name}"] for name, _ in _OUTS)
```

```python
import math
from collections import namedtuple
from contextlib import ExitStack, contextmanager

import numpy as np

import concourse.bass as bass
from concourse import mybir
from concourse.alu_op_type import AluOpType as ALU

ACT = mybir.ActivationFunctionType
AX = mybir.AxisListType
F32 = mybir.dt.float32
U32 = mybir.dt.uint32
I32 = mybir.dt.int32

P = 128
DM, SEQ, DB, DS, PAST, PAGE = 1024, 1024, 8, 4, 4096, 128
HD, NH, NG, REP = 64, 8, 2, 4
CSTRIDE, CHID, SELB, TOPN, WIN = 16, 64, 64, 15, 512
NBUCK, MAXDIST = 32, 128
DKV = NG * HD
DATT, DSSD, DCONV = NH * HD, 512, 768
DFF = 2816
OFF_GATE = DATT + 6 * DKV
OFF_Z = OFF_GATE + 3 * NH
OFF_XBC = OFF_Z + DSSD
OFF_DT = OFF_XBC + DCONV
DIN = OFF_DT + 8
EPS = 1e-6
NEG = -1e30
NT = SEQ // P
NS = DB * DS
KT = DM // P
TOK = SEQ + NS
PER = 4
B4 = 4
BIASW = 384
PZ_Z, PZ_XBC, PZ_DT = 0, DSSD, DSSD + DCONV
PZ = PZ_DT + 8

F32R = mybir.dt.float32r
HI, LO = 0, 1
TERMS = ((HI, HI), (HI, LO), (LO, HI))

CONST_COLS = {}


def _shape_constants():
    p = np.arange(P)
    row_s = (p // REP) % DS
    t = np.arange(NS)
    parts = {
        "ident": np.eye(P),
        "ones": np.ones((P, P)),
        "tri": p[:, None] <= p[None, :],
        "after": np.where(p[:, None] <= p[None, :], 0.0, NEG),
        "far": np.where(p[None, :] > p[:, None], 0.0, NEG),
        "rep_sum": (p[:, None] // REP) == (p[None, :] // REP),
        "s_tri": np.pad(((t[:, None] // DS) == (t[None, :] // DS)) & (t[:, None] <= t[None, :]), ((0, P - NS), (0, 0))),
        "s_after": np.pad(np.where(((t[:, None] // DS) == (t[None, :] // DS)) & (t[:, None] <= t[None, :]), 0.0, NEG),
                          ((0, P - NS), (0, 0))),
        "s_ones": np.pad((t[:, None] // DS) == (t[None, :] // DS), ((0, P - NS), (0, 0))),
        "s_of_b": np.pad((t[:, None] // DS) == np.arange(DB)[None, :], ((0, P - NS), (0, 0))),
        "win_old": np.where(np.arange(4)[None, :] <= row_s[:, None], NEG, 0.0),
        "page_of": (8 * p[:, None] <= p[None, :]) & (p[None, :] < 8 * p[:, None] + 8),
        "p_mod": (p % 8)[:, None],
        "eps": np.full((P, 1), EPS),
        "zero": np.zeros((P, 1)),
        "one": np.ones((P, 1)),
    }
    at, out = 0, []
    for name, a in parts.items():
        CONST_COLS[name] = (at, at + a.shape[1])
        at += a.shape[1]
        out.append(np.asarray(a, np.float32))
    return np.concatenate(out, axis=1)


def _bucket_columns():
    oh = np.zeros((NBUCK + 1, BIASW), np.float32)
    for y in range(BIASW):
        n = 255 - y
        if n < 0:
            oh[NBUCK, y] = 1.0
            continue
        half = NBUCK // 2
        if n < half:
            b = n
        else:
            b = half + int(np.float32(np.log(np.float32(n) / np.float32(half))) / np.float32(math.log(MAXDIST / half))
                           * np.float32(NBUCK - half))
        b = min(b, NBUCK - 1)
        oh[b, y] += 1.0
        oh[NBUCK - 1, y] -= 1.0
    return oh


CONSTS = _shape_constants()
BUCKETS = _bucket_columns()


def named(**values):
    return namedtuple("Named", list(values))(**values)


class Buffers:
    pass


@contextmanager
def stage(nc, names):
    with ExitStack() as ctx:
        found = {}
        nums = []
        for name in names.split():
            count = 1
            if "*" in name:
                name, count = name.split("*")
            sems = [ctx.enter_context(nc.semaphore(f"{name}_{i}")) for i in range(int(count))]
            nums += [x.num for x in sems]
            found[name] = sems[0] if count == 1 else sems
        yield named(**found)
        with nc.Block() as block:
            @block.sync
            def _(sp):
                for n in sorted(nums):
                    sp.sem_clear(range(n, n + 1))


class Chain:

    def __init__(self, engine, sem):
        self.engine, self.sem, self.n = engine, sem, 0

    def __call__(self, instruction):
        self.n += 1
        instruction.then_inc(self.sem, 1)
        self.engine.wait_ge(self.sem, self.n)
        return instruction


def load_setup(nc, io, m):
    c = m.c
    with stage(nc, "loaded filled bias_mm bias_row bias_stored head_decay scaled page_float page_mm") as s:
        with nc.Block() as block:
            @block.sync
            def _(sp):
                loads = [
                    (m.consts[:, :], io.consts), (m.onehot[:, :], io.buckets),
                    (m.gmix[:, :], io.norm_mix.rearrange("o (c p) -> p (o c)", p=P)),
                    (m.gffn[:, :], io.norm_ffn.rearrange("o (c p) -> p (o c)", p=P)),
                    (m.qn[:, :], bass.AP(io.q_norm.tensor, 0, [[0, P], [1, HD]])),
                    (m.kn[:, :], bass.AP(io.k_norm.tensor, 0, [[0, P], [1, HD]])),
                    (m.convb[:, :], io.conv_b.rearrange("o (c p) -> p (o c)", p=P)),
                    (m.dtb[:, :], bass.AP(io.dt_bias.tensor, 0, [[0, P], [1, 8]])),
                    (m.alog[:, :], bass.AP(io.a_log.tensor, 0, [[0, P], [1, 8]])),
                    (m.dskip[:, :], bass.AP(io.d_skip.tensor, 0, [[0, P], [1, 8]])),
                    (m.ssdn[:, :], bass.AP(io.ssd_norm.tensor, 0, [[0, P], [1, DSSD]])),
                    (m.pages[:, :], bass.AP(io.page_table.tensor, 0, [[1, 16], [16, 16]])),
                ] + [(m.convw[:, k, :], io.conv_w[0, k, :].rearrange("(c p) -> p c", p=P)) for k in range(4)]
                for dst, src in loads:
                    sp.dma_start(dst, src, allow_slow_non_contiguous=True).then_inc(s.loaded, 16)
                sp.wait_ge(s.filled, 1)
                sp.dma_start(m.relx[0:NBUCK, :], io.rel_bias).then_inc(s.loaded, 16)
                sp.wait_ge(s.bias_row, 1)
                sp.dma_start(m.bias_dram, m.biasrow[:, :].unsqueeze(1).broadcast_to([NH, P, BIASW])).then_inc(s.bias_stored, 16)
                sp.wait_ge(s.bias_stored, 16)

            @block.vector
            def _(dve):
                chain = Chain(dve, s.scaled)
                nc.vector.memset(m.relx[:, :], NEG).then_inc(s.filled, 1)
                dve.wait_ge(s.loaded, 16 * 17)
                nc.vector.tensor_copy(m.pagef[:, :], m.pages[:, :]).then_inc(s.page_float, 1)
                dve.wait_ge(s.page_mm, 1)
                chain(nc.vector.tensor_scalar(m.rowf[:, :], m.bank[1][:, 0:2 * DB], 8.0, c("p_mod"), ALU.mult, ALU.add))
                nc.vector.tensor_copy(m.rows[:, :], m.rowf[:, :])
                nc.vector.tensor_scalar(m.qn[:, :], m.qn[:, :], float(HD) ** -0.5, None, ALU.mult)
                dve.wait_ge(s.head_decay, 1)
                nc.vector.tensor_scalar(m.alog[:, :], m.alog[:, :], -1.0, None, ALU.mult)
                dve.wait_ge(s.bias_mm, 1)
                nc.vector.tensor_copy(m.biasrow[:, :], m.bank[0][0:NH, 0:BIASW]).then_inc(s.bias_row, 1)

            @block.scalar
            def _(act):
                act.wait_ge(s.loaded, 16 * 17)
                nc.scalar.activation(m.alog[:, :], m.alog[:, :], ACT.Exp).then_inc(s.head_decay, 1)

            @block.tensor
            def _(pe):
                pe.wait_ge(s.page_float, 1)
                nc.tensor.matmul(m.bank[1][:, 0:2 * DB], c("page_of")[0:16, :], m.pagef[:, :],
                                 start=True, stop=True).then_inc(s.page_mm, 1)
                pe.wait_ge(s.loaded, 16 * 17)
                nc.tensor.matmul(m.bank[0][0:NH, 0:BIASW], m.relx[:, :], m.onehot[:, :],
                                 start=True, stop=True).then_inc(s.bias_mm, 1)


def stage_project(nc, io, m, heads):
    c = m.c
    n = NT + 1
    rows = [P] * NT + [NS]
    first = 0 if heads else OFF_Z
    width = OFF_Z if heads else DIN - OFF_Z
    chunks = [(0, 512), (512, 1024), (1024, width)]
    TA, TB = m.bank[6], m.bank[7]
    a = Region(nc, m.att_end, m.end)
    wp = a("w_in_parts", [P, 2, KT, width], F32R)
    raw = a("w_in_raw", [P, 2, width])
    XS = 3 if heads else 2
    x = a("x_tile", [P, XS, DM])
    u = a("u_parts", [P, 2, 2, KT, P], F32R)
    b = Region(nc, m.sample_end, m.pz_end) if heads else a
    ut = b("u_whole", [P, KT, P])
    if heads:
        q_raw = b("q_raw", [P, DATT])
        kv_raw = b("kv_raw", [P, 2, 6, DKV])
        qk = b("qk_normed", [P, 2, 6, P])
        sq = b("squares", [P, 768])
        junk = b("junk", [P, DM], mybir.dt.bfloat16)
        ss = b("ss", [P, 4])
        hs = b("hs", [P, 36])
    rows_of = lambda ap: ap.rearrange("(n p) c -> p n c", p=P)
    kv_rows = lambda o: o.rearrange("a b t g d -> (a b t) (g d)")
    out_rows = lambda o, j: kv_rows(o)[j * P:(j + 1) * P, :]
    four = lambda bank, r: bank[:, :].rearrange("p (k q) -> p k q", k=4)[:, :, 0:r]
    xp, xsm = rows_of(io.x_prompt.rearrange("o t c -> (o t) c")), io.x_sample.rearrange("b t c -> (b t) c")

    def stores(j):
        if j == NT:
            return [(kv_rows(io.s_k_cmp), 0, None), (kv_rows(io.s_v_cmp), 1, None), (kv_rows(io.s_k_sel), None, 4),
                    (kv_rows(io.s_v_sel), 3, None), (io.kw_new, None, 5), (io.vw_new, 5, None)]
        out = [(out_rows(io.p_k_cmp, j), 0, None), (out_rows(io.p_v_cmp, j), 1, None),
               (out_rows(io.p_k_sel, j), None, 4), (out_rows(io.p_v_sel, j), 3, None)]
        i = j - (SEQ - WIN) // P
        return out + ([(out_rows(io.p_k_win, i), None, 5), (out_rows(io.p_v_win, i), 5, None)] if i >= 0 else [])

    stored_by = [[0], [0]]
    for j in range(n):
        stored_by[j % 2].append(stored_by[j % 2][-1] + len(stores(j)))

    with stage(nc, "x_loaded*3 w_landed*2 w_hi w_split x_rstd x_scaled x_turned u_whole u_hi u_ready projected "
                   "chunk_taken z_taken squared head_sums head_rstd normed qk_turned qk_taken stored*2 tables kept act_c dve_c") as s:
        def sample_bias_tables(sp):
            t = m.bias_dram.tensor
            for p0 in range(0, P, 16):
                g = (p0 // 16) % NG
                for q in range(DS):
                    sp.dma_start(m.srow[p0 + q * REP:p0 + (q + 1) * REP, :],
                                 bass.AP(t, g * REP * P * BIASW + 127 - q, [[P * BIASW, REP], [1, 132]])
                                 ).then_inc(s.tables, 16)

        def window_caches(sp):
            flat = lambda o: o.rearrange("o b t g d -> (o b) t (g d)")
            for dst, old, new in ((io.s_k_win, io.cache_k_win, io.kw_new), (io.s_v_win, io.cache_v_win, io.vw_new)):
                sp.dma_start(flat(dst)[:, 0:WIN - DS, :], flat(old)[:, DS:WIN, :]).then_inc(s.kept, 16)
                sp.dma_start(flat(dst)[:, WIN - DS:WIN, :], new.rearrange("(b t) c -> b t c", b=DB)).then_inc(s.kept, 16)

        with nc.Block() as block:
            @block.sync
            def _(sp):
                def load_x(j):
                    if j >= XS:
                        sp.wait_ge(s.x_turned, 2 * (j - XS + 1))
                    sp.dma_start(x[0:rows[j], j % XS, :], xp[:, j, :] if j < NT else xsm).then_inc(s.x_loaded[j % XS], 16)

                load_x(0)
                for k in range(KT):
                    if k >= 2:
                        sp.wait_ge(s.w_split, k - 1)
                    sp.dma_start(raw[:, k % 2, :], io.w_in[0, k * P:(k + 1) * P, first:first + width]
                                 ).then_inc(s.w_landed[k % 2], 16)
                    if 1 <= k < XS:
                        load_x(k)
                for j in range(n):
                    if j + XS < n:
                        load_x(j + XS)
                    if j == 1:
                        if heads:
                            sample_bias_tables(sp)
                        else:
                            window_caches(sp)
                    if heads:
                        sp.wait_ge(s.normed, j + 1)
                        for dst, plain, done in stores(j):
                            src = kv_raw[0:rows[j], j % 2, plain, :] if done is None else qk[0:rows[j], j % 2, done, :]
                            sp.dma_start(dst, src).then_inc(s.stored[j % 2], 16)
                if heads:
                    for k in range(2):
                        sp.wait_ge(s.stored[k], 16 * stored_by[k][-1])
                    sp.wait_ge(s.tables, 16 * 32)
                else:
                    sp.wait_ge(s.kept, 16 * 4)

            @block.tensor
            def _(pe):
                def turn_x(j):
                    r = rows[j]
                    pe.wait_ge(s.x_scaled, j + 1)
                    if j >= 1:
                        pe.wait_ge(s.u_whole, 2 * j)
                    if heads and j >= 3:
                        pe.wait_ge(s.qk_taken, 2 * (j - 2))
                    for k in range(KT):
                        i = nc.tensor.transpose((TA, TB)[k // 4][:, (k % 4) * P:(k % 4) * P + r],
                                                x[0:r, j % XS, k * P:(k + 1) * P], c("ident")[0:r, 0:r])
                        if k % 4 == 3:
                            i.then_inc(s.x_turned, 1)

                def turn_heads(j):
                    r = rows[j]
                    pe.wait_ge(s.normed, j + 1)
                    pe.wait_ge(s.u_whole, 2 * min(j + 3, n))
                    if j >= 1:
                        pe.wait_ge(s.qk_taken, 2 * j)
                    for k in range(6):
                        i = nc.tensor.transpose((TA, TB)[k // 4][:, (k % 4) * P:(k % 4) * P + r], qk[0:r, j % 2, k, :],
                                                c("ident")[0:r, 0:r])
                        if k in (3, 5):
                            i.then_inc(s.qk_turned, 1)

                def term(j, i, k):
                    lo_col, hi_col = chunks[i]
                    for pa, pb in TERMS:
                        mm = nc.tensor.matmul(m.bank[3 * (j % 2) + i][0:rows[j], 0:hi_col - lo_col],
                                              u[:, j % 2, pa, k, 0:rows[j]], wp[:, pb, k, lo_col:hi_col],
                                              start=(k == 0 and (pa, pb) == TERMS[0]),
                                              stop=(k == KT - 1 and (pa, pb) == TERMS[-1]))
                    if k == KT - 1:
                        mm.then_inc(s.projected, 1)

                turn_x(0)
                for j in range(n):
                    pe.wait_ge(s.u_ready, 2 * (j + 1))
                    if j == 0:
                        for k in range(KT):
                            pe.wait_ge(s.w_split, k + 1)
                            for i in range(3):
                                term(j, i, k)
                        turn_x(1)
                        continue
                    for i in range(3):
                        if j >= 2:
                            if heads:
                                pe.wait_ge(s.chunk_taken, 3 * (j - 2) + i + 1)
                            elif i == 0:
                                pe.wait_ge(s.z_taken, j - 1)
                            else:
                                pe.wait_ge(s.chunk_taken, 2 * (j - 2) + i)
                        for k in range(KT):
                            term(j, i, k)
                        if i == 0 and j + 1 < n:
                            turn_x(j + 1)
                    if heads:
                        turn_heads(j - 1)
                if heads:
                    turn_heads(n - 1)

            @block.scalar
            def _(act):
                chain = Chain(act, s.act_c)

                def logs_and_roots(head_tile, x_tile):
                    if x_tile < n:
                        rx, at = rows[x_tile], x_tile % XS
                        act.wait_ge(s.x_loaded[at], 16 * (x_tile // XS + 1))
                        chain(nc.scalar.activation(junk[0:rx, :], x[0:rx, at, :], ACT.Square,
                                                   accum_out=ss[0:rx, at:at + 1]))
                    if head_tile >= 0:
                        r = rows[head_tile]
                        act.wait_ge(s.head_sums, head_tile + 1)
                        chain(nc.scalar.activation(hs[0:r, 12:24], hs[0:r, 0:12], ACT.Ln, scale=1.0 / HD,
                                                   bias=c("eps")[0:r, :]))
                    if x_tile < n:
                        chain(nc.scalar.activation(ss[0:rx, 3:4], ss[0:rx, at:at + 1], ACT.Ln, scale=1.0 / DM,
                                                   bias=c("eps")[0:rx, :]))
                    if head_tile >= 0:
                        nc.scalar.activation(hs[0:r, 24:36], hs[0:r, 12:24], ACT.Exp, scale=-0.5).then_inc(s.head_rstd, 1)
                    if x_tile < n:
                        nc.scalar.activation(m.rstd[0:rx, x_tile:x_tile + 1], ss[0:rx, 3:4], ACT.Exp,
                                             scale=-0.5).then_inc(s.x_rstd, 1)

                def u_hi(j):
                    for h in range(2):
                        act.wait_ge(s.u_whole, 2 * j + h + 1)
                        if j >= 2:
                            act.wait_ge(s.projected, 3 * (j - 1))
                        nc.scalar.activation(u[:, j % 2, HI, 4 * h:4 * h + 4, 0:rows[j]],
                                             ut[:, 4 * h:4 * h + 4, 0:rows[j]], ACT.Copy).then_inc(s.u_hi, 1)

                def take_heads(j):
                    r, qs = rows[j], slice(j * P, j * P + rows[j])
                    act.wait_ge(s.qk_turned, 2 * j + 1)
                    nc.scalar.activation(m.qT[:, j, :, :] if j < NT else m.qTs[:, :, :], four(TA, r),
                                         ACT.Copy).then_inc(s.qk_taken, 1)
                    act.wait_ge(s.qk_turned, 2 * j + 2)
                    nc.scalar.activation(m.ksT[:, qs] if j < NT else m.ksTs[:, :], TB[:, 0:r], ACT.Copy)
                    nc.scalar.activation(m.kwT[:, qs] if j < NT else m.kwTs[:, :], TB[:, P:P + r],
                                         ACT.Copy).then_inc(s.qk_taken, 1)

                if heads:
                    logs_and_roots(-1, 0)
                u_hi(0)
                for k in range(KT):
                    act.wait_ge(s.w_landed[k % 2], 16 * (k // 2 + 1))
                    nc.scalar.activation(wp[:, HI, k, :], raw[:, k % 2, :], ACT.Copy).then_inc(s.w_hi, 1)
                if heads:
                    logs_and_roots(-1, 1)
                    logs_and_roots(-1, 2)
                for j in range(n):
                    r = rows[j]
                    if not heads:
                        if j + 1 < n:
                            u_hi(j + 1)
                        act.wait_ge(s.projected, 3 * j + 1)
                        nc.scalar.activation(m.pz[0:r, j, PZ_Z:PZ_Z + DSSD], m.bank[3 * (j % 2)][0:r, :],
                                             ACT.Silu).then_inc(s.z_taken, 1)
                        continue
                    act.wait_ge(s.projected, 3 * j + 1)
                    if j >= 1:
                        act.wait_ge(s.normed, j)
                    if j >= 2:
                        act.wait_ge(s.stored[j % 2], 16 * stored_by[j % 2][j // 2])
                    bank = m.bank[3 * (j % 2):3 * (j % 2) + 3]
                    nc.scalar.activation(q_raw[0:r, :], bank[0][0:r, :], ACT.Copy).then_inc(s.chunk_taken, 1)
                    if j + 1 < n:
                        u_hi(j + 1)
                    act.wait_ge(s.projected, 3 * j + 2)
                    nc.scalar.activation(kv_raw[0:r, j % 2, 0:4, :], bank[1][0:r, :].rearrange("p (a b) -> p a b", a=4),
                                         ACT.Copy).then_inc(s.chunk_taken, 1)
                    act.wait_ge(s.projected, 3 * j + 3)
                    nc.scalar.activation(kv_raw[0:r, j % 2, 4:6, :],
                                         bank[2][0:r, 0:256].rearrange("p (a b) -> p a b", a=2), ACT.Copy)
                    nc.scalar.activation(m.gates[0:r, j, :], bank[2][0:r, 256:280], ACT.Copy).then_inc(s.chunk_taken, 1)
                    if j >= 1:
                        take_heads(j - 1)
                    act.wait_ge(s.chunk_taken, 3 * (j + 1))
                    if j >= 1:
                        act.wait_ge(s.head_sums, j)
                    nc.scalar.activation(sq[0:r, 0:512], q_raw[0:r, :], ACT.Square)
                    nc.scalar.activation(sq[0:r, 512:640], kv_raw[0:r, j % 2, 2, :], ACT.Square)
                    nc.scalar.activation(sq[0:r, 640:768], kv_raw[0:r, j % 2, 4, :], ACT.Square).then_inc(s.squared, 1)
                    nc.scalar.activation(m.v[0:r, j, 0, :], kv_raw[0:r, j % 2, 3, :], ACT.Copy)
                    nc.scalar.activation(m.v[0:r, j, 1, :], kv_raw[0:r, j % 2, 5, :], ACT.Copy)
                    logs_and_roots(j, j + 3)
                if heads:
                    take_heads(n - 1)

            @block.vector
            def _(dve):
                chain = Chain(dve, s.dve_c)

                def scale_x(j):
                    r = rows[j]
                    dve.wait_ge(s.x_loaded[j % XS], 16 * (j // XS + 1))
                    if heads:
                        dve.wait_ge(s.x_rstd, j + 1)
                    nc.vector.tensor_scalar(x[0:r, j % XS, :], x[0:r, j % XS, :], m.rstd[0:r, j:j + 1], None,
                                            ALU.mult).then_inc(s.x_scaled, 1)

                def make_u(j):
                    r = rows[j]
                    for h in range(2):
                        dve.wait_ge(s.x_turned, 2 * j + h + 1)
                        if j >= 1:
                            dve.wait_ge(s.u_ready, 2 * (j - 1) + h + 1)
                        nc.vector.tensor_tensor(ut[:, 4 * h:4 * h + 4, 0:r], four((TA, TB)[h], r),
                                                m.gmix[:, 4 * h:4 * h + 4].unsqueeze(2).broadcast_to([P, 4, r]),
                                                ALU.mult).then_inc(s.u_whole, 1)
                    for h in range(2):
                        dve.wait_ge(s.u_hi, 2 * j + h + 1)
                        nc.vector.tensor_tensor(u[:, j % 2, LO, 4 * h:4 * h + 4, 0:r], ut[:, 4 * h:4 * h + 4, 0:r],
                                                u[:, j % 2, HI, 4 * h:4 * h + 4, 0:r].bitcast(F32),
                                                ALU.subtract).then_inc(s.u_ready, 1)

                scale_x(0)
                make_u(0)
                for k in range(KT):
                    dve.wait_ge(s.w_hi, k + 1)
                    nc.vector.tensor_tensor(wp[:, LO, k, :], raw[:, k % 2, :], wp[:, HI, k, :].bitcast(F32),
                                            ALU.subtract).then_inc(s.w_split, 1)
                scale_x(1)
                for j in range(n):
                    r = rows[j]
                    if j + 1 < n:
                        make_u(j + 1)
                    if j + 2 < n:
                        scale_x(j + 2)
                    if not heads:
                        for i, (at, end) in list(enumerate(chunks))[1:]:
                            dve.wait_ge(s.projected, 3 * j + i + 1)
                            nc.vector.tensor_copy(m.pz[0:r, j, at:end], m.bank[3 * (j % 2) + i][0:r, 0:end - at]
                                                  ).then_inc(s.chunk_taken, 1)
                        continue
                    dve.wait_ge(s.squared, j + 1)
                    if j >= 1:
                        dve.wait_ge(s.head_rstd, j)
                    nc.vector.tensor_reduce(hs[0:r, 0:12], sq[0:r, :].rearrange("p (h d) -> p h d", d=HD), AX.X,
                                            ALU.add).then_inc(s.head_sums, 1)
                    dve.wait_ge(s.head_rstd, j + 1)
                    if j >= 2:
                        dve.wait_ge(s.stored[j % 2], 16 * stored_by[j % 2][j // 2])
                        dve.wait_ge(s.qk_turned, 2 * (j - 1))
                    nc.vector.tensor_tensor(
                        qk[0:r, j % 2, 0:4, :].rearrange("p r (g d) -> p g r d", g=NG),
                        q_raw[0:r, :].rearrange("p (g r d) -> p g r d", g=NG, r=REP),
                        hs[0:r, 24:32].rearrange("p (g r) -> p g r", g=NG).unsqueeze(3).broadcast_to([r, NG, REP, HD]),
                        ALU.mult)
                    chain(nc.vector.tensor_tensor(
                        qk[0:r, j % 2, 4:6, :].rearrange("p b (g d) -> p b g d", g=NG),
                        kv_raw[0:r, j % 2, 2:6:2, :].rearrange("p b (g d) -> p b g d", g=NG),
                        hs[0:r, 32:36].rearrange("p (b g) -> p b g", g=NG).unsqueeze(3).broadcast_to([r, 2, NG, HD]),
                        ALU.mult))
                    for part, gain, count in ((slice(0, 4), m.qn, NH), (slice(4, 6), m.kn, 4)):
                        v = qk[0:r, j % 2, part, :].rearrange("p r (g d) -> p (r g) d", g=NG)
                        i = nc.vector.tensor_tensor(v, v, gain[0:r, :].unsqueeze(1).broadcast_to([r, count, HD]), ALU.mult)
                    i.then_inc(s.normed, 1)


def stage_pointwise(nc, io, m):
    c = m.c
    sb = Region(nc, m.att_end, m.end)
    m.dt = nc.alloc_sbuf_tensor_at("dt", [P, NT + 1, 16], F32, offset=m.dt_start)
    t1 = sb("dt_low", [P, NT + 1, 8])
    t2 = sb("dt_exp", [P, NT + 1, 8])
    parts = [(slice(0, P), slice(0, NT)), (slice(0, NS), slice(NT, NT + 1))]
    w = place_compression(nc, m)
    with stage(nc, "act_c dve_c low_ready log_ready stored") as s:
        with nc.Block() as block:
            @block.sync
            def _(sp):
                for kv in range(2):
                    for j in range(2):
                        src = io.cmp_w1[0, kv, 16 * j:16 * (j + 1), :, :].rearrange("(q s) d h -> (s d) q h", s=2)
                        sp.dma_start(w.w1[:, kv, :, j, :], src).then_inc(m.cmp_loaded, 16)
                    sp.dma_start(w.w2[:, kv, :], io.cmp_w2[0, kv, :, :]).then_inc(m.cmp_loaded, 16)
                    sp.dma_start(w.pe[:, kv, :], io.cmp_pe[0, kv, :, :].rearrange("(q s) d -> (s d) q", s=2),
                                 allow_slow_non_contiguous=True).then_inc(m.cmp_loaded, 16)
                sp.dma_start(io.p_conv[0, 0, :, :], m.pz[P - 3:P, NT - 1, PZ_XBC:PZ_XBC + DCONV]).then_inc(s.stored, 16)
                for b in range(DB):
                    sp.dma_start(io.s_conv[0, b, :, :],
                                 m.pz[b * DS + 1:(b + 1) * DS, NT, PZ_XBC:PZ_XBC + DCONV]).then_inc(s.stored, 16)
                sp.wait_ge(s.stored, 16 * (1 + DB))

            @block.scalar
            def _(act):
                for rows, tiles in parts:
                    nc.scalar.activation(m.gates[rows, tiles, :], m.gates[rows, tiles, :], ACT.Sigmoid)
                chain = Chain(act, s.act_c)
                act.wait_ge(s.low_ready, 1)
                for rows, tiles in parts:
                    chain(nc.scalar.activation(t2[rows, tiles, :], t1[rows, tiles, :], ACT.Exp))
                for rows, tiles in parts:
                    nc.scalar.activation(t2[rows, tiles, :], t2[rows, tiles, :], ACT.Ln,
                                         bias=c("one")[rows, :]).then_inc(s.log_ready, 1)

            @block.vector
            def _(dve):
                chain = Chain(dve, s.dve_c)
                for rows, tiles in parts:
                    n = tiles.stop - tiles.start
                    r = rows.stop
                    x, low = m.dt[rows, tiles, 0:8], t1[rows, tiles, :]
                    chain(nc.vector.tensor_tensor(x, m.pz[rows, tiles, PZ_DT:PZ_DT + 8],
                                                  m.dtb[rows, :].unsqueeze(1).broadcast_to([r, n, 8]), ALU.add))
                    chain(nc.vector.tensor_scalar(low, x, -1.0, None, ALU.mult))
                    chain(nc.vector.tensor_tensor(low, low, x, ALU.min))
                nc.vector.tensor_scalar(t1[0:1, 0, 0:1], t1[0:1, 0, 0:1], 1.0, None, ALU.mult).then_inc(s.low_ready, 1)
                dve.wait_ge(s.log_ready, 2)
                for rows, tiles in parts:
                    n = tiles.stop - tiles.start
                    r = rows.stop
                    x = m.dt[rows, tiles, 0:8]
                    chain(nc.vector.tensor_scalar(x, x, 0.0, None, ALU.max))
                    chain(nc.vector.tensor_tensor(x, x, t2[rows, tiles, :], ALU.add))
                    nc.vector.tensor_tensor(m.dt[rows, tiles, 8:16], x,
                                            m.alog[rows, :].unsqueeze(1).broadcast_to([r, n, 8]), ALU.mult)


def by_head_pair(ap):
    return ap.rearrange("o b (i h) p n -> (h p) (o b) i n", h=2)


def stage_conv(nc, io, m):
    c = m.c
    NCB = DCONV // P
    sb = Region(nc, m.qT_start, m.work_end)
    m.xc = sb("conv_out", [P, NCB, TOK])
    m.hin = sb("state_in", [P, DB, 2, NG, HD])
    m.conv_end = sb.at
    raw = sb("conv_in", [P, NCB, 3 + SEQ])
    raws = sb("conv_in_s", [P, NCB, DB, 3 + DS])
    state = sb("conv_state", [DB * 3, DCONV])
    with stage(nc, "ssm_loaded state_loaded padded turned taken tapped summed sample_taken dve_c") as s:
        with nc.Block() as block:
            @block.sync
            def _(sp):
                sp.dma_start(state[:, :], io.state_conv.rearrange("o b k c -> (o b k) c")).then_inc(s.state_loaded, 16)
                for i in range(4):
                    sp.dma_start(m.hin[:, :, i % 2, i // 2, :], by_head_pair(io.state_ssm)[:, :, i, :]
                                 ).then_inc(s.ssm_loaded, 16)
                sp.wait_ge(s.ssm_loaded, 64)

            @block.gpsimd
            def _(pool):
                nc.gpsimd.memset(raw[:, :, 0:3], 0.0).then_inc(s.padded, 1)

            @block.tensor
            def _(pe):
                for b in range(NCB):
                    for h in range(2):
                        n = 2 * b + h
                        if n >= 6:
                            pe.wait_ge(s.taken, n - 5)
                        for k in range(4):
                            i = nc.tensor.transpose(m.bank[n % 6][:, k * P:(k + 1) * P],
                                                    m.pz[:, 4 * h + k, PZ_XBC + b * P:PZ_XBC + (b + 1) * P], c("ident"))
                        i.then_inc(s.turned, 1)
                pe.wait_ge(s.state_loaded, 16)
                for b in range(NCB):
                    nc.tensor.transpose(m.bank[6][:, b * NS:(b + 1) * NS],
                                        m.pz[0:NS, NT, PZ_XBC + b * P:PZ_XBC + (b + 1) * P], c("ident")[0:NS, 0:NS])
                    i = nc.tensor.transpose(m.bank[7][:, b * 24:(b + 1) * 24], state[:, b * P:(b + 1) * P],
                                            c("ident")[0:24, 0:24])
                i.then_inc(s.turned, 1)

            @block.scalar
            def _(act):
                act.wait_ge(s.padded, 1)
                for b in range(NCB):
                    for h in range(2):
                        n = 2 * b + h
                        act.wait_ge(s.turned, n + 1)
                        nc.scalar.activation(raw[:, b, 3 + 512 * h:3 + 512 * (h + 1)], m.bank[n % 6][:, :],
                                             ACT.Copy).then_inc(s.taken, 1)
                    act.wait_ge(s.taken, 2 * b + 2)
                    nc.scalar.activation(m.xc[:, b, 0:SEQ], raw[:, b, 0:SEQ], ACT.Identity, bias=m.convb[:, b:b + 1],
                                         scale=m.convw[:, 0, b:b + 1]).then_inc(s.tapped, 1)
                act.wait_ge(s.turned, 2 * NCB + 1)
                nc.scalar.activation(raws[:, :, :, 3:3 + DS], m.bank[6][:, 0:NCB * NS].rearrange(
                    "p (c b t) -> p c b t", c=NCB, b=DB), ACT.Copy)
                nc.scalar.activation(raws[:, :, :, 0:3], m.bank[7][:, 0:NCB * 24].rearrange(
                    "p (c b t) -> p c b t", c=NCB, b=DB), ACT.Copy).then_inc(s.sample_taken, 1)
                act.wait_ge(s.sample_taken, 1)
                for b in range(NCB):
                    nc.scalar.activation(m.xc[:, b, SEQ:TOK].rearrange("p (b t) -> p b t", b=DB), raws[:, b, :, 0:DS],
                                         ACT.Identity, bias=m.convb[:, b:b + 1],
                                         scale=m.convw[:, 0, b:b + 1]).then_inc(s.tapped, 1)
                for b in range(NCB):
                    act.wait_ge(s.summed, b + 1)
                    nc.scalar.activation(m.xc[:, b, 0:SEQ], m.xc[:, b, 0:SEQ], ACT.Silu)
                act.wait_ge(s.summed, 2 * NCB)
                nc.scalar.activation(m.xc[:, :, SEQ:TOK], m.xc[:, :, SEQ:TOK], ACT.Silu)

            @block.vector
            def _(dve):
                chain = Chain(dve, s.dve_c)
                for b in range(NCB):
                    dve.wait_ge(s.tapped, b + 1)
                    for k in range(1, 4):
                        i = nc.vector.scalar_tensor_tensor(m.xc[:, b, 0:SEQ], raw[:, b, k:k + SEQ], m.convw[:, k, b:b + 1],
                                                           m.xc[:, b, 0:SEQ], ALU.mult, ALU.add)
                        if k < 3:
                            chain(i)
                    i.then_inc(s.summed, 1)
                for b in range(NCB):
                    dve.wait_ge(s.tapped, NCB + b + 1)
                    out = m.xc[:, b, SEQ:TOK].rearrange("p (b t) -> p b t", b=DB)
                    for k in range(1, 4):
                        i = nc.vector.scalar_tensor_tensor(out, raws[:, b, :, k:k + DS], m.convw[:, k, b:b + 1],
                                                           out, ALU.mult, ALU.add)
                        if k < 3:
                            chain(i)
                    i.then_inc(s.summed, 1)


def ssd_chunks(nc, m, w, chunks):
    c = m.c
    n = len(chunks)
    R = chunks[0].rows
    sample = chunks[0].sample
    tri, after, ones = (("s_tri", "s_after", "s_ones") if sample else ("tri", "after", "ones"))
    tri, after, ones = c(tri)[0:R, 0:R], c(after)[0:R, 0:R], c(ones)[0:R, 0:R]
    heads = lambda ap: ap.unsqueeze(2).broadcast_to([R, 8, HD])
    with stage(nc, "xs_ready dt_ready td_ready turned sums_ready x_taken small_taken diff_ready ex_ready cb_ready "
                   "acb_ready seg_done e_ready m_ready xdt_ready xe_ready yo_ready yd_ready st_ready state_ready "
                   "state_scaled xd_ready y_ready yr_ready y_done act_c dve_c pe_c") as s:
        with nc.Block() as block:
            @block.tensor
            def _(pe):
                chain = Chain(pe, s.pe_c)

                def front(j):
                    q = j % 2
                    pe.wait_ge(s.xs_ready, j + 1)
                    if j >= 1:
                        pe.wait_ge(s.x_taken, j)
                        pe.wait_ge(s.small_taken, j)
                    for k in range(4):
                        nc.tensor.transpose(m.bank[0][0:R, k * P:(k + 1) * P], w.xs[:, q, k, 0:R], c("ident"))
                    nc.tensor.transpose(m.bank[1][0:R, 0:P], w.xs[:, q, 4, 0:R], c("ident")).then_inc(s.turned, 1)
                    pe.wait_ge(s.dt_ready, j + 1)
                    nc.tensor.matmul(m.bank[1][0:R, P:P + 8], tri, w.dt[0:R, q, 8:16], start=True, stop=True)
                    nc.tensor.matmul(m.bank[1][0:R, P + 8:P + 16], ones, w.dt[0:R, q, 8:16], start=True,
                                     stop=True).then_inc(s.sums_ready, 1)
                    if j >= 1:
                        pe.wait_ge(s.seg_done, j)
                    pe.wait_ge(s.td_ready, j + 1)
                    for h in range(2):
                        mm = nc.tensor.matmul(m.bank[4 + h][0:R, 0:4 * R], c("ones")[0:R, 0:R],
                                              w.td[0:R, 4 * h:4 * h + 4, 0:R], start=True, stop=True)
                    mm.then_inc(s.acb_ready, 1)

                def c_times_b(j):
                    q = j % 2
                    if j >= 1:
                        pe.wait_ge(s.m_ready, j)
                    for g in range(NG):
                        mm = nc.tensor.matmul(m.bank[2][0:R, g * P:g * P + R], w.xs[64 * g:64 * g + 64, q, 4, 0:R],
                                              w.xs[64 * g:64 * g + 64, q, 5, 0:R], start=True, stop=True)
                        chain(mm)
                    nc.tensor.nop().then_inc(s.cb_ready, 1)

                def back(j):
                    q = j % 2
                    if j >= 1:
                        pe.wait_ge(s.y_ready, j)
                        pe.wait_ge(s.state_ready, j)
                    if not sample:
                        for g in range(NG):
                            mm = nc.tensor.matmul(m.bank[6][0:R, 256 * g:256 * (g + 1)],
                                                  w.xs[64 * g:64 * g + 64, q, 5, 0:R],
                                                  w.state[64 * g:64 * g + 64, :], start=True, stop=True)
                            chain(mm)
                    else:
                        for g in range(NG):
                            for b in range(DB):
                                mm = nc.tensor.matmul(m.bank[6][0:R, 256 * g:256 * (g + 1)],
                                                      w.cm[64 * g:64 * g + 64, b, :], w.s0[64 * g:64 * g + 64, b, :],
                                                      start=(b == 0), stop=(b == DB - 1))
                            chain(mm)
                    nc.tensor.nop().then_inc(s.yo_ready, 1)
                    pe.wait_ge(s.m_ready, j + 1)
                    pe.wait_ge(s.xdt_ready, j + 1)
                    for h in range(8):
                        mm = nc.tensor.matmul(m.bank[7][0:R, HD * h:HD * (h + 1)], w.seg[0:R, h, 0:R],
                                              w.xdt[0:R, HD * h:HD * (h + 1)], start=True, stop=True)
                    mm.then_inc(s.yd_ready, 1)
                    if not sample:
                        pe.wait_ge(s.xe_ready, j + 1)
                        nc.tensor.matmul(m.bank[3][:, :], w.small[0:R, q, 0:P], w.xe[0:R, :], start=True,
                                         stop=True).then_inc(s.st_ready, 1)

                front(0)
                c_times_b(0)
                for j in range(n):
                    if j + 1 < n:
                        front(j + 1)
                    back(j)
                    if j + 1 < n:
                        c_times_b(j + 1)

            @block.scalar
            def _(act):
                chain = Chain(act, s.act_c)

                def slice_chunk(j):
                    if j >= 2:
                        act.wait_ge(s.yo_ready, j - 1)
                    nc.scalar.activation(w.xs[:, j % 2, :, 0:R], chunks[j].xc, ACT.Copy).then_inc(s.xs_ready, 1)

                def y_norm(j):
                    q = j % 2
                    act.wait_ge(s.y_ready, j + 1)
                    for g in range(NG):
                        chain(nc.scalar.activation(w.junk[0:R, :], w.y[0:R, q, 256 * g:256 * (g + 1)], ACT.Square,
                                                   accum_out=w.yr[0:R, q, g:g + 1]))
                    chain(nc.scalar.activation(w.yr[0:R, q, 2:4], w.yr[0:R, q, 0:2], ACT.Ln, scale=1.0 / 256,
                                               bias=c("eps")[0:R, :]))
                    nc.scalar.activation(w.yr[0:R, q, 4:6], w.yr[0:R, q, 2:4], ACT.Exp, scale=-0.5).then_inc(s.yr_ready, 1)

                slice_chunk(0)
                for j in range(n):
                    q = j % 2
                    act.wait_ge(s.turned, j + 1)
                    if j >= 1:
                        act.wait_ge(s.xe_ready, j)
                        act.wait_ge(s.xd_ready, j)
                    nc.scalar.activation(w.xt[0:R, :], m.bank[0][0:R, :], ACT.Copy).then_inc(s.x_taken, 1)
                    if j + 1 < n:
                        slice_chunk(j + 1)
                    act.wait_ge(s.diff_ready, j + 1)
                    if j >= 2:
                        act.wait_ge(s.y_ready, j - 1)
                    nc.scalar.activation(w.ex[0:R, q, :], w.small[0:R, q, P:P + 24], ACT.Exp).then_inc(s.ex_ready, 1)
                    act.wait_ge(s.seg_done, j + 1)
                    nc.scalar.activation(w.seg[0:R, :, 0:R], w.seg[0:R, :, 0:R], ACT.Exp).then_inc(s.e_ready, 1)
                    if j >= 1:
                        y_norm(j - 1)
                y_norm(n - 1)

            @block.gpsimd
            def _(pool):
                for j in range(n):
                    pool.wait_ge(s.x_taken, j + 1)
                    if j >= 1:
                        pool.wait_ge(s.y_ready, j)
                    nc.gpsimd.tensor_tensor(w.xd[0:R, :].rearrange("p (h d) -> p h d", h=8),
                                            w.xt[0:R, :].rearrange("p (h d) -> p h d", h=8), heads(m.dskip[0:R, :]),
                                            ALU.mult).then_inc(s.xd_ready, 1)

            @block.vector
            def _(dve):
                chain = Chain(dve, s.dve_c)

                def steps(j):
                    q = j % 2
                    if j >= 2:
                        dve.wait_ge(s.xe_ready, j - 1)
                    nc.vector.tensor_copy(w.dt[0:R, q, :], chunks[j].dt).then_inc(s.dt_ready, 1)
                    dve.wait_ge(s.dt_ready, j + 1)
                    if j >= 1:
                        dve.wait_ge(s.acb_ready, j)
                    nc.vector.tensor_tensor(w.td[0:R, :, 0:R], tri.unsqueeze(1).broadcast_to([R, 8, R]),
                                            w.dt[0:R, q, 8:16].unsqueeze(2).broadcast_to([R, 8, R]),
                                            ALU.mult).then_inc(s.td_ready, 1)

                def finish(j):
                    q = j % 2
                    dve.wait_ge(s.yr_ready, j + 1)
                    for g in range(NG):
                        i = nc.vector.scalar_tensor_tensor(chunks[j].out[:, 256 * g:256 * (g + 1)],
                                                           w.y[0:R, q, 256 * g:256 * (g + 1)], w.yr[0:R, q, 4 + g:5 + g],
                                                           m.ssdn[0:R, 256 * g:256 * (g + 1)], ALU.mult, ALU.mult)
                    i.then_inc(s.y_done, 1)

                steps(0)
                for j in range(n):
                    q = j % 2
                    ch = chunks[j]
                    dve.wait_ge(s.sums_ready, j + 1)
                    if j >= 2:
                        dve.wait_ge(s.ex_ready, j - 1)
                    nc.vector.tensor_copy(w.small[0:R, q, 0:P + 16], m.bank[1][0:R, 0:P + 16]).then_inc(s.small_taken, 1)
                    dve.wait_ge(s.small_taken, j + 1)
                    nc.vector.tensor_tensor(w.small[0:R, q, P + 16:P + 24], w.small[0:R, q, P + 8:P + 16],
                                            w.small[0:R, q, P:P + 8], ALU.subtract).then_inc(s.diff_ready, 1)
                    dve.wait_ge(s.acb_ready, j + 1)
                    if j >= 1:
                        dve.wait_ge(s.yd_ready, j)
                    for h in range(8):
                        i = nc.vector.scalar_tensor_tensor(w.seg[0:R, h, 0:R],
                                                           m.bank[4 + h // 4][0:R, (h % 4) * R:(h % 4 + 1) * R],
                                                           w.small[0:R, q, P + h:P + h + 1], after,
                                                           ALU.subtract, ALU.add)
                    i.then_inc(s.seg_done, 1)
                    if j + 1 < n:
                        steps(j + 1)
                    dve.wait_ge(s.x_taken, j + 1)
                    nc.vector.tensor_tensor(w.xdt[0:R, :].rearrange("p (h d) -> p h d", h=8),
                                            w.xt[0:R, :].rearrange("p (h d) -> p h d", h=8), heads(w.dt[0:R, q, 0:8]),
                                            ALU.mult).then_inc(s.xdt_ready, 1)
                    dve.wait_ge(s.xdt_ready, j + 1)
                    dve.wait_ge(s.ex_ready, j + 1)
                    if j >= 1:
                        dve.wait_ge(s.state_ready, j)
                    nc.vector.tensor_tensor(w.xe[0:R, :].rearrange("p (h d) -> p h d", h=8),
                                            w.xdt[0:R, :].rearrange("p (h d) -> p h d", h=8), heads(w.ex[0:R, q, 16:24]),
                                            ALU.mult).then_inc(s.xe_ready, 1)
                    dve.wait_ge(s.e_ready, j + 1)
                    dve.wait_ge(s.cb_ready, j + 1)
                    for g in range(NG):
                        i = nc.vector.tensor_tensor(w.seg[0:R, 4 * g:4 * g + 4, 0:R], w.seg[0:R, 4 * g:4 * g + 4, 0:R],
                                                    m.bank[2][0:R, g * P:g * P + R].unsqueeze(1).broadcast_to([R, 4, R]),
                                                    ALU.mult)
                    i.then_inc(s.m_ready, 1)
                    if j >= 1:
                        finish(j - 1)
                    dve.wait_ge(s.yo_ready, j + 1)
                    if not sample:
                        for g in range(NG):
                            st = w.state[64 * g:64 * g + 64, :].rearrange("p (r d) -> p r d", r=4)
                            chain(nc.vector.tensor_tensor(
                                st, st, w.ex[64 * g:64 * g + 64, q, 8 + 4 * g:12 + 4 * g].unsqueeze(2).broadcast_to(
                                    [64, 4, HD]), ALU.mult))
                        dve.wait_ge(s.st_ready, j + 1)
                        for g in range(NG):
                            i = nc.vector.tensor_tensor(w.state[64 * g:64 * g + 64, :], w.state[64 * g:64 * g + 64, :],
                                                        m.bank[3][64 * g:64 * g + 64, 256 * g:256 * (g + 1)], ALU.add)
                        i.then_inc(s.state_ready, 1)
                    y = w.y[0:R, q, :]
                    if j >= 2:
                        dve.wait_ge(s.y_done, j - 1)
                    chain(nc.vector.tensor_tensor(y.rearrange("p (h d) -> p h d", h=8),
                                                  m.bank[6][0:R, :].rearrange("p (h d) -> p h d", h=8),
                                                  heads(w.ex[0:R, q, 0:8]), ALU.mult))
                    dve.wait_ge(s.yd_ready, j + 1)
                    chain(nc.vector.tensor_tensor(y, y, m.bank[7][0:R, :], ALU.add))
                    dve.wait_ge(s.xd_ready, j + 1)
                    chain(nc.vector.tensor_tensor(y, y, w.xd[0:R, :], ALU.add))
                    nc.vector.tensor_tensor(y, y, ch.z, ALU.mult).then_inc(s.y_ready, 1)
                finish(n - 1)


def stage_ssd(nc, io, m):
    c = m.c
    sb = Region(nc, m.conv_end, m.work_end)
    w = Buffers()
    w.xs = sb("chunk", [P, 2, 6, P])
    w.dt = sb("chunk_dt", [P, 2, 16])
    w.td = sb("dt_steps", [P, 8, P])
    w.small = sb("b_and_sums", [P, 2, P + 24])
    w.ex = sb("decays", [P, 2, 24])
    w.seg = sb("seg", [P, 8, P])
    w.xt = sb("x_tok", [P, DSSD])
    w.xdt = sb("xdt", [P, DSSD])
    w.xe = sb("x_to_end", [P, DSSD])
    w.xd = sb("x_skip", [P, DSSD])
    w.y = sb("y_ssd", [P, 2, DSSD])
    w.yr = sb("y_rstd", [P, 2, 6])
    w.junk = sb("junk_y", [P, 256])
    w.state = sb("state", [P, 256])
    w.s0 = sb("state0", [P, DB, 256])
    w.cm = sb("c_masked", [P, DB, NS])
    w.bm = sb("b_masked", [NS, DB, P])
    w.db = sb("dta_of_b", [NS, DB, 8])
    w.dec = sb("decay_of_b", [P, DB, 8])
    w.hin = m.hin
    w.hout = sb("state_out", [P, DB, 2, NG, HD])
    hd = by_head_pair

    with stage(nc, "zeroed turned taken") as s:
        with nc.Block() as block:
            @block.gpsimd
            def _(pool):
                nc.gpsimd.memset(w.state[:, :], 0.0)
                nc.gpsimd.memset(w.cm[:, :, :], 0.0).then_inc(s.zeroed, 1)

            @block.tensor
            def _(pe):
                for b in range(DB):
                    for i in range(2):
                        t = nc.tensor.transpose(m.bank[b // 2][:, ((b % 2) * 2 + i) * P:((b % 2) * 2 + i + 1) * P],
                                                w.hin[:, b, i, :, :], c("ident"))
                t.then_inc(s.turned, 1)

            @block.vector
            def _(dve):
                dve.wait_ge(s.zeroed, 1)
                nc.vector.tensor_copy(bass.AP(w.cm[:, :, :].tensor, 0, [[DB * NS, P], [NS + DS, DB], [1, DS]]),
                                      m.xc[:, 5, SEQ:TOK].rearrange("p (b t) -> p b t", b=DB))
                dve.wait_ge(s.turned, 1)
                for k in range(4):
                    nc.vector.tensor_copy(w.s0[:, 2 * k:2 * k + 2, :], m.bank[k][:, :].rearrange("p (b x) -> p b x", b=2))

    with nc.Fori(0, NT // PER) as turn:
        chunks = []
        for j in range(PER):
            i = turn * PER + j
            flat = lambda ap: ap.rearrange("p o c -> p (o c)")
            chunks.append(named(rows=P, sample=False, xc=m.xc[:, :, bass.ds(i * P, P)],
                               dt=flat(m.dt[:, bass.ds(i, 1), :]), z=flat(m.pz[:, bass.ds(i, 1), PZ_Z:PZ_Z + DSSD]),
                               out=flat(m.mix[:, bass.ds(i, 1), DATT:DM])))
        ssd_chunks(nc, m, w, chunks)
    ssd_chunks(nc, m, w, [named(rows=NS, sample=True, xc=m.xc[:, :, SEQ:TOK], dt=m.dt[0:NS, NT, :],
                               z=m.pz[0:NS, NT, PZ_Z:PZ_Z + DSSD], out=m.mix[0:NS, NT, DATT:DM])])

    with stage(nc, "dta_ready sums_ready decayed b_ready multiplied scaled added turned taken stored") as s:
        with nc.Block() as block:
            @block.tensor
            def _(pe):
                pe.wait_ge(s.dta_ready, 1)
                nc.tensor.matmul(m.bank[7][:, 0:64], c("ones")[0:NS, :], w.db[:, :, :], start=True,
                                 stop=True).then_inc(s.sums_ready, 1)
                pe.wait_ge(s.b_ready, 1)
                for b in range(DB):
                    if b >= 4:
                        pe.wait_ge(s.added, b - 3)
                    nc.tensor.matmul(m.bank[b % 4][:, :], w.bm[:, b, :], w.xe[0:NS, :], start=True,
                                     stop=True).then_inc(s.multiplied, 1)
                for b in range(DB + 1):
                    src = w.s0[:, b, :] if b < DB else w.state[:, :]
                    if b < DB:
                        pe.wait_ge(s.added, b + 1)
                    if b >= 2:
                        pe.wait_ge(s.taken, b - 1)
                    for i in range(2):
                        t = nc.tensor.transpose(m.bank[4 + b % 2][:, i * P:(i + 1) * P], src[:, i * P:(i + 1) * P],
                                                c("ident"))
                    t.then_inc(s.turned, 1)

            @block.scalar
            def _(act):
                act.wait_ge(s.sums_ready, 1)
                nc.scalar.activation(w.dec[:, :, :], m.bank[7][:, 0:64].rearrange("p (b h) -> p b h", b=DB),
                                     ACT.Exp).then_inc(s.decayed, 1)
                for b in range(DB + 1):
                    act.wait_ge(s.turned, b + 1)
                    dst = w.hout[:, b, :, :, :] if b < DB else w.hin[:, 0, :, :, :]
                    nc.scalar.activation(dst.rearrange("p i g n -> p (i g n)"), m.bank[4 + b % 2][:, 0:256],
                                         ACT.Copy).then_inc(s.taken, 1)

            @block.vector
            def _(dve):
                nc.vector.tensor_tensor(w.db[:, :, :], m.dt[0:NS, NT, 8:16].unsqueeze(1).broadcast_to([NS, DB, 8]),
                                        c("s_of_b")[0:NS, :].unsqueeze(2).broadcast_to([NS, DB, 8]),
                                        ALU.mult).then_inc(s.dta_ready, 1)
                nc.vector.tensor_tensor(w.bm[:, :, :], w.small[0:NS, 0, 0:P].unsqueeze(1).broadcast_to([NS, DB, P]),
                                        c("s_of_b")[0:NS, :].unsqueeze(2).broadcast_to([NS, DB, P]),
                                        ALU.mult).then_inc(s.b_ready, 1)
                dve.wait_ge(s.decayed, 1)
                for b in range(DB):
                    for g in range(NG):
                        st = w.s0[64 * g:64 * g + 64, b, :].rearrange("p (r d) -> p r d", r=4)
                        i = nc.vector.tensor_tensor(st, st, w.dec[64 * g:64 * g + 64, b, 4 * g:4 * g + 4].unsqueeze(
                            2).broadcast_to([64, 4, HD]), ALU.mult)
                    i.then_inc(s.scaled, 1)
                    dve.wait_ge(s.scaled, b + 1)
                    dve.wait_ge(s.multiplied, b + 1)
                    for g in range(NG):
                        i = nc.vector.tensor_tensor(w.s0[64 * g:64 * g + 64, b, :], w.s0[64 * g:64 * g + 64, b, :],
                                                    m.bank[b % 4][64 * g:64 * g + 64, 256 * g:256 * (g + 1)], ALU.add)
                    i.then_inc(s.added, 1)

            @block.sync
            def _(sp):
                for b in range(0, DB, 2):
                    sp.wait_ge(s.taken, b + 2)
                    for i in range(4):
                        sp.dma_start(hd(io.s_ssm)[:, b:b + 2, i, :], w.hout[:, b:b + 2, i % 2, i // 2, :]
                                     ).then_inc(s.stored, 16)
                sp.wait_ge(s.taken, DB + 1)
                for i in range(4):
                    sp.dma_start(hd(io.p_ssm)[:, 0, i, :], w.hin[:, 0, i % 2, i // 2, :]).then_inc(s.stored, 16)
                sp.wait_ge(s.stored, 16 * (4 * DB // 2 + 4))


SUBS = PAGE // CSTRIDE
CW = CSTRIDE * DKV


def place_compression(nc, m):
    sb = Region(nc, m.work_end, m.mix_start)
    w = m.cmp = Buffers()
    w.w1 = sb("cmp_w1", [P, 2, 8, 2, CHID])
    w.w2 = sb("cmp_w2", [CHID, 2, HD])
    w.pe = sb("cmp_pe", [P, 2, 16])
    w.pre = sb("cmp_pe_sum", [CHID, 2])
    return w


def stage_prompt_compress(nc, io, m):
    c = m.c
    sb = Region(nc, m.att_end, m.work_end)
    N = SEQ // CSTRIDE
    m.kcT = sb("kcT", [P, N])
    m.vc = sb("vc", [N, DKV])
    m.bias = sb("bias", [P, NH, 256])
    m.prompt_att_start = sb.at
    w = m.cmp
    x = sb("rows16", [N, 2, CW])
    xr = sb("rows16_by_group", [N, 2, CW])
    xt = sb("rows16_T", [P, 2, 8, NG, N])
    up = sb("second_half", [CHID, 2, NG, N])
    hid = sb("hidden", [CHID, 2, NG, N])
    kc = sb("kc_tok", [N, DKV])
    sq = sb("kc_square", [N, DKV])
    st = sb("kc_stats", [N, 6])
    with stage(nc, "loaded*2 grouped turned taken summed shifted added hidden_done projected kc_raw squared stats rstd "
                   "normed kc_turned bias_loaded gates_out gates_in zeroed pe_summed act_c dve_c") as s:
        with nc.Block() as block:
            @block.sync
            def _(sp):
                for kv, src in enumerate((io.p_k_cmp, io.p_v_cmp)):
                    sp.dma_start(x[:, kv, :], src.rearrange("a b (n s) g d -> (a b n) (s g d)", s=CSTRIDE)
                                 ).then_inc(s.loaded[kv], 16)
                t = m.bias_dram.tensor
                sp.dma_start(m.bias[:, :, :], bass.AP(t, 127, [[BIASW - 1, P], [P * BIASW, NH], [1, 256]])).then_inc(s.bias_loaded, 16)
                sp.dma_start(io.gate_dram, m.gates[0:NS, NT, :]).then_inc(s.gates_out, 16)
                sp.wait_ge(s.gates_out, 16)
                for b in range(DB):
                    for g in range(NG):
                        src = bass.AP(io.gate_dram.tensor, b * DS * 3 * NH + g * 3 * REP, [[3 * NH, DS], [3, REP], [1, 3]])
                        p0 = (b % B4) * 32 + g * 16
                        sp.dma_start(m.gate_rows[p0:p0 + 16, b // B4, :], src).then_inc(s.gates_in, 16)
                sp.wait_ge(s.gates_in, 16 * DB * NG)
                sp.wait_ge(s.bias_loaded, 16)

            @block.gpsimd
            def _(pool):
                nc.gpsimd.memset(hid[:, :, :, :], 0.0).then_inc(s.zeroed, 1)

            @block.tensor
            def _(pe):
                pe.wait_ge(m.cmp_loaded, 16 * 8)
                for kv in range(2):
                    for n in range(16):
                        mm = nc.tensor.matmul(m.bank[7][0:CHID, kv:kv + 1], w.w1[:, kv, n % 8, n // 8, :],
                                              w.pe[:, kv, n:n + 1], start=(n == 0), stop=(n == 15))
                mm.then_inc(s.pe_summed, 1)
                for kv in range(2):
                    pe.wait_ge(s.grouped, kv + 1)
                    for a in range(4):
                        n = 4 * kv + a
                        if n >= 2:
                            pe.wait_ge(s.taken, n - 1)
                        for k in range(4):
                            g, q = k % 2, 2 * a + k // 2
                            t = nc.tensor.transpose(m.bank[n % 2][:, k * N:(k + 1) * N],
                                                    xr[:, kv, g * 1024 + q * P:g * 1024 + (q + 1) * P], c("ident")[0:N, 0:N])
                        t.then_inc(s.turned, 1)
                    pe.wait_ge(s.taken, 4 * kv + 4)
                    for q in range(8):
                        mm = nc.tensor.matmul(m.bank[2 + kv][:, 0:NG * N], w.w1[:, kv, q, :, :].rearrange("p j h -> p (j h)"),
                                              xt[:, kv, q, :, :], start=(q == 0), stop=(q == 7))
                    mm.then_inc(s.summed, 1)
                for kv in range(2):
                    pe.wait_ge(s.hidden_done, kv + 1)
                    for g in range(NG):
                        mm = nc.tensor.matmul(m.bank[4 + kv][0:N, g * HD:(g + 1) * HD], hid[:, kv, g, :], w.w2[:, kv, :],
                                              start=True, stop=True)
                    mm.then_inc(s.projected, 1)
                pe.wait_ge(s.normed, 1)
                nc.tensor.transpose(m.bank[6][:, 0:N], kc[:, :], c("ident")[0:N, 0:N]).then_inc(s.kc_turned, 1)

            @block.scalar
            def _(act):
                chain = Chain(act, s.act_c)
                act.wait_ge(s.zeroed, 1)
                for kv in range(2):
                    act.wait_ge(s.summed, kv + 1)
                    nc.scalar.activation(up[:, kv, :, :], m.bank[2 + kv][CHID:P, 0:NG * N].rearrange(
                        "p (g n) -> p g n", g=NG), ACT.Copy).then_inc(s.shifted, 1)
                    act.wait_ge(s.added, kv + 1)
                    nc.scalar.activation(hid[:, kv, :, 0:N - 1], up[:, kv, :, 0:N - 1], ACT.Silu,
                                         bias=w.pre[:, kv:kv + 1]).then_inc(s.hidden_done, 1)
                act.wait_ge(s.kc_raw, 1)
                nc.scalar.activation(sq[:, :], kc[:, :], ACT.Square).then_inc(s.squared, 1)
                act.wait_ge(s.stats, 1)
                chain(nc.scalar.activation(st[:, 2:4], st[:, 0:2], ACT.Ln, scale=1.0 / HD, bias=c("eps")[0:N, :]))
                nc.scalar.activation(st[:, 4:6], st[:, 2:4], ACT.Exp, scale=-0.5).then_inc(s.rstd, 1)

            @block.vector
            def _(dve):
                chain = Chain(dve, s.dve_c)
                for kv in range(2):
                    dve.wait_ge(s.loaded[kv], 16)
                    nc.vector.tensor_copy(xr[:, kv, :].rearrange("p (g s d) -> p g s d", g=NG, s=CSTRIDE),
                                          x[:, kv, :].rearrange("p (s g d) -> p g s d", g=NG, s=CSTRIDE)
                                          ).then_inc(s.grouped, 1)
                    for a in range(4):
                        n = 4 * kv + a
                        dve.wait_ge(s.turned, n + 1)
                        nc.vector.tensor_copy(xt[:, kv, 2 * a:2 * a + 2, :, :],
                                              m.bank[n % 2][:, 0:4 * N].rearrange("p (q g n) -> p q g n", q=2, g=NG)
                                              ).then_inc(s.taken, 1)
                dve.wait_ge(s.pe_summed, 1)
                nc.vector.tensor_copy(w.pre[:, :], m.bank[7][0:CHID, 0:2])
                for kv in range(2):
                    dve.wait_ge(s.shifted, kv + 1)
                    nc.vector.tensor_tensor(up[:, kv, :, 0:N - 1], up[:, kv, :, 1:N],
                                            m.bank[2 + kv][0:CHID, 0:NG * N].rearrange("p (g n) -> p g n", g=NG)[:, :, 0:N - 1],
                                            ALU.add).then_inc(s.added, 1)
                dve.wait_ge(s.projected, 2)
                nc.vector.tensor_copy(m.vc[:, :], m.bank[5][0:N, 0:DKV])
                nc.vector.tensor_copy(kc[:, :], m.bank[4][0:N, 0:DKV]).then_inc(s.kc_raw, 1)
                dve.wait_ge(s.squared, 1)
                nc.vector.tensor_reduce(st[:, 0:2], sq[:, :].rearrange("p (g d) -> p g d", g=NG), AX.X,
                                        ALU.add).then_inc(s.stats, 1)
                dve.wait_ge(s.rstd, 1)
                k3 = kc[:, :].rearrange("p (g d) -> p g d", g=NG)
                chain(nc.vector.tensor_tensor(k3, k3, st[:, 4:6].unsqueeze(2).broadcast_to([N, NG, HD]), ALU.mult))
                nc.vector.tensor_tensor(k3, k3, m.kn[0:N, :].unsqueeze(1).broadcast_to([N, NG, HD]),
                                        ALU.mult).then_inc(s.normed, 1)
                dve.wait_ge(s.kc_turned, 1)
                nc.vector.tensor_copy(m.kcT[:, :], m.bank[6][:, 0:N])


def stage_prompt_attention(nc, io, m):
    c = m.c
    assert SEQ // SELB <= 16
    sb = Region(nc, m.prompt_att_start, m.work_end)
    qp = sb("q_padded", [P, NG, NT, P])
    psel = sb("p_sel", [P, 2, SEQ])
    pwc = sb("p_win_cmp", [P, 2, 768])
    pt = sb("p_T", [P, 4, 512])
    negmax = sb("neg_max", [P, NG * NT, 3])
    sums = sb("row_sums", [P, NG * NT, 3])
    scale = sb("row_scale", [P, NG * NT, 3])
    o_raw = sb("o_by_branch", [P, NG * NT, 3, HD])
    CMP, SEL, WINB = 0, 1, 2
    CC = 640
    units = [(t, g) for t in range(NT) for g in range(NG)]

    def parts(n):
        t, g = units[n // 2]
        if n % 2 == 0:
            return [(SEL, k, k * P, P) for k in range(t + 1)]
        lo = max(0, t - 4)
        return [(WINB, k, (k - lo) * P, P) for k in range(lo, t + 1)] + [(CMP, 0, CC, 8 * t + 7)]

    def groups(n):
        p = parts(n)
        return [p[i:i + 4] for i in range(0, len(p), 4)]

    first_group = [0]
    for n in range(2 * len(units)):
        first_group.append(first_group[-1] + len(groups(n)))

    with stage(nc, "zeroed") as s:
        with nc.Block() as block:
            @block.gpsimd
            def _(pool):
                nc.gpsimd.memset(qp[:, :, :, :], 0.0)

    with nc.Fori(0, REP) as r, stage(
            nc, "q_ready scored prepared exp_done turned copied weighted o_taken dve_c act_c") as s:
        with nc.Block() as block:
            @block.tensor
            def _(pe):
                def scores(n):
                    t, g = units[n // 2]
                    if n >= 2:
                        pe.wait_ge(s.exp_done, n - 1)
                    if n % 2 == 0:
                        for a in range(0, (t + 1) * P, 512):
                            b = min(a + 512, (t + 1) * P)
                            mm = nc.tensor.matmul(m.psum[:, a:b], qp[:, g, t, :], m.ksT[:, a:b], start=True, stop=True)
                    else:
                        lo = max(0, t - 4) * P
                        for a in range(lo, (t + 1) * P, 512):
                            b = min(a + 512, (t + 1) * P)
                            nc.tensor.matmul(m.psum[:, 1024 + a - lo:1024 + b - lo], qp[:, g, t, :], m.kwT[:, a:b],
                                             start=True, stop=True)
                        mm = nc.tensor.matmul(m.psum[:, 1024 + CC:1024 + CC + 8 * t + 7], qp[:, g, t, :],
                                              m.kcT[:, 0:8 * t + 7], start=True, stop=True)
                    mm.then_inc(s.scored, 1)

                def turn(n, i):
                    G = first_group[n] + i
                    src = psel if n % 2 == 0 else pwc
                    if G >= 2:
                        pe.wait_ge(s.copied, G - 1)
                    for k, (_, _, col, width) in enumerate(groups(n)[i]):
                        x = nc.tensor.transpose(m.bank[4 + G % 2][0:width, k * P:(k + 1) * P],
                                                src[:, (n // 2) % 2, col:col + width], c("ident"))
                    x.then_inc(s.turned, 1)

                def weight(n, i):
                    t, g = units[n // 2]
                    G = first_group[n] + i
                    pe.wait_ge(s.copied, G + 1)
                    if n % 2 == 0 and n >= 4 and i == 0:
                        pe.wait_ge(s.o_taken, n // 2 - 1)
                    lo = max(0, t - 4)
                    for k, (br, kt, col, width) in enumerate(groups(n)[i]):
                        v = (m.vc[0:width, g * HD:(g + 1) * HD] if br == CMP else
                             m.v[:, kt, 0 if br == SEL else 1, g * HD:(g + 1) * HD])
                        mm = nc.tensor.matmul(m.bank[6 + (n // 2) % 2][:, br * HD:(br + 1) * HD],
                                              pt[0:width, G % 4, k * P:(k + 1) * P], v,
                                              start=(br == CMP or kt == (0 if br == SEL else lo)),
                                              stop=(br == CMP or kt == t))
                    mm.then_inc(s.weighted, 1)

                pe.wait_ge(s.q_ready, 2)
                scores(0)
                scores(1)
                order = [(n, i) for n in range(2 * len(units)) for i in range(len(groups(n)))]
                for k, (n, i) in enumerate(order):
                    if i == 0:
                        if n + 2 < 2 * len(units):
                            scores(n + 2)
                        pe.wait_ge(s.exp_done, n + 1)
                    turn(n, i)
                    if k:
                        weight(*order[k - 1])
                weight(*order[-1])

            def copy_group(engine, sem, copy, n, i):
                G = first_group[n] + i
                engine.wait_ge(s.turned, G + 1)
                if G >= 4:
                    engine.wait_ge(s.weighted, G - 3)
                p = groups(n)[i]
                whole = [x for x in p if x[3] == P]
                if whole:
                    x = copy(pt[:, G % 4, 0:len(whole) * P], m.bank[4 + G % 2][:, 0:len(whole) * P])
                if len(whole) < len(p):
                    k, width = len(p) - 1, p[-1][3]
                    x = copy(pt[0:width, G % 4, k * P:(k + 1) * P], m.bank[4 + G % 2][0:width, k * P:(k + 1) * P])
                x.then_inc(sem, 1)

            @block.scalar
            def _(act):
                def exps(n):
                    t, g = units[n // 2]
                    u = n // 2
                    act.wait_ge(s.prepared, n + 1)
                    if n >= 4:
                        act.wait_ge(s.weighted, first_group[n - 3])
                    if n % 2 == 0:
                        act_ = nc.scalar.activation(psel[:, u % 2, 0:(t + 1) * P], m.psum[:, 0:(t + 1) * P], ACT.Exp,
                                                    bias=negmax[:, u, SEL:SEL + 1], accum_out=sums[:, u, SEL:SEL + 1])
                    else:
                        k = min(t, 4) + 1
                        nc.scalar.activation(pwc[:, u % 2, 0:k * P], m.psum[:, 1024:1024 + k * P], ACT.Exp,
                                             bias=negmax[:, u, WINB:WINB + 1], accum_out=sums[:, u, WINB:WINB + 1])
                        act_ = nc.scalar.activation(pwc[:, u % 2, CC:CC + 8 * t + 7], m.psum[:, 1024 + CC:1024 + CC + 8 * t + 7],
                                                    ACT.Exp, bias=negmax[:, u, CMP:CMP + 1],
                                                    accum_out=sums[:, u, CMP:CMP + 1])
                    act_.then_inc(s.exp_done, 1)

                exps(0)
                exps(1)
                for n in range(2 * len(units)):
                    for i in range(len(groups(n))):
                        copy_group(act, s.copied, lambda o, a: nc.scalar.activation(o, a, ACT.Copy), n, i)
                    if n + 2 < 2 * len(units):
                        exps(n + 2)

            @block.vector
            def _(dve):
                chain = Chain(dve, s.dve_c)
                for g in range(NG):
                    rows = slice(64 * g, 64 * g + 64)
                    nc.vector.tensor_copy(qp[rows, g, :, :],
                                          m.qT[rows, :, bass.ds(r, 1), :].rearrange("p t o q -> p t (o q)")
                                          ).then_inc(s.q_ready, 1)

                def add(region, table):
                    chain(nc.vector.tensor_tensor(region, region, table, ALU.add))

                def top(region, u, br):
                    return nc.vector.tensor_reduce(negmax[:, u, br:br + 1], region, AX.X, ALU.max, negate=True)

                def prepare(n):
                    t, g = units[n // 2]
                    u = n // 2
                    bias = m.bias[:, bass.ds(g * REP + r, 1), :].rearrange("p o k -> p (o k)")
                    dve.wait_ge(s.scored, n + 1)
                    if n % 2 == 0:
                        lo = max(0, t - 1)
                        add(m.psum[:, lo * P:(t + 1) * P], bias[:, 0:256] if t else bias[:, P:256])
                        i = top(m.psum[:, 0:(t + 1) * P], u, SEL)
                    else:
                        k = min(t, 4) + 1
                        lo = max(0, k - 2)
                        add(m.psum[:, 1024 + lo * P:1024 + k * P], bias[:, 0:256] if t else bias[:, P:256])
                        if t >= 4:
                            add(m.psum[:, 1024:1024 + P], c("far"))
                        top(m.psum[:, 1024:1024 + k * P], u, WINB)
                        first = max(0, 8 * t - 9)
                        col = 159 + 16 * (first - 8 * t)
                        add(m.psum[:, 1024 + CC + first:1024 + CC + 8 * t + 7], bias[:, col:256:16])
                        chain(top(m.psum[:, 1024 + CC:1024 + CC + 8 * t + 7], u, CMP))
                        i = nc.vector.tensor_scalar(negmax[:, u, CMP:CMP + 1], negmax[:, u, CMP:CMP + 1], 1e29, None,
                                                    ALU.min)
                    i.then_inc(s.prepared, 1)

                def take_o(u):
                    dve.wait_ge(s.weighted, first_group[2 * u + 2])
                    nc.vector.tensor_copy(o_raw[:, u, :, :].rearrange("p b d -> p (b d)"),
                                          m.bank[6 + u % 2][:, 0:3 * HD]).then_inc(s.o_taken, 1)

                def finish(k):
                    us, ts = slice(4 * k, 4 * k + 4), slice(2 * k, 2 * k + 2)
                    sc, o = scale[:, us, :], o_raw[:, us, :, :]
                    gate = m.gates[:, ts, :].rearrange("p t (g r b) -> p t g r b", g=NG, r=REP)[:, :, :, bass.ds(r, 1), :]
                    out = m.mix[:, ts, 0:DATT].rearrange("p t (g r d) -> p t g r d", g=NG, r=REP)[
                        :, :, :, bass.ds(r, 1), :].rearrange("p t g o d -> p t g (o d)")
                    dve.wait_ge(s.o_taken, 4 * k + 4)
                    chain(nc.vector.tensor_scalar(sc, sums[:, us, :], 1e-30, None, ALU.max))
                    chain(nc.vector.reciprocal(sc, sc))
                    sc4 = sc.rearrange("p (t g) b -> p t g b", g=NG)
                    chain(nc.vector.tensor_tensor(sc4, sc4, gate.rearrange("p t g o b -> p t g (o b)"), ALU.mult))
                    chain(nc.vector.tensor_tensor(o, o, sc.unsqueeze(3).broadcast_to([P, 4, 3, HD]), ALU.mult))
                    chain(nc.vector.tensor_tensor(o[:, :, 0, :], o[:, :, 0, :], o[:, :, 1, :], ALU.add))
                    nc.vector.tensor_tensor(out, o[:, :, 0, :].rearrange("p (t g) d -> p t g d", g=NG),
                                            o[:, :, 2, :].rearrange("p (t g) d -> p t g d", g=NG), ALU.add)

                prepare(0)
                prepare(1)
                for n in range(2 * len(units)):
                    if n + 2 < 2 * len(units):
                        prepare(n + 2)
                    if n % 2 == 0 and n >= 2:
                        take_o(n // 2 - 1)
                    if n % 8 == 1 and n > 1:
                        finish((n - 9) // 8)
                take_o(len(units) - 1)
                finish(len(units) // 4 - 1)


def prepare_sample_attention(nc, io, m, w):
    with stage(nc, "zeroed") as s:
        with nc.Block() as block:
            @block.gpsimd
            def _(pool):
                nc.gpsimd.memset(w.q_all[:, :, :, :], 0.0).then_inc(s.zeroed, 1)

            @block.vector
            def _(dve):
                nc.vector.memset(w.hid[:, :, :], 0.0)
                nc.vector.memset(w.pc[:, :], 0.0)
                nc.vector.memset(w.imp[:, :], 0.0)
                nc.vector.memset(w.score[:, SCORES - 1:SCORES], 2e30)
                dve.wait_ge(s.zeroed, 1)
                for g in range(NG):
                    rows = slice(64 * g, 64 * g + 64)
                    for b in range(B4):
                        for hb in range(2):
                            q0 = (hb * B4 + b) * DS
                            nc.vector.tensor_copy(
                                w.q_all[rows, hb, b, b * 32 + g * 16:b * 32 + g * 16 + 16].rearrange("p (t r) -> p r t", t=DS),
                                m.qTs[rows, :, q0:q0 + DS])


SCORES = PAST // SELB + 1
RING = 4


def sample_attention_turn(nc, io, m, w, hb):
    c = m.c
    NA, NB_, NC_ = 16, 8, 8
    caches = [io.cache_k_cmp, io.cache_v_cmp, io.cache_k_sel, io.cache_v_sel]
    chunks = [(caches[kv], b, h) for b in range(B4) for kv in range(2) for h in range(2)]
    chunks += [(caches[2], b, h) for h in range(2) for b in range(B4)]
    chunks += [(caches[3], b, h) for b in range(B4) for h in range(2)]
    fill_a = lambda u, i: 8 * u + i
    fill_b = lambda k, i: 64 + i if k == 0 else 70 + 4 * (k - 1) + i
    fill_k = lambda i: 68 + i
    fill_w = lambda b: 98 + b
    fill_p = lambda i: 102 + i
    PCMP, PWIN, PNEW, PSEL = 0, 2, 6, 8
    p_pieces = ([(w.pc, k * P, P) for k in range(2)] + [(w.sw, k * P, P) for k in range(4)] +
                [(w.ss, PAST, DS), (w.sw, WIN, DS)] + [(w.ss, k * P, P) for k in range(32)])

    with stage(nc, "rows_ready v_used win_loaded kn_ready q_ready grouped turned copied_v copied_a summed "
                   "shifted added hidden_done projected taken squared k_sums k_rstd k_normed c_scored c_ready c_exp "
                   "c_weights imp_done masked s_scored s_taken w_scored n_scored w_taken w_ready s_ready w_exp s_exp "
                   "p_final o_ready stored dve_c act_c") as s:
        with nc.Block() as block:
            @block.sync
            def _(sp):
                for dst, src in ((w.wk, io.cache_k_win), (w.wv, io.cache_v_win)):
                    v = src.rearrange("o b (p k) g d -> p (o b) (k g d)", k=4)
                    sp.dma_start(dst[:, :, :], v[:, bass.ds(hb * B4, B4), :]).then_inc(s.win_loaded, 16)
                vs = io.s_v_sel.rearrange("o b t g d -> t (o b) (g d)")
                vw = io.vw_new.rearrange("(b t) c -> t b c", b=DB)
                sp.dma_start(w.vn[:, :, 0, :], vs[:, bass.ds(hb * B4, B4), :]).then_inc(s.win_loaded, 16)
                sp.dma_start(w.vn[:, :, 1, :], vw[:, bass.ds(hb * B4, B4), :]).then_inc(s.win_loaded, 16)
                sp.wait_ge(s.o_ready, 1)
                for b in range(B4):
                    for g in range(NG):
                        dst = io.o_dram[bass.ds(hb * B4 * DS + b * DS, DS), :].rearrange("t (g r d) -> t g r d", g=NG, r=REP)
                        sp.dma_start(dst[:, g, :, :], w.os[g * 16:g * 16 + 16, b, g * HD:(g + 1) * HD]
                                     ).then_inc(s.stored, 16)
                sp.wait_ge(s.stored, 16 * 8)

            @block.gpsimd
            def _(pool):
                pool.wait_ge(s.rows_ready, 1)
                for n, (cache, b, h) in enumerate(chunks):
                    k = n - RING
                    if 0 <= k < NA:
                        pool.wait_ge(s.grouped, k + 1)
                    elif NA <= k < NA + NB_:
                        pool.wait_ge(s.turned, fill_b(k - NA, 3) + 1)
                    elif k >= 0:
                        pool.wait_ge(s.v_used, k - NA - NB_ + 1)
                    nc.gpsimd.indirect_dma_start(
                        w.ring[:, n % RING, :], None,
                        cache.rearrange("o n (a s) g d -> (o n a) (s g d)", s=CSTRIDE),
                        bass.IndirectOffsetOnAxis(ap=w.rows[:, 2 * b + h:2 * b + h + 1], axis=0)
                    ).then_inc(w.landed[n % RING], 16)

            def chunk_here(engine, n):
                engine.wait_ge(w.landed[n % RING], hb * (16 * len(chunks) // RING) + 16 * (n // RING + 1))

            @block.tensor
            def _(pe):
                def bank_free(f):
                    if f >= 2:
                        pe.wait_ge(s.copied_a if f % 2 else s.copied_v, f // 2)

                def turn(f, pieces):
                    bank_free(f)
                    for k, (src, width) in enumerate(pieces):
                        x = nc.tensor.transpose(m.bank[4 + f % 2][0:width, k * P:(k + 1) * P], src, c("ident"))
                    x.then_inc(s.turned, 1)

                def copied(f):
                    pe.wait_ge(s.copied_a if f % 2 else s.copied_v, f // 2 + 1)

                def turn_a(u, i):
                    n = 2 * u + i // 4
                    pe.wait_ge(s.grouped, n + 1)
                    a = i % 4
                    turn(fill_a(u, i), [(w.xr[:, n % 2, g * 1024 + q * P:g * 1024 + (q + 1) * P], P)
                                        for q in (2 * a, 2 * a + 1) for g in range(NG)])

                def project(u):
                    pe.wait_ge(s.hidden_done, u + 1)
                    if u >= 2:
                        pe.wait_ge(s.taken, u - 1)
                    for h in range(2):
                        for g in range(NG):
                            mm = nc.tensor.matmul(m.bank[2 + u % 2][:, (2 * h + g) * HD:(2 * h + g + 1) * HD],
                                                  w.hid[:, g, h * P:(h + 1) * P], m.cmp.w2[:, u % 2, :],
                                                  start=True, stop=True)
                    mm.then_inc(s.projected, 1)

                for i in range(8):
                    turn_a(0, i)
                for u in range(8):
                    if u >= 2:
                        pe.wait_ge(s.added, u - 1)
                    for q in range(8):
                        if q == 0:
                            copied(fill_a(u, 6))
                            copied(fill_a(u, 7))
                        mm = nc.tensor.matmul(m.bank[u % 2][:, :], m.cmp.w1[:, u % 2, q, :, :].rearrange("p j h -> p (j h)"),
                                              w.xt[:, u % 2, q, :, :], start=(q == 0), stop=(q == 7))
                        if q == 7:
                            mm.then_inc(s.summed, 1)
                        if u < 7:
                            turn_a(u + 1, q)
                    if u:
                        project(u - 1)
                project(7)

                def turn_b(k, i):
                    if i == 0:
                        chunk_here(pe, NA + k)
                    x = w.ring[:, (NA + k) % RING, :]
                    turn(fill_b(k, i), [(x[:, (4 * i + j) * P:(4 * i + j + 1) * P], P) for j in range(4)])

                for i in range(4):
                    turn_b(0, i)
                pe.wait_ge(s.k_normed, 1)
                for i in range(2):
                    turn(fill_k(i), [(w.kraw[:, (4 * i + j) * P:(4 * i + j + 1) * P], P) for j in range(4)])
                copied(fill_k(0))
                copied(fill_k(1))
                pe.wait_ge(s.q_ready, 1)
                for b in range(B4):
                    mm = nc.tensor.matmul(m.bank[6][:, 0:255], w.q[:, b, :], w.kcT[:, b * 256:b * 256 + 255],
                                          start=(b == 0), stop=(b == B4 - 1))
                mm.then_inc(s.c_scored, 1)
                for k in range(NB_):
                    if k == B4:
                        pe.wait_ge(s.s_taken, 4)
                    if k == 2:
                        pe.wait_ge(s.c_weights, 1)
                        nc.tensor.matmul(m.bank[7][:, 0:255], c("rep_sum"), w.pc[:, 0:255], start=True,
                                         stop=True).then_inc(s.imp_done, 1)
                    if k == 0:
                        pe.wait_ge(s.taken, 8)
                        pe.wait_ge(s.added, 8)
                    for i in range(4):
                        copied(fill_b(k, i))
                        mm = nc.tensor.matmul(m.bank[i][:, :], w.q[:, k % B4, :], w.kt[:, k % 2, i * 512:(i + 1) * 512],
                                              start=(k % B4 == 0), stop=(k % B4 == B4 - 1))
                        if i == 3:
                            mm.then_inc(s.s_scored, 1)
                        if k + 1 < NB_:
                            turn_b(k + 1, i)
                pe.wait_ge(s.win_loaded, 64)
                for b in range(B4):
                    turn(fill_w(b), [(w.wk[:, b, j * P:(j + 1) * P], P) for j in range(4)])
                pe.wait_ge(s.c_exp, 1)
                for b in range(B4):
                    copied(fill_w(b))
                    mm = nc.tensor.matmul(m.bank[6][:, :], w.q[:, b, :], w.kt[:, 0, b * 512:(b + 1) * 512],
                                          start=(b == 0), stop=(b == B4 - 1))
                mm.then_inc(s.w_scored, 1)
                pe.wait_ge(s.masked, 1)
                pe.wait_ge(s.kn_ready, 1)
                for br in range(2):
                    for b in range(B4):
                        mm = nc.tensor.matmul(m.bank[7][:, 4 * br:4 * br + 4], w.q[:, b, :], w.kn[:, br, b * DS:(b + 1) * DS],
                                              start=(b == 0), stop=(b == B4 - 1))
                mm.then_inc(s.n_scored, 1)
                pe.wait_ge(s.p_final, 3)
                for i in range(10):
                    turn(fill_p(i), [(src[:, col:col + width], width) for src, col, width in p_pieces[4 * i:4 * i + 4]])
                copied(fill_p(8))
                copied(fill_p(9))
                pe.wait_ge(s.w_taken, 2)
                for b in range(B4):
                    terms = [(w.pt[:, PCMP + h, :], w.vc[:, b, h, :]) for h in range(2)]
                    terms += [(w.pt[:, PWIN + k, :], w.wv[:, b, k * P:(k + 1) * P]) for k in range(4)]
                    terms += [(w.pt[0:DS, PNEW + br, :], w.vn[:, b, br, :]) for br in range(2)]
                    terms += [(w.pt[:, PSEL + k, :], None) for k in range(32)]
                    for n, (weights, v) in enumerate(terms):
                        h, k = divmod(n - PSEL, 16)
                        if v is None:
                            chunk = NA + NB_ + 2 * b + h
                            if k == 0:
                                chunk_here(pe, chunk)
                            v = w.ring[:, chunk % RING, k * P:(k + 1) * P]
                        mm = nc.tensor.matmul(m.bank[7][0:32, b * P:(b + 1) * P], weights[:, b * 32:(b + 1) * 32], v,
                                              start=(n == 0), stop=(n == len(terms) - 1))
                        if n >= PSEL and k == 15:
                            mm.then_inc(s.v_used, 1)

            def copy(engine, f, dst, src_view=None, width=P):
                act = engine is w.act
                engine.wait_ge(s.turned, f + 1)
                src = m.bank[4 + f % 2][0:width, :] if src_view is None else src_view(m.bank[4 + f % 2])
                x = nc.scalar.activation(dst, src, ACT.Copy) if act else nc.vector.tensor_copy(dst, src)
                x.then_inc(s.copied_a if act else s.copied_v, 1)

            def copy_a(engine, u, i):
                if i < 2 and u >= 2:
                    engine.wait_ge(s.summed, u - 1)
                h, a = divmod(i, 4)
                copy(engine, fill_a(u, i), w.xt[:, u % 2, 2 * a:2 * a + 2, :, h * P:(h + 1) * P],
                     lambda bank: bank[:, :].rearrange("p (q g n) -> p q g n", q=2, g=NG))

            def copy_b(engine, k, i):
                if k >= 2 and i < 2:
                    engine.wait_ge(s.s_scored, k - 1)
                copy(engine, fill_b(k, i), w.kt[:, k % 2, i * 512:(i + 1) * 512])

            def copy_w(engine, b):
                if b < 2:
                    engine.wait_ge(s.s_scored, NB_ - 1)
                copy(engine, fill_w(b), w.kt[:, 0, b * 512:(b + 1) * 512])

            def copy_p(engine, i):
                if i == 1:
                    engine.wait_ge(s.turned, fill_p(1) + 1)
                    bank = m.bank[4 + fill_p(1) % 2]
                    nc.scalar.activation(w.pt[:, 4:6, :].rearrange("p a b -> p (a b)"), bank[:, 0:256], ACT.Copy)
                    nc.scalar.activation(w.pt[0:DS, 6:8, :].rearrange("p a b -> p (a b)"), bank[0:DS, 256:512],
                                         ACT.Copy).then_inc(s.copied_a, 1)
                else:
                    copy(engine, fill_p(i), w.pt[:, 4 * i:4 * i + 4, :].rearrange("p a b -> p (a b)"))

            @block.scalar
            def _(act):
                w.act = act
                chain = Chain(act, s.act_c)
                nc.scalar.activation(w.q[:, :, :], w.q_all[:, bass.ds(hb, 1), :, :].rearrange("p o b q -> p (o b) q"),
                                     ACT.Copy).then_inc(s.q_ready, 1)
                for i in (1, 3, 5, 7):
                    copy_a(act, 0, i)
                for u in range(8):
                    if u < 7:
                        for i in (1, 3, 5, 7):
                            copy_a(act, u + 1, i)
                    act.wait_ge(s.summed, u + 1)
                    if u >= 1:
                        act.wait_ge(s.hidden_done, u)
                    nc.scalar.activation(w.up[:, :, :], m.bank[u % 2][CHID:P, :].rearrange("p (g n) -> p g n", g=NG),
                                         ACT.Copy).then_inc(s.shifted, 1)
                    act.wait_ge(s.added, u + 1)
                    if u >= 1:
                        act.wait_ge(s.projected, u)
                    nc.scalar.activation(w.hid[:, :, 0:255], w.up[:, :, 0:255], ACT.Silu,
                                         bias=m.cmp.pre[:, u % 2:u % 2 + 1]).then_inc(s.hidden_done, 1)
                for i in (1, 3):
                    copy_b(act, 0, i)
                act.wait_ge(s.taken, 7)
                act.wait_ge(s.turned, 64)
                nc.scalar.activation(w.sq[:, :], w.kraw[:, :], ACT.Square).then_inc(s.squared, 1)
                act.wait_ge(s.k_sums, 1)
                chain(nc.scalar.activation(w.kst[:, 16:32], w.kst[:, 0:16], ACT.Ln, scale=1.0 / HD, bias=c("eps")))
                nc.scalar.activation(w.kst[:, 32:48], w.kst[:, 16:32], ACT.Exp, scale=-0.5).then_inc(s.k_rstd, 1)
                copy(act, fill_k(1), w.kcT[:, 512:1024])
                act.wait_ge(s.c_ready, 1)
                nc.scalar.activation(w.pc[:, 0:255], m.bank[6][:, 0:255], ACT.Exp, bias=w.nm[:, 0:1],
                                     accum_out=w.sum[:, 0:1]).then_inc(s.c_exp, 1)
                for k in range(1, NB_):
                    for i in (1, 3):
                        copy_b(act, k, i)
                for b in (1, 3):
                    copy_w(act, b)
                act.wait_ge(s.w_ready, 1)
                nc.scalar.activation(w.sw[:, :], w.sw[:, :], ACT.Exp, bias=w.nm[:, 1:2],
                                     accum_out=w.sum[:, 1:2]).then_inc(s.w_exp, 1)
                act.wait_ge(s.s_ready, 1)
                nc.scalar.activation(w.ss[:, :], w.ss[:, :], ACT.Exp, bias=w.nm[:, 2:3],
                                     accum_out=w.sum[:, 2:3]).then_inc(s.s_exp, 1)
                for i in (1, 3, 5, 7, 9):
                    copy_p(act, i)
                act.wait_ge(s.v_used, 8)
                nc.scalar.activation(w.os[:, :, :].rearrange("p b x -> p (b x)"), m.bank[7][0:32, :],
                                     ACT.Copy).then_inc(s.o_ready, 1)

            @block.vector
            def _(dve):
                chain = Chain(dve, s.dve_c)
                nc.vector.tensor_copy(w.rows[:, :], m.rows[:, bass.ds(hb * 2 * B4, 2 * B4)]).then_inc(s.rows_ready, 1)
                nc.vector.tensor_copy(w.kn[:, 0, :], m.ksTs[:, bass.ds(hb * 16, 16)])
                nc.vector.tensor_copy(w.kn[:, 1, :], m.kwTs[:, bass.ds(hb * 16, 16)]).then_inc(s.kn_ready, 1)
                nc.vector.tensor_copy(w.gt[:, :], w.gate[:, bass.ds(hb, 1), :].rearrange("p o x -> p (o x)"))

                def group(n):
                    chunk_here(dve, n)
                    if n >= 2:
                        dve.wait_ge(s.turned, 4 * (n - 1))
                    nc.vector.tensor_copy(w.xr[:, n % 2, :].rearrange("p (g s d) -> p g s d", g=NG, s=CSTRIDE),
                                          w.ring[:, n % RING, :].rearrange("p (s g d) -> p g s d", g=NG, s=CSTRIDE)
                                          ).then_inc(s.grouped, 1)

                def take(u):
                    dve.wait_ge(s.projected, u + 1)
                    dst = (w.kraw[:, (u // 2) * 256:(u // 2 + 1) * 256] if u % 2 == 0 else
                           w.vc[:, u // 2, :, :].rearrange("p h x -> p (h x)"))
                    nc.vector.tensor_copy(dst, m.bank[2 + u % 2][:, 0:256]).then_inc(s.taken, 1)

                group(0)
                group(1)
                for i in (0, 2, 4, 6):
                    copy_a(dve, 0, i)
                for u in range(8):
                    if u < 7:
                        group(2 * u + 2)
                        for i in (0, 2):
                            copy_a(dve, u + 1, i)
                        group(2 * u + 3)
                        for i in (4, 6):
                            copy_a(dve, u + 1, i)
                    if u:
                        take(u - 1)
                    dve.wait_ge(s.shifted, u + 1)
                    nc.vector.tensor_tensor(w.up[:, :, 0:255], w.up[:, :, 1:256],
                                            m.bank[u % 2][0:CHID, :].rearrange("p (g n) -> p g n", g=NG)[:, :, 0:255],
                                            ALU.add).then_inc(s.added, 1)
                take(7)
                for i in (0, 2):
                    copy_b(dve, 0, i)
                dve.wait_ge(s.squared, 1)
                nc.vector.tensor_reduce(w.kst[:, 0:16], w.sq[:, :].rearrange("p (a d) -> p a d", d=HD), AX.X,
                                        ALU.add).then_inc(s.k_sums, 1)
                dve.wait_ge(s.k_rstd, 1)
                k3 = w.kraw[:, :].rearrange("p (a d) -> p a d", d=HD)
                chain(nc.vector.tensor_tensor(k3, k3, w.kst[:, 32:48].unsqueeze(2).broadcast_to([P, 16, HD]), ALU.mult))
                nc.vector.tensor_tensor(k3, k3, m.kn[:, :].unsqueeze(1).broadcast_to([P, 16, HD]),
                                        ALU.mult).then_inc(s.k_normed, 1)
                copy(dve, fill_k(0), w.kcT[:, 0:512])
                dve.wait_ge(s.c_scored, 1)
                near = m.bank[6][:, 247:255]
                chain(nc.vector.tensor_tensor(near, near, m.srow[:, 15:128:16], ALU.add))
                nc.vector.tensor_reduce(w.nm[:, 0:1], m.bank[6][:, 0:255], AX.X, ALU.max,
                                        negate=True).then_inc(s.c_ready, 1)
                for k in (1,):
                    for i in (0, 2):
                        copy_b(dve, k, i)
                dve.wait_ge(s.c_exp, 1)
                chain(nc.vector.tensor_scalar(w.rs[:, 0:1], w.sum[:, 0:1], 1e-30, None, ALU.max))
                chain(nc.vector.reciprocal(w.rs[:, 0:1], w.rs[:, 0:1]))
                nc.vector.tensor_scalar(w.pc[:, 0:255], w.pc[:, 0:255], w.rs[:, 0:1], None, ALU.mult
                                        ).then_inc(s.c_weights, 1)
                for i in (0, 2):
                    copy_b(dve, 2, i)
                dve.wait_ge(s.imp_done, 1)
                chain(nc.vector.tensor_copy(w.imp[:, 1:256], m.bank[7][:, 0:255]))
                chain(nc.vector.tensor_reduce(w.score[:, 0:64], w.imp[:, 1:257].rearrange("p (j x) -> p j x", x=4),
                                              AX.X, ALU.add))
                chain(nc.vector.tensor_tensor(w.score[:, 0:64], w.score[:, 0:64], w.imp[:, 0:256:4], ALU.add))
                chain(nc.vector.memset(w.score[:, 0:64:63], 1e30))
                chain(nc.vector.max(w.top[:, 0:8], w.score[:, :]))
                chain(nc.vector.match_replace(w.left[:, :], w.top[:, 0:8], w.score[:, :], -1.0))
                chain(nc.vector.max(w.top[:, 8:16], w.left[:, :]))
                chain(nc.vector.match_replace(w.left[:, :], w.top[:, 8:16], w.left[:, :], -1.0))
                nc.vector.tensor_scalar(w.mask[:, :], w.left[:, 0:64], 0.0, NEG, ALU.is_ge, ALU.mult).then_inc(s.masked, 1)
                nc.vector.tensor_scalar(w.pc[:, 0:255], w.pc[:, 0:255], w.gt[:, 0:1], None,
                                        ALU.mult).then_inc(s.p_final, 1)
                dve.wait_ge(s.masked, 1)
                dve.wait_ge(s.p_final, 1)
                for k in (3,):
                    for i in (0, 2):
                        copy_b(dve, k, i)

                def take_scores(h):
                    dve.wait_ge(s.s_scored, 4 * (h + 1))
                    for i in range(4):
                        nc.vector.tensor_tensor(
                            w.ss[:, h * 2048 + i * 512:h * 2048 + (i + 1) * 512].rearrange("p (s j x) -> p s j x", s=4, x=4),
                            m.bank[i][:, :].rearrange("p (s j x) -> p s j x", s=4, x=4),
                            w.mask[:, 32 * h:32 * h + 32].unsqueeze(1).unsqueeze(3).broadcast_to([P, 4, 32, 4]),
                            ALU.add).then_inc(s.s_taken, 1)

                for i in (0, 2):
                    copy_b(dve, 4, i)
                take_scores(0)
                for k in range(5, NB_):
                    for i in (0, 2):
                        copy_b(dve, k, i)
                for b in (0, 2):
                    copy_w(dve, b)
                dve.wait_ge(s.w_scored, 1)
                nc.vector.tensor_copy(w.sw[:, 0:WIN], m.bank[6][:, :]).then_inc(s.w_taken, 1)
                dve.wait_ge(s.n_scored, 1)
                nc.vector.tensor_tensor(w.sw[:, WIN:WIN + DS], m.bank[7][:, 4:8], m.srow[:, P:P + DS], ALU.add)
                nc.vector.tensor_tensor(w.ss[:, PAST:PAST + DS], m.bank[7][:, 0:4], m.srow[:, P:P + DS],
                                        ALU.add).then_inc(s.w_taken, 1)
                dve.wait_ge(s.w_taken, 2)
                old = w.sw[:, 0:WIN].rearrange("p (k n) -> p k n", k=4)
                chain(nc.vector.tensor_tensor(old[:, :, 0], old[:, :, 0], c("win_old"), ALU.add))
                chain(nc.vector.tensor_tensor(old[:, :, 96:128], old[:, :, 96:128],
                                              m.srow[:, 0:P].rearrange("p (n k) -> p k n", k=4), ALU.add))
                nc.vector.tensor_reduce(w.nm[:, 1:2], w.sw[:, :], AX.X, ALU.max, negate=True).then_inc(s.w_ready, 1)
                take_scores(1)
                dve.wait_ge(s.s_taken, 8)
                near = w.ss[:, 2048:4096].rearrange("p (s n) -> p s n", s=16)[:, :, 120:128]
                chain(nc.vector.tensor_tensor(near, near, m.srow[:, 0:P].rearrange("p (n s) -> p s n", s=16), ALU.add))
                nc.vector.tensor_reduce(w.nm[:, 2:3], w.ss[:, :], AX.X, ALU.max, negate=True).then_inc(s.s_ready, 1)
                for k, (buf, done) in enumerate(((w.sw, s.w_exp), (w.ss, s.s_exp))):
                    a = slice(k + 1, k + 2)
                    dve.wait_ge(done, 1)
                    chain(nc.vector.tensor_scalar(w.rs[:, a], w.sum[:, a], 1e-30, None, ALU.max))
                    chain(nc.vector.reciprocal(w.rs[:, a], w.rs[:, a]))
                    gate = w.gt[:, 2:3] if k == 0 else w.gt[:, 1:2]
                    nc.vector.tensor_scalar(buf[:, :], buf[:, :], w.rs[:, a], gate, ALU.mult,
                                            ALU.mult).then_inc(s.p_final, 1)
                for i in (0, 2, 4, 6, 8):
                    copy_p(dve, i)


def stage_sample_attention(nc, io, m):
    sb = Region(nc, m.sample_end, m.work_end)
    w = Buffers()
    w.ring = sb("cache_ring", [P, RING, CW])
    both = sb("rows_T_or_weights_T", [P, 2 * 8 * NG * 256])
    w.xt = both[:, :].rearrange("p (u q g n) -> p u q g n", u=2, q=8, g=NG)
    w.pt = both[:, 0:40 * P].rearrange("p (k n) -> p k n", k=40)
    both = sb("rows_grouped_or_scores", [P, PAST + DS])
    w.xr = both[:, 0:2 * CW].rearrange("p (k x) -> p k x", k=2)
    w.sq = both[:, 0:1024]
    w.ss = both[:, :]
    w.kt = sb("keys_T", [P, 2, CW])
    w.wk = sb("win_k", [P, B4, 4 * DKV])
    w.wv = sb("win_v", [P, B4, 4 * DKV])
    w.vn = sb("new_v", [DS, B4, 2, DKV])
    w.kn = sb("new_k", [P, 2, 16])
    w.up = sb("second_half_s", [CHID, NG, 256])
    w.hid = sb("hidden_s", [CHID, NG, 256])
    w.kraw = sb("kc_s", [P, 1024])
    w.kcT = sb("kcT_s", [P, 1024])
    w.vc = sb("vc_s", [P, B4, 2, DKV])
    w.kst = sb("kc_stats_s", [P, 48])
    w.pc = sb("p_cmp_s", [P, 256])
    w.imp = sb("importance", [P, 257])
    w.score = sb("score", [P, SCORES])
    w.left = sb("not_selected", [P, SCORES])
    w.top = sb("top", [P, 16])
    w.mask = sb("block_mask", [P, 64])
    w.sw = sb("p_win_s", [P, WIN + DS])
    w.os = sb("out_s", [32, B4, P])
    w.q_all = sb("q_padded_all", [P, 2, B4, P])
    w.q = sb("q_padded_s", [P, B4, P])
    w.gate = m.gate_rows
    w.gt = sb("gate_rows_now", [P, 3])
    w.rows = sb("rows_now", [P, 2 * B4], U32)
    w.nm = sb("neg_max_s", [P, 3])
    w.sum = sb("row_sums_s", [P, 3])
    w.rs = sb("row_scale_s", [P, 3])
    prepare_sample_attention(nc, io, m, w)
    with ExitStack() as ctx:
        w.landed = [ctx.enter_context(nc.semaphore(f"ring_landed_{i}")) for i in range(RING)]
        with nc.Fori(0, 2) as hb:
            sample_attention_turn(nc, io, m, w, hb)



def stage_finish_mixer(nc, io, m):
    c = m.c
    low = Region(nc, m.base_end, m.mix_start)
    m.u2 = low("u_parts", [P, 2, KT, TOK], F32R)
    m.gT_start = low.at
    raw = nc.alloc_sbuf_tensor_at("w_out_raw", [P, KT, DM], F32, offset=m.base_end)
    wo = low("w_out", [P, 2, KT, DM], F32R)
    mT = low("mixT", [P, 2, 2, KT, P], F32R)
    x = low("x_again", [P, 3, DM])
    ut = low("u_whole", [P, KT, P])
    ss = nc.alloc_sbuf_tensor_at("ss2", [P, 4], F32, offset=low.at)
    xp = io.x_prompt.rearrange("o (n p) c -> p (o n) c", p=P)
    hp = io.h_dram[0:SEQ, :].rearrange("(n p) c -> p n c", p=P)
    n = NT + 1
    rows = [P] * NT + [NS]
    four = lambda bank, r: bank[:, :].rearrange("p (k q) -> p k q", k=4)[:, :, 0:r]
    with stage(nc, "o_loaded x_loaded*3 w_loaded*8 w_hi w_split turned mT_hi mT_ready mixed h_ready h_stored h_normed "
                   "h_turned u_whole u_hi u_taken h_rstd act_c") as s:
        with nc.Block() as block:
            @block.sync
            def _(sp):
                def store(j):
                    sp.wait_ge(s.h_ready, 2 * j + 2)
                    sp.dma_start(hp[:, j, :] if j < NT else io.h_dram[SEQ:TOK, :], m.mix[0:rows[j], j, :]
                                 ).then_inc(s.h_stored, 16)

                for j in range(n):
                    if j >= 3:
                        sp.wait_ge(s.h_turned, 2 * (j - 2))
                    sp.dma_start(x[0:rows[j], j % 3, :], xp[:, j, :] if j < NT else
                                 io.x_sample.rearrange("b t c -> (b t) c")).then_inc(s.x_loaded[j % 3], 16)
                    if j == 0:
                        for k in range(KT):
                            sp.dma_start(raw[:, k, :], io.w_out[0, k * P:(k + 1) * P, :]).then_inc(s.w_loaded[k], 16)
                        sp.dma_start(m.mix[0:NS, NT, 0:DATT], io.o_dram).then_inc(s.o_loaded, 16)
                    if j >= 3:
                        store(j - 3)
                for j in range(n - 3, n):
                    store(j)
                sp.wait_ge(s.h_stored, 16 * n)

            @block.scalar
            def _(act):
                chain = Chain(act, s.act_c)

                def mix_hi(j):
                    for h in range(2):
                        act.wait_ge(s.turned, 2 * j + h + 1)
                        if j >= 2:
                            act.wait_ge(s.mixed, 2 * (j - 1))
                        nc.scalar.activation(mT[:, j % 2, HI, 4 * h:4 * h + 4, 0:rows[j]], four(m.bank[6 + h], rows[j]),
                                             ACT.Copy).then_inc(s.mT_hi, 1)

                def statistics(j):
                    r = rows[j]
                    act.wait_ge(s.h_ready, 2 * j + 2)
                    chain(nc.scalar.activation(x[0:r, j % 3, :], m.mix[0:r, j, :], ACT.Square, accum_out=ss[0:r, 0:1]))
                    chain(nc.scalar.activation(ss[0:r, 1:2], ss[0:r, 0:1], ACT.Ln, scale=1.0 / DM, bias=c("eps")[0:r, :]))
                    nc.scalar.activation(ss[0:r, 2 + j % 2:3 + j % 2], ss[0:r, 1:2], ACT.Exp,
                                         scale=-0.5).then_inc(s.h_rstd, 1)

                mix_hi(0)
                for k in range(KT):
                    act.wait_ge(s.w_loaded[k], 16)
                    nc.scalar.activation(wo[:, HI, k, :], raw[:, k, :], ACT.Copy).then_inc(s.w_hi, 1)
                for j in range(n + 1):
                    if j + 1 < n:
                        mix_hi(j + 1)
                    if j >= 1:
                        i = j - 1
                        statistics(i)
                        for h in range(2):
                            act.wait_ge(s.u_whole, 2 * i + h + 1)
                            nc.scalar.activation(m.u2[:, HI, 4 * h:4 * h + 4, i * P:i * P + rows[i]],
                                                 ut[:, 4 * h:4 * h + 4, 0:rows[i]], ACT.Copy).then_inc(s.u_hi, 1)

            @block.tensor
            def _(pe):
                def turn(src, r, banks, sem):
                    for k in range(KT):
                        i = nc.tensor.transpose(m.bank[banks[k // 4]][:, (k % 4) * P:(k % 4) * P + r],
                                                src[:, k * P:(k + 1) * P], c("ident")[0:r, 0:r])
                        if k % 4 == 3:
                            i.then_inc(sem, 1)

                def turn_mix(j):
                    if j == NT:
                        pe.wait_ge(s.o_loaded, 16)
                    if j >= 1:
                        pe.wait_ge(s.mT_ready, 2 * j)
                    turn(m.mix[0:rows[j], j, :], rows[j], (6, 7), s.turned)

                def turn_h(j):
                    pe.wait_ge(s.h_normed, j + 1)
                    if j >= 1:
                        pe.wait_ge(s.u_whole, 2 * j)
                    turn(x[0:rows[j], j % 3, :], rows[j], (4, 5), s.h_turned)

                turn_mix(0)
                for j in range(n):
                    r = rows[j]
                    if j + 1 < n:
                        turn_mix(j + 1)
                    pe.wait_ge(s.mT_ready, 2 * j + 2)
                    if j >= 2:
                        pe.wait_ge(s.h_ready, 2 * (j - 1))
                    for h in range(2):
                        for k in range(KT):
                            if j == 0 and h == 0:
                                pe.wait_ge(s.w_split, k + 1)
                            for a, b in TERMS:
                                mm = nc.tensor.matmul(m.bank[2 * (j % 2) + h][0:r, :], mT[:, j % 2, a, k, 0:r],
                                                      wo[:, b, k, h * 512:(h + 1) * 512],
                                                      start=(k == 0 and (a, b) == TERMS[0]),
                                                      stop=(k == KT - 1 and (a, b) == TERMS[-1]))
                        mm.then_inc(s.mixed, 1)
                    if j >= 1:
                        turn_h(j - 1)
                turn_h(n - 1)

            @block.vector
            def _(dve):
                def mix_lo(j):
                    for h in range(2):
                        dve.wait_ge(s.mT_hi, 2 * j + h + 1)
                        nc.vector.tensor_tensor(mT[:, j % 2, LO, 4 * h:4 * h + 4, 0:rows[j]], four(m.bank[6 + h], rows[j]),
                                                mT[:, j % 2, HI, 4 * h:4 * h + 4, 0:rows[j]].bitcast(F32),
                                                ALU.subtract).then_inc(s.mT_ready, 1)

                mix_lo(0)
                for k in range(KT):
                    dve.wait_ge(s.w_hi, k + 1)
                    nc.vector.tensor_tensor(wo[:, LO, k, :], raw[:, k, :], wo[:, HI, k, :].bitcast(F32),
                                            ALU.subtract).then_inc(s.w_split, 1)
                for j in range(n + 1):
                    if j + 1 < n:
                        mix_lo(j + 1)
                    if j >= 1:
                        i = j - 1
                        r = rows[i]
                        dve.wait_ge(s.x_loaded[i % 3], 16 * (i // 3 + 1))
                        for h in range(2):
                            dve.wait_ge(s.mixed, 2 * i + h + 1)
                            part = m.mix[0:r, i, h * 512:(h + 1) * 512]
                            nc.vector.tensor_tensor(part, m.bank[2 * (i % 2) + h][0:r, :],
                                                    x[0:r, i % 3, h * 512:(h + 1) * 512], ALU.add).then_inc(s.h_ready, 1)
                        dve.wait_ge(s.h_rstd, i + 1)
                        nc.vector.tensor_scalar(x[0:r, i % 3, :], m.mix[0:r, i, :], ss[0:r, 2 + i % 2:3 + i % 2], None,
                                                ALU.mult).then_inc(s.h_normed, 1)
                        for h in range(2):
                            dve.wait_ge(s.h_turned, 2 * i + h + 1)
                            if i >= 1:
                                dve.wait_ge(s.u_taken, 2 * (i - 1) + h + 1)
                            nc.vector.tensor_tensor(ut[:, 4 * h:4 * h + 4, 0:r], four(m.bank[4 + h], r),
                                                    m.gffn[:, 4 * h:4 * h + 4].unsqueeze(2).broadcast_to([P, 4, r]),
                                                    ALU.mult).then_inc(s.u_whole, 1)
                        for h in range(2):
                            dve.wait_ge(s.u_hi, 2 * i + h + 1)
                            nc.vector.tensor_tensor(m.u2[:, LO, 4 * h:4 * h + 4, i * P:i * P + r],
                                                    ut[:, 4 * h:4 * h + 4, 0:r],
                                                    m.u2[:, HI, 4 * h:4 * h + 4, i * P:i * P + r].bitcast(F32),
                                                    ALU.subtract).then_inc(s.u_taken, 1)


FT = DFF // P
PIECE = TOK // 3


def stage_ffn_up(nc, io, m):
    U = 2
    UNITS = [(f, side) for f in range(U) for side in range(2)]
    sb = Region(nc, m.gT_start, m.end)
    m.gT = sb("gT", [P, FT, TOK])
    m.after_gT = sb.at
    raw = sb("w_raw", [P, 2, KT, P])
    wp = sb("w_parts", [P, len(UNITS), 2, KT, P], F32R)
    e = sb("silu_gate", [P, 2, PIECE])
    sides = [io.w_gate.rearrange("o (c p) (f q) -> p (o c) f q", p=P, q=P),
             io.w_up.rearrange("o (c p) (f q) -> p (o c) f q", p=P, q=P)]
    last = FT // U - 1

    with stage(nc, "landed*2 w_hi w_split multiplied silu_done piece_done") as s:
        with nc.Block() as block:
            @block.sync
            def _(sp):
                def load(t, i):
                    f, side = UNITS[i]
                    sp.dma_start(raw[:, side, :, :],
                                 sides[side][:, :, bass.ds(t * U + f, 1), :].rearrange("p c o q -> p (c o) q")
                                 ).then_inc(s.landed[side], 16)

                for i in range(4):
                    if i >= 2:
                        sp.wait_ge(s.w_split, i - 1)
                    load(0, i)
                with sp.Fori(0, last) as t:
                    for i in range(4):
                        sp.wait_ge(s.w_split, t * 4 + 3 + i)
                        load(t + 1, i)

            @block.scalar
            def _(act):
                def hi(t, i):
                    f, side = UNITS[i]
                    act.wait_ge(s.landed[side], t * (16 * U) + 16 * (f + 1))
                    nc.scalar.activation(wp[:, i, HI, :, :], raw[:, side, :, :], ACT.Copy).then_inc(s.w_hi, 1)

                def turn(t, more):
                    for f in range(U):
                        for q in range(3):
                            act.wait_ge(s.multiplied, t * 12 + 6 * f + q + 1)
                            act.wait_ge(s.piece_done, t * 6 + 3 * f + q + 2)
                            nc.scalar.activation(e[:, (3 * f + q) % 2, :], m.bank[q][:, 0:PIECE], ACT.Silu).then_inc(s.silu_done, 1)
                        if more:
                            for i in (2 * f, 2 * f + 1):
                                act.wait_ge(s.multiplied, t * 12 + 3 * i + 3)
                                hi(t + 1, i)

                for i in range(4):
                    hi(0, i)
                with act.Fori(0, last) as t:
                    turn(t, True)
                turn(last, False)

            @block.tensor
            def _(pe):
                def turn(t):
                    for i, (f, side) in enumerate(UNITS):
                        pe.wait_ge(s.w_split, t * 4 + i + 1)
                        for q in range(3):
                            pe.wait_ge(s.piece_done, t * 6 + 3 * f + q + 1)
                            for k in range(KT):
                                for a, b in TERMS:
                                    mm = nc.tensor.matmul(m.bank[3 * side + q][:, 0:PIECE], wp[:, i, a, k, :],
                                                          m.u2[:, b, k, q * PIECE:(q + 1) * PIECE],
                                                          start=(k == 0 and (a, b) == TERMS[0]),
                                                          stop=(k == KT - 1 and (a, b) == TERMS[-1]))
                            mm.then_inc(s.multiplied, 1)

                with pe.Fori(0, last) as t:
                    turn(t)
                turn(last)

            @block.vector
            def _(dve):
                def lo(t, i):
                    dve.wait_ge(s.w_hi, t * 4 + i + 1)
                    nc.vector.tensor_tensor(wp[:, i, LO, :, :], raw[:, UNITS[i][1], :, :],
                                            wp[:, i, HI, :, :].bitcast(F32), ALU.subtract).then_inc(s.w_split, 1)

                def turn(t, more):
                    for f in range(U):
                        for q in range(3):
                            dve.wait_ge(s.silu_done, t * 6 + 3 * f + q + 1)
                            dve.wait_ge(s.multiplied, t * 12 + 6 * f + 3 + q + 1)
                            nc.vector.tensor_tensor(
                                m.gT[:, bass.ds(t * U + f, 1), q * PIECE:(q + 1) * PIECE].rearrange("p o t -> p (o t)"),
                                e[:, (3 * f + q) % 2, :], m.bank[3 + q][:, 0:PIECE], ALU.mult).then_inc(s.piece_done, 1)
                        if more:
                            lo(t + 1, 2 * f)
                            lo(t + 1, 2 * f + 1)

                nc.vector.memset(e[:, :, 0:1], 0.0).then_inc(s.piece_done, 3)
                for i in range(4):
                    lo(0, i)
                with dve.Fori(0, last) as t:
                    turn(t, True)
                turn(last, False)


def stage_ffn_down(nc, io, m):
    NC, GR, RG, RW = 512, 2, 4, 4
    NGR = FT // GR
    IN_B = 19
    a, b = Region(nc, m.base_end, m.gT_start), Region(nc, m.after_gT, m.end)
    whi = a("w_down_hi", [P, FT, NC], F32R)
    wlo_a = a("w_down_lo_a", [P, FT - IN_B, NC], F32R)
    gp = a("g_parts", [P, RG, 2, GR, P], F32R)
    raw = a("w_down_raw", [P, RW, NC])
    wlo_b = b("w_down_lo_b", [P, IN_B, NC], F32R)
    y = b("y_tile", [P, 2, NC])
    part_of = lambda part, f: (whi[:, f, :] if part == HI else wlo_b[:, f, :] if f < IN_B
                               else wlo_a[:, f - IN_B, :])
    wd = io.w_down.rearrange("o (f p) n -> p (o f) n", p=P)
    yp = io.y_prompt.rearrange("o (n p) c -> p (o n) c", p=P)
    hp = io.h_dram[0:SEQ, :].rearrange("(n p) c -> p n c", p=P)
    ysm = io.y_sample.rearrange("b t c -> (b t) c")
    HALVES, PER_HALF = DM // NC, NT + 1

    def tile(at, t):
        half, j = at // PER_HALF, at % PER_HALF + 2 * t
        sample = at % PER_HALF == NT
        rows = NS if sample else P
        cols = slice(half * NC, (half + 1) * NC)
        return named(at=at, t=t, n=at + 2 * t, slot=at % 2, uses=at // 2 + t, half=half, rows=rows,
                     opens=at % PER_HALF == 0,
                     h=io.h_dram[SEQ:TOK, cols] if sample else hp[:, bass.ds(j, 1), cols],
                     y=ysm[:, cols] if sample else yp[:, bass.ds(j, 1), cols],
                     tokens=slice(SEQ, TOK) if sample else bass.ds(j * P, P))

    def over_tiles(engine, body):
        for half in range(HALVES):
            start = half * PER_HALF
            body(tile(start, 0))
            body(tile(start + 1, 0))
            with engine.Fori(0, (NT - 2) // 2) as t:
                body(tile(start + 2, t))
                body(tile(start + 3, t))
            body(tile(start + NT, 0))

    with stage(nc, "landed*4 w_hi w_split g_hi g_split used h_loaded*2 y_ready stored*2") as s:
        def group_free(engine, x, g):
            if g >= RG:
                engine.wait_ge(s.used, x.n * NGR + g - RG + 1)
            elif x.at > 0:
                before = max(k for k in range(NGR) if k % RG == g)
                engine.wait_ge(s.used, (x.n - 1) * NGR + before + 1)

        with nc.Block() as block:
            @block.sync
            def _(sp):
                def store(x):
                    sp.wait_ge(s.y_ready, x.n + 1)
                    sp.dma_start(x.y, y[0:x.rows, x.slot, :]).then_inc(s.stored[x.slot], 16)

                def body(x):
                    if x.at >= 2:
                        sp.wait_ge(s.stored[x.slot], x.uses * 16)
                    sp.dma_start(y[0:x.rows, x.slot, :], x.h).then_inc(s.h_loaded[x.slot], 16)
                    if x.opens:
                        for f in range(FT):
                            i = x.half * FT + f
                            if i >= RW:
                                sp.wait_ge(s.w_split, i - RW + 1)
                            sp.dma_start(raw[:, i % RW, :], wd[:, f, x.half * NC:(x.half + 1) * NC]
                                         ).then_inc(s.landed[i % RW], 16)
                    if x.at >= 1:
                        store(tile(x.at - 1, x.t))

                over_tiles(sp, body)
                last = HALVES * PER_HALF - 1
                store(tile(last, 0))
                for k in range(2):
                    sp.wait_ge(s.stored[k], 16 * (HALVES * PER_HALF // 2))

            @block.scalar
            def _(act):
                def body(x):
                    for g in range(NGR):
                        if x.opens:
                            if x.half > 0:
                                act.wait_ge(s.used, (x.at - 1) * NGR + g + 1)
                            for f in range(g * GR, (g + 1) * GR):
                                i = x.half * FT + f
                                act.wait_ge(s.landed[i % RW], 16 * (i // RW + 1))
                                nc.scalar.activation(part_of(HI, f), raw[:, i % RW, :], ACT.Copy).then_inc(s.w_hi, 1)
                        group_free(act, x, g)
                        nc.scalar.activation(gp[:, g % RG, HI, :, 0:x.rows], m.gT[:, g * GR:(g + 1) * GR, x.tokens],
                                             ACT.Copy).then_inc(s.g_hi, 1)

                over_tiles(act, body)

            @block.tensor
            def _(pe):
                def body(x):
                    if x.at >= 2:
                        pe.wait_ge(s.y_ready, x.n - 1)
                    for g in range(NGR):
                        if x.opens:
                            pe.wait_ge(s.w_split, x.half * FT + (g + 1) * GR)
                        pe.wait_ge(s.g_split, x.n * NGR + g + 1)
                        for k in range(GR):
                            f = g * GR + k
                            for pa, pb in TERMS:
                                mm = nc.tensor.matmul(m.bank[x.slot][0:x.rows, :], gp[:, g % RG, pa, k, 0:x.rows],
                                                      part_of(pb, f), start=(f == 0 and (pa, pb) == TERMS[0]),
                                                      stop=(f == FT - 1 and (pa, pb) == TERMS[-1]))
                        mm.then_inc(s.used, 1)

                over_tiles(pe, body)

            @block.vector
            def _(dve):
                def take(x):
                    dve.wait_ge(s.used, (x.n + 1) * NGR)
                    dve.wait_ge(s.h_loaded[x.slot], x.uses * 16 + 16)
                    nc.vector.tensor_tensor(y[0:x.rows, x.slot, :], m.bank[x.slot][0:x.rows, :],
                                            y[0:x.rows, x.slot, :], ALU.add).then_inc(s.y_ready, 1)

                def body(x):
                    for g in range(NGR):
                        if x.opens:
                            for f in range(g * GR, (g + 1) * GR):
                                i = x.half * FT + f
                                dve.wait_ge(s.w_hi, i + 1)
                                nc.vector.tensor_tensor(part_of(LO, f), raw[:, i % RW, :], part_of(HI, f).bitcast(F32),
                                                        ALU.subtract).then_inc(s.w_split, 1)
                        dve.wait_ge(s.g_hi, x.n * NGR + g + 1)
                        nc.vector.tensor_tensor(gp[:, g % RG, LO, :, 0:x.rows], m.gT[:, g * GR:(g + 1) * GR, x.tokens],
                                                gp[:, g % RG, HI, :, 0:x.rows].bitcast(F32),
                                                ALU.subtract).then_inc(s.g_split, 1)
                        if g == RG - 1 and x.at >= 1:
                            take(tile(x.at - 1, x.t))

                over_tiles(dve, body)
                take(tile(HALVES * PER_HALF - 1, 0))


class Region:

    def __init__(self, nc, start, end):
        self.nc, self.at, self.end = nc, start, end

    def __call__(self, name, shape, dtype=F32):
        size = int(np.prod(shape[1:])) * (2 if dtype == mybir.dt.bfloat16 else 4)
        t = self.nc.alloc_sbuf_tensor_at(name, list(shape), dtype, offset=self.at)
        self.at += -(-size // 32) * 32
        assert self.at <= self.end, (name, self.at, self.end)
        return t


class Memory:

    def __init__(self, nc):
        self.psum = nc.alloc_psum_tensor("banks", [P, 8 * 512], F32)
        self.bank = [self.psum[:, i * 512:(i + 1) * 512] for i in range(8)]
        start, end = -(-nc.sbuf_base // 32) * 32, nc.sbuf_usable_end // 32 * 32
        sb = Region(nc, start, end)
        self.consts = sb("consts", list(CONSTS.shape))
        self.gmix = sb("gmix", [P, KT])
        self.gffn = sb("gffn", [P, KT])
        self.qn = sb("qn", [P, HD])
        self.kn = sb("kn", [P, HD])
        self.convw = sb("convw", [P, 4, 6])
        self.convb = sb("convb", [P, 6])
        self.dtb = sb("dtb", [P, 8])
        self.alog = sb("alog", [P, 8])
        self.dskip = sb("dskip", [P, 8])
        self.ssdn = sb("ssdn", [P, DSSD])
        self.rows = sb("rows", [P, 2 * DB], U32)
        self.srow = sb("srow", [P, 132])
        self.gates = sb("gates", [P, NT + 1, 3 * NH])
        self.gate_rows = sb("gate_rows", [P, 2, 3])
        self.rstd = sb("rstd", [P, NT + 1])
        self.bias_dram = nc.dram_tensor("bias_by_distance", (NH, P, BIASW), F32, kind="Internal").ap()
        self.base_end = sb.at
        self.qTs = sb("qTs", [P, REP, NS])
        self.ksTs = sb("ksTs", [P, NS])
        self.kwTs = sb("kwTs", [P, NS])
        self.dt_start = sb.at
        sb("dt_place", [P, NT + 1, 16])
        self.sample_end = sb.at
        self.pz = sb("pz", [P, NT + 1, PZ])
        self.pz_end = sb.at
        self.qT_start = sb.at
        self.qT = sb("qT", [P, NT, REP, P])
        self.ksT = sb("ksT", [P, SEQ])
        self.kwT = sb("kwT", [P, SEQ])
        self.v = sb("v", [P, NT + 1, 2, DKV])
        self.att_end = sb.at
        self.end = end
        self.mix_start = end - (NT + 1) * DM * 4
        self.work_end = self.mix_start - 8960
        self.mix = nc.alloc_sbuf_tensor_at("mix", [P, NT + 1, DM], F32, offset=self.mix_start)

    def c(self, name):
        a, b = CONST_COLS[name]
        return self.consts[:, a:b]


def stage_setup(nc, io, m):
    sb = Region(nc, m.sample_end, m.end)
    m.relx = sb("relx", [NBUCK + 1, NH])
    m.onehot = sb("onehot", [NBUCK + 1, BIASW])
    m.biasrow = sb("biasrow", [NH, BIASW])
    m.pages = sb("pages", [16, 2 * DB], I32)
    m.pagef = sb("pagef", [16, 2 * DB])
    m.rowf = sb("rowf", [P, 2 * DB])

    load_setup(nc, io, m)


def stage_project_heads(nc, io, m):
    stage_project(nc, io, m, heads=True)


def stage_project_ssd(nc, io, m):
    stage_project(nc, io, m, heads=False)


def program(nc, io):
    m = Memory(nc)
    with nc.semaphore("cmp_loaded") as m.cmp_loaded:
        for f in STAGES:
            f(nc, io, m)


STAGES = [stage_setup, stage_project_heads, stage_project_ssd, stage_pointwise, stage_prompt_compress,
          stage_prompt_attention, stage_conv, stage_ssd, stage_sample_attention,
          stage_finish_mixer, stage_ffn_up, stage_ffn_down]


_INS = ['x_prompt', 'x_sample', 'cache_k_cmp', 'cache_v_cmp', 'cache_k_sel', 'cache_v_sel', 'cache_k_win', 'cache_v_win',
        'state_conv', 'state_ssm', 'page_table', 'norm_mix', 'w_in', 'q_norm', 'k_norm', 'cmp_pe', 'cmp_w1', 'cmp_w2',
        'rel_bias', 'conv_w', 'conv_b', 'dt_bias', 'a_log', 'd_skip', 'ssd_norm', 'w_out', 'norm_ffn', 'w_gate', 'w_up',
        'w_down']
_OUTS = [('y_prompt', (1, SEQ, DM)), ('y_sample', (DB, DS, DM))] + \
    [(f'p_{n}', (1, 1, SEQ, NG, HD)) for n in ('k_cmp', 'v_cmp', 'k_sel', 'v_sel')] + \
    [(f'p_{n}', (1, 1, WIN, NG, HD)) for n in ('k_win', 'v_win')] + \
    [('p_conv', (1, 1, 3, DCONV)), ('p_ssm', (1, 1, 8, HD, HD))] + \
    [(f's_{n}', (1, DB, DS, NG, HD)) for n in ('k_cmp', 'v_cmp', 'k_sel', 'v_sel')] + \
    [(f's_{n}', (1, DB, WIN, NG, HD)) for n in ('k_win', 'v_win')] + \
    [('s_conv', (1, DB, 3, DCONV)), ('s_ssm', (1, DB, 8, HD, HD))]

_SCRATCH = [("kw_new", (NS, DKV)), ("vw_new", (NS, DKV)), ("h_dram", (TOK, DM)), ("gate_dram", (NS, 3 * NH)),
            ("o_dram", (NS, DATT))]


def kernel(**inputs):
    import numpy as _np
    import concourse.bacc as _bacc
    from concourse.bass_utils import run_bass_kernel_spmd as _run

    nc = _bacc.Bacc("TRN2", target_bir_lowering=False, num_devices=1)
    aps, arrays = {}, {}
    given = {name: inputs[name] for name in _INS}
    given["consts"], given["buckets"] = CONSTS, BUCKETS
    for name, a in given.items():
        a = _np.ascontiguousarray(a)
        arrays[f"in_{name}"] = a
        aps[name] = nc.dram_tensor(f"in_{name}", a.shape, mybir.dt.from_np(a.dtype), kind="ExternalInput").ap()
    for name, shape in _OUTS:
        aps[name] = nc.dram_tensor(f"out_{name}", shape, F32, kind="ExternalOutput").ap()
    for name, shape in _SCRATCH:
        aps[name] = nc.dram_tensor(name, shape, F32, kind="Internal").ap()
    program(nc, named(**aps))
    r = _run(nc, [arrays], core_ids=[0])
    return tuple(r.results[0][f"out_{name}"] for name, _ in _OUTS)
```
